# Optimizing a Trainium2 kernel written in Bass

```python
import math
import jax, jax.numpy as jnp
from jax import lax
import numpy as np

D_MODEL = 1024
BATCH = 1
SEQ = 1024
DEPTH = 1
DEC_BATCH = 8
DEC_SEQ = 4
PAST_LEN = 4096
PAGE_SIZE = 128

EPS = 1e-6
M_HEADS = 4
M_HD = 128
M_DIM = M_HEADS * M_HD
M_CONV = 4
M_CHUNK = 64
N_HEADS = 8
N_KV = 2
N_HPG = N_HEADS // N_KV
N_HD = 64
N_DIM = N_HEADS * N_HD
CMP_BLK = 32
SEL_BLK = 64
TOPK = 16
WINDOW = 512
SEL_QBLK = 64
WIN_QBLK = 128
FORCE_SCORE = 1e4
NB = 32
MAX_DIST = 1024
MEM_LEN = 256
X_HEADS = 4
X_HD = D_MODEL // X_HEADS
D_FF = 2816
F_CONV = 3
IN_SIZES = (M_DIM, M_DIM, M_HEADS, M_HEADS, M_DIM, N_DIM, 2 * N_KV * N_HD, 2 * N_KV * N_HD, 2 * N_KV * N_HD, 3 * N_HEADS, D_MODEL, D_MODEL)
IN_DIM = 3 * M_DIM + 2 * M_HEADS + N_DIM + 6 * N_KV * N_HD + 3 * N_HEADS + 2 * D_MODEL

kernel_name = 'hybrid_mlstm_nsa_decoder_step'

def rmsnorm(x, g):
    xf = x.astype(jnp.float32)
    y = xf * lax.rsqrt(jnp.mean(xf * xf, axis=-1, keepdims=True) + EPS)
    return (y * g.astype(jnp.float32)).astype(x.dtype)

def causal_dwconv(x, buf, w, b):
    width = w.shape[0]
    t = x.shape[1]
    xx = jnp.concatenate([buf.astype(x.dtype), x], axis=1)
    y = b + sum(w[k] * xx[:, k:k + t] for k in range(width))
    return y, xx[:, xx.shape[1] - (width - 1):]

def t5_bucket(dist):
    d = jnp.maximum(dist, 0)
    exact = NB // 2
    large = exact + (jnp.log(jnp.maximum(d, 1).astype(jnp.float32) / exact) / math.log(MAX_DIST / exact) * (NB - exact)).astype(jnp.int32)
    large = jnp.minimum(large, NB - 1)
    return jnp.where(d < exact, d, large)

def masked_softmax(s, mask):
    p = jax.nn.softmax(jnp.where(mask, s, -1e30), axis=-1)
    return jnp.where(mask, p, 0.0)

def split_in(z):
    outs = []
    start = 0
    for s in IN_SIZES:
        outs.append(z[..., start:start + s])
        start += s
    return outs

def mlstm_chunked(q, k, v, ig, lf, C0, n0, m0):
    B, T, H, D = q.shape
    L = math.gcd(T, M_CHUNK)
    nc = T // L

    def to_chunks(a):
        a = a.reshape((B, nc, L, H) + a.shape[3:])
        return jnp.moveaxis(jnp.moveaxis(a, 1, 0), 3, 2)

    causal = jnp.tril(jnp.ones((L, L), bool))

    def step(carry, inp):
        C, n, m = carry
        qc, kc, vc, ic, fc = inp
        b = jnp.cumsum(fc, axis=-1)
        logD = jnp.where(causal, b[..., :, None] - b[..., None, :] + ic[..., None, :], -jnp.inf)
        m_inter = b + m[..., None]
        mt = jnp.maximum(m_inter, jnp.max(logD, axis=-1))
        Dm = jnp.exp(logD - mt[..., None])
        sc = jnp.exp(m_inter - mt)
        s = jnp.einsum('bhtd,bhsd->bhts', qc, kc) * Dm
        num = sc[..., None] * jnp.einsum('bhvk,bhtk->bhtv', C, qc) + jnp.einsum('bhts,bhsv->bhtv', s, vc)
        den = sc * jnp.einsum('bhk,bhtk->bht', n, qc) + jnp.sum(s, axis=-1)
        h = num / jnp.maximum(jnp.abs(den), jnp.exp(-mt))[..., None]
        wl = Dm[..., -1, :]
        C = sc[..., -1, None, None] * C + jnp.einsum('bhs,bhsv,bhsk->bhvk', wl, vc, kc)
        n = sc[..., -1, None] * n + jnp.einsum('bhs,bhsk->bhk', wl, kc)
        return (C, n, mt[..., -1]), h

    (C, n, m), h = lax.scan(step, (C0, n0, m0), (to_chunks(q), to_chunks(k), to_chunks(v), to_chunks(ig), to_chunks(lf)))
    h = jnp.transpose(h, (1, 0, 3, 2, 4)).reshape(B, T, H, D)
    return h, C, n, m

def mlstm_mixer(xm, v, ig, fg, og, conv_buf, C0, n0, m0, p):
    B, T, _ = xm.shape
    f32 = jnp.float32
    xc, conv_new = causal_dwconv(xm, conv_buf, p['m_conv_w'], p['m_conv_b'])
    xc = jax.nn.silu(xc).reshape(B, T, M_HEADS, M_HD)
    q = jnp.einsum('bthd,hde->bthe', xc, p['m_wq']).astype(f32)
    k = jnp.einsum('bthd,hde->bthe', xc, p['m_wk']).astype(f32) * (M_HD ** -0.5)
    vh = v.reshape(B, T, M_HEADS, M_HD).astype(f32)
    i_pre = (ig + p['m_gate_b'][0]).astype(f32)
    log_f = jax.nn.log_sigmoid((fg + p['m_gate_b'][1]).astype(f32))
    h, C, n, m = mlstm_chunked(q, k, vh, i_pre, log_f, C0.astype(f32), n0.astype(f32), m0.astype(f32))
    h = h * lax.rsqrt(jnp.mean(h * h, axis=-1, keepdims=True) + EPS) * p['m_norm'].astype(f32)
    h = jax.nn.sigmoid(og.astype(f32)) * h.reshape(B, T, M_DIM)
    return h.astype(xm.dtype), C, n, m, conv_new

def nsa_compress(kb, w1, w2, pe):
    B, T, G, D = kb.shape
    nc = T // CMP_BLK
    blk = kb.reshape(B, nc, CMP_BLK, G, D) + pe[None, None, :, None, :]
    flat = jnp.moveaxis(blk, 3, 2).reshape(B, nc, G, CMP_BLK * D)
    return jax.nn.gelu(flat @ w1) @ w2

def nsa_cmp_sel(q, qpos, kc, vc, ks, vs, rel_table, p):
    B, Tq, H, D = q.shape
    Tk = kc.shape[1]
    pad = (-Tk) % SEL_BLK
    padk = lambda a: jnp.pad(a, ((0, 0), (0, pad), (0, 0), (0, 0)))
    kc, vc, ks, vs = padk(kc), padk(vc), padk(ks), padk(vs)
    Tp = Tk + pad
    nc = Tp // CMP_BLK
    nsb = Tp // SEL_BLK
    scale = N_HD ** -0.5
    qg = q.reshape(B, Tq, N_KV, N_HPG, D)
    kcmp = nsa_compress(kc, p['cmp_w1'][0], p['cmp_w2'][0], p['cmp_pe'][0])
    vcmp = nsa_compress(vc, p['cmp_w1'][1], p['cmp_w2'][1], p['cmp_pe'][1])
    blk_end = jnp.arange(nc, dtype=jnp.int32) * CMP_BLK + (CMP_BLK - 1)
    dist = qpos[:, None] - blk_end[None, :]
    bias = rel_table[t5_bucket(dist)].reshape(Tq, nc, N_KV, N_HPG).transpose(2, 3, 0, 1)
    s = jnp.einsum('btghd,bcgd->bghtc', qg, kcmp).astype(jnp.float32) * scale + bias
    pc = masked_softmax(s, dist >= 0)
    o_cmp = jnp.einsum('bghtc,bcgd->btghd', pc.astype(vcmp.dtype), vcmp).reshape(B, Tq, H, D)
    imp = pc.sum(axis=2).reshape(B, N_KV, Tq, nsb, SEL_BLK // CMP_BLK).sum(axis=-1)
    sb = jnp.arange(nsb, dtype=jnp.int32)
    valid = sb[None, :] * SEL_BLK <= qpos[:, None]
    forced = (sb[None, :] == 0) | (sb[None, :] == (qpos // SEL_BLK)[:, None])
    imp = jnp.where(forced, FORCE_SCORE, jnp.where(valid, imp, -1.0))
    kk = min(TOPK, nsb)
    _, idx = lax.top_k(imp, kk)
    Qb = math.gcd(Tq, SEL_QBLK)
    nqb = Tq // Qb
    ks_t = jnp.moveaxis(ks, 2, 1)
    vs_t = jnp.moveaxis(vs, 2, 1)
    table_g = rel_table.reshape(NB, N_KV, N_HPG).transpose(1, 0, 2)
    offs = jnp.arange(SEL_BLK, dtype=jnp.int32)
    bi = jnp.arange(B)[:, None, None, None]
    gi = jnp.arange(N_KV)[None, :, None, None]

    def sel_block(args):
        qb, pb, ib = args
        tok = (ib[..., None] * SEL_BLK + offs).reshape(B, N_KV, Qb, kk * SEL_BLK)
        kg = ks_t[bi, gi, tok]
        vg = vs_t[bi, gi, tok]
        d = pb[None, None, :, None] - tok
        bsel = jnp.moveaxis(table_g[gi, t5_bucket(d)], -1, 2)
        sq = jnp.einsum('bqghd,bgqsd->bghqs', qb, kg).astype(jnp.float32) * scale + bsel
        ps = masked_softmax(sq, (d >= 0)[:, :, None])
        return jnp.einsum('bghqs,bgqsd->bqghd', ps.astype(vg.dtype), vg)

    q_blocks = jnp.moveaxis(qg.reshape(B, nqb, Qb, N_KV, N_HPG, D), 1, 0)
    p_blocks = qpos.reshape(nqb, Qb)
    i_blocks = jnp.moveaxis(idx.reshape(B, N_KV, nqb, Qb, kk), 2, 0)
    o_sel = lax.map(sel_block, (q_blocks, p_blocks, i_blocks))
    o_sel = jnp.moveaxis(o_sel, 0, 1).reshape(B, Tq, H, D)
    return o_cmp, o_sel

def nsa_window(q, qpos, kw, vw, kpos, rel_table):
    B, Tq, H, D = q.shape
    Tk = kw.shape[1]
    Qb = math.gcd(Tq, WIN_QBLK)
    nqb = Tq // Qb
    Kb = WINDOW + Qb
    kpad = jnp.pad(kw, ((0, 0), (Kb, 0), (0, 0), (0, 0)))
    vpad = jnp.pad(vw, ((0, 0), (Kb, 0), (0, 0), (0, 0)))
    ppad = jnp.concatenate([jnp.full((Kb,), -1, jnp.int32), kpos])
    idx = Tk - Tq + (jnp.arange(nqb, dtype=jnp.int32)[:, None] + 1) * Qb + jnp.arange(Kb, dtype=jnp.int32)[None, :]
    kb = kpad[:, idx]
    vb = vpad[:, idx]
    pb = ppad[idx]
    qb = q.reshape(B, nqb, Qb, N_KV, N_HPG, D)
    qp = qpos.reshape(nqb, Qb)
    d = qp[:, :, None] - pb[:, None, :]
    mask = (pb[:, None, :] >= 0) & (d >= 0) & (d < WINDOW)
    bias = rel_table[t5_bucket(d)].reshape(nqb, Qb, Kb, N_KV, N_HPG).transpose(0, 3, 4, 1, 2)
    s = jnp.einsum('bnqghd,bnkgd->bnghqk', qb, kb).astype(jnp.float32) * (N_HD ** -0.5) + bias
    pw = masked_softmax(s, mask[:, None, None])
    return jnp.einsum('bnghqk,bnkgd->bnqghd', pw.astype(vb.dtype), vb).reshape(B, Tq, H, D)

def nsa_mixer(q, kv_cmp, kv_sel, kv_win, gates, qpos, past, win_buf, wb, rel_table, p):
    B, T = q.shape[:2]
    new_rows = jnp.concatenate([kv_cmp, kv_sel], axis=2)
    full = new_rows if past is None else jnp.concatenate([past.astype(new_rows.dtype), new_rows], axis=1)
    o_cmp, o_sel = nsa_cmp_sel(q, qpos, full[:, :, 0], full[:, :, 1], full[:, :, 2], full[:, :, 3], rel_table, p)
    if win_buf is None:
        kw_all, kpos = kv_win, qpos
    else:
        kw_all = jnp.concatenate([win_buf.astype(kv_win.dtype), kv_win], axis=1)
        kpos = jnp.concatenate([qpos[0] - wb + jnp.arange(wb, dtype=jnp.int32), qpos])
    o_win = nsa_window(q, qpos, kw_all[:, :, 0], kw_all[:, :, 1], kpos, rel_table)
    tk = kw_all.shape[1]
    if tk >= wb:
        new_win = kw_all[:, tk - wb:]
    else:
        new_win = jnp.pad(kw_all, ((0, 0), (wb - tk, 0), (0, 0), (0, 0), (0, 0)))
    g = jax.nn.sigmoid(gates.astype(jnp.float32)).reshape(B, T, N_HEADS, 3, 1)
    o = g[:, :, :, 0] * o_cmp + g[:, :, :, 1] * o_sel + g[:, :, :, 2] * o_win
    return o.reshape(B, T, N_DIM).astype(q.dtype), new_rows, new_win

def layer(x, qpos, mem_k, mem_v, past, win_buf, wb, C0, n0, m0, mconv, fconv, rel_table, p):
    B, T, _ = x.shape
    nrm = p['norms']
    h = rmsnorm(x, nrm[0])
    xm, v, ig, fg, og, qn, kvc, kvs, kvw, gn, ga, gb = split_in(h @ p['w_in'])
    hm, C, n, m, mconv_new = mlstm_mixer(xm, v, ig, fg, og, mconv, C0, n0, m0, p)
    on, new_rows, new_win = nsa_mixer(qn.reshape(B, T, N_HEADS, N_HD), kvc.reshape(B, T, 2, N_KV, N_HD), kvs.reshape(B, T, 2, N_KV, N_HD), kvw.reshape(B, T, 2, N_KV, N_HD), gn, qpos, past, win_buf, wb, rel_table, p)
    merged = jax.nn.sigmoid(ga) * (hm @ p['w_up_m']) + jax.nn.sigmoid(gb) * (on @ p['w_up_n'])
    x = x + rmsnorm(merged @ p['w_out'], nrm[1])
    h = rmsnorm(x, nrm[2])
    qx = (h @ p['x_wq']).reshape(B, T, X_HEADS, X_HD)
    s = jnp.einsum('bthd,bmhd->bhtm', qx, mem_k.astype(qx.dtype)).astype(jnp.float32) * (X_HD ** -0.5)
    px = jax.nn.softmax(s, axis=-1).astype(x.dtype)
    ox = jnp.einsum('bhtm,bmhd->bthd', px, mem_v.astype(x.dtype)).reshape(B, T, D_MODEL)
    x = x + rmsnorm(ox @ p['x_wo'], nrm[3])
    h = rmsnorm(x, nrm[4])
    u, fconv_new = causal_dwconv(h @ p['f_wu'], fconv, p['f_conv_w'], p['f_conv_b'])
    x = x + rmsnorm((jax.nn.gelu(u) * (h @ p['f_wg'])) @ p['f_wd'], nrm[5])
    return x, new_rows, new_win, C, n, m, mconv_new, fconv_new

def setup_inputs(seed: int = 0) -> dict:
    key = jax.random.key(seed)
    ks = iter(jax.random.split(key, 48))

    def nrm(shape, scale):
        return jax.random.normal(next(ks), shape, jnp.float32) * scale

    n_pages = PAST_LEN // PAGE_SIZE
    n_pool = (DEC_BATCH * n_pages * 5 + 3) // 4
    wb = min(WINDOW, PAST_LEN)
    page_table = jax.random.permutation(next(ks), n_pool)[:DEC_BATCH * n_pages].reshape(DEC_BATCH, n_pages).astype(jnp.int32)
    f_bias = jnp.broadcast_to(jnp.linspace(3.0, 6.0, M_HEADS), (DEPTH, M_HEADS)) + nrm((DEPTH, M_HEADS), 0.1)
    m_gate_b = jnp.stack([nrm((DEPTH, M_HEADS), 0.1), f_bias], axis=1)
    return {
        'x_prompt': nrm((BATCH, SEQ, D_MODEL), 1.0),
        'x_sample': nrm((DEC_BATCH, DEC_SEQ, D_MODEL), 1.0),
        'mem_prompt': nrm((BATCH, MEM_LEN, D_MODEL), 1.0),
        'cache_nsa_kv': nrm((DEPTH, n_pool, PAGE_SIZE, 4, N_KV, N_HD), 1.0),
        'cache_win_kv': nrm((DEPTH, DEC_BATCH, wb, 2, N_KV, N_HD), 1.0),
        'state_mlstm_C': nrm((DEPTH, DEC_BATCH, M_HEADS, M_HD, M_HD), 0.3),
        'state_mlstm_n': nrm((DEPTH, DEC_BATCH, M_HEADS, M_HD), 1.0),
        'state_mlstm_m': nrm((DEPTH, DEC_BATCH, M_HEADS), 0.5) + 1.0,
        'state_mlstm_conv': nrm((DEPTH, DEC_BATCH, M_CONV - 1, M_DIM), 1.0),
        'state_ffn_conv': nrm((DEPTH, DEC_BATCH, F_CONV - 1, D_FF), 1.0),
        'cache_mem_kv': nrm((DEPTH, DEC_BATCH, MEM_LEN, 2, X_HEADS, X_HD), 1.0),
        'page_table': page_table,
        'rel_bias': nrm((NB, N_HEADS), 0.5),
        'norms': 1.0 + nrm((DEPTH, 6, D_MODEL), 0.05),
        'w_in': nrm((DEPTH, D_MODEL, IN_DIM), D_MODEL ** -0.5),
        'm_gate_b': m_gate_b,
        'm_conv_w': nrm((DEPTH, M_CONV, M_DIM), 0.5),
        'm_conv_b': nrm((DEPTH, M_DIM), 0.02),
        'm_wq': nrm((DEPTH, M_HEADS, M_HD, M_HD), M_HD ** -0.5),
        'm_wk': nrm((DEPTH, M_HEADS, M_HD, M_HD), M_HD ** -0.5),
        'm_norm': 1.0 + nrm((DEPTH, M_HEADS, M_HD), 0.05),
        'cmp_w1': nrm((DEPTH, 2, CMP_BLK * N_HD, N_HD), (CMP_BLK * N_HD) ** -0.5),
        'cmp_w2': nrm((DEPTH, 2, N_HD, N_HD), N_HD ** -0.5),
        'cmp_pe': nrm((DEPTH, 2, CMP_BLK, N_HD), 0.1),
        'w_up_m': nrm((DEPTH, M_DIM, D_MODEL), M_DIM ** -0.5),
        'w_up_n': nrm((DEPTH, N_DIM, D_MODEL), N_DIM ** -0.5),
        'w_out': nrm((DEPTH, D_MODEL, D_MODEL), D_MODEL ** -0.5),
        'x_wq': nrm((DEPTH, D_MODEL, D_MODEL), D_MODEL ** -0.5),
        'x_wkv': nrm((DEPTH, D_MODEL, 2 * D_MODEL), D_MODEL ** -0.5),
        'x_wo': nrm((DEPTH, D_MODEL, D_MODEL), D_MODEL ** -0.5),
        'f_wu': nrm((DEPTH, D_MODEL, D_FF), D_MODEL ** -0.5),
        'f_wg': nrm((DEPTH, D_MODEL, D_FF), D_MODEL ** -0.5),
        'f_wd': nrm((DEPTH, D_FF, D_MODEL), D_FF ** -0.5),
        'f_conv_w': nrm((DEPTH, F_CONV, D_FF), 0.5),
        'f_conv_b': nrm((DEPTH, D_FF), 0.02),
    }

def reference(x_prompt, x_sample, mem_prompt, cache_nsa_kv, cache_win_kv, state_mlstm_C, state_mlstm_n, state_mlstm_m, state_mlstm_conv, state_ffn_conv, cache_mem_kv, page_table, rel_bias, norms, w_in, m_gate_b, m_conv_w, m_conv_b, m_wq, m_wk, m_norm, cmp_w1, cmp_w2, cmp_pe, w_up_m, w_up_n, w_out, x_wq, x_wkv, x_wo, f_wu, f_wg, f_wd, f_conv_w, f_conv_b):
    bp, tp, _ = x_prompt.shape
    bs, ts, _ = x_sample.shape
    n_pages = page_table.shape[1]
    past_len = n_pages * PAGE_SIZE
    wb = cache_win_kv.shape[2]
    qpos_p = jnp.arange(tp, dtype=jnp.int32)
    qpos_s = past_len + jnp.arange(ts, dtype=jnp.int32)
    f32 = jnp.float32
    xp, xs = x_prompt, x_sample
    p_states, s_states = [], []
    for l in range(DEPTH):
        p = {'norms': norms[l], 'w_in': w_in[l], 'm_gate_b': m_gate_b[l], 'm_conv_w': m_conv_w[l], 'm_conv_b': m_conv_b[l], 'm_wq': m_wq[l], 'm_wk': m_wk[l], 'm_norm': m_norm[l], 'cmp_w1': cmp_w1[l], 'cmp_w2': cmp_w2[l], 'cmp_pe': cmp_pe[l], 'w_up_m': w_up_m[l], 'w_up_n': w_up_n[l], 'w_out': w_out[l], 'x_wq': x_wq[l], 'x_wo': x_wo[l], 'f_wu': f_wu[l], 'f_wg': f_wg[l], 'f_wd': f_wd[l], 'f_conv_w': f_conv_w[l], 'f_conv_b': f_conv_b[l]}
        mkv = (mem_prompt @ x_wkv[l]).reshape(bp, MEM_LEN, 2, X_HEADS, X_HD)
        xp, rows_p, win_p, C_p, n_p, m_p, mc_p, fc_p = layer(xp, qpos_p, mkv[:, :, 0], mkv[:, :, 1], None, None, wb, jnp.zeros((bp, M_HEADS, M_HD, M_HD), f32), jnp.zeros((bp, M_HEADS, M_HD), f32), jnp.zeros((bp, M_HEADS), f32), jnp.zeros((bp, M_CONV - 1, M_DIM), xp.dtype), jnp.zeros((bp, F_CONV - 1, D_FF), xp.dtype), rel_bias, p)
        p_states.append((rows_p, win_p, C_p, n_p, m_p, mc_p, fc_p, mkv))
        past = cache_nsa_kv[l][page_table].reshape(bs, past_len, 4, N_KV, N_HD)
        xs, rows_s, win_s, C_s, n_s, m_s, mc_s, fc_s = layer(xs, qpos_s, cache_mem_kv[l][:, :, 0], cache_mem_kv[l][:, :, 1], past, cache_win_kv[l], wb, state_mlstm_C[l], state_mlstm_n[l], state_mlstm_m[l], state_mlstm_conv[l], state_ffn_conv[l], rel_bias, p)
        s_states.append((rows_s, win_s, C_s, n_s, m_s, mc_s, fc_s))
    p_rows, p_win, p_C, p_n, p_m, p_mc, p_fc, p_mkv = zip(*p_states)
    s_rows, s_win, s_C, s_n, s_m, s_mc, s_fc = zip(*s_states)
    return (xp, xs, jnp.stack(p_rows), jnp.stack(p_win), jnp.stack(p_C), jnp.stack(p_n), jnp.stack(p_m), jnp.stack(p_mc), jnp.stack(p_fc), jnp.stack(p_mkv), jnp.stack(s_rows), jnp.stack(s_win), jnp.stack(s_C), jnp.stack(s_n), jnp.stack(s_m), jnp.stack(s_mc), jnp.stack(s_fc))


_drawn_inputs = setup_inputs


def setup_inputs(seed=0):
    import zlib

    import numpy as np

    out = dict(_drawn_inputs(seed))
    spreads = {}
    factors = {'f_conv_b': 5.179}
    for name, (base, spread) in spreads.items():
        noise = np.random.default_rng([zlib.crc32(name.encode()), seed]).standard_normal(out[name].shape)
        drawn = base * np.exp(spread * noise) if base else spread * noise
        out[name] = __import__('jax').numpy.asarray(drawn.astype(out[name].dtype))
    for name, factor in factors.items():
        out[name] = (out[name] * factor).astype(out[name].dtype)
    return out
```

```python
from contextlib import ExitStack, contextmanager

import concourse.bass as bass
import numpy as np
from concourse import mybir

F32 = mybir.dt.float32
I32 = mybir.dt.int32
ACT = mybir.ActivationFunctionType
ALU = mybir.AluOpType
AX = mybir.AxisListType
ds = bass.ds

P = 128
D = 1024
KD = D // P
TP = 1024
NTILE = TP // P
NSEQ, TS = 8, 4
NS = NSEQ * TS
T = TP + NS
NG = 3
GW = T // NG
EPS = 1e-6
MH, MD = 4, 128
NH, HD = 8, 64
NPAIR = NH // 2
CB = 32
SB = 64
TOPK = 16
WIN = 512
PAST, PAGE = 4096, 128
NPAGE = PAST // PAGE
NBUCKET, MAX_DIST = 32, 1024
MEM = 256
XH = 4
DFF = 2816
KF = DFF // P
NEG = -1.0e30
CMP_SCALE = float(HD) ** -0.5
C_V, C_OG = 0, 512
N_VSEL, N_VWIN, N_IG, N_FG, N_GN, N_END = 0, 128, 256, 260, 264, 288
TOKW = 1312
Q_XM, Q_QN, Q_KCMP, Q_VCMP, Q_KSEL, Q_KWIN = 0, 4, 8, 9, 10, 11
NFEAT = 12


class Chain:

    def __init__(self, eng, sem, base=0):
        self.eng, self.sem, self.base, self.n = eng, sem, base, 0

    def link(self, ins):
        self.n += 1
        ins.then_inc(self.sem, 1)
        self.eng.wait_ge(self.sem, self.base + self.n)


def bias_buckets(dist):
    d = np.maximum(dist, 0)
    exact = NBUCKET // 2
    ratio = np.log(np.maximum(d, 1).astype(np.float32) / np.float32(exact)) / np.float32(np.log(MAX_DIST / exact))
    large = np.minimum(exact + (ratio * np.float32(NBUCKET - exact)).astype(np.int32), NBUCKET - 1)
    return np.where(d < exact, d, large)


@contextmanager
def stage(nc, name):
    with ExitStack() as outer:
        used = []

        def sem(n):
            used.append(outer.enter_context(nc.semaphore(f"{name}_{n}")))
            return used[-1]

        with ExitStack() as ctx:
            yield ctx, sem
        for s in used:
            nc.sync.sem_clear(s)
        nc.all_engine_barrier(sem_only=True)




def rms_norm(nc, name, K, src, gain, out, sq, rstd, ss, add=False):
    with stage(nc, name) as (ctx, sem):
        sq_ready, sq_used, out_ready, rstd_ready, mean_ready, root_ready, scaled = map(
            sem, ("sq_ready", "sq_used", "out_ready", "rstd_ready", "mean_ready", "root_ready", "scaled"))
        block = ctx.enter_context(nc.Block())

        @block.scalar
        def _(act):
            for c in range(KD):
                if c >= 2:
                    act.wait_ge(sq_used, c - 1)
                nc.scalar.activation(sq[:, c % 2, :], src[:, c, :], ACT.Square).then_inc(sq_ready, 1)
            act.wait_ge(mean_ready, 1)
            nc.scalar.activation(rstd[:, :], rstd[:, :], ACT.Sqrt).then_inc(root_ready, 1)

        @block.tensor
        def _(pe):
            for c in range(KD):
                pe.wait_ge(sq_ready, c + 1)
                for g in range(NG):
                    last = nc.tensor.matmul(ss[:, g, 0:GW], K["ones"][:, :], sq[:, c % 2, g * GW:(g + 1) * GW],
                                            start=(c == 0), stop=(c == KD - 1))
                last.then_inc(sq_used, 1)

        @block.vector
        def _(ve):
            ve.wait_ge(sq_used, KD)
            nc.vector.tensor_scalar(rstd[:, :].rearrange("p (g t) -> p g t", g=NG), ss[:, :, 0:GW], 1.0 / D, EPS,
                                    ALU.mult, ALU.add).then_inc(mean_ready, 1)
            ve.wait_ge(root_ready, 1)
            nc.vector.reciprocal(rstd[:, :], rstd[:, :]).then_inc(rstd_ready, 1)
            ve.wait_ge(rstd_ready, 1)
            tmp = out if not add else src
            for c in range(KD):
                nc.vector.scalar_tensor_tensor(out=tmp[:, c, :], in0=src[:, c, :], scalar=gain[:, c:c + 1],
                                               in1=rstd[:, :], op0=ALU.mult, op1=ALU.mult).then_inc(scaled, 1)
            if add:
                for c in range(KD):
                    ve.wait_ge(scaled, c + 1)
                    nc.vector.tensor_tensor(out[:, c, :], out[:, c, :], src[:, c, :], ALU.add).then_inc(out_ready, 1)


def project(nc, name, w, n_chunks, kc, rhs, dst, ring, acc, width=T, groups=NG, preload=None):
    gw = width // groups
    with stage(nc, name) as (ctx, sem):
        w_loaded = [sem("w_loaded0"), sem("w_loaded1")]
        acc_ready, acc_free, rhs_loaded = map(sem, ("acc_ready", "acc_free", "rhs_loaded"))
        block = ctx.enter_context(nc.Block())
        assert n_chunks % 2 == 0

        @block.sync
        def _(sp):
            if preload:
                sp.dma_start(*preload).then_inc(rhs_loaded, 16)
            for j in range(2):
                sp.dma_start(ring[:, j, 0:kc * P], w[j]).then_inc(w_loaded[j], 16)
            with sp.Fori(1, n_chunks // 2) as i:
                for j in range(2):
                    sp.wait_ge(acc_ready, 2 * i + j - 1)
                    sp.dma_start(ring[:, j, 0:kc * P], w[ds(2 * i + j, 1), :, :].rearrange("a p k -> p (a k)")
                                 ).then_inc(w_loaded[j], 16)

        @block.tensor
        def _(pe):
            if preload:
                pe.wait_ge(rhs_loaded, 16)
            with pe.Fori(0, n_chunks // 2) as i:
                for j in range(2):
                    pe.wait_ge(w_loaded[j], 16 * i + 16)
                    pe.wait_ge(acc_free, 2 * i + j + 1)
                    for g in range(groups):
                        for k in range(kc):
                            last = nc.tensor.matmul(acc[:, 3 * j + g, 0:gw], ring[:, j, k * P:(k + 1) * P],
                                                    rhs[:, k, g * gw:(g + 1) * gw], start=(k == 0), stop=(k == kc - 1))
                    last.then_inc(acc_ready, 1)

        @block.vector
        def _(ve):
            ve.sem_inc(acc_free, 2)
            with ve.Fori(0, n_chunks // 2) as i:
                for j in range(2):
                    ve.wait_ge(acc_ready, 2 * i + j + 1)
                    out = dst[:, ds(2 * i + j, 1), :].rearrange("p a (g t) -> p (a g) t", g=groups)
                    nc.vector.tensor_scalar(out, acc[:, 3 * j:3 * j + groups, 0:gw], 1.0, None, ALU.mult
                                            ).then_inc(acc_free, 1)


def project_tokens(nc, name, w, h, outs, acc, sizes=(P,) * NTILE + (NS,)):
    with stage(nc, name) as (ctx, sem):
        wt = ctx.enter_context(nc.sbuf_tensor(name + "_wt", [P, 2, KD, max(n for _, n, _ in outs)], F32))
        w_loaded = [sem("w_loaded0"), sem("w_loaded1")]
        acc_ready, acc_free = map(sem, ("acc_ready", "acc_free"))
        block = ctx.enter_context(nc.Block())
        n = len(sizes)

        @block.sync
        def _(sp):
            for j, (c, width, _) in enumerate(outs):
                if j >= 2:
                    sp.wait_ge(acc_ready, (j - 1) * n)
                sp.dma_start(wt[:, j % 2, :, 0:width], w[:, :, c:c + width]).then_inc(w_loaded[j % 2], 16)

        @block.tensor
        def _(pe):
            for j, (_, width, _) in enumerate(outs):
                pe.wait_ge(w_loaded[j % 2], 16 * (j // 2 + 1))
                for t in range(n):
                    m = sizes[t]
                    u = j * n + t
                    if u >= 2:
                        pe.wait_ge(acc_free, u - 1)
                    for k in range(KD):
                        last = nc.tensor.matmul(acc[0:m, u % 2, 0:width], h[:, k, t * P:t * P + m],
                                                wt[:, j % 2, k, 0:width], start=(k == 0), stop=(k == KD - 1))
                    last.then_inc(acc_ready, 1)

        @block.vector
        def _(ve):
            for j, (c, width, dst) in enumerate(outs):
                for t in range(n):
                    m = sizes[t]
                    u = j * n + t
                    ve.wait_ge(acc_ready, u + 1)
                    nc.vector.tensor_copy(dst[0:m, t, :], acc[0:m, u % 2, 0:width]).then_inc(acc_free, 1)



def conv_mlstm(nc, A, O, K, zm, hm):
    with stage(nc, "mconv") as (ctx, sem):
        sb = lambda n, s: ctx.enter_context(nc.sbuf_tensor(n, s, F32))
        cw = sb("cw", [P, 4, 5])
        xs = sb("xs", [P, 4, NSEQ, 3 + TS])
        ys = sb("ys", [P, 4, NSEQ, TS])
        loaded, staged, steps, conv_ready, stored, act_done = map(
            sem, ("loaded", "staged", "steps", "conv_ready", "stored", "act_done"))
        block = ctx.enter_context(nc.Block())

        @block.sync
        def _(sp):
            sp.dma_start(cw[:, :, :], A["m_conv"]).then_inc(loaded, 16)
            sp.dma_start(xs[:, :, :, 0:3], A["m_state"]).then_inc(loaded, 16)
            sp.dma_start(O["p_mconv"], zm[:, :, TP - 3:TP]).then_inc(stored, 16)
            sp.wait_ge(staged, 4)
            sp.dma_start(O["s_mconv"], xs[:, :, :, TS:TS + 3]).then_inc(stored, 16)
            sp.wait_ge(stored, 32)

        @block.vector
        def _(ve):
            ve.wait_ge(loaded, 32)
            for c in range(4):
                nc.vector.tensor_copy(xs[:, c, :, 3:3 + TS],
                                      zm[:, c, TP:T].rearrange("p (b t) -> p b t", t=TS)).then_inc(staged, 1)
            ve.wait_ge(staged, 4)
            chain = Chain(ve, steps)
            for c in range(4):
                nc.vector.tensor_scalar(hm[:, c, 0:TP], zm[:, c, 0:TP], cw[:, c, 3:4], cw[:, c, 4:5],
                                        ALU.mult, ALU.add)
                chain.link(nc.vector.tensor_scalar(ys[:, c, :, :], xs[:, c, :, 3:3 + TS], cw[:, c, 3:4],
                                                   cw[:, c, 4:5], ALU.mult, ALU.add))
            for k in range(3):
                d = 3 - k
                for c in range(4):
                    nc.vector.scalar_tensor_tensor(out=hm[:, c, d:TP], in0=zm[:, c, 0:TP - d], scalar=cw[:, c, k:k + 1],
                                                   in1=hm[:, c, d:TP], op0=ALU.mult, op1=ALU.add)
                    chain.link(nc.vector.scalar_tensor_tensor(
                        out=ys[:, c, :, :], in0=xs[:, c, :, k:k + TS], scalar=cw[:, c, k:k + 1],
                        in1=ys[:, c, :, :], op0=ALU.mult, op1=ALU.add))
            for c in range(4):
                nc.vector.tensor_copy(hm[:, c, TP:T].rearrange("p (b t) -> p b t", t=TS), ys[:, c, :, :]
                                      ).then_inc(conv_ready, 1)

        @block.scalar
        def _(act):
            for c in range(4):
                act.wait_ge(conv_ready, c + 1)
                nc.scalar.activation(hm[:, c, :], hm[:, c, :], ACT.Silu).then_inc(act_done, 1)


def gates(nc, A, K, tokm, tokn, sm, psum):
    lf, b, a, g, tmp = sm["lf"], sm["b"], sm["a"], sm["g"], sm["tmp"]
    n = NTILE + 1
    with stage(nc, "gates") as (ctx, sem):
        gb = ctx.enter_context(nc.sbuf_tensor("gb", [P, 8], F32))
        loaded, steps, act_steps, cum_ready, og_done = map(sem, ("loaded", "steps", "act_steps", "cum_ready", "og_done"))
        block = ctx.enter_context(nc.Block())
        fg = tokn[:, :, N_FG:N_FG + MH]

        @block.sync
        def _(sp):
            sp.dma_start(gb[:, :], A["gate_b"].partition_broadcast(P)).then_inc(loaded, 16)

        @block.vector
        def _(ve):
            ve.wait_ge(loaded, 16)
            chain = Chain(ve, steps)
            chain.link(nc.vector.tensor_tensor(tokn[:, :, N_IG:N_IG + 8], tokn[:, :, N_IG:N_IG + 8],
                                               gb[:, :].unsqueeze(1).to_broadcast([P, n, 8]), ALU.add))
            nc.vector.tensor_scalar(lf[:, :, :], fg, 0.0, None, ALU.min)
            chain.link(nc.vector.scalar_tensor_tensor(out=tmp[:, :, :], in0=fg, scalar=-1.0, in1=fg,
                                                      op0=ALU.mult, op1=ALU.min))
            ve.wait_ge(act_steps, 1)
            chain.link(nc.vector.tensor_scalar(tmp[:, :, :], tmp[:, :, :], 1.0, None, ALU.add))
            ve.wait_ge(act_steps, 2)
            chain.link(nc.vector.tensor_tensor(lf[:, :, :], lf[:, :, :], tmp[:, :, :], ALU.subtract))
            ve.wait_ge(cum_ready, 2)
            nc.vector.tensor_copy(b[:, 0:NTILE, :], psum[:, 0, 0:NTILE * MH].rearrange("p (t h) -> p t h", h=MH))
            chain.link(nc.vector.tensor_copy(b[:, NTILE, :], psum[:, 1, 0:MH]))
            chain.link(nc.vector.tensor_tensor(a[:, :, :], tokn[:, :, N_IG:N_IG + MH], b[:, :, :], ALU.subtract))

        @block.scalar
        def _(act):
            act.wait_ge(steps, 2)
            nc.scalar.activation(tmp[:, :, :], tmp[:, :, :], ACT.Exp).then_inc(act_steps, 1)
            act.wait_ge(steps, 3)
            nc.scalar.activation(tmp[:, :, :], tmp[:, :, :], ACT.Ln).then_inc(act_steps, 1)
            nc.scalar.activation(g[:, :, :], tokn[:, :, N_GN:N_END], ACT.Sigmoid).then_inc(act_steps, 1)
            for t in range(n):
                m = P if t < NTILE else NS
                nc.scalar.activation(tokm[0:m, t, C_OG:C_OG + 512], tokm[0:m, t, C_OG:C_OG + 512], ACT.Sigmoid
                                     ).then_inc(og_done, 1)

        @block.tensor
        def _(pe):
            pe.wait_ge(steps, 4)
            nc.tensor.matmul(psum[:, 0, 0:NTILE * MH], K["tri"][:, :], lf[:, 0:NTILE, :].rearrange("p t h -> p (t h)"),
                             start=True, stop=True).then_inc(cum_ready, 1)
            nc.tensor.matmul(psum[:, 1, 0:MH], K["stri"][:, :], lf[:, NTILE, :], start=True, stop=True
                             ).then_inc(cum_ready, 1)


def mlstm(nc, A, O, K, hm, tokm, sm, psum):
    with stage(nc, "mlstm") as (ctx, sem):
        sb = lambda n, s: ctx.enter_context(nc.sbuf_tensor(n, s, F32))
        wqk = sb("wqk", [P, 2, MH, MD])
        mnorm = sb("mnorm", [P, MH, MD])
        xc = sb("xc", [P, MH, P])
        qT, kT, kt = sb("qT", [P, MH, P]), sb("kT", [P, MH, P]), sb("kt", [P, MH, P])
        va = sb("va", [P, MH, MD + 1])
        kw = sb("kw", [P, MH, MD])
        dec = sb("dec", [P, MH, P])
        num = sb("num", [P, MH, MD + 1])
        C = sb("C", [P, MH, MD + 1])
        mc, M, Mb, ML = sb("mc", [P, MH]), sb("M", [P, MH]), sb("Mb", [P, 2 * MH]), sb("ML", [P, 2 * MH])
        sc, wl, sl, emt, r1, r2 = (sb(n, [P, MH]) for n in ("sc", "wl", "sl", "emt", "r1", "r2"))
        tmp = sb("tmpm", [P, MH, P])
        ac = sb("ac", [P, MH])
        names = ("loaded", "xc_ready", "qk_ready", "qk_copied", "arow_ready", "steps", "mrow_ready", "last_ready",
                 "exps_ready", "scores_ready", "inter_ready", "intra_ready", "update_ready", "turned", "h_stored",
                 "finished", "diag_a_ready", "diag_m_ready", "exponents_ready", "differences_ready", "weighted_ready",
                 "square_ready", "root_ready", "gated_ready", "stored")
        S = {n: sem(n) for n in names}
        block = ctx.enter_context(nc.Block())
        row4 = lambda bank: psum[:, bank, :].rearrange("p (h t) -> p h t", h=MH)
        wide = lambda bank: psum[:, bank:bank + 2, :].rearrange("p b (h t) -> p (b h) t", h=2)[:, :, 0:MD + 1]
        per_head = lambda v, n: v.unsqueeze(2).to_broadcast([P, MH, n])
        per_all = lambda v: v.unsqueeze(1).to_broadcast([P, MH, P])
        STEPS = 19

        @block.sync
        def _(sp):
            sp.dma_start(wqk[:, :, :, :], A["m_wqk"]).then_inc(S["loaded"], 16)
            sp.dma_start(mnorm[:, :, :], A["m_norm"].partition_broadcast(P)).then_inc(S["loaded"], 16)
            sp.wait_ge(S["finished"], 2)
            sp.dma_start(O["p_C"], tmp[:, :, :]).then_inc(S["stored"], 16)
            sp.dma_start(O["p_n"], r1[:, :]).then_inc(S["stored"], 16)
            sp.dma_start(O["p_m"], mc[0:1, :]).then_inc(S["stored"], 16)
            sp.wait_ge(S["stored"], 48)

        @block.scalar
        def _(act):
            act.wait_ge(S["loaded"], 32)
            with act.Fori(0, NTILE) as i:
                act.wait_ge(S["h_stored"], i + 1)
                act.wait_ge(S["loaded"], 32)
                nc.scalar.activation(xc[:, :, :], hm[:, :, ds(i * P, P)], ACT.Copy).then_inc(S["xc_ready"], 1)
                act.wait_ge(S["qk_ready"], i + 1)
                nc.scalar.activation(qT[:, :, :], row4(0), ACT.Copy).then_inc(S["qk_copied"], 1)
                nc.scalar.activation(kT[:, :, :], row4(1), ACT.Copy, scale=MD ** -0.5).then_inc(S["qk_copied"], 1)
                nc.scalar.activation(kt[:, :, :], row4(2), ACT.Copy, scale=MD ** -0.5).then_inc(S["qk_copied"], 1)
                act.wait_ge(S["exponents_ready"], i + 1)
                for h in range(MH):
                    nc.scalar.activation(dec[:, h, :], dec[:, h, :], ACT.Exp,
                                         bias=ac[:, h:h + 1]
                                         ).then_inc(S["exps_ready"], 1)
                act.wait_ge(S["differences_ready"], i + 1)
                for v in (sc, emt, wl, sl):
                    nc.scalar.activation(v[:, :], v[:, :], ACT.Exp).then_inc(S["exps_ready"], 1)
                act.wait_ge(S["square_ready"], i + 1)
                nc.scalar.activation(r1[:, :], r1[:, :], ACT.Sqrt).then_inc(S["root_ready"], 1)

        @block.tensor
        def _(pe):
            pe.wait_ge(S["loaded"], 32)
            with pe.Fori(0, NTILE) as i:
                pe.wait_ge(S["h_stored"], i + 1)
                pe.wait_ge(S["xc_ready"], i + 1)
                for h in range(MH):
                    hs = slice(h * P, (h + 1) * P)
                    nc.tensor.matmul(psum[:, 0, hs], wqk[:, 0, h, :], xc[:, h, :], start=True, stop=True)
                    nc.tensor.matmul(psum[:, 1, hs], wqk[:, 1, h, :], xc[:, h, :], start=True, stop=True)
                    last = nc.tensor.matmul(psum[:, 2, hs], xc[:, h, :], wqk[:, 1, h, :], start=True, stop=True)
                last.then_inc(S["qk_ready"], 1)
                pe.wait_ge(S["diag_a_ready"], i + 1)
                nc.tensor.matmul(psum[:, 4, :], K["ones"][:, :], tmp[:, :, :].rearrange("p h t -> p (h t)"),
                                 start=True, stop=True).then_inc(S["arow_ready"], 1)
                pe.wait_ge(S["qk_copied"], 3 * i + 3)
                for h in range(MH):
                    last = nc.tensor.matmul(psum[:, 3, h * P:(h + 1) * P], kT[:, h, :], qT[:, h, :], start=True, stop=True)
                last.then_inc(S["scores_ready"], 1)
                for h in range(MH):
                    last = nc.tensor.matmul(wide(5)[:, h, :], qT[:, h, :], C[:, h, :], start=True, stop=True)
                last.then_inc(S["inter_ready"], 1)
                pe.wait_ge(S["diag_m_ready"], i + 1)
                nc.tensor.matmul(psum[:, 4, :], K["ones"][:, :], tmp[:, :, :].rearrange("p h t -> p (h t)"),
                                 start=True, stop=True).then_inc(S["mrow_ready"], 1)
                nc.tensor.matmul(psum[:, 7, 0:2 * MH], K["last"][:, :], Mb[:, :], start=True, stop=True
                                 ).then_inc(S["last_ready"], 1)
                pe.wait_ge(S["weighted_ready"], i + 1)
                for h in range(MH):
                    last = nc.tensor.matmul(wide(0)[:, h, :], dec[:, h, :], va[:, h, :], start=True, stop=True)
                last.then_inc(S["intra_ready"], 1)
                for h in range(MH):
                    last = nc.tensor.matmul(wide(2)[:, h, :], kw[:, h, :], va[:, h, :], start=True, stop=True)
                last.then_inc(S["update_ready"], 1)
                pe.wait_ge(S["gated_ready"], i + 1)
                for h in range(MH):
                    last = nc.tensor.transpose(psum[:, 4, h * P:(h + 1) * P], num[:, h, 0:MD], K["ident"][:, :])
                last.then_inc(S["turned"], 1)
            pe.wait_ge(S["h_stored"], NTILE + 1)
            for h in range(MH):
                last = nc.tensor.transpose(psum[:, 4, h * P:(h + 1) * P], C[:, h, 0:MD], K["ident"][:, :])
            last.then_inc(S["turned"], 1)

        @block.vector
        def _(ve):
            ve.wait_ge(S["loaded"], 32)
            pre = Chain(ve, S["finished"])
            nc.vector.memset(C[:, :, :], 0.0)
            nc.vector.memset(va[:, :, MD:MD + 1], 1.0)
            pre.link(nc.vector.memset(mc[:, :], 0.0))
            ve.sem_inc(S["h_stored"], 1)
            with ve.Fori(0, NTILE) as i:
                ch = Chain(ve, S["steps"], i * STEPS)

                def signal(ins, name):
                    ins.then_inc(S[name], 1)
                    ve.wait_ge(S[name], i + 1)

                a = ac[:, :]
                ch.link(nc.vector.tensor_copy(a, sm["a"][:, ds(i, 1), :].rearrange("p a h -> p (a h)")))
                b = sm["b"][:, ds(i, 1), :].rearrange("p a h -> p (a h)")
                nc.vector.tensor_tensor(tmp[:, :, :], per_all(K["ident"][:, :]), per_head(a, P), ALU.mult
                                        ).then_inc(S["diag_a_ready"], 1)
                nc.vector.tensor_copy(va[:, :, 0:MD], tokm[:, ds(i, 1), C_V:C_V + 512].rearrange("p a (h v) -> p (a h) v", h=MH))
                ve.wait_ge(S["arow_ready"], i + 1)
                ch.link(nc.vector.tensor_tensor(dec[:, :, :], row4(4), per_all(K["causal"][:, :]), ALU.add))
                ch.link(nc.vector.tensor_reduce(M[:, :], dec[:, :, :], AX.X, ALU.max))
                ch.link(nc.vector.tensor_tensor(M[:, :], M[:, :], mc[:, :], ALU.max))
                nc.vector.tensor_copy(Mb[:, 0:MH], M[:, :])
                ch.link(nc.vector.tensor_tensor(Mb[:, MH:2 * MH], M[:, :], b, ALU.add))
                nc.vector.tensor_tensor(tmp[:, :, :], per_all(K["ident"][:, :]), per_head(M[:, :], P), ALU.mult
                                        ).then_inc(S["diag_m_ready"], 1)
                nc.vector.tensor_tensor(sc[:, :], mc[:, :], M[:, :], ALU.subtract)
                nc.vector.tensor_scalar(emt[:, :], Mb[:, MH:2 * MH], -1.0, None, ALU.mult)
                ve.wait_ge(S["mrow_ready"], i + 1)
                nc.vector.tensor_tensor(dec[:, :, :], per_all(K["causal_t"][:, :]), row4(4), ALU.subtract
                                        ).then_inc(S["exponents_ready"], 1)
                ve.wait_ge(S["last_ready"], i + 1)
                ch.link(nc.vector.tensor_copy(ML[:, :], psum[:, 7, 0:2 * MH]))
                nc.vector.tensor_tensor(wl[:, :], a, ML[:, 0:MH], ALU.subtract)
                ch.link(nc.vector.tensor_tensor(sl[:, :], mc[:, :], ML[:, 0:MH], ALU.subtract))
                signal(nc.vector.tensor_copy(mc[:, :], ML[:, MH:2 * MH]), "differences_ready")
                ve.wait_ge(S["scores_ready"], i + 1)
                ve.wait_ge(S["exps_ready"], 8 * i + 8)
                nc.vector.tensor_tensor(dec[:, :, :], dec[:, :, :], row4(3), ALU.mult)
                signal(nc.vector.tensor_tensor(kw[:, :, :], kt[:, :, :], per_head(wl[:, :], MD), ALU.mult), "weighted_ready")
                ve.wait_ge(S["inter_ready"], i + 1)
                ch.link(nc.vector.tensor_tensor(num[:, :, :], wide(5), per_head(sc[:, :], MD + 1), ALU.mult))
                ve.wait_ge(S["intra_ready"], i + 1)
                ch.link(nc.vector.tensor_tensor(num[:, :, :], num[:, :, :], wide(0), ALU.add))
                den = num[:, :, MD]
                ch.link(nc.vector.scalar_tensor_tensor(out=r2[:, :], in0=den, scalar=-1.0, in1=den, op0=ALU.mult, op1=ALU.max))
                ch.link(nc.vector.tensor_tensor(r2[:, :], r2[:, :], emt[:, :], ALU.max))
                ch.link(nc.vector.reciprocal(r2[:, :], r2[:, :]))
                ch.link(nc.vector.tensor_tensor(num[:, :, 0:MD], num[:, :, 0:MD], per_head(r2[:, :], MD), ALU.mult))
                ch.link(nc.vector.tensor_tensor(tmp[:, :, :], num[:, :, 0:MD], num[:, :, 0:MD], ALU.mult))
                ch.link(nc.vector.tensor_reduce(r1[:, :], tmp[:, :, :], AX.X, ALU.add))
                signal(nc.vector.tensor_scalar(r1[:, :], r1[:, :], 1.0 / MD, EPS, ALU.mult, ALU.add), "square_ready")
                ve.wait_ge(S["root_ready"], i + 1)
                ch.link(nc.vector.reciprocal(r1[:, :], r1[:, :]))
                ch.link(nc.vector.tensor_tensor(num[:, :, 0:MD], num[:, :, 0:MD], per_head(r1[:, :], MD), ALU.mult))
                ch.link(nc.vector.tensor_tensor(num[:, :, 0:MD], num[:, :, 0:MD], mnorm[:, :, :], ALU.mult))
                signal(nc.vector.tensor_tensor(
                    num[:, :, 0:MD], num[:, :, 0:MD],
                    tokm[:, ds(i, 1), C_OG:C_OG + 512].rearrange("p a (h v) -> p (a h) v", h=MH), ALU.mult), "gated_ready")
                ve.wait_ge(S["update_ready"], i + 1)
                for h in range(MH):
                    last = nc.vector.scalar_tensor_tensor(out=C[:, h, :], in0=C[:, h, :], scalar=sl[:, h:h + 1],
                                                          in1=wide(2)[:, h, :], op0=ALU.mult, op1=ALU.add)
                ch.link(last)
                assert ch.n == STEPS, ch.n
                ve.wait_ge(S["turned"], i + 1)
                nc.vector.tensor_scalar(hm[:, :, ds(i * P, P)], row4(4), 1.0, None, ALU.mult).then_inc(S["h_stored"], 1)
            ve.wait_ge(S["turned"], NTILE + 1)
            nc.vector.tensor_copy(r1[:, :], C[:, :, MD])
            pre.link(nc.vector.tensor_copy(tmp[:, :, :], row4(4)))


def mlstm_sample(nc, A, O, K, hm, tokm, sm, psum):
    with stage(nc, "smlstm") as (ctx, sem):
        sb = lambda n, s: ctx.enter_context(nc.sbuf_tensor("sm_" + n, s, F32))
        wqk = sb("wqk", [P, 2, MH, MD])
        mnorm = sb("mnorm", [NS, MH, MD])
        C = sb("C", [P, NSEQ, MH, MD])
        n0, m0 = sb("n0", [NS, MH, MD]), sb("m0", [NS, MH])
        n8, sl8 = sb("n8", [NSEQ, MH, MD]), sb("sl8", [NSEQ, 2 * MH])
        qT, kT = sb("qT", [P, MH, NS]), sb("kT", [P, MH, NS])
        kt, qt = sb("kt", [NS, MH, MD]), sb("qt", [NS, MH, MD])
        kw, kwm = sb("kw", [NS, MH, MD]), sb("kwm", [NS, NSEQ, MH * MD])
        va = sb("va", [NS, MH, MD + 1])
        dec, tmp = sb("dec", [NS, MH, NS]), sb("tmpm", [NS, MH, NS])
        num, sq = sb("num", [NS, MH, MD + 1]), sb("sqm", [NS, MH, MD])
        inter = sb("inter", [P, MH, NS])
        slrow, slb = sb("slrow", [NS, NSEQ, MH]), sb("slb", [P, NSEQ, MH])
        M, Mb, ML = sb("M", [NS, MH]), sb("Mb", [NS, 2 * MH]), sb("ML", [NS, 2 * MH])
        sc, wl, sl, emt, r1, r2, nq = (sb(n, [NS, MH]) for n in ("sc", "wl", "sl", "emt", "r1", "r2", "nq"))
        names = ("loaded", "qk_ready", "qk_copied", "diag_a_ready", "arow_ready", "steps", "diag_m_ready", "mrow_ready",
                 "last_ready", "exponents_ready", "exps_ready", "differences_ready", "scores_ready", "weighted_ready",
                 "intra_ready", "inter_ready", "inter_copied", "inter_turned", "scale_ready", "scale_spread",
                 "masked_ready", "update_ready", "updated", "norm_ready", "square_ready", "root_ready", "gated_ready",
                 "turned", "stored")
        S = {n: sem(n) for n in names}
        block = ctx.enter_context(nc.Block())
        last = NTILE
        a, b = sm["a"][0:NS, last, :], sm["b"][0:NS, last, :]
        ones, ident = K["ones"], K["ident"]
        small = lambda bank: psum[0:NS, bank, 0:MH * NS].rearrange("p (h t) -> p h t", h=MH)
        wide = lambda bank: psum[0:NS, bank:bank + 2, :].rearrange("p b (h t) -> p (b h) t", h=2)[:, :, 0:MD + 1]
        per_head = lambda v, n: v.unsqueeze(2).to_broadcast([NS, MH, n])
        per_all = lambda v: v.unsqueeze(1).to_broadcast([NS, MH, NS])

        @block.sync
        def _(sp):
            sp.dma_start(wqk[:, :, :, :], A["m_wqk"]).then_inc(S["loaded"], 16)
            sp.dma_start(mnorm[:, :, :], A["m_norm"].partition_broadcast(NS)).then_inc(S["loaded"], 16)
            sp.dma_start(C[:, :, :, :], A["s_C0"]).then_inc(S["loaded"], 16)
            sp.dma_start(n0[:, :, :], A["s_n0t"]).then_inc(S["loaded"], 16)
            sp.dma_start(n8[:, :, :], A["s_n0"]).then_inc(S["loaded"], 16)
            sp.dma_start(m0[:, :], A["s_m0t"]).then_inc(S["loaded"], 16)
            sp.wait_ge(S["updated"], NSEQ)
            sp.dma_start(O["s_C"], C[:, :, :, :]).then_inc(S["stored"], 16)
            sp.wait_ge(S["norm_ready"], 1)
            sp.dma_start(O["s_n"], n8[:, :, :]).then_inc(S["stored"], 16)
            sp.dma_start(O["s_m"], sl8[:, MH:2 * MH]).then_inc(S["stored"], 16)
            sp.wait_ge(S["stored"], 48)

        @block.tensor
        def _(pe):
            pe.wait_ge(S["loaded"], 96)
            for h in range(MH):
                x = hm[:, h, TP:T]
                nc.tensor.matmul(psum[:, 0, h * NS:(h + 1) * NS], wqk[:, 0, h, :], x, start=True, stop=True)
                nc.tensor.matmul(psum[:, 1, h * NS:(h + 1) * NS], wqk[:, 1, h, :], x, start=True, stop=True)
                nc.tensor.matmul(psum[0:NS, 2, h * MD:(h + 1) * MD], x, wqk[:, 1, h, :], start=True, stop=True)
                mm = nc.tensor.matmul(psum[0:NS, 3, h * MD:(h + 1) * MD], x, wqk[:, 0, h, :], start=True, stop=True)
            mm.then_inc(S["qk_ready"], 1)
            pe.wait_ge(S["diag_a_ready"], 1)
            nc.tensor.matmul(psum[0:NS, 4, 0:MH * NS], ones[0:NS, 0:NS], tmp[:, :, :].rearrange("p h t -> p (h t)"),
                             start=True, stop=True).then_inc(S["arow_ready"], 1)
            pe.wait_ge(S["qk_copied"], 4)
            for h in range(MH):
                mm = nc.tensor.matmul(psum[0:NS, 5, h * NS:(h + 1) * NS], kT[:, h, :], qT[:, h, :], start=True, stop=True)
            mm.then_inc(S["scores_ready"], 1)
            for h in range(MH):
                for q in range(NSEQ):
                    c = slice(h * NS + q * TS, h * NS + (q + 1) * TS)
                    mm = nc.tensor.matmul(psum[:, 6, c], C[:, q, h, :], qT[:, h, q * TS:(q + 1) * TS], start=True, stop=True)
            mm.then_inc(S["inter_ready"], 1)
            pe.wait_ge(S["diag_m_ready"], 1)
            nc.tensor.matmul(psum[0:NS, 4, 0:MH * NS], ones[0:NS, 0:NS], tmp[:, :, :].rearrange("p h t -> p (h t)"),
                             start=True, stop=True).then_inc(S["mrow_ready"], 1)
            nc.tensor.matmul(psum[0:NS, 7, 0:2 * MH], K["slast"][0:NS, 0:NS], Mb[:, :], start=True, stop=True
                             ).then_inc(S["last_ready"], 1)
            pe.wait_ge(S["inter_copied"], 1)
            for h in range(MH):
                mm = nc.tensor.transpose(psum[0:NS, 6, h * MD:(h + 1) * MD], inter[:, h, :], ident[:, :])
            mm.then_inc(S["inter_turned"], 1)
            pe.wait_ge(S["weighted_ready"], 1)
            for h in range(MH):
                mm = nc.tensor.matmul(wide(0)[:, h, :], dec[:, h, :], va[:, h, :], start=True, stop=True)
            mm.then_inc(S["intra_ready"], 1)
            pe.wait_ge(S["scale_ready"], 1)
            nc.tensor.matmul(psum[:, 4, 0:NSEQ * MH], ones[0:NS, :], slrow[:, :, :].rearrange("p b h -> p (b h)"),
                             start=True, stop=True)
            nc.tensor.matmul(psum[0:NSEQ, 7, 0:MH], K["slast8"][0:NS, 0:NSEQ], sl[:, :], start=True, stop=True)
            nc.tensor.matmul(psum[0:NSEQ, 7, MH:2 * MH], K["slast8"][0:NS, 0:NSEQ], Mb[:, MH:2 * MH], start=True, stop=True)
            nc.tensor.matmul(psum[0:NSEQ, 5, :], K["sseq8"][0:NS, 0:NSEQ], kw[:, :, :].rearrange("p h k -> p (h k)"),
                             start=True, stop=True).then_inc(S["scale_spread"], 1)
            for q in range(NSEQ):
                pe.wait_ge(S["masked_ready"], q + 1)
                if q >= 2:
                    pe.wait_ge(S["updated"], q - 1)
                for h in range(MH):
                    mm = nc.tensor.matmul(psum[:, 2 + q % 2, h * MD:(h + 1) * MD], kwm[:, q, h * MD:(h + 1) * MD],
                                          va[:, h, 0:MD], start=True, stop=True)
                mm.then_inc(S["update_ready"], 1)
            pe.wait_ge(S["gated_ready"], 1)
            for h in range(MH):
                mm = nc.tensor.transpose(psum[:, 0, h * NS:(h + 1) * NS], num[:, h, 0:MD], ident[0:NS, 0:NS])
            mm.then_inc(S["turned"], 1)

        @block.scalar
        def _(act):
            act.wait_ge(S["qk_ready"], 1)
            k = MD ** -0.5
            nc.scalar.activation(qT[:, :, :], psum[:, 0, 0:MH * NS].rearrange("p (h t) -> p h t", h=MH), ACT.Copy
                                 ).then_inc(S["qk_copied"], 1)
            nc.scalar.activation(kT[:, :, :], psum[:, 1, 0:MH * NS].rearrange("p (h t) -> p h t", h=MH), ACT.Copy, scale=k
                                 ).then_inc(S["qk_copied"], 1)
            nc.scalar.activation(kt[:, :, :], psum[0:NS, 2, :].rearrange("p (h t) -> p h t", h=MH), ACT.Copy, scale=k
                                 ).then_inc(S["qk_copied"], 1)
            nc.scalar.activation(qt[:, :, :], psum[0:NS, 3, :].rearrange("p (h t) -> p h t", h=MH), ACT.Copy
                                 ).then_inc(S["qk_copied"], 1)
            act.wait_ge(S["exponents_ready"], 1)
            for h in range(MH):
                nc.scalar.activation(dec[:, h, :], dec[:, h, :], ACT.Exp, bias=sm["a"][0:NS, last, h:h + 1]
                                     ).then_inc(S["exps_ready"], 1)
            act.wait_ge(S["differences_ready"], 1)
            for v in (sc, emt, wl, sl):
                nc.scalar.activation(v[:, :], v[:, :], ACT.Exp).then_inc(S["exps_ready"], 1)
            act.wait_ge(S["inter_ready"], 1)
            nc.scalar.activation(inter[:, :, :], psum[:, 6, 0:MH * NS].rearrange("p (h t) -> p h t", h=MH), ACT.Copy
                                 ).then_inc(S["inter_copied"], 1)
            act.wait_ge(S["square_ready"], 1)
            nc.scalar.activation(r1[:, :], r1[:, :], ACT.Sqrt).then_inc(S["root_ready"], 1)

        @block.vector
        def _(ve):
            ch = Chain(ve, S["steps"])

            def signal(ins, name):
                ins.then_inc(S[name], 1)
                ve.wait_ge(S[name], 1)

            nc.vector.memset(va[:, :, MD:MD + 1], 1.0)
            nc.vector.tensor_tensor(tmp[:, :, :], per_all(ident[0:NS, 0:NS]), per_head(a, NS), ALU.mult
                                    ).then_inc(S["diag_a_ready"], 1)
            nc.vector.tensor_copy(va[:, :, 0:MD], tokm[0:NS, last, C_V:C_V + 512].rearrange("p (h v) -> p h v", h=MH))
            ve.wait_ge(S["loaded"], 96)
            ve.wait_ge(S["arow_ready"], 1)
            ch.link(nc.vector.tensor_tensor(dec[:, :, :], small(4), per_all(K["scausal"][0:NS, 0:NS]), ALU.add))
            ch.link(nc.vector.tensor_reduce(M[:, :], dec[:, :, :], AX.X, ALU.max))
            ch.link(nc.vector.tensor_tensor(M[:, :], M[:, :], m0[:, :], ALU.max))
            nc.vector.tensor_copy(Mb[:, 0:MH], M[:, :])
            ch.link(nc.vector.tensor_tensor(Mb[:, MH:2 * MH], M[:, :], b, ALU.add))
            nc.vector.tensor_tensor(tmp[:, :, :], per_all(ident[0:NS, 0:NS]), per_head(M[:, :], NS), ALU.mult
                                    ).then_inc(S["diag_m_ready"], 1)
            nc.vector.tensor_tensor(sc[:, :], m0[:, :], M[:, :], ALU.subtract)
            nc.vector.tensor_scalar(emt[:, :], Mb[:, MH:2 * MH], -1.0, None, ALU.mult)
            ve.wait_ge(S["mrow_ready"], 1)
            nc.vector.tensor_tensor(dec[:, :, :], per_all(K["scausal_t"][0:NS, 0:NS]), small(4), ALU.subtract
                                    ).then_inc(S["exponents_ready"], 1)
            ve.wait_ge(S["last_ready"], 1)
            ch.link(nc.vector.tensor_copy(ML[:, :], psum[0:NS, 7, 0:2 * MH]))
            nc.vector.tensor_tensor(wl[:, :], a, ML[:, 0:MH], ALU.subtract)
            signal(nc.vector.tensor_tensor(sl[:, :], m0[:, :], ML[:, 0:MH], ALU.subtract), "differences_ready")
            ve.wait_ge(S["scores_ready"], 1)
            ve.wait_ge(S["exps_ready"], 8)
            ve.wait_ge(S["qk_copied"], 4)
            ch.link(nc.vector.tensor_tensor(sq[:, :, :], qt[:, :, :], n0[:, :, :], ALU.mult))
            ch.link(nc.vector.tensor_reduce(nq[:, :], sq[:, :, :], AX.X, ALU.add))
            ch.link(nc.vector.tensor_tensor(nq[:, :], nq[:, :], sc[:, :], ALU.mult))
            nc.vector.tensor_tensor(dec[:, :, :], dec[:, :, :], small(5), ALU.mult)
            signal(nc.vector.tensor_tensor(kw[:, :, :], kt[:, :, :], per_head(wl[:, :], MD), ALU.mult), "weighted_ready")
            signal(nc.vector.tensor_tensor(slrow[:, :, :], K["slast8"][0:NS, 0:NSEQ].unsqueeze(2).to_broadcast([NS, NSEQ, MH]),
                                           sl[:, :].unsqueeze(1).to_broadcast([NS, NSEQ, MH]), ALU.mult), "scale_ready")
            for q in range(NSEQ):
                nc.vector.tensor_scalar(kwm[:, q, :], kw[:, :, :].rearrange("p h k -> p (h k)"), K["sseq8"][0:NS, q:q + 1],
                                        None, ALU.mult).then_inc(S["masked_ready"], 1)
            ve.wait_ge(S["inter_turned"], 1)
            ve.wait_ge(S["intra_ready"], 1)
            ch.link(nc.vector.tensor_tensor(num[:, :, 0:MD], psum[0:NS, 6, :].rearrange("p (h v) -> p h v", h=MH),
                                            per_head(sc[:, :], MD), ALU.mult))
            ch.link(nc.vector.tensor_tensor(num[:, :, 0:MD], num[:, :, 0:MD], wide(0)[:, :, 0:MD], ALU.add))
            ch.link(nc.vector.tensor_tensor(nq[:, :], nq[:, :], wide(0)[:, :, MD], ALU.add))
            ch.link(nc.vector.scalar_tensor_tensor(out=r2[:, :], in0=nq[:, :], scalar=-1.0, in1=nq[:, :], op0=ALU.mult, op1=ALU.max))
            ch.link(nc.vector.tensor_tensor(r2[:, :], r2[:, :], emt[:, :], ALU.max))
            ch.link(nc.vector.reciprocal(r2[:, :], r2[:, :]))
            ch.link(nc.vector.tensor_tensor(num[:, :, 0:MD], num[:, :, 0:MD], per_head(r2[:, :], MD), ALU.mult))
            ch.link(nc.vector.tensor_tensor(sq[:, :, :], num[:, :, 0:MD], num[:, :, 0:MD], ALU.mult))
            ch.link(nc.vector.tensor_reduce(r1[:, :], sq[:, :, :], AX.X, ALU.add))
            signal(nc.vector.tensor_scalar(r1[:, :], r1[:, :], 1.0 / MD, EPS, ALU.mult, ALU.add), "square_ready")
            ve.wait_ge(S["scale_spread"], 1)
            ch.link(nc.vector.tensor_copy(slb[:, :, :], psum[:, 4, 0:NSEQ * MH].rearrange("p (b h) -> p b h", h=MH)))
            ch.link(nc.vector.tensor_copy(sl8[:, :], psum[0:NSEQ, 7, 0:2 * MH]))
            ch.link(nc.vector.tensor_tensor(n8[:, :, :], n8[:, :, :], sl8[:, 0:MH].unsqueeze(2).to_broadcast([NSEQ, MH, MD]), ALU.mult))
            signal(nc.vector.tensor_tensor(n8[:, :, :], n8[:, :, :], psum[0:NSEQ, 5, :].rearrange("p (h k) -> p h k", h=MH),
                                           ALU.add), "norm_ready")
            for q in range(NSEQ):
                ve.wait_ge(S["update_ready"], q + 1)
                ve.wait_ge(S["inter_ready"], 1)
                ch.link(nc.vector.tensor_tensor(C[:, q, :, :], C[:, q, :, :], slb[:, q, :].unsqueeze(2).to_broadcast([P, MH, MD]), ALU.mult))
                nc.vector.tensor_tensor(C[:, q, :, :], C[:, q, :, :], psum[:, 2 + q % 2, :].rearrange("p (h v) -> p h v", h=MH),
                                        ALU.add).then_inc(S["updated"], 1)
            ve.wait_ge(S["root_ready"], 1)
            ch.link(nc.vector.reciprocal(r1[:, :], r1[:, :]))
            ch.link(nc.vector.tensor_tensor(num[:, :, 0:MD], num[:, :, 0:MD], per_head(r1[:, :], MD), ALU.mult))
            ch.link(nc.vector.tensor_tensor(num[:, :, 0:MD], num[:, :, 0:MD], mnorm[:, :, :], ALU.mult))
            signal(nc.vector.tensor_tensor(num[:, :, 0:MD], num[:, :, 0:MD],
                                           tokm[0:NS, last, C_OG:C_OG + 512].rearrange("p (h v) -> p h v", h=MH), ALU.mult),
                   "gated_ready")
            ve.wait_ge(S["turned"], 1)
            nc.vector.tensor_copy(hm[:, :, TP:T], psum[:, 0, 0:MH * NS].rearrange("p (h t) -> p h t", h=MH))


HEADS_AT_ONCE = 2
BRANCHES = CMP, SEL, SLIDE = range(3)
NCMP = TP // CB
RAWW = 1920
STRIPW, CSTRIPW, WSTRIPW = TP, NCMP + 4 * (NTILE - 1), WIN + P


def compress_setup(nc, A, K, N, zn, psum):
    with stage(nc, "cmp") as (ctx, sem):
        sb = lambda n, s: ctx.enter_context(nc.sbuf_tensor("cmp_" + n, s, F32))
        pe_in = sb("pe", [P, 2, CB])
        act_out = sb("act", [P, 2, NCMP])
        rel, onehot, rmask, rv = sb("rel", [NBUCKET, NH]), sb("onehot", [NBUCKET, 2048]), sb("rmask", [NH, 2048]), sb("rv", [NH, 2048])
        loaded, layer1_ready, bias_ready, act_ready, layer2_ready, copied, vec_ready, vec_masked, stored = map(sem, (
            "loaded", "layer1_ready", "bias_ready", "act_ready", "layer2_ready", "copied", "vec_ready", "vec_masked", "stored"))
        block = ctx.enter_context(nc.Block())

        @block.sync
        def _(sp):
            for dst, src in ((N["w1"][:, :, :, :], A["cmp_w1"]), (N["w2"][:, :, :], A["cmp_w2"]), (pe_in[:, :, :], A["cmp_pe"]),
                             (rel[:, :], A["rel"]), (onehot[:, :], A["onehot"]), (rmask[:, :], A["rmask"])):
                sp.dma_start(dst, src).then_inc(loaded, 16)
            sp.wait_ge(vec_masked, 4)
            sp.dma_start(A["bias_vec"], rv[:, :]).then_inc(stored, 16)
            sp.wait_ge(stored, 16)

        @block.tensor
        def _(pe):
            pe.wait_ge(loaded, 96)
            for q in range(4):
                nc.tensor.matmul(psum[0:NH, q, :], rel[:, :], onehot[:, q * 512:(q + 1) * 512], start=True, stop=True
                                 ).then_inc(vec_ready, 1)
            for kv in range(2):
                for j in range(CB):
                    nc.tensor.matmul(psum[:, 4 + kv, 0:1], N["w1"][:, kv, j, :], pe_in[:, kv, j:j + 1],
                                     start=(j == 0), stop=(j == CB - 1))
                for j in range(CB):
                    last = nc.tensor.matmul(psum[:, 6 + kv, 0:NCMP], N["w1"][:, kv, j, :],
                                            zn[:, Q_KCMP - 4 + kv, j:TP:CB], start=(j == 0), stop=(j == CB - 1))
            last.then_inc(layer1_ready, 1)
            pe.wait_ge(act_ready, 2)
            nc.tensor.matmul(psum[:, 4, 0:NCMP], N["w2"][:, 0, :], act_out[:, 0, :], start=True, stop=True)
            nc.tensor.matmul(psum[0:NCMP, 5, 0:P], act_out[:, 1, :], N["w2"][:, 1, :], start=True, stop=True
                             ).then_inc(layer2_ready, 1)

        @block.vector
        def _(ve):
            ve.wait_ge(loaded, 96)
            for q in range(4):
                ve.wait_ge(vec_ready, q + 1)
                c = slice(q * 512, (q + 1) * 512)
                nc.vector.tensor_tensor(rv[:, c], psum[0:NH, q, :], rmask[:, c], ALU.add).then_inc(vec_masked, 1)
            ve.wait_ge(layer1_ready, 1)
            nc.vector.tensor_copy(N["pb"][:, :], psum[:, 4:6, 0]).then_inc(bias_ready, 1)
            ve.wait_ge(layer2_ready, 1)
            nc.vector.tensor_copy(N["kcmp"][:, :], psum[:, 4, 0:NCMP])
            nc.vector.tensor_copy(N["vcmp"][:, :], psum[0:NCMP, 5, 0:P])

        @block.scalar
        def _(act):
            act.wait_ge(bias_ready, 1)
            for kv in range(2):
                nc.scalar.activation(act_out[:, kv, :], psum[:, 6 + kv, 0:NCMP], ACT.Gelu_apprx_tanh,
                                     bias=N["pb"][:, kv:kv + 1]).then_inc(act_ready, 1)


def nsa_prompt(nc, A, K, N, zn, tokn, gates, on, psum):
    units = [(br, t, g) for t in range(NTILE) for br in BRANCHES for g in range(HEADS_AT_ONCE)]
    U = len(units)

    def keys(u):
        br, t, _ = units[u]
        if br == CMP:
            return 0, NCMP
        first = 0 if br == SEL else max(0, t - WIN // P)
        return first, (t + 1 - first) * P

    turns = []
    for u in range(U):
        nt = -(-keys(u)[1] // P)
        turns += [(u, k, min(4, nt - k)) for k in range(0, nt, 4)]
    by_unit = [[q for q, x in enumerate(turns) if x[0] == u] for u in range(U)]
    NTURN = [(len(turns) + 1) // 2, len(turns) // 2]

    with stage(nc, "nsap") as (ctx, sem):
        sb = lambda n, s: ctx.enter_context(nc.sbuf_tensor("np_" + n, s, F32))
        raw = sb("raw", [P, 2, RAWW])
        strip, wstrip, cstrip = sb("strip", [P, 2, STRIPW]), sb("wstrip", [P, 2, WSTRIPW]), sb("cstrip", [P, 2, CSTRIPW])
        qs = sb("qs", [P, TP])
        pb = sb("p", [P, 2, TP])
        pt = sb("pt", [P, 2, NTILE, P])
        o = sb("o", [P, NTILE, 2, HD])
        gp = sb("gp", [P, 2, NTILE, 3])
        mx, nm, sums, rs = sb("mx", [P, 2]), sb("nm", [P, 2]), sb("sums", [P, 2]), sb("rs", [P, 2])
        names = ("raw_loaded", "flipped", "setup_ready", "scores_ready", "logits_ready", "max_ready", "exp_ready", "turn_ready",
                 "copied_act", "copied_dve", "pv_ready", "out_ready", "o_turned", "on_stored", "steps", "strips_copied")
        S = {n: sem(n) for n in names}
        block = ctx.enter_context(nc.Block())

        @block.sync
        def _(sp):
            for p in range(NPAIR):
                if p:
                    sp.wait_ge(S["flipped"], p)
                for g in range(2):
                    h = p + NPAIR * g
                    src = A["bias_vec"][h:h + 1, 0:RAWW]
                    src = bass.AP(tensor=src.tensor, offset=src.offset, ap=[[1, P], [1, RAWW]])
                    sp.dma_start(raw[:, g, :], src).then_inc(S["raw_loaded"], 16)

        @block.tensor
        def _(pe):
            def scores(i, u):
                br, t, g = units[u]
                k0, nk = keys(u)
                if u >= 2:
                    pe.wait_ge(S["logits_ready"], i * U + u - 1)
                hs = slice(g * HD, (g + 1) * HD)
                src = {CMP: N["kcmp"], SEL: zn[:, Q_KSEL - 4, :], SLIDE: zn[:, Q_KWIN - 4, :]}[br]
                for c in range(0, nk, 512):
                    w = min(512, nk - c)
                    last = nc.tensor.matmul(psum[:, 2 * (u % 2) + c // 512, 0:w], qs[hs, t * P:(t + 1) * P],
                                            src[hs, k0 * P + c:k0 * P + c + w], start=True, stop=True)
                last.then_inc(S["scores_ready"], 1)

            def turn(i, u):
                pe.wait_ge(S["exp_ready"], i * U + u + 1)
                nk = keys(u)[1]
                for q in by_unit[u]:
                    _, k, n = turns[q]
                    if q >= 2:
                        pe.wait_ge(S[("copied_act", "copied_dve")[q % 2]], i * NTURN[q % 2] + q // 2)
                    for j in range(n):
                        w = min(P, nk - (k + j) * P)
                        last = nc.tensor.transpose(psum[0:w, 4 + q % 2, j * P:(j + 1) * P],
                                                   pb[:, u % 2, (k + j) * P:(k + j) * P + w], K["ident"][:, :])
                    last.then_inc(S["turn_ready"], 1)

            def values(i, u):
                br, t, g = units[u]
                k0, nk = keys(u)
                for q in by_unit[u]:
                    pe.wait_ge(S[("copied_act", "copied_dve")[q % 2]], i * NTURN[q % 2] + q // 2 + 1)
                if u >= 2:
                    pe.wait_ge(S["out_ready"], i * U + u - 1)
                nt = -(-nk // P)
                for j in range(nt):
                    if br == CMP:
                        v = N["vcmp"][0:NCMP, g * HD:(g + 1) * HD]
                    else:
                        c = (N_VSEL if br == SEL else N_VWIN) + g * HD
                        v = tokn[:, k0 + j, c:c + HD]
                    w = min(P, nk)
                    last = nc.tensor.matmul(psum[:, 6 + u % 2, 0:HD], pt[0:w, u % 2, j, :], v, start=(j == 0), stop=(j == nt - 1))
                last.then_inc(S["pv_ready"], 1)

            with pe.Fori(0, NPAIR) as i:
                pe.wait_ge(S["on_stored"], 2 * i + 2)
                pe.wait_ge(S["raw_loaded"], 32 * i + 32)
                for g in range(2):
                    for c in range(2):
                        nc.tensor.matmul(psum[:, 2 * g + c, :], K["flip"][:, :], raw[:, g, c * 512:(c + 1) * 512], start=True, stop=True)
                for g in range(2):
                    last = nc.tensor.matmul(psum[:, 4, g * 64:g * 64 + CSTRIPW], K["flip"][:, :],
                                            raw[:, g, CB - 1:CB - 1 + CB * (CSTRIPW - 1) + 1:CB], start=True, stop=True)
                last.then_inc(S["flipped"], 1)
                pe.wait_ge(S["setup_ready"], i + 1)
                scores(i, 0)
                for u in range(U):
                    if u + 1 < U:
                        scores(i, u + 1)
                    turn(i, u)
                    values(i, u)
                pe.wait_ge(S["out_ready"], i * U + U)
                for t in range(NTILE):
                    last = nc.tensor.transpose(psum[:, 4 + t // 4, (t % 4) * P:(t % 4 + 1) * P],
                                               o[:, t, :, :].rearrange("p g d -> p (g d)"), K["ident"][:, :])
                last.then_inc(S["o_turned"], 1)

        def copy_turned(eng, sem_name, i, q, ready):
            u, k, n = turns[q]
            nk = keys(u)[1]
            w = min(P, nk)
            eng.wait_ge(S["turn_ready"], i * len(turns) + q + 1)
            return pt[0:w, u % 2, k:k + n, :], psum[0:w, 4 + q % 2, 0:n * P].rearrange("p (n q) -> p n q", n=n)

        @block.scalar
        def _(act):
            def exp(i, u):
                nk = keys(u)[1]
                act.wait_ge(S["max_ready"], i * U + u + 1)
                nc.scalar.activation(pb[:, u % 2, 0:nk], pb[:, u % 2, 0:nk], ACT.Exp, bias=nm[:, u % 2:u % 2 + 1],
                                     accum_out=sums[:, u % 2:u % 2 + 1]).then_inc(S["exp_ready"], 1)

            with act.Fori(0, NPAIR) as i:
                exp(i, 0)
                for u in range(U):
                    if u + 1 < U:
                        exp(i, u + 1)
                    for q in by_unit[u]:
                        if q % 2 == 0:
                            if u >= 2:
                                act.wait_ge(S["pv_ready"], i * U + u - 1)
                            dst, src = copy_turned(act, "copied_act", i, q, None)
                            nc.scalar.activation(dst, src, ACT.Copy).then_inc(S["copied_act"], 1)

        @block.vector
        def _(ve):
            STEPS = 2 * U + 5

            def logits(i, u, ch):
                br, t, g = units[u]
                k0, nk = keys(u)
                if br == CMP:
                    bias = cstrip[:, g, 4 * (NTILE - 1 - t):4 * (NTILE - 1 - t) + nk]
                elif br == SEL or t < WIN // P:
                    bias = strip[:, g, (NTILE - 1 - t) * P:TP]
                else:
                    bias = wstrip[:, g, :]
                ve.wait_ge(S["scores_ready"], i * U + u + 1)
                if u >= 2:
                    ve.wait_ge(S["turn_ready"], i * len(turns) + by_unit[u - 2][-1] + 1)
                x = pb[:, u % 2, 0:nk]
                s = psum[:, 2 * (u % 2):2 * (u % 2) + 2, :].rearrange("p a b -> p (a b)")[:, 0:nk]
                nc.vector.tensor_tensor(x, s, bias, ALU.add).then_inc(S["logits_ready"], 1)
                ve.wait_ge(S["logits_ready"], i * U + u + 1)
                if u >= 2:
                    ve.wait_ge(S["exp_ready"], i * U + u - 1)
                nc.vector.tensor_reduce(nm[:, u % 2:u % 2 + 1], x, AX.X, ALU.max, negate=True).then_inc(S["max_ready"], 1)

            ve.sem_inc(S["on_stored"], 2)
            with ve.Fori(0, NPAIR) as i:
                ch = Chain(ve, S["steps"], i * STEPS)
                nc.vector.tensor_scalar(qs[:, :], zn[:, ds(i, 1), 0:TP].rearrange("p a t -> p (a t)"), CMP_SCALE, None, ALU.mult)
                for g in range(2):
                    ch.link(nc.vector.tensor_copy(gp[:, g, :, :], gates[:, 0:NTILE, ds(3 * (i + NPAIR * g), 3)]))
                for g in range(2):
                    ch.link(nc.vector.tensor_tensor(gp[:, g, 0, CMP:CMP + 1], gp[:, g, 0, CMP:CMP + 1], K["seen"][:, :], ALU.mult))
                ve.wait_ge(S["flipped"], i + 1)
                for g in range(2):
                    full = psum[:, 2 * g:2 * g + 2, :].rearrange("p a b -> p (a b)")
                    nc.vector.tensor_copy(strip[:, g, :], full)
                    nc.vector.tensor_copy(wstrip[:, g, P:WSTRIPW], full[:, TP - WIN:TP])
                    nc.vector.tensor_tensor(wstrip[:, g, 0:P], full[:, TP - WSTRIPW:TP - WIN], K["wmask"][:, :], ALU.add)
                nc.vector.tensor_copy(cstrip[:, :, :], psum[:, 4, 0:128].rearrange("p (g x) -> p g x", g=2)[:, :, 0:CSTRIPW]
                                      ).then_inc(S["setup_ready"], 1)
                ve.wait_ge(S["setup_ready"], i + 1)
                logits(i, 0, ch)
                for u in range(U):
                    br, t, g = units[u]
                    if u + 1 < U:
                        logits(i, u + 1, ch)
                    for q in by_unit[u]:
                        if q % 2 == 1:
                            if u >= 2:
                                ve.wait_ge(S["pv_ready"], i * U + u - 1)
                            dst, src = copy_turned(ve, "copied_dve", i, q, None)
                            nc.vector.tensor_copy(dst, src).then_inc(S["copied_dve"], 1)
                    r = rs[:, u % 2:u % 2 + 1]
                    ve.wait_ge(S["exp_ready"], i * U + u + 1)
                    ch.link(nc.vector.reciprocal(r, sums[:, u % 2:u % 2 + 1]))
                    ch.link(nc.vector.tensor_tensor(r, r, gp[:, g, t, br:br + 1], ALU.mult))
                    ve.wait_ge(S["pv_ready"], i * U + u + 1)
                    x = psum[:, 6 + u % 2, 0:HD]
                    if br == CMP:
                        nc.vector.tensor_scalar(o[:, t, g, :], x, r, None, ALU.mult).then_inc(S["out_ready"], 1)
                    else:
                        nc.vector.scalar_tensor_tensor(out=o[:, t, g, :], in0=x, scalar=r, in1=o[:, t, g, :],
                                                       op0=ALU.mult, op1=ALU.add).then_inc(S["out_ready"], 1)
                ve.wait_ge(S["o_turned"], i + 1)
                for c in range(2):
                    nc.vector.tensor_scalar(on[:, ds(i, 1), c * 512:(c + 1) * 512].rearrange("p a t -> p (a t)"),
                                            psum[:, 4 + c, :], 1.0, None, ALU.mult).then_inc(S["on_stored"], 1)
                ch.link(nc.vector.tensor_copy(mx[:, :], rs[:, :]))
                assert ch.n == 2 * U + 5, ch.n


def compress_sample(nc, A, K, N, pages, psum):
    with stage(nc, "cmps") as (ctx, sem):
        sb = lambda n, s: ctx.enter_context(nc.sbuf_tensor("cs_" + n, s, F32))
        kv_in = sb("kv", [P, 2, NPAGE, 2 * PAGE])
        act_out = sb("act", [P, 2, P])
        loaded = [sem("loaded0"), sem("loaded1")]
        layer1_ready, act_ready, layer2_ready, copied = map(sem, ("layer1_ready", "act_ready", "layer2_ready", "copied"))
        block = ctx.enter_context(nc.Block())
        NB = PAST // CB

        @block.sync
        def _(sp):
            def load(i, j):
                with sp.Fori(0, NPAGE) as p:
                    page = sp.value_load(pages[0:1, ds(((2 * i if i is not None else 0) + j) * NPAGE + p, 1)], min_val=0, max_val=N["n_pool"] - 1)
                    if i is not None:
                        sp.wait_ge(layer1_ready, 2 * i + j - 1)
                    sp.dma_start(kv_in[:, j, ds(p, 1), :].rearrange("p a x -> p (a x)"),
                                 A["pool"][ds(page, 1), :, 0:2 * PAGE].rearrange("a p x -> (a p) x")).then_inc(loaded[j], 16)

            for j in range(2):
                load(None, j)
            with sp.Fori(1, NSEQ // 2) as i:
                for j in range(2):
                    load(i, j)

        @block.tensor
        def _(pe):
            with pe.Fori(0, NSEQ // 2) as i:
                for j in range(2):
                    pe.wait_ge(loaded[j], 16 * NPAGE * i + 16 * NPAGE)
                    pe.wait_ge(copied, 2 * i + j + 1)
                    for kv in range(2):
                        for r in range(CB):
                            last = nc.tensor.matmul(psum[:, kv, 0:NB], N["w1"][:, kv, r, :],
                                                    kv_in[:, j, :, kv * PAGE + r:(kv + 1) * PAGE:CB],
                                                    start=(r == 0), stop=(r == CB - 1))
                    last.then_inc(layer1_ready, 1)
                    pe.wait_ge(act_ready, 4 * i + 2 * j + 2)
                    nc.tensor.matmul(psum[:, 2, 0:NB], N["w2"][:, 0, :], act_out[:, 0, :], start=True, stop=True)
                    nc.tensor.matmul(psum[:, 3, 0:P], act_out[:, 1, :], N["w2"][:, 1, :], start=True, stop=True
                                     ).then_inc(layer2_ready, 1)

        @block.scalar
        def _(act):
            with act.Fori(0, NSEQ // 2) as i:
                for j in range(2):
                    act.wait_ge(layer1_ready, 2 * i + j + 1)
                    for kv in range(2):
                        nc.scalar.activation(act_out[:, kv, :], psum[:, kv, 0:NB], ACT.Gelu_apprx_tanh,
                                             bias=N["pb"][:, kv:kv + 1]).then_inc(act_ready, 1)

        @block.vector
        def _(ve):
            ve.sem_inc(copied, 1)
            with ve.Fori(0, NSEQ // 2) as i:
                for j in range(2):
                    ve.wait_ge(layer2_ready, 2 * i + j + 1)
                    nc.vector.tensor_scalar(N["kc"][:, ds(2 * i + j, 1), :].rearrange("p a x -> p (a x)"), psum[:, 2, 0:NB],
                                            1.0, None, ALU.mult)
                    nc.vector.tensor_scalar(N["vc"][:, ds(2 * i + j, 1), :].rearrange("p a x -> p (a x)"), psum[:, 3, 0:P],
                                            1.0, None, ALU.mult).then_inc(copied, 1)


CMPC, TAILC = 1024, 1152
BW = TAILC + NS


def nsa_sample(nc, A, O, K, N, zn, tokn, gates, pages, on, psum):
    with stage(nc, "nsas") as (ctx, sem):
        sb = lambda n, s: ctx.enter_context(nc.sbuf_tensor("ns_" + n, s, F32))
        qf, qz = sb("qf", [P, 2, P]), sb("qz", [P, NSEQ, P])
        relq, onehot, delta = sb("relq", [P, NH]), sb("onehot", [P, BW]), sb("delta", [P, TS])
        relr = sb("relr", [P, 4, NH, TS])
        bias = sb("bias", [P, BW])
        group, tmask, wmask = sb("group", [P, P]), sb("tmask", [P, 2, NS]), sb("wmask", [P, TS])
        gr = sb("gr", [P, 2, 3])
        kbuf, vbuf = sb("kbuf", [P, 2, 4, 4 * PAGE]), sb("vbuf", [P, 2, 4, 4 * PAGE])
        win = sb("win", [P, 4, 2, WIN])
        ss = sb("ss", [P, PAST + NS])
        ws = sb("ws", [P, WIN + NS])
        pc, pcg = sb("pc", [P, P]), sb("pcg", [P, P])
        imp, top, bmask = sb("imp", [P, SB + 1]), sb("top", [P, 16]), sb("bmask", [P, SB + 1])
        nm, sums, rs = sb("nm", [P, 3]), sb("sums", [P, 3]), sb("rs", [P, 3])
        pt = sb("pt", [P, 2, 4, P])
        names = ("loaded", "win_loaded0", "win_loaded1", "gates_stored", "gates_loaded", "k_loaded0", "k_loaded1", "v_loaded0", "v_loaded1",
                 "q_ready", "rel_ready", "bias_ready", "bias_copied", "score_ready", "score_drained", "pc_ready", "max_ready",
                 "exp_ready", "scale_ready", "probs_ready", "turn_ready", "turn_copied", "pv_ready", "out_copied", "steps",
                 "kept", "gpass")
        S = {n: sem(n) for n in names}
        block = ctx.enter_context(nc.Block())
        CMPJ, WINJ, WTAIL, IMP, SEL0, STAIL = 0, 1, 2, 3, 4, 12
        NJ = 13
        TC, TW, TWT, TS0, TST, NT = 0, 1, 2, 3, 11, 12
        NBLK = PAST // SB

        @block.sync
        def _(sp):
            for dst, src in ((relq[:, :], A["relq"]), (onehot[:, :], A["onehot_s"]), (delta[:, :], A["delta"]),
                             (group[:, :], A["group"]), (tmask[:, :, :], A["tmask"]), (wmask[:, :], A["wmask_s"])):
                sp.dma_start(dst, src).then_inc(S["loaded"], 16)
            sp.dma_start(A["gate_rows"], gates[0:NS, NTILE, :]).then_inc(S["gates_stored"], 16)
            sp.dma_start(O["winp"], A["winp"]).then_inc(S["kept"], 16)
            sp.dma_start(O["zkv"], zn[:, 4:8, :]).then_inc(S["kept"], 16)
            sp.dma_start(O["tkv"], tokn[:, :, 0:2 * P]).then_inc(S["kept"], 16)
            sp.wait_ge(S["gates_stored"], 16)
            for q in range(NSEQ):
                src = A["gate_rows"][q * TS:(q + 1) * TS, :].rearrange("q (h r) -> h q r", r=3)
                for h in range(NH):
                    r = (q % 4) * 32 + h * TS
                    sp.dma_start(gr[r:r + TS, q // 4, :], src[h, :, :]).then_inc(S["gates_loaded"], 16)
            for s in range(2):
                if s:
                    sp.wait_ge(S["pv_ready"], TWT + 1)
                for b in range(4):
                    sp.dma_start(win[:, b, :, :], A["winp"][4 * s + b]).then_inc(S[f"win_loaded{s}"], 16)

                def load(buf, at, done, j, c):
                    for b in range(4):
                        for p in range(4):
                            n = (4 * s + b) * NPAGE + p
                            page = sp.value_load(pages[0:1, ds(4 * c + n, 1)], min_val=0, max_val=N["n_pool"] - 1)
                            sp.dma_start(buf[:, j, b, p * PAGE:(p + 1) * PAGE],
                                         A["pool"][ds(page, 1), :, at:at + PAGE].rearrange("a p x -> (a p) x")).then_inc(done[j], 16)

                kd, vd = (S["k_loaded0"], S["k_loaded1"]), (S["v_loaded0"], S["v_loaded1"])
                with sp.Fori(0, 4) as i:
                    for j in range(2):
                        if s == 0:
                            sp.wait_ge(S["score_ready"], 2 * i + j + SEL0 - 1)
                        else:
                            sp.wait_ge(S["score_ready"], 2 * i + j + NJ + SEL0 - 1)
                        load(kbuf, 2 * PAGE, kd, j, 2 * i + j)
                with sp.Fori(0, 4) as i:
                    for j in range(2):
                        sp.wait_ge(S["pv_ready"], 2 * i + j + s * NT + TS0 - 1)
                        load(vbuf, 3 * PAGE, vd, j, 2 * i + j)
            sp.wait_ge(S["kept"], 48)

        @block.tensor
        def _(pe):
            pe.wait_ge(S["rel_ready"], 1)
            for n, c in enumerate(range(0, BW, 512)):
                w = min(512, BW - c)
                last = nc.tensor.matmul(psum[:, 5 + n, 0:w], relr[:, :, :, :].rearrange("p b h q -> p (b h q)"),
                                        onehot[:, c:c + w], start=True, stop=True)
            last.then_inc(S["bias_ready"], 1)
            pe.wait_ge(S["q_ready"], 1)
            for s in range(2):
                def job(n):
                    n += s * NJ
                    if n >= 2:
                        pe.wait_ge(S["score_drained"], n - 1)
                    return psum[:, n % 2, :]

                def per_sequence(n, rhs, w):
                    out = job(n)
                    for b in range(4):
                        last = nc.tensor.matmul(out[:, 0:w], qz[:, 4 * s + b, :], rhs(b), start=(b == 0), stop=(b == 3))
                    last.then_inc(S["score_ready"], 1)

                per_sequence(CMPJ, lambda b: N["kc"][:, 4 * s + b, :], P)
                pe.wait_ge(S[f"win_loaded{s}"], 64)
                per_sequence(WINJ, lambda b: win[:, b, 0, :], WIN)
                nc.tensor.matmul(job(WTAIL)[:, 0:NS], qf[:, s, :], zn[:, Q_KWIN - 4, TP:T], start=True, stop=True
                                 ).then_inc(S["score_ready"], 1)
                out = job(IMP)
                pe.wait_ge(S["pc_ready"], s + 1)
                nc.tensor.matmul(out[:, 0:P], group[:, :], pc[:, :], start=True, stop=True).then_inc(S["score_ready"], 1)
                for c in range(8):
                    pe.wait_ge(S[f"k_loaded{c % 2}"], 256 * (4 * s + c // 2 + 1))
                    per_sequence(SEL0 + c, lambda b: kbuf[:, c % 2, b, :], 4 * PAGE)
                nc.tensor.matmul(job(STAIL)[:, 0:NS], qf[:, s, :], zn[:, Q_KSEL - 4, TP:T], start=True, stop=True
                                 ).then_inc(S["score_ready"], 1)

                def turn(n, src, w, k):
                    n += s * NT
                    if n >= 2:
                        pe.wait_ge(S["turn_copied"], n - 1)
                    for j in range(k):
                        last = nc.tensor.transpose(psum[0:w, 2 + n % 2, j * P:(j + 1) * P], src[:, j * w:(j + 1) * w], K["ident"][:, :])
                    last.then_inc(S["turn_ready"], 1)

                def products(n, w, k, value):
                    first, last_job = n == TC, n == TST
                    n += s * NT
                    pe.wait_ge(S["turn_copied"], n + 1)
                    if first:
                        pe.wait_ge(S["out_copied"], s + 1)
                    for j in range(k):
                        for b in range(4):
                            last = nc.tensor.matmul(psum[:, 4 + b, 0:32], value(b, j), pt[0:w, n % 2, j, b * 32:(b + 1) * 32],
                                                    start=first and j == 0, stop=last_job and j == k - 1)
                    last.then_inc(S["pv_ready"], 1)

                pe.wait_ge(S["probs_ready"], 3 * s + 1)
                turn(TC, pcg[:, :], P, 1)
                products(TC, P, 1, lambda b, j: N["vc"][:, 4 * s + b, :])
                pe.wait_ge(S["probs_ready"], 3 * s + 2)
                turn(TW, ws[:, 0:WIN], P, 4)
                products(TW, P, 4, lambda b, j: win[:, b, 1, j * P:(j + 1) * P])
                turn(TWT, ws[:, WIN:WIN + NS], NS, 1)
                products(TWT, NS, 1, lambda b, j: tokn[0:NS, NTILE, N_VWIN:N_VWIN + P])
                pe.wait_ge(S["probs_ready"], 3 * s + 3)
                turn(TS0, ss[:, 0:4 * P], P, 4)
                for c in range(8):
                    if c < 7:
                        turn(TS0 + c + 1, ss[:, (c + 1) * 4 * P:(c + 2) * 4 * P], P, 4)
                    pe.wait_ge(S[f"v_loaded{c % 2}"], 256 * (4 * s + c // 2 + 1))
                    products(TS0 + c, P, 4, lambda b, j: vbuf[:, c % 2, b, j * P:(j + 1) * P])
                turn(TST, ss[:, PAST:PAST + NS], NS, 1)
                products(TST, NS, 1, lambda b, j: tokn[0:NS, NTILE, N_VSEL:N_VSEL + P])

        @block.scalar
        def _(act):
            for s in range(2):
                def exp(k, x):
                    act.wait_ge(S["max_ready"], 3 * s + k + 1)
                    nc.scalar.activation(x, x, ACT.Exp, bias=nm[:, k:k + 1], accum_out=sums[:, k:k + 1]).then_inc(S["exp_ready"], 1)

                def gate(k, dst, x):
                    act.wait_ge(S["scale_ready"], 3 * s + k + 1)
                    act.wait_ge(S["exp_ready"], 3 * s + k + 1)
                    nc.scalar.activation(dst, x, ACT.Copy, scale=rs[:, k:k + 1]).then_inc(S["probs_ready"], 1)

                def copy(n, w, k):
                    n += s * NT
                    act.wait_ge(S["turn_ready"], n + 1)
                    if n >= 2:
                        act.wait_ge(S["pv_ready"], n - 1)
                    nc.scalar.activation(pt[0:w, n % 2, 0:k, :], psum[0:w, 2 + n % 2, 0:k * P].rearrange("p (k r) -> p k r", k=k),
                                         ACT.Copy).then_inc(S["turn_copied"], 1)

                exp(0, pc[:, :])
                exp(1, ws[:, :])
                gate(0, pcg[:, :], pc[:, :])
                gate(1, ws[:, :], ws[:, :])
                exp(2, ss[:, :])
                gate(2, ss[:, :], ss[:, :])
                copy(TC, P, 1)
                copy(TW, P, 4)
                copy(TWT, NS, 1)
                for c in range(8):
                    copy(TS0 + c, P, 4)
                copy(TST, NS, 1)

        @block.vector
        def _(ve):
            ch = Chain(ve, S["steps"])
            ve.wait_ge(S["loaded"], 96)
            dst = relr[:, :, :, :].rearrange("p b h q -> p b (h q)")
            ch.link(nc.vector.tensor_copy(relr[:, 0, :, :], relq[:, :].unsqueeze(2).to_broadcast([P, NH, TS])))
            ch.link(nc.vector.tensor_tensor(relr[:, 0, :, :], relr[:, 0, :, :], delta[:, :].unsqueeze(1).to_broadcast([P, NH, TS]), ALU.mult))
            nc.vector.tensor_copy(relr[:, 1:4, :, :].rearrange("p b h q -> p b (h q)"),
                                  relr[:, 0, :, :].rearrange("p h q -> p (h q)").unsqueeze(1).to_broadcast([P, 3, NH * TS])
                                  ).then_inc(S["rel_ready"], 1)
            nc.vector.memset(qz[:, :, :], 0.0)
            ch.link(nc.vector.memset(qf[:, :, :], 0.0))
            for s in range(2):
                for g in range(2):
                    half = slice(g * HD, (g + 1) * HD)
                    for b in range(4):
                        q = 4 * s + b
                        last = nc.vector.tensor_scalar(
                            qf[half, s, b * 32 + g * 16:b * 32 + (g + 1) * 16].rearrange("p (i q) -> p i q", q=TS),
                            zn[half, 0:NPAIR, TP + q * TS:TP + (q + 1) * TS], CMP_SCALE, None, ALU.mult)
            ch.link(last)
            for q in range(NSEQ):
                c = slice((q % 4) * 32, (q % 4 + 1) * 32)
                last = nc.vector.tensor_copy(qz[:, q, c], qf[:, q // 4, c])
            last.then_inc(S["q_ready"], 1)
            ve.wait_ge(S["bias_ready"], 1)
            for n, c in enumerate(range(0, BW, 512)):
                w = min(512, BW - c)
                last = nc.vector.tensor_copy(bias[:, c:c + w], psum[:, 5 + n, 0:w])
            last.then_inc(S["out_copied"], 1)
            ve.wait_ge(S["out_copied"], 1)
            ve.wait_ge(S["gates_loaded"], 16 * 64)
            for s in range(2):
                def job(n):
                    n += s * NJ
                    ve.wait_ge(S["score_ready"], n + 1)
                    return psum[:, n % 2, :]

                def most(k, x):
                    nc.vector.tensor_reduce(nm[:, k:k + 1], x, AX.X, ALU.max, negate=True).then_inc(S["max_ready"], 1)

                def scale(k, g):
                    ve.wait_ge(S["exp_ready"], 3 * s + k + 1)
                    ch.link(nc.vector.reciprocal(rs[:, k:k + 1], sums[:, k:k + 1]))
                    if k == 0:
                        ch.link(nc.vector.tensor_scalar(pc[:, :], pc[:, :], rs[:, 0:1], None, ALU.mult))
                        nc.vector.tensor_copy(rs[:, 0:1], gr[:, s, 0:1]).then_inc(S["scale_ready"], 1)
                    else:
                        nc.vector.tensor_tensor(rs[:, k:k + 1], rs[:, k:k + 1], gr[:, s, g:g + 1], ALU.mult).then_inc(S["scale_ready"], 1)

                def drained(ins, n):
                    ins.then_inc(S["score_drained"], 1)
                    ve.wait_ge(S["score_drained"], s * NJ + n + 1)

                if s:
                    ve.wait_ge(S["turn_ready"], NT)
                x = job(CMPJ)
                drained(nc.vector.tensor_tensor(pc[:, :], x[:, 0:P], bias[:, CMPC:CMPC + P], ALU.add), CMPJ)
                most(0, pc[:, :])
                x = job(WINJ)
                drained(nc.vector.tensor_tensor(ws[:, 0:WIN], x, bias[:, WIN:2 * WIN], ALU.add), WINJ)
                ch.link(nc.vector.tensor_tensor(ws[:, 0:TS], ws[:, 0:TS], wmask[:, :], ALU.add))
                x = job(WTAIL)
                drained(nc.vector.tensor_tensor(ws[:, WIN:WIN + NS], x[:, 0:NS], bias[:, TAILC:BW], ALU.add), WTAIL)
                ch.link(nc.vector.tensor_tensor(ws[:, WIN:WIN + NS], ws[:, WIN:WIN + NS], tmask[:, s, :], ALU.add))
                most(1, ws[:, :])
                scale(0, 0)
                nc.vector.memset(imp[:, NBLK:NBLK + 1], 1.0e4).then_inc(S["pc_ready"], 1)
                x = job(IMP)
                drained(nc.vector.tensor_reduce(imp[:, 0:NBLK], x[:, 0:P].rearrange("p (b c) -> p b c", c=SB // CB), AX.X, ALU.add), IMP)
                ch.link(nc.vector.memset(imp[:, 0:1], 1.0e4))
                for r in range(TOPK // 8):
                    ch.link(nc.vector.max(top[:, 8 * r:8 * r + 8], imp[:, :]))
                    ch.link(nc.vector.match_replace(imp[:, :], top[:, 8 * r:8 * r + 8], imp[:, :], -4.0))
                ch.link(nc.vector.tensor_scalar(bmask[:, :], imp[:, :], -2.0, NEG, ALU.is_gt, ALU.mult))
                for c in range(8):
                    x = job(SEL0 + c)
                    out = ss[:, c * 512:(c + 1) * 512].rearrange("p (b t) -> p b t", t=SB)
                    mask = bmask[:, 8 * c:8 * c + 8].unsqueeze(2).to_broadcast([P, 8, SB])
                    x3 = x.rearrange("p (b t) -> p b t", t=SB)
                    if c < 6:
                        drained(nc.vector.scalar_tensor_tensor(out=out, in0=x3, scalar=bias[:, 0:1], in1=mask,
                                                               op0=ALU.add, op1=ALU.add), SEL0 + c)
                    else:
                        drained(nc.vector.tensor_tensor(ss[:, c * 512:(c + 1) * 512], x, bias[:, (c - 6) * 512:(c - 5) * 512],
                                                        ALU.add), SEL0 + c)
                        ch.link(nc.vector.tensor_tensor(out, out, mask, ALU.add))
                x = job(STAIL)
                drained(nc.vector.tensor_tensor(ss[:, PAST:PAST + NS], x[:, 0:NS], bias[:, TAILC:BW], ALU.add), STAIL)
                ch.link(nc.vector.tensor_tensor(ss[:, PAST:PAST + NS], ss[:, PAST:PAST + NS], tmask[:, s, :], ALU.add))
                scale(1, 2)
                most(2, ss[:, :])
                scale(2, 1)
                ve.wait_ge(S["pv_ready"], (s + 1) * NT)
                for g in range(2):
                    half = slice(g * HD, (g + 1) * HD)
                    for b in range(4):
                        q = 4 * s + b
                        last = nc.vector.tensor_copy(on[half, 0:NPAIR, TP + q * TS:TP + (q + 1) * TS],
                                                     psum[half, 4 + b, g * 16:(g + 1) * 16].rearrange("p (i q) -> p i q", q=TS))
                last.then_inc(S["out_copied"], 1)


def merge(nc, A, h, hm, on, dst, acc):
    SPAN = 2 * (KD + 4) * P
    with stage(nc, "merge") as (ctx, sem):
        ring = ctx.enter_context(nc.sbuf_tensor("mg_ring", [P, 2, SPAN], F32))
        sg = ctx.enter_context(nc.sbuf_tensor("mg_gate", [P, 2, T], F32))
        part = ctx.enter_context(nc.sbuf_tensor("mg_part", [P, T], F32))
        w_loaded = [sem("w_loaded0"), sem("w_loaded1")]
        gate_ready, branch_ready, gate_drained, branch_drained, parts = map(
            sem, ("gate_ready", "branch_ready", "gate_drained", "branch_drained", "parts"))
        block = ctx.enter_context(nc.Block())
        n_chunks = D // P

        @block.sync
        def _(sp):
            for j in range(2):
                sp.dma_start(ring[:, j, :], A["w_merge"][j]).then_inc(w_loaded[j], 16)
            with sp.Fori(1, n_chunks // 2) as i:
                for j in range(2):
                    sp.wait_ge(branch_ready, 4 * i + 2 * j - 2)
                    sp.dma_start(ring[:, j, :], A["w_merge"][ds(2 * i + j, 1), :, :].rearrange("a p k -> p (a k)")
                                 ).then_inc(w_loaded[j], 16)

        @block.tensor
        def _(pe):
            with pe.Fori(0, n_chunks // 2) as i:
                for j in range(2):
                    pe.wait_ge(w_loaded[j], 16 * i + 16)
                    for r, (branch, x) in enumerate(((0, hm), (1, on))):
                        base = r * (KD + 4) * P
                        pe.wait_ge(gate_drained, 4 * i + 2 * j + r + 1)
                        for g in range(NG):
                            for k in range(KD):
                                last = nc.tensor.matmul(acc[:, g, 0:GW], ring[:, j, base + k * P:base + (k + 1) * P],
                                                        h[:, k, g * GW:(g + 1) * GW], start=(k == 0), stop=(k == KD - 1))
                        last.then_inc(gate_ready, 1)
                        base += KD * P
                        pe.wait_ge(branch_drained, 4 * i + 2 * j + r + 2)
                        for g in range(NG):
                            for k in range(4):
                                last = nc.tensor.matmul(acc[:, 3 + g, 0:GW], ring[:, j, base + k * P:base + (k + 1) * P],
                                                        x[:, k, g * GW:(g + 1) * GW], start=(k == 0), stop=(k == 3))
                        last.then_inc(branch_ready, 1)

        @block.scalar
        def _(act):
            act.sem_inc(gate_drained, 1)
            with act.Fori(0, n_chunks) as i:
                for r in range(2):
                    act.wait_ge(gate_ready, 2 * i + r + 1)
                    if r == 0:
                        act.wait_ge(branch_drained, 2 * i + 1)
                    else:
                        act.wait_ge(parts, i + 1)
                    nc.scalar.activation(sg[:, r, :].rearrange("p (g t) -> p g t", g=NG), acc[:, 0:NG, 0:GW], ACT.Sigmoid
                                         ).then_inc(gate_drained, 1)

        @block.vector
        def _(ve):
            ve.sem_inc(branch_drained, 2)
            ve.sem_inc(parts, 1)
            with ve.Fori(0, n_chunks) as i:
                for r in range(2):
                    ve.wait_ge(gate_drained, 2 * i + r + 2)
                    ve.wait_ge(branch_ready, 2 * i + r + 1)
                    gate = sg[:, r, :].rearrange("p (g t) -> p g t", g=NG)
                    if r == 0:
                        ve.wait_ge(parts, i + 1)
                    dst_r = part[:, :].rearrange("p (g t) -> p g t", g=NG) if r == 0 else gate
                    nc.vector.tensor_tensor(dst_r, acc[:, NG:2 * NG, 0:GW], gate, ALU.mult).then_inc(branch_drained, 1)
                    ve.wait_ge(branch_drained, 2 * i + r + 3)
                nc.vector.tensor_tensor(dst[:, ds(i, 1), :].rearrange("p a t -> p (a t)"), part[:, :], sg[:, 1, :], ALU.add
                                        ).then_inc(parts, 1)


def cross_prompt(nc, K, qx, mk, mv, ox, psum):
    with stage(nc, "xp") as (ctx, sem):
        sb = lambda n, s: ctx.enter_context(nc.sbuf_tensor("xp_" + n, s, F32))
        q = sb("q", [P, KD, P])
        p, pt = sb("p", [P, 2, MEM]), sb("pt", [P, 2, 2, P])
        nm, sums = sb("nm", [P, 2]), sb("sums", [P, 2])
        names = ("q_ready", "score_ready", "max_ready", "exp_ready", "inverted", "probs_ready", "turn_ready", "turn_copied",
                 "pv_ready", "out_ready")
        S = {n: sem(n) for n in names}
        block = ctx.enter_context(nc.Block())
        DC = KD // XH

        @block.tensor
        def _(pe):
            def scores(i, h):
                for c in range(DC):
                    last = nc.tensor.matmul(psum[:, h % 2, 0:MEM], q[:, DC * h + c, :], mk[:, DC * h + c, :],
                                            start=(c == 0), stop=(c == DC - 1))
                last.then_inc(S["score_ready"], 1)

            with pe.Fori(0, NTILE) as i:
                pe.wait_ge(S["q_ready"], i + 1)
                scores(i, 0)
                for h in range(XH):
                    if h + 1 < XH:
                        if h >= 1:
                            pe.wait_ge(S["exp_ready"], XH * i + h)
                        scores(i, h + 1)
                    pe.wait_ge(S["probs_ready"], XH * i + h + 1)
                    for m in range(2):
                        last = nc.tensor.transpose(psum[:, 2 + h % 2, m * P:(m + 1) * P], p[:, h % 2, m * P:(m + 1) * P], K["ident"][:, :])
                    last.then_inc(S["turn_ready"], 1)
                    pe.wait_ge(S["turn_copied"], XH * i + h + 1)
                    for c in range(DC):
                        for m in range(2):
                            last = nc.tensor.matmul(psum[:, 4 + h % 2, c * P:(c + 1) * P], mv[:, m, (DC * h + c) * P:(DC * h + c + 1) * P],
                                                    pt[:, h % 2, m, :], start=(m == 0), stop=(m == 1))
                    last.then_inc(S["pv_ready"], 1)

        @block.scalar
        def _(act):
            with act.Fori(0, NTILE) as i:
                for h in range(XH):
                    act.wait_ge(S["max_ready"], XH * i + h + 1)
                    nc.scalar.activation(p[:, h % 2, :], psum[:, h % 2, 0:MEM], ACT.Exp, bias=nm[:, h % 2:h % 2 + 1],
                                         accum_out=sums[:, h % 2:h % 2 + 1]).then_inc(S["exp_ready"], 1)
                    act.wait_ge(S["turn_ready"], XH * i + h + 1)
                    nc.scalar.activation(pt[:, h % 2, :, :], psum[:, 2 + h % 2, 0:2 * P].rearrange("p (m q) -> p m q", m=2), ACT.Copy
                                         ).then_inc(S["turn_copied"], 1)

        @block.vector
        def _(ve):
            with ve.Fori(0, NTILE) as i:
                nc.vector.tensor_scalar(q[:, :, :], qx[:, :, ds(i * P, P)], float(D // XH) ** -0.5, None, ALU.mult
                                        ).then_inc(S["q_ready"], 1)

                def most(h):
                    ve.wait_ge(S["score_ready"], XH * i + h + 1)
                    nc.vector.tensor_reduce(nm[:, h % 2:h % 2 + 1], psum[:, h % 2, 0:MEM], AX.X, ALU.max, negate=True
                                            ).then_inc(S["max_ready"], 1)

                most(0)
                for h in range(XH):
                    s = sums[:, h % 2:h % 2 + 1]
                    ve.wait_ge(S["exp_ready"], XH * i + h + 1)
                    nc.vector.reciprocal(s, s).then_inc(S["inverted"], 1)
                    ve.wait_ge(S["inverted"], XH * i + h + 1)
                    nc.vector.tensor_scalar(p[:, h % 2, :], p[:, h % 2, :], s, None, ALU.mult).then_inc(S["probs_ready"], 1)
                    if h + 1 < XH:
                        most(h + 1)
                    ve.wait_ge(S["pv_ready"], XH * i + h + 1)
                    nc.vector.tensor_scalar(ox[:, DC * h:DC * (h + 1), ds(i * P, P)],
                                            psum[:, 4 + h % 2, 0:DC * P].rearrange("p (c q) -> p c q", c=DC), 1.0, None, ALU.mult
                                            ).then_inc(S["out_ready"], 1)
                ve.wait_ge(S["out_ready"], XH * i + XH)


def cross_sample(nc, A, K, qx, ox, psum):
    with stage(nc, "xs") as (ctx, sem):
        sb = lambda n, s: ctx.enter_context(nc.sbuf_tensor("xs_" + n, s, F32))
        qz = sb("qz", [P, NSEQ, KD, P])
        kv = sb("kv", [P, 2, KD * MEM])
        p, pt = sb("p", [P, MEM]), sb("pt", [P, 2, P])
        nm, sums = sb("nm", [P, 1]), sb("sums", [P, 1])
        cleared, q_ready, k_used, score_ready, max_ready, exp_ready, inverted, probs_ready, turn_ready, turn_copied, v_used = map(sem, (
            "cleared", "q_ready", "k_used", "score_ready", "max_ready", "exp_ready", "inverted", "probs_ready", "turn_ready",
            "turn_copied", "v_used"))
        loaded = [sem("loaded0"), sem("loaded1")]
        block = ctx.enter_context(nc.Block())
        DC = KD // XH

        @block.sync
        def _(sp):
            for n in range(2 * NSEQ):
                if n >= 2:
                    used, at = (k_used, n - 1) if n - 2 < NSEQ else (v_used, n - 1 - NSEQ)
                    sp.wait_ge(used, at)
                src = A["mem_k"][n] if n < NSEQ else A["mem_v"][n - NSEQ]
                sp.dma_start(kv[:, n % 2, :], src).then_inc(loaded[n % 2], 16)

        @block.gpsimd
        def _(pool):
            nc.gpsimd.memset(qz[:, :, :, :], 0.0).then_inc(cleared, 1)

        @block.vector
        def _(ve):
            ve.wait_ge(cleared, 1)
            for b in range(NSEQ):
                for h in range(XH):
                    r = b * XH * TS + h * TS
                    nc.vector.tensor_scalar(qz[:, b, DC * h:DC * (h + 1), r:r + TS],
                                            qx[:, DC * h:DC * (h + 1), TP + b * TS:TP + (b + 1) * TS],
                                            float(D // XH) ** -0.5, None, ALU.mult).then_inc(q_ready, 1)
            ve.wait_ge(k_used, NSEQ)
            nc.vector.tensor_reduce(nm[:, :], psum[:, 0, 0:MEM], AX.X, ALU.max, negate=True).then_inc(max_ready, 1)
            ve.wait_ge(exp_ready, 1)
            nc.vector.reciprocal(sums[:, :], sums[:, :]).then_inc(inverted, 1)
            ve.wait_ge(inverted, 1)
            nc.vector.tensor_scalar(p[:, :], p[:, :], sums[:, 0:1], None, ALU.mult).then_inc(probs_ready, 1)
            ve.wait_ge(v_used, NSEQ)
            nc.vector.tensor_copy(ox[:, :, TP:T], psum[:, 2, 0:KD * NS].rearrange("p (c t) -> p c t", c=KD))

        @block.scalar
        def _(act):
            act.wait_ge(max_ready, 1)
            nc.scalar.activation(p[:, :], psum[:, 0, 0:MEM], ACT.Exp, bias=nm[:, 0:1], accum_out=sums[:, 0:1]).then_inc(exp_ready, 1)
            act.wait_ge(turn_ready, 1)
            nc.scalar.activation(pt[:, :, :], psum[:, 1, 0:2 * P].rearrange("p (m q) -> p m q", m=2), ACT.Copy).then_inc(turn_copied, 1)

        @block.tensor
        def _(pe):
            pe.wait_ge(q_ready, NSEQ * XH)
            for b in range(NSEQ):
                pe.wait_ge(loaded[b % 2], 16 * (b // 2 + 1))
                for c in range(KD):
                    last = nc.tensor.matmul(psum[:, 0, 0:MEM], qz[:, b, c, :], kv[:, b % 2, c * MEM:(c + 1) * MEM],
                                            start=(b == 0 and c == 0), stop=(b == NSEQ - 1 and c == KD - 1))
                last.then_inc(k_used, 1)
            pe.wait_ge(probs_ready, 1)
            for m in range(2):
                last = nc.tensor.transpose(psum[:, 1, m * P:(m + 1) * P], p[:, m * P:(m + 1) * P], K["ident"][:, :])
            last.then_inc(turn_ready, 1)
            pe.wait_ge(turn_copied, 1)
            for b in range(NSEQ):
                n = NSEQ + b
                pe.wait_ge(loaded[n % 2], 16 * (n // 2 + 1))
                for c in range(KD):
                    r = b * XH * TS + (c // DC) * TS
                    for m in range(2):
                        last = nc.tensor.matmul(psum[:, 2, c * NS + b * TS:c * NS + (b + 1) * TS],
                                                kv[:, n % 2, m * D + c * P:m * D + (c + 1) * P], pt[:, m, r:r + TS],
                                                start=(m == 0), stop=(m == 1))
                last.then_inc(v_used, 1)


def ffn(nc, A, O, h, mid, ring, acc):
    with stage(nc, "ffn") as (ctx, sem):
        sb = lambda n, s: ctx.enter_context(nc.sbuf_tensor("ff_" + n, s, F32))
        taps = sb("taps", [P, KF, 4])
        state = sb("state", [P, KF, NSEQ, 2])
        pstate = sb("pstate", [P, KF, 2])
        tap = sb("tap", [P, 4])
        u, cv = sb("u", [P, T]), sb("cv", [P, T])
        us, cs = sb("us", [P, NSEQ, 2 + TS]), sb("cs", [P, NSEQ, TS])
        names = ("loaded", "wu_loaded", "wg_loaded", "u_ready", "u_copied", "gate_ready", "conv_ready", "gelu_ready", "mid_ready",
                 "steps", "stored")
        S = {n: sem(n) for n in names}
        block = ctx.enter_context(nc.Block())

        @block.sync
        def _(sp):
            sp.dma_start(taps[:, :, :], A["f_conv"]).then_inc(S["loaded"], 16)
            sp.dma_start(state[:, :, :, :], A["f_state"]).then_inc(S["loaded"], 16)
            sp.dma_start(ring[:, 0, :], A["f_wu"][0]).then_inc(S["wu_loaded"], 16)
            sp.dma_start(ring[:, 1, :], A["f_wg"][0]).then_inc(S["wg_loaded"], 16)
            with sp.Fori(1, KF) as i:
                sp.wait_ge(S["u_ready"], i)
                sp.dma_start(ring[:, 0, :], A["f_wu"][ds(i, 1), :, :].rearrange("a p k -> p (a k)")).then_inc(S["wu_loaded"], 16)
                sp.wait_ge(S["gate_ready"], i)
                sp.dma_start(ring[:, 1, :], A["f_wg"][ds(i, 1), :, :].rearrange("a p k -> p (a k)")).then_inc(S["wg_loaded"], 16)
            sp.wait_ge(S["mid_ready"], KF + 1)
            sp.dma_start(O["p_fconv"], pstate[:, :, :]).then_inc(S["stored"], 16)
            sp.dma_start(O["s_fconv"], state[:, :, :, :]).then_inc(S["stored"], 16)
            sp.wait_ge(S["stored"], 32)

        @block.tensor
        def _(pe):
            with pe.Fori(0, KF) as i:
                for j, (wl, ready, free) in enumerate((("wu_loaded", "u_ready", "u_copied"), ("wg_loaded", "gate_ready", "mid_ready"))):
                    pe.wait_ge(S[wl], 16 * i + 16)
                    pe.wait_ge(S[free], i + 1)
                    for g in range(NG):
                        for k in range(KD):
                            last = nc.tensor.matmul(acc[:, 3 * j + g, 0:GW], ring[:, j, k * P:(k + 1) * P],
                                                    h[:, k, g * GW:(g + 1) * GW], start=(k == 0), stop=(k == KD - 1))
                    last.then_inc(S[ready], 1)

        @block.scalar
        def _(act):
            act.sem_inc(S["u_copied"], 1)
            with act.Fori(0, KF) as i:
                act.wait_ge(S["u_ready"], i + 1)
                act.wait_ge(S["mid_ready"], i + 1)
                nc.scalar.activation(u[:, :].rearrange("p (g t) -> p g t", g=NG), acc[:, 0:NG, 0:GW], ACT.Copy
                                     ).then_inc(S["u_copied"], 1)
                act.wait_ge(S["conv_ready"], i + 1)
                nc.scalar.activation(cv[:, :], cv[:, :], ACT.Gelu_apprx_tanh).then_inc(S["gelu_ready"], 1)

        @block.vector
        def _(ve):
            STEPS = 7
            ve.wait_ge(S["loaded"], 32)
            ve.sem_inc(S["mid_ready"], 1)
            with ve.Fori(0, KF) as i:
                ch = Chain(ve, S["steps"], i * STEPS)
                nc.vector.tensor_copy(us[:, :, 0:2], state[:, ds(i, 1), :, :].rearrange("p a b t -> p (a b) t"))
                ch.link(nc.vector.tensor_copy(tap[:, :], taps[:, ds(i, 1), :].rearrange("p a k -> p (a k)")))
                ve.wait_ge(S["u_copied"], i + 2)
                nc.vector.tensor_scalar(cv[:, 0:TP], u[:, 0:TP], tap[:, 2:3], tap[:, 3:4], ALU.mult, ALU.add)
                ch.link(nc.vector.tensor_copy(us[:, :, 2:2 + TS], u[:, TP:T].rearrange("p (b t) -> p b t", t=TS)))
                nc.vector.tensor_scalar(pstate[:, ds(i, 1), :].rearrange("p a t -> p (a t)"), u[:, TP - 2:TP], 1.0, None, ALU.mult)
                nc.vector.tensor_scalar(state[:, ds(i, 1), :, :].rearrange("p a b t -> p (a b) t"), us[:, :, TS:TS + 2], 1.0, None, ALU.mult)
                ch.link(nc.vector.tensor_scalar(cs[:, :, :], us[:, :, 2:2 + TS], tap[:, 2:3], tap[:, 3:4], ALU.mult, ALU.add))
                for k in (1, 0):
                    d = 2 - k
                    ch.link(nc.vector.scalar_tensor_tensor(out=cv[:, d:TP], in0=u[:, 0:TP - d], scalar=tap[:, k:k + 1],
                                                           in1=cv[:, d:TP], op0=ALU.mult, op1=ALU.add))
                    ch.link(nc.vector.scalar_tensor_tensor(out=cs[:, :, :], in0=us[:, :, k:k + TS], scalar=tap[:, k:k + 1],
                                                           in1=cs[:, :, :], op0=ALU.mult, op1=ALU.add))
                nc.vector.tensor_copy(cv[:, TP:T].rearrange("p (b t) -> p b t", t=TS), cs[:, :, :]).then_inc(S["conv_ready"], 1)
                ve.wait_ge(S["gelu_ready"], i + 1)
                ve.wait_ge(S["gate_ready"], i + 1)
                nc.vector.tensor_tensor(mid[:, ds(i, 1), :].rearrange("p a (g t) -> p (a g) t", g=NG), acc[:, NG:2 * NG, 0:GW],
                                        cv[:, :].rearrange("p (g t) -> p g t", g=NG), ALU.mult).then_inc(S["mid_ready"], 1)
                ve.wait_ge(S["mid_ready"], i + 2)
                assert ch.n == STEPS, ch.n


def transfer(nc, name, pairs):
    with stage(nc, name) as (ctx, sem):
        done = sem("done")
        block = ctx.enter_context(nc.Block())

        @block.sync
        def _(sp):
            for dst, src in pairs:
                sp.dma_start(dst, src).then_inc(done, 16)
            sp.wait_ge(done, 16 * len(pairs))


def build(nc, A, O):
    with ExitStack() as ctx:
        K = {}

        def sb(name, shape, c=ctx):
            return c.enter_context(nc.sbuf_tensor(name, shape, F32))

        psum = ctx.enter_context(nc.psum_tensor("psum", [P, 8, 512], F32))
        consts = sb("consts", [P, N_CONST])
        for n, (a, w) in CONST_AT.items():
            K[n] = consts[:, a:a + w]
        gains = sb("gains", [P, 6, KD])
        ring = sb("ring", [P, 2, KD * P])
        pages = ctx.enter_context(nc.sbuf_tensor("pages", [1, NSEQ * NPAGE], I32))
        with stage(nc, "load") as (c, sem):
            loaded = sem("loaded")
            block = c.enter_context(nc.Block())

            @block.sync
            def _(sp):
                sp.dma_start(consts[:, :], A["consts"]).then_inc(loaded, 16)
                sp.dma_start(gains[:, :, :], A["gains"]).then_inc(loaded, 16)
                sp.dma_start(pages[:, :], A["page_table"]).then_inc(loaded, 16)
                sp.wait_ge(loaded, 48)

        mix = ctx.enter_context(ExitStack())
        hm = sb("hm", [P, 4, T], mix)
        zm = sb("zm", [P, 4, T], mix)
        late = ctx.enter_context(ExitStack())
        zn = sb("zn", [P, NFEAT - 4, T], late)
        tokn = sb("tokn", [P, NTILE + 1, N_END], late)
        branch_gates = sb("branch_gates", [P, NTILE + 1, 3 * NH], late)

        early = ctx.enter_context(ExitStack())
        tokm = sb("tokm", [P, NTILE + 1, C_OG + 512], early)
        with ExitStack() as c:
            h = sb("h", [P, KD, T], c)
            with stage(nc, "load_x") as (c2, sem):
                loaded = sem("loaded")
                block = c2.enter_context(nc.Block())

                @block.sync
                def _(sp):
                    sp.dma_start(h[:, :, :], A["x"]).then_inc(loaded, 16)
                    sp.wait_ge(loaded, 16)

                @block.vector
                def _(ve):
                    nc.vector.memset(tokn[:, NTILE, :], 0.0)
            with ExitStack() as c2:
                sq = sb("sq", [P, 2, T], c2)
                rstd = sb("rstd", [P, T], c2)
                rms_norm(nc, "norm0", K, h, gains[:, 0, :], h, sq, rstd, psum[:, 0:3, :])
            project(nc, "inm", A["w_in"][0:4], 4, KD, h, zm, ring, psum)
            project(nc, "inn", A["w_in"][4:12], 8, KD, h, zn, ring, psum)
            project_tokens(nc, "int", A["w_tok"], h, [(0, 512, tokm[:, :, 0:512]), (512, 512, tokm[:, :, 512:1024]),
                                                      (1024, TOKW - 1024, tokn)], psum)
            with stage(nc, "spill") as (c2, sem):
                stored = sem("stored")
                block = c2.enter_context(nc.Block())

                @block.sync
                def _(sp):
                    sp.dma_start(A["h_spill"], h[:, :, :]).then_inc(stored, 16)
                    sp.wait_ge(stored, 16)

        with ExitStack() as c:
            n = NTILE + 1
            sm = {m: sb("s_" + m, [P, n, w], c) for m, w in (("lf", MH), ("b", MH), ("a", MH), ("tmp", MH))}
            sm["g"] = branch_gates
            conv_mlstm(nc, A, O, K, zm, hm)
            gates(nc, A, K, tokm, tokn, sm, psum)
            mlstm(nc, A, O, K, hm, tokm, sm, psum)
            mlstm_sample(nc, A, O, K, hm, tokm, sm, psum)
        early.close()
        with ExitStack() as c:
            N = {"kcmp": sb("kcmp", [P, NCMP], c), "vcmp": sb("vcmp", [NCMP, P], c),
                 "kc": sb("kc", [P, NSEQ, P], c), "vc": sb("vc", [P, NSEQ, P], c), "n_pool": A["pool"].shape[0]}
            with ExitStack() as c2:
                N.update({"w1": sb("w1", [P, 2, CB, P], c2), "w2": sb("w2", [P, 2, P], c2), "pb": sb("pb", [P, 2], c2)})
                compress_setup(nc, A, K, N, zn, psum)
                compress_sample(nc, A, K, N, pages, psum)
            nsa_prompt(nc, A, K, N, zn, tokn, branch_gates, zm, psum)
            nsa_sample(nc, A, O, K, N, zn, tokn, branch_gates, pages, zm, psum)

        late.close()
        with ExitStack() as c:
            dst = sb("merged", [P, KD, T], c)
            h = sb("h2", [P, KD, T], c)
            transfer(nc, "reload", [(h[:, :, :], A["h_spill"])])
            merge(nc, A, h, hm, zm, dst, psum)
            project(nc, "wout", A["w_out"], KD, KD, dst, h, ring, psum)
            transfer(nc, "spill_y", [(A["h_spill"], h[:, :, :])])
        mix.close()
        x = sb("x", [P, KD, T])
        h = sb("h3", [P, KD, T])

        def norms(name, g, last=False):
            with ExitStack() as c:
                sq, rstd = sb(name + "_sq", [P, 2, T], c), sb(name + "_rstd", [P, T], c)
                rms_norm(nc, name + "a", K, h, gains[:, g, :], x, sq, rstd, psum[:, 0:3, :], add=True)
                if not last:
                    rms_norm(nc, name + "b", K, x, gains[:, g + 1, :], h, sq, rstd, psum[:, 0:3, :])

        transfer(nc, "reload_y", [(h[:, :, :], A["h_spill"]), (x[:, :, :], A["x"])])
        norms("norm1", 1)
        with ExitStack() as c:
            qx = sb("qx", [P, KD, T], c)
            project(nc, "xq", A["x_wq"], KD, KD, h, qx, ring, psum)
            with ExitStack() as c2:
                mk, mv = sb("mk", [P, KD, MEM], c2), sb("mv", [P, 2, D], c2)
                with ExitStack() as c3:
                    mem = sb("mem", [P, KD, MEM], c3)
                    transfer(nc, "memory", [(mem[:, :, :], A["mem"])])
                    project(nc, "xk", A["x_wk"], KD, KD, mem, mk, ring, psum, width=MEM, groups=1)
                    project_tokens(nc, "xv", A["x_wv"], mem, [(0, 512, mv[:, :, 0:512]), (512, 512, mv[:, :, 512:1024])], psum, (P, P))
                transfer(nc, "memory_out", [(O["mk"], mk[:, :, :]), (O["mv"], mv[:, :, :])])
                cross_prompt(nc, K, qx, mk, mv, h, psum)
            cross_sample(nc, A, K, qx, h, psum)
            project(nc, "xo", A["x_wo"], KD, KD, h, qx, ring, psum)
            transfer(nc, "xo_spill", [(A["h_spill"], qx[:, :, :])])
        transfer(nc, "xo_reload", [(h[:, :, :], A["h_spill"])])
        norms("norm2", 3)
        with ExitStack() as c:
            mid = sb("mid", [P, KF, T], c)
            ffn(nc, A, O, h, mid, ring, psum)
            with ExitStack() as c2:
                wide = sb("wide_ring", [P, 2, KF * P], c2)
                project(nc, "down", A["f_wd"], KD, KF, mid, h, wide, psum)
        norms("norm3", 5, last=True)
        transfer(nc, "store", [(O["y"], x[:, :, :])])




def shape_constants():
    i = np.arange(P)
    c = {}
    c["ident"] = np.eye(P)
    c["ones"] = np.ones((P, P))
    c["tri"] = (i[:, None] <= i[None, :]) * 1.0
    same = (i[:, None] // TS == i[None, :] // TS) & (i[:, None] < NS) & (i[None, :] < NS)
    c["stri"] = same * c["tri"]
    c["last"] = (i[:, None] == P - 1) * np.ones((1, P))
    seq = np.arange(NSEQ)
    c["slast"] = same * (i[:, None] % TS == TS - 1)
    c["slast8"] = (i[:, None] == seq[None, :] * TS + TS - 1) * 1.0
    c["sseq8"] = (i[:, None] // TS == seq[None, :]) * 1.0
    c["scausal"] = np.where(c["stri"].T > 0, 0.0, NEG)[:, 0:NS]
    c["scausal_t"] = np.where(c["stri"] > 0, 0.0, NEG)[:, 0:NS]
    c["flip"] = np.eye(P)[::-1]
    c["seen"] = (i[:, None] >= CB - 1) * 1.0
    c["wmask"] = np.where(i[None, :] <= i[:, None], NEG, 0.0)
    c["causal"] = np.where(i[None, :] <= i[:, None], 0.0, NEG)
    c["causal_t"] = np.ascontiguousarray(c["causal"].T)
    return c


CONST = shape_constants()
CONST_AT, N_CONST = {}, 0
for _n, _v in CONST.items():
    CONST_AT[_n] = (N_CONST, _v.shape[1])
    N_CONST += _v.shape[1]


def chunked(w):
    k, m = w.shape
    return np.ascontiguousarray(w.reshape(k // P, P, m // P, P).transpose(2, 1, 0, 3)).reshape(m // P, P, k)


def feature_rows(a):
    return np.ascontiguousarray(a.reshape(a.shape[0], -1, P).transpose(2, 1, 0))


def lay_out(v):
    L = {}
    x = np.concatenate([v["x_prompt"].reshape(TP, D), v["x_sample"].reshape(NS, D)])
    L["x"] = feature_rows(x)
    L["consts"] = np.concatenate([CONST[n] for n in CONST_AT], axis=1).astype(np.float32)
    L["gains"] = np.ascontiguousarray(v["norms"][0].reshape(6, KD, P).transpose(2, 0, 1))
    w = v["w_in"][0]
    at, parts = 0, []
    for n in (512, 512, 4, 4, 512, 512, 256, 256, 256, 24, 1024, 1024):
        parts.append(w[:, at:at + n])
        at += n
    xm, val, ig, fg, og, qn, kvc, kvs, kvw, gn, ga, gb = parts
    pair = np.array([h * HD + e for i in range(NPAIR) for h in (i, NPAIR + i) for e in range(HD)])
    L["w_in"] = chunked(np.concatenate([xm, qn[:, pair], kvc, kvs[:, 0:128], kvw[:, 0:128]], axis=1))
    tok = np.concatenate([val, og, kvs[:, 128:], kvw[:, 128:], ig, fg, gn], axis=1)
    L["w_tok"] = np.ascontiguousarray(tok.reshape(KD, P, TOKW).transpose(1, 0, 2))
    L["m_conv"] = np.ascontiguousarray(np.concatenate([v["m_conv_w"][0], v["m_conv_b"]]).reshape(5, 4, P).transpose(2, 1, 0))
    L["m_state"] = np.ascontiguousarray(v["state_mlstm_conv"][0].reshape(NSEQ, 3, 4, P).transpose(3, 2, 0, 1))
    L["gate_b"] = v["m_gate_b"].reshape(8)
    L["m_wqk"] = np.ascontiguousarray(np.stack([v["m_wq"][0], v["m_wk"][0]]).transpose(2, 0, 1, 3))
    L["m_norm"] = v["m_norm"][0]
    dist = TP - 1 - np.arange(2048)
    L["onehot"] = (bias_buckets(dist)[None, :] == np.arange(NBUCKET)[:, None]).astype(np.float32)
    L["rmask"] = np.tile(np.where(dist >= 0, 0.0, NEG), (NH, 1)).astype(np.float32)
    L["rel"] = v["rel_bias"]
    w1 = v["cmp_w1"][0].reshape(2, CB, HD, HD)
    w2 = v["cmp_w2"][0]
    both = np.zeros((P, 2, CB, P), np.float32)
    both2 = np.zeros((P, 2, P), np.float32)
    for g in range(2):
        half = slice(g * HD, (g + 1) * HD)
        both[half, :, :, half] = w1.transpose(2, 0, 1, 3)
        both2[half, :, half] = w2.transpose(1, 0, 2)
    L["cmp_w1"], L["cmp_w2"] = both, both2
    pe = v["cmp_pe"][0].transpose(2, 0, 1)
    L["cmp_pe"] = np.ascontiguousarray(np.concatenate([pe, pe]))
    cache = v["cache_nsa_kv"][0].reshape(-1, PAGE, 4, P)
    pool = cache.transpose(0, 3, 2, 1).copy()
    pool[:, :, 3, :] = cache[:, :, 3, :]
    L["pool"] = pool.reshape(-1, P, 4 * PAGE)
    L["page_table"] = v["page_table"].reshape(1, NSEQ * NPAGE)
    w = v["cache_win_kv"][0].reshape(NSEQ, WIN, 2, P)
    winp = np.empty((NSEQ, P, 2, WIN), np.float32)
    winp[:, :, 0] = w[:, :, 0].transpose(0, 2, 1)
    winp[:, :, 1] = w[:, :, 1].reshape(NSEQ, 4, P, P).transpose(0, 2, 1, 3).reshape(NSEQ, P, WIN)
    L["winp"] = winp
    L["relq"] = np.tile(v["rel_bias"], (TS, 1))
    qd = np.arange(P) // NBUCKET
    near = PAST + qd[:, None] - (PAST - 1024 + np.arange(1024))[None, :]
    blocks = PAST + qd[:, None] - (np.arange(P) * CB + CB - 1)[None, :]
    tail = qd[:, None] - (np.arange(NS) % TS)[None, :]
    dist = np.concatenate([near, blocks, tail], axis=1)
    L["onehot_s"] = (bias_buckets(dist) == (np.arange(P) % NBUCKET)[:, None]).astype(np.float32)
    L["delta"] = (qd[:, None] == np.arange(TS)[None, :]).astype(np.float32)
    row = np.arange(P)
    rb, rg, rq = row // 32, row // 16 % 2, row % TS
    L["group"] = ((rb[:, None] == rb) & (rg[:, None] == rg) & (rq[:, None] == rq)).astype(np.float32)
    tok = np.arange(NS)
    ok = [(tok // TS == 4 * s + rb[:, None]) & (tok % TS <= rq[:, None]) for s in range(2)]
    L["tmask"] = np.where(np.stack(ok, 1), 0.0, NEG).astype(np.float32)
    L["wmask_s"] = np.where(np.arange(TS) <= rq[:, None], NEG, 0.0).astype(np.float32)
    ca, cb = chunked(ga), chunked(gb)
    um, un = chunked(v["w_up_m"][0]), chunked(v["w_up_n"][0][pair])
    L["w_merge"] = np.concatenate([ca, um, cb, un], axis=2)
    L["w_out"] = chunked(v["w_out"][0])
    L["x_wq"], L["x_wo"] = chunked(v["x_wq"][0]), chunked(v["x_wo"][0])
    L["mem"] = feature_rows(v["mem_prompt"][0])
    L["x_wk"] = chunked(v["x_wkv"][0][:, 0:D])
    L["x_wv"] = np.ascontiguousarray(v["x_wkv"][0][:, D:].reshape(KD, P, D).transpose(1, 0, 2))
    mem = v["cache_mem_kv"][0].reshape(NSEQ, MEM, 2, KD, P)
    L["mem_k"] = np.ascontiguousarray(mem[:, :, 0].transpose(0, 3, 2, 1)).reshape(NSEQ, P, KD * MEM)
    L["mem_v"] = np.ascontiguousarray(mem[:, :, 1].reshape(NSEQ, 2, P, D).transpose(0, 2, 1, 3)).reshape(NSEQ, P, 2 * D)
    L["f_wu"], L["f_wg"], L["f_wd"] = chunked(v["f_wu"][0]), chunked(v["f_wg"][0]), chunked(v["f_wd"][0])
    L["f_conv"] = np.ascontiguousarray(np.concatenate([v["f_conv_w"][0], v["f_conv_b"]]).reshape(4, KF, P).transpose(2, 1, 0))
    L["f_state"] = np.ascontiguousarray(v["state_ffn_conv"][0].reshape(NSEQ, 2, KF, P).transpose(3, 2, 0, 1))
    L["s_C0"] = np.ascontiguousarray(v["state_mlstm_C"][0].transpose(3, 0, 1, 2))
    L["s_n0"] = v["state_mlstm_n"][0]
    L["s_n0t"] = np.repeat(v["state_mlstm_n"][0], TS, axis=0)
    L["s_m0t"] = np.repeat(v["state_mlstm_m"][0], TS, axis=0)
    return L


SCRATCH = {"gate_rows": (NS, 3 * NH), "bias_vec": (NH, 2048), "h_spill": (P, KD, T)}
OUTS = {"y": (P, KD, T), "p_mconv": (P, 4, 3), "s_mconv": (P, 4, NSEQ, 3), "p_C": (P, MH, MD), "p_n": (P, MH),
        "p_m": (1, MH), "s_C": (P, NSEQ, MH, MD), "s_n": (NSEQ, MH, MD), "s_m": (NSEQ, MH), "winp": (NSEQ, P, 2, WIN),
        "mk": (P, KD, MEM), "mv": (P, 2, D), "p_fconv": (P, KF, 2), "s_fconv": (P, KF, NSEQ, 2), "zkv": (P, 4, T), "tkv": (P, NTILE + 1, 2 * P)}


def kernel(**inputs):
    import concourse.bacc as bacc
    from concourse.bass_utils import run_bass_kernel_spmd

    v = {n: np.asarray(a) for n, a in inputs.items()}
    nc = bacc.Bacc("TRN2", target_bir_lowering=False, num_devices=1)
    L = lay_out(v)
    A = {n: nc.dram_tensor("in_" + n, a.shape, mybir.dt.from_np(a.dtype), kind="ExternalInput").ap() for n, a in L.items()}
    for n, s in SCRATCH.items():
        A[n] = nc.dram_tensor(n, s, F32, kind="Internal").ap()
    O = {n: nc.dram_tensor("out_" + n, s, F32, kind="ExternalOutput").ap() for n, s in OUTS.items()}
    build(nc, A, O)
    r = run_bass_kernel_spmd(nc, [{"in_" + n: a for n, a in L.items()}], core_ids=[0]).results[0]
    R = {n: r["out_" + n] for n in OUTS}

    y = R["y"].transpose(2, 1, 0).reshape(T, D)
    kz, kt = R["zkv"].transpose(2, 1, 0), R["tkv"].transpose(1, 0, 2).reshape(-1, 2, P)[:T]
    rows = np.stack([kz[:, 0], kz[:, 1], kz[:, 2], kt[:, 0]], axis=1).reshape(T, 4, 2, HD)
    wnew = np.stack([kz[:, 3], kt[:, 1]], axis=1).reshape(T, 2, 2, HD)
    wold = np.stack([R["winp"][:, :, 0].transpose(0, 2, 1),
                     R["winp"][:, :, 1].reshape(NSEQ, P, 4, P).transpose(0, 2, 1, 3).reshape(NSEQ, WIN, P)], axis=2)
    swin = np.concatenate([wold.reshape(NSEQ, WIN, 2, 2, HD)[:, TS:], wnew[TP:].reshape(NSEQ, TS, 2, 2, HD)], axis=1)
    mkv = np.stack([R["mk"].transpose(2, 1, 0).reshape(MEM, D), R["mv"].transpose(1, 0, 2).reshape(MEM, D)], axis=1)
    fix = lambda a: np.ascontiguousarray(a)
    return tuple(fix(a) for a in (
        y[None, :TP], y[TP:].reshape(NSEQ, TS, D),
        rows[None, None, :TP], wnew[None, None, TP - WIN:TP],
        R["p_C"].transpose(1, 0, 2)[None, None], R["p_n"].T[None, None], R["p_m"][None],
        R["p_mconv"].transpose(2, 1, 0).reshape(1, 1, 3, MH * MD), R["p_fconv"].transpose(2, 1, 0).reshape(1, 1, 2, DFF),
        mkv.reshape(1, 1, MEM, 2, XH, D // XH),
        rows[TP:].reshape(1, NSEQ, TS, 4, 2, HD), swin[None],
        R["s_C"].transpose(1, 2, 3, 0)[None], R["s_n"][None], R["s_m"][None],
        R["s_mconv"].transpose(2, 3, 1, 0).reshape(1, NSEQ, 3, MH * MD), R["s_fconv"].transpose(2, 3, 1, 0).reshape(1, NSEQ, 2, DFF)))
```

```python
from contextlib import ExitStack, contextmanager

import concourse.bass as bass
import numpy as np
from concourse import mybir

F32 = mybir.dt.float32
I32 = mybir.dt.int32
ACT = mybir.ActivationFunctionType
ALU = mybir.AluOpType
AX = mybir.AxisListType
ds = bass.ds

P = 128
D = 1024
KD = D // P
TP = 1024
NTILE = TP // P
NSEQ, TS = 8, 4
NS = NSEQ * TS
T = TP + NS
NG = 3
GW = T // NG
EPS = 1e-6
MH, MD = 4, 128
NH, HD = 8, 64
NPAIR = NH // 2
CB = 32
SB = 64
TOPK = 16
WIN = 512
PAST, PAGE = 4096, 128
NPAGE = PAST // PAGE
NBUCKET, MAX_DIST = 32, 1024
MEM = 256
XH = 4
DFF = 2816
KF = DFF // P
NEG = -1.0e30
CMP_SCALE = float(HD) ** -0.5
C_V, C_OG = 0, 512
N_VSEL, N_VWIN, N_IG, N_FG, N_GN, N_END = 0, 128, 256, 260, 264, 288
TOKW = 1312
Q_XM, Q_QN, Q_KCMP, Q_VCMP, Q_KSEL, Q_KWIN = 0, 4, 8, 9, 10, 11
NFEAT = 12


class Chain:

    def __init__(self, eng, sem, base=0):
        self.eng, self.sem, self.base, self.n = eng, sem, base, 0

    def link(self, ins):
        self.n += 1
        ins.then_inc(self.sem, 1)
        self.eng.wait_ge(self.sem, self.base + self.n)


def bias_buckets(dist):
    d = np.maximum(dist, 0)
    exact = NBUCKET // 2
    ratio = np.log(np.maximum(d, 1).astype(np.float32) / np.float32(exact)) / np.float32(np.log(MAX_DIST / exact))
    large = np.minimum(exact + (ratio * np.float32(NBUCKET - exact)).astype(np.int32), NBUCKET - 1)
    return np.where(d < exact, d, large)


@contextmanager
def stage(nc, name):
    with ExitStack() as outer:
        used = []

        def sem(n):
            used.append(outer.enter_context(nc.semaphore(f"{name}_{n}")))
            return used[-1]

        with ExitStack() as ctx:
            yield ctx, sem
        for s in used:
            nc.sync.sem_clear(s)
        nc.all_engine_barrier(sem_only=True)




def rms_norm(nc, name, K, src, gain, out, sq, rstd, ss, load=None, clear=None):
    with stage(nc, name) as (ctx, sem):
        sq_ready, sq_used, out_ready, rstd_ready, mean_ready, root_ready = map(
            sem, ("sq_ready", "sq_used", "out_ready", "rstd_ready", "mean_ready", "root_ready"))
        loaded = [sem(f"loaded{c}") for c in range(KD)]
        block = ctx.enter_context(nc.Block())

        @block.sync
        def _(sp):
            for c in range(KD):
                sp.dma_start(src[:, c, :], load[:, c, :]).then_inc(loaded[c], 16)

        @block.gpsimd
        def _(pool):
            nc.gpsimd.memset(clear, 0.0)

        @block.scalar
        def _(act):
            for c in range(KD):
                act.wait_ge(loaded[c], 16)
                if c >= 2:
                    act.wait_ge(sq_used, c - 1)
                nc.scalar.activation(sq[:, c % 2, :], src[:, c, :], ACT.Square).then_inc(sq_ready, 1)
            act.wait_ge(mean_ready, 1)
            nc.scalar.activation(rstd[:, :], rstd[:, :], ACT.Sqrt).then_inc(root_ready, 1)

        @block.tensor
        def _(pe):
            for c in range(KD):
                pe.wait_ge(sq_ready, c + 1)
                for g in range(NG):
                    last = nc.tensor.matmul(ss[:, g, 0:GW], K["ones"][:, :], sq[:, c % 2, g * GW:(g + 1) * GW],
                                            start=(c == 0), stop=(c == KD - 1))
                last.then_inc(sq_used, 1)

        @block.vector
        def _(ve):
            ve.wait_ge(sq_used, KD)
            nc.vector.tensor_scalar(rstd[:, :].rearrange("p (g t) -> p g t", g=NG), ss[:, :, 0:GW], 1.0 / D, EPS,
                                    ALU.mult, ALU.add).then_inc(mean_ready, 1)
            ve.wait_ge(root_ready, 1)
            nc.vector.reciprocal(rstd[:, :], rstd[:, :]).then_inc(rstd_ready, 1)
            ve.wait_ge(rstd_ready, 1)
            for c in range(KD):
                nc.vector.scalar_tensor_tensor(out=out[:, c, :], in0=src[:, c, :], scalar=gain[:, c:c + 1],
                                               in1=rstd[:, :], op0=ALU.mult, op1=ALU.mult).then_inc(out_ready, 1)


def residual_norm(nc, name, K, src, gains, g, x, h, sq, rstd, ss, store=None):
    with stage(nc, name) as (ctx, sem):
        sq_ready, sq_used, rstd_ready, mean_ready, root_ready, scaled, summed, out_ready, stored = map(
            sem, ("sq_ready", "sq_used", "rstd_ready", "mean_ready", "root_ready", "scaled", "summed", "out_ready", "stored"))
        rounds = 1 if store is not None else 2
        block = ctx.enter_context(nc.Block())

        @block.sync
        def _(sp):
            if store is not None:
                for c in range(KD):
                    sp.wait_ge(summed, c + 1)
                    sp.dma_start(store[:, c, :], x[:, c, :]).then_inc(stored, 16)
                sp.wait_ge(stored, 16 * KD)

        @block.scalar
        def _(act):
            for r in range(rounds):
                for c in range(KD):
                    n = r * KD + c
                    if n >= 2:
                        act.wait_ge(sq_used, n - 1)
                    if r:
                        act.wait_ge(summed, c + 1)
                    nc.scalar.activation(sq[:, c % 2, :], (src, x)[r][:, c, :], ACT.Square).then_inc(sq_ready, 1)
                act.wait_ge(mean_ready, r + 1)
                nc.scalar.activation(rstd[:, r, :], rstd[:, r, :], ACT.Sqrt).then_inc(root_ready, 1)

        @block.tensor
        def _(pe):
            for n in range(rounds * KD):
                c = n % KD
                pe.wait_ge(sq_ready, n + 1)
                if n == KD:
                    pe.wait_ge(mean_ready, 1)
                for q in range(NG):
                    last = nc.tensor.matmul(ss[:, q, 0:GW], K["ones"][:, :], sq[:, c % 2, q * GW:(q + 1) * GW],
                                            start=(c == 0), stop=(c == KD - 1))
                last.then_inc(sq_used, 1)

        @block.vector
        def _(ve):
            for r in range(rounds):
                ve.wait_ge(sq_used, KD * (r + 1))
                nc.vector.tensor_scalar(rstd[:, r, :].rearrange("p (g t) -> p g t", g=NG), ss[:, :, 0:GW], 1.0 / D, EPS,
                                        ALU.mult, ALU.add).then_inc(mean_ready, 1)
                ve.wait_ge(root_ready, r + 1)
                nc.vector.reciprocal(rstd[:, r, :], rstd[:, r, :]).then_inc(rstd_ready, 1)
                ve.wait_ge(rstd_ready, r + 1)
                if r:
                    ve.wait_ge(summed, KD)
                for c in range(KD):
                    nc.vector.scalar_tensor_tensor(out=(src, h)[r][:, c, :], in0=(src, x)[r][:, c, :],
                                                   scalar=gains[:, g + r, c:c + 1], in1=rstd[:, r, :], op0=ALU.mult,
                                                   op1=ALU.mult).then_inc((scaled, out_ready)[r], 1)

        @block.gpsimd
        def _(pool):
            for c in range(KD):
                pool.wait_ge(scaled, c + 1)
                nc.gpsimd.tensor_tensor(x[:, c, :], x[:, c, :], src[:, c, :], ALU.add).then_inc(summed, 1)


def project(nc, name, w, n_chunks, kc, rhs, dst, ring, acc, width=T, groups=NG, aside=()):
    gw = width // groups
    with stage(nc, name) as (ctx, sem):
        w_loaded = [sem("w_loaded0"), sem("w_loaded1")]
        acc_ready, acc_free, moved = map(sem, ("acc_ready", "acc_free", "moved"))
        block = ctx.enter_context(nc.Block())
        assert n_chunks % 2 == 0

        @block.scalar
        def _(act):
            if aside:
                for to, src in aside:
                    act.dma_start(to, src).then_inc(moved, 16)
                act.wait_ge(moved, 16 * len(aside))

        @block.sync
        def _(sp):
            for j in range(2):
                sp.dma_start(ring[:, j, 0:kc * P], w[j]).then_inc(w_loaded[j], 16)
            with sp.Fori(1, n_chunks // 2) as i:
                for j in range(2):
                    sp.wait_ge(acc_ready, 2 * i + j - 1)
                    sp.dma_start(ring[:, j, 0:kc * P], w[ds(2 * i + j, 1), :, :].rearrange("a p k -> p (a k)")
                                 ).then_inc(w_loaded[j], 16)

        @block.tensor
        def _(pe):
            with pe.Fori(0, n_chunks // 2) as i:
                for j in range(2):
                    pe.wait_ge(w_loaded[j], 16 * i + 16)
                    pe.wait_ge(acc_free, 2 * i + j + 1)
                    for g in range(groups):
                        for k in range(kc):
                            last = nc.tensor.matmul(acc[:, 3 * j + g, 0:gw], ring[:, j, k * P:(k + 1) * P],
                                                    rhs[:, k, g * gw:(g + 1) * gw], start=(k == 0), stop=(k == kc - 1))
                    last.then_inc(acc_ready, 1)

        @block.vector
        def _(ve):
            ve.sem_inc(acc_free, 2)
            with ve.Fori(0, n_chunks // 2) as i:
                for j in range(2):
                    ve.wait_ge(acc_ready, 2 * i + j + 1)
                    out = dst[:, ds(2 * i + j, 1), :].rearrange("p a (g t) -> p (a g) t", g=groups)
                    nc.vector.tensor_scalar(out, acc[:, 3 * j:3 * j + groups, 0:gw], 1.0, None, ALU.mult
                                            ).then_inc(acc_free, 1)


def project_tokens(nc, name, w, h, outs, acc, sizes=(P,) * NTILE + (NS,)):
    with stage(nc, name) as (ctx, sem):
        wt = ctx.enter_context(nc.sbuf_tensor(name + "_wt", [P, 2, KD, max(n for _, n, _ in outs)], F32))
        w_loaded = [sem("w_loaded0"), sem("w_loaded1")]
        acc_ready, acc_free = map(sem, ("acc_ready", "acc_free"))
        block = ctx.enter_context(nc.Block())
        n = len(sizes)

        @block.sync
        def _(sp):
            for j, (c, width, _) in enumerate(outs):
                if j >= 2:
                    sp.wait_ge(acc_ready, (j - 1) * n)
                sp.dma_start(wt[:, j % 2, :, 0:width], w[:, :, c:c + width]).then_inc(w_loaded[j % 2], 16)

        @block.tensor
        def _(pe):
            for j, (_, width, _) in enumerate(outs):
                pe.wait_ge(w_loaded[j % 2], 16 * (j // 2 + 1))
                for t in range(n):
                    m = sizes[t]
                    u = j * n + t
                    if u >= 2:
                        pe.wait_ge(acc_free, u - 1)
                    for k in range(KD):
                        last = nc.tensor.matmul(acc[0:m, u % 2, 0:width], h[:, k, t * P:t * P + m],
                                                wt[:, j % 2, k, 0:width], start=(k == 0), stop=(k == KD - 1))
                    last.then_inc(acc_ready, 1)

        @block.vector
        def _(ve):
            for j, (c, width, dst) in enumerate(outs):
                for t in range(n):
                    m = sizes[t]
                    u = j * n + t
                    ve.wait_ge(acc_ready, u + 1)
                    nc.vector.tensor_copy(dst[0:m, t, :], acc[0:m, u % 2, 0:width]).then_inc(acc_free, 1)



def conv_mlstm(nc, A, O, K, zm, hm):
    with stage(nc, "mconv") as (ctx, sem):
        sb = lambda n, s: ctx.enter_context(nc.sbuf_tensor(n, s, F32))
        cw = sb("cw", [P, 4, 5])
        xs = sb("xs", [P, 4, NSEQ, 3 + TS])
        ys = sb("ys", [P, 4, NSEQ, TS])
        loaded, staged, steps, conv_ready, stored, act_done = map(
            sem, ("loaded", "staged", "steps", "conv_ready", "stored", "act_done"))
        block = ctx.enter_context(nc.Block())

        @block.sync
        def _(sp):
            sp.dma_start(cw[:, :, :], A["m_conv"]).then_inc(loaded, 16)
            sp.dma_start(xs[:, :, :, 0:3], A["m_state"]).then_inc(loaded, 16)
            sp.dma_start(O["p_mconv"], zm[:, :, TP - 3:TP]).then_inc(stored, 16)
            sp.wait_ge(staged, 4)
            sp.dma_start(O["s_mconv"], xs[:, :, :, TS:TS + 3]).then_inc(stored, 16)
            sp.wait_ge(stored, 32)

        @block.vector
        def _(ve):
            ve.wait_ge(loaded, 32)
            for c in range(4):
                nc.vector.tensor_copy(xs[:, c, :, 3:3 + TS],
                                      zm[:, c, TP:T].rearrange("p (b t) -> p b t", t=TS)).then_inc(staged, 1)
            ve.wait_ge(staged, 4)
            chain = Chain(ve, steps)
            for c in range(4):
                nc.vector.tensor_scalar(hm[:, c, 0:TP], zm[:, c, 0:TP], cw[:, c, 3:4], cw[:, c, 4:5],
                                        ALU.mult, ALU.add)
                chain.link(nc.vector.tensor_scalar(ys[:, c, :, :], xs[:, c, :, 3:3 + TS], cw[:, c, 3:4],
                                                   cw[:, c, 4:5], ALU.mult, ALU.add))
            for k in range(3):
                d = 3 - k
                for c in range(4):
                    nc.vector.scalar_tensor_tensor(out=hm[:, c, d:TP], in0=zm[:, c, 0:TP - d], scalar=cw[:, c, k:k + 1],
                                                   in1=hm[:, c, d:TP], op0=ALU.mult, op1=ALU.add)
                    chain.link(nc.vector.scalar_tensor_tensor(
                        out=ys[:, c, :, :], in0=xs[:, c, :, k:k + TS], scalar=cw[:, c, k:k + 1],
                        in1=ys[:, c, :, :], op0=ALU.mult, op1=ALU.add))
            for c in range(4):
                nc.vector.tensor_copy(hm[:, c, TP:T].rearrange("p (b t) -> p b t", t=TS), ys[:, c, :, :]
                                      ).then_inc(conv_ready, 1)

        @block.scalar
        def _(act):
            for c in range(4):
                act.wait_ge(conv_ready, c + 1)
                nc.scalar.activation(hm[:, c, :], hm[:, c, :], ACT.Silu).then_inc(act_done, 1)


def gates(nc, A, K, tokm, tokn, sm, psum):
    lf, b, a, g, tmp = sm["lf"], sm["b"], sm["a"], sm["g"], sm["tmp"]
    n = NTILE + 1
    with stage(nc, "gates") as (ctx, sem):
        gb = ctx.enter_context(nc.sbuf_tensor("gb", [P, 8], F32))
        loaded, steps, act_steps, cum_ready, og_done = map(sem, ("loaded", "steps", "act_steps", "cum_ready", "og_done"))
        block = ctx.enter_context(nc.Block())
        fg = tokn[:, :, N_FG:N_FG + MH]

        @block.sync
        def _(sp):
            sp.dma_start(gb[:, :], A["gate_b"].partition_broadcast(P)).then_inc(loaded, 16)

        @block.vector
        def _(ve):
            ve.wait_ge(loaded, 16)
            chain = Chain(ve, steps)
            chain.link(nc.vector.tensor_tensor(tokn[:, :, N_IG:N_IG + 8], tokn[:, :, N_IG:N_IG + 8],
                                               gb[:, :].unsqueeze(1).to_broadcast([P, n, 8]), ALU.add))
            nc.vector.tensor_scalar(lf[:, :, :], fg, 0.0, None, ALU.min)
            chain.link(nc.vector.scalar_tensor_tensor(out=tmp[:, :, :], in0=fg, scalar=-1.0, in1=fg,
                                                      op0=ALU.mult, op1=ALU.min))
            ve.wait_ge(act_steps, 1)
            chain.link(nc.vector.tensor_scalar(tmp[:, :, :], tmp[:, :, :], 1.0, None, ALU.add))
            ve.wait_ge(act_steps, 2)
            chain.link(nc.vector.tensor_tensor(lf[:, :, :], lf[:, :, :], tmp[:, :, :], ALU.subtract))
            ve.wait_ge(cum_ready, 2)
            nc.vector.tensor_copy(b[:, 0:NTILE, :], psum[:, 0, 0:NTILE * MH].rearrange("p (t h) -> p t h", h=MH))
            chain.link(nc.vector.tensor_copy(b[:, NTILE, :], psum[:, 1, 0:MH]))
            chain.link(nc.vector.tensor_tensor(a[:, :, :], tokn[:, :, N_IG:N_IG + MH], b[:, :, :], ALU.subtract))

        @block.scalar
        def _(act):
            act.wait_ge(steps, 2)
            nc.scalar.activation(tmp[:, :, :], tmp[:, :, :], ACT.Exp).then_inc(act_steps, 1)
            act.wait_ge(steps, 3)
            nc.scalar.activation(tmp[:, :, :], tmp[:, :, :], ACT.Ln).then_inc(act_steps, 1)
            nc.scalar.activation(g[:, :, :], tokn[:, :, N_GN:N_END], ACT.Sigmoid).then_inc(act_steps, 1)
            for t in range(n):
                m = P if t < NTILE else NS
                nc.scalar.activation(tokm[0:m, t, C_OG:C_OG + 512], tokm[0:m, t, C_OG:C_OG + 512], ACT.Sigmoid
                                     ).then_inc(og_done, 1)

        @block.tensor
        def _(pe):
            pe.wait_ge(steps, 4)
            nc.tensor.matmul(psum[:, 0, 0:NTILE * MH], K["tri"][:, :], lf[:, 0:NTILE, :].rearrange("p t h -> p (t h)"),
                             start=True, stop=True).then_inc(cum_ready, 1)
            nc.tensor.matmul(psum[:, 1, 0:MH], K["stri"][:, :], lf[:, NTILE, :], start=True, stop=True
                             ).then_inc(cum_ready, 1)


def mlstm(nc, A, O, K, hm, tokm, sm, psum):
    with stage(nc, "mlstm") as (ctx, sem):
        sb = lambda n, s: ctx.enter_context(nc.sbuf_tensor(n, s, F32))
        wqk = sb("wqk", [P, 2, MH, MD])
        mnorm = sb("mnorm", [P, MH, MD])
        xc = sb("xc", [P, MH, P])
        qT, kT, kt = sb("qT", [P, MH, P]), sb("kT", [P, MH, P]), sb("kt", [P, MH, P])
        va = sb("va", [P, MH, MD + 1])
        kw = sb("kw", [P, MH, MD])
        dec = sb("dec", [P, MH, P])
        num = sb("num", [P, MH, MD + 1])
        C = sb("C", [P, MH, MD + 1])
        mc, M, Mb, ML = sb("mc", [P, MH]), sb("M", [P, MH]), sb("Mb", [P, 2 * MH]), sb("ML", [P, 2 * MH])
        sc, wl, sl, emt, r1, r2 = (sb(n, [P, MH]) for n in ("sc", "wl", "sl", "emt", "r1", "r2"))
        tmp = sb("tmpm", [P, MH, P])
        ac = sb("ac", [P, MH])
        names = ("loaded", "xc_ready", "qk_ready", "qk_copied", "arow_ready", "steps", "mrow_ready", "last_ready",
                 "exps_ready", "scores_ready", "inter_ready", "intra_ready", "update_ready", "turned", "h_stored",
                 "finished", "diag_a_ready", "diag_m_ready", "exponents_ready", "differences_ready", "weighted_ready",
                 "square_ready", "root_ready", "gated_ready", "stored")
        S = {n: sem(n) for n in names}
        block = ctx.enter_context(nc.Block())
        row4 = lambda bank: psum[:, bank, :].rearrange("p (h t) -> p h t", h=MH)
        wide = lambda bank: psum[:, bank:bank + 2, :].rearrange("p b (h t) -> p (b h) t", h=2)[:, :, 0:MD + 1]
        per_head = lambda v, n: v.unsqueeze(2).to_broadcast([P, MH, n])
        per_all = lambda v: v.unsqueeze(1).to_broadcast([P, MH, P])
        STEPS = 19

        @block.sync
        def _(sp):
            sp.dma_start(wqk[:, :, :, :], A["m_wqk"]).then_inc(S["loaded"], 16)
            sp.dma_start(mnorm[:, :, :], A["m_norm"].partition_broadcast(P)).then_inc(S["loaded"], 16)
            sp.wait_ge(S["finished"], 2)
            sp.dma_start(O["p_C"], tmp[:, :, :]).then_inc(S["stored"], 16)
            sp.dma_start(O["p_n"], r1[:, :]).then_inc(S["stored"], 16)
            sp.dma_start(O["p_m"], mc[0:1, :]).then_inc(S["stored"], 16)
            sp.wait_ge(S["stored"], 48)

        @block.scalar
        def _(act):
            act.wait_ge(S["loaded"], 32)
            with act.Fori(0, NTILE) as i:
                act.wait_ge(S["h_stored"], i + 1)
                act.wait_ge(S["loaded"], 32)
                nc.scalar.activation(xc[:, :, :], hm[:, :, ds(i * P, P)], ACT.Copy).then_inc(S["xc_ready"], 1)
                act.wait_ge(S["qk_ready"], i + 1)
                nc.scalar.activation(qT[:, :, :], row4(0), ACT.Copy).then_inc(S["qk_copied"], 1)
                nc.scalar.activation(kT[:, :, :], row4(1), ACT.Copy, scale=MD ** -0.5).then_inc(S["qk_copied"], 1)
                nc.scalar.activation(kt[:, :, :], row4(2), ACT.Copy, scale=MD ** -0.5).then_inc(S["qk_copied"], 1)
                act.wait_ge(S["exponents_ready"], i + 1)
                for h in range(MH):
                    nc.scalar.activation(dec[:, h, :], dec[:, h, :], ACT.Exp,
                                         bias=ac[:, h:h + 1]
                                         ).then_inc(S["exps_ready"], 1)
                act.wait_ge(S["differences_ready"], i + 1)
                for v in (sc, emt, wl, sl):
                    nc.scalar.activation(v[:, :], v[:, :], ACT.Exp).then_inc(S["exps_ready"], 1)
                act.wait_ge(S["square_ready"], i + 1)
                nc.scalar.activation(r1[:, :], r1[:, :], ACT.Sqrt).then_inc(S["root_ready"], 1)

        @block.tensor
        def _(pe):
            pe.wait_ge(S["loaded"], 32)
            with pe.Fori(0, NTILE) as i:
                pe.wait_ge(S["h_stored"], i + 1)
                pe.wait_ge(S["xc_ready"], i + 1)
                for h in range(MH):
                    hs = slice(h * P, (h + 1) * P)
                    nc.tensor.matmul(psum[:, 0, hs], wqk[:, 0, h, :], xc[:, h, :], start=True, stop=True)
                    nc.tensor.matmul(psum[:, 1, hs], wqk[:, 1, h, :], xc[:, h, :], start=True, stop=True)
                    last = nc.tensor.matmul(psum[:, 2, hs], xc[:, h, :], wqk[:, 1, h, :], start=True, stop=True)
                last.then_inc(S["qk_ready"], 1)
                pe.wait_ge(S["diag_a_ready"], i + 1)
                nc.tensor.matmul(psum[:, 4, :], K["ones"][:, :], tmp[:, :, :].rearrange("p h t -> p (h t)"),
                                 start=True, stop=True).then_inc(S["arow_ready"], 1)
                pe.wait_ge(S["qk_copied"], 3 * i + 3)
                for h in range(MH):
                    last = nc.tensor.matmul(psum[:, 3, h * P:(h + 1) * P], kT[:, h, :], qT[:, h, :], start=True, stop=True)
                last.then_inc(S["scores_ready"], 1)
                for h in range(MH):
                    last = nc.tensor.matmul(wide(5)[:, h, :], qT[:, h, :], C[:, h, :], start=True, stop=True)
                last.then_inc(S["inter_ready"], 1)
                pe.wait_ge(S["diag_m_ready"], i + 1)
                nc.tensor.matmul(psum[:, 4, :], K["ones"][:, :], tmp[:, :, :].rearrange("p h t -> p (h t)"),
                                 start=True, stop=True).then_inc(S["mrow_ready"], 1)
                nc.tensor.matmul(psum[:, 7, 0:2 * MH], K["last"][:, :], Mb[:, :], start=True, stop=True
                                 ).then_inc(S["last_ready"], 1)
                pe.wait_ge(S["weighted_ready"], i + 1)
                for h in range(MH):
                    last = nc.tensor.matmul(wide(0)[:, h, :], dec[:, h, :], va[:, h, :], start=True, stop=True)
                last.then_inc(S["intra_ready"], 1)
                for h in range(MH):
                    last = nc.tensor.matmul(wide(2)[:, h, :], kw[:, h, :], va[:, h, :], start=True, stop=True)
                last.then_inc(S["update_ready"], 1)
                pe.wait_ge(S["gated_ready"], i + 1)
                for h in range(MH):
                    last = nc.tensor.transpose(psum[:, 4, h * P:(h + 1) * P], num[:, h, 0:MD], K["ident"][:, :])
                last.then_inc(S["turned"], 1)
            pe.wait_ge(S["h_stored"], NTILE + 1)
            for h in range(MH):
                last = nc.tensor.transpose(psum[:, 4, h * P:(h + 1) * P], C[:, h, 0:MD], K["ident"][:, :])
            last.then_inc(S["turned"], 1)

        @block.vector
        def _(ve):
            ve.wait_ge(S["loaded"], 32)
            pre = Chain(ve, S["finished"])
            nc.vector.memset(C[:, :, :], 0.0)
            nc.vector.memset(va[:, :, MD:MD + 1], 1.0)
            pre.link(nc.vector.memset(mc[:, :], 0.0))
            ve.sem_inc(S["h_stored"], 1)
            with ve.Fori(0, NTILE) as i:
                ch = Chain(ve, S["steps"], i * STEPS)

                def signal(ins, name):
                    ins.then_inc(S[name], 1)
                    ve.wait_ge(S[name], i + 1)

                a = ac[:, :]
                ch.link(nc.vector.tensor_copy(a, sm["a"][:, ds(i, 1), :].rearrange("p a h -> p (a h)")))
                b = sm["b"][:, ds(i, 1), :].rearrange("p a h -> p (a h)")
                nc.vector.tensor_tensor(tmp[:, :, :], per_all(K["ident"][:, :]), per_head(a, P), ALU.mult
                                        ).then_inc(S["diag_a_ready"], 1)
                nc.vector.tensor_copy(va[:, :, 0:MD], tokm[:, ds(i, 1), C_V:C_V + 512].rearrange("p a (h v) -> p (a h) v", h=MH))
                ve.wait_ge(S["arow_ready"], i + 1)
                ch.link(nc.vector.tensor_tensor(dec[:, :, :], row4(4), per_all(K["causal"][:, :]), ALU.add))
                ch.link(nc.vector.tensor_reduce(M[:, :], dec[:, :, :], AX.X, ALU.max))
                ch.link(nc.vector.tensor_tensor(M[:, :], M[:, :], mc[:, :], ALU.max))
                nc.vector.tensor_copy(Mb[:, 0:MH], M[:, :])
                ch.link(nc.vector.tensor_tensor(Mb[:, MH:2 * MH], M[:, :], b, ALU.add))
                nc.vector.tensor_tensor(tmp[:, :, :], per_all(K["ident"][:, :]), per_head(M[:, :], P), ALU.mult
                                        ).then_inc(S["diag_m_ready"], 1)
                nc.vector.tensor_tensor(sc[:, :], mc[:, :], M[:, :], ALU.subtract)
                nc.vector.tensor_scalar(emt[:, :], Mb[:, MH:2 * MH], -1.0, None, ALU.mult)
                ve.wait_ge(S["mrow_ready"], i + 1)
                nc.vector.tensor_tensor(dec[:, :, :], per_all(K["causal_t"][:, :]), row4(4), ALU.subtract
                                        ).then_inc(S["exponents_ready"], 1)
                ve.wait_ge(S["last_ready"], i + 1)
                ch.link(nc.vector.tensor_copy(ML[:, :], psum[:, 7, 0:2 * MH]))
                nc.vector.tensor_tensor(wl[:, :], a, ML[:, 0:MH], ALU.subtract)
                ch.link(nc.vector.tensor_tensor(sl[:, :], mc[:, :], ML[:, 0:MH], ALU.subtract))
                signal(nc.vector.tensor_copy(mc[:, :], ML[:, MH:2 * MH]), "differences_ready")
                ve.wait_ge(S["scores_ready"], i + 1)
                ve.wait_ge(S["exps_ready"], 8 * i + 8)
                nc.vector.tensor_tensor(dec[:, :, :], dec[:, :, :], row4(3), ALU.mult)
                signal(nc.vector.tensor_tensor(kw[:, :, :], kt[:, :, :], per_head(wl[:, :], MD), ALU.mult), "weighted_ready")
                ve.wait_ge(S["inter_ready"], i + 1)
                ch.link(nc.vector.tensor_tensor(num[:, :, :], wide(5), per_head(sc[:, :], MD + 1), ALU.mult))
                ve.wait_ge(S["intra_ready"], i + 1)
                ch.link(nc.vector.tensor_tensor(num[:, :, :], num[:, :, :], wide(0), ALU.add))
                den = num[:, :, MD]
                ch.link(nc.vector.scalar_tensor_tensor(out=r2[:, :], in0=den, scalar=-1.0, in1=den, op0=ALU.mult, op1=ALU.max))
                ch.link(nc.vector.tensor_tensor(r2[:, :], r2[:, :], emt[:, :], ALU.max))
                ch.link(nc.vector.reciprocal(r2[:, :], r2[:, :]))
                ch.link(nc.vector.tensor_tensor(num[:, :, 0:MD], num[:, :, 0:MD], per_head(r2[:, :], MD), ALU.mult))
                ch.link(nc.vector.tensor_tensor(tmp[:, :, :], num[:, :, 0:MD], num[:, :, 0:MD], ALU.mult))
                ch.link(nc.vector.tensor_reduce(r1[:, :], tmp[:, :, :], AX.X, ALU.add))
                signal(nc.vector.tensor_scalar(r1[:, :], r1[:, :], 1.0 / MD, EPS, ALU.mult, ALU.add), "square_ready")
                ve.wait_ge(S["root_ready"], i + 1)
                ch.link(nc.vector.reciprocal(r1[:, :], r1[:, :]))
                ch.link(nc.vector.tensor_tensor(num[:, :, 0:MD], num[:, :, 0:MD], per_head(r1[:, :], MD), ALU.mult))
                ch.link(nc.vector.tensor_tensor(num[:, :, 0:MD], num[:, :, 0:MD], mnorm[:, :, :], ALU.mult))
                signal(nc.vector.tensor_tensor(
                    num[:, :, 0:MD], num[:, :, 0:MD],
                    tokm[:, ds(i, 1), C_OG:C_OG + 512].rearrange("p a (h v) -> p (a h) v", h=MH), ALU.mult), "gated_ready")
                ve.wait_ge(S["update_ready"], i + 1)
                for h in range(MH):
                    last = nc.vector.scalar_tensor_tensor(out=C[:, h, :], in0=C[:, h, :], scalar=sl[:, h:h + 1],
                                                          in1=wide(2)[:, h, :], op0=ALU.mult, op1=ALU.add)
                ch.link(last)
                assert ch.n == STEPS, ch.n
                ve.wait_ge(S["turned"], i + 1)
                nc.vector.tensor_scalar(hm[:, :, ds(i * P, P)], row4(4), 1.0, None, ALU.mult).then_inc(S["h_stored"], 1)
            ve.wait_ge(S["turned"], NTILE + 1)
            nc.vector.tensor_copy(r1[:, :], C[:, :, MD])
            pre.link(nc.vector.tensor_copy(tmp[:, :, :], row4(4)))


def mlstm_sample(nc, A, O, K, hm, tokm, sm, psum):
    with stage(nc, "smlstm") as (ctx, sem):
        sb = lambda n, s: ctx.enter_context(nc.sbuf_tensor("sm_" + n, s, F32))
        wqk = sb("wqk", [P, 2, MH, MD])
        mnorm = sb("mnorm", [NS, MH, MD])
        C = sb("C", [P, NSEQ, MH, MD])
        n0, m0 = sb("n0", [NS, MH, MD]), sb("m0", [NS, MH])
        n8, sl8 = sb("n8", [NSEQ, MH, MD]), sb("sl8", [NSEQ, 2 * MH])
        qT, kT = sb("qT", [P, MH, NS]), sb("kT", [P, MH, NS])
        kt, qt = sb("kt", [NS, MH, MD]), sb("qt", [NS, MH, MD])
        kw, kwm = sb("kw", [NS, MH, MD]), sb("kwm", [NS, NSEQ, MH * MD])
        va = sb("va", [NS, MH, MD + 1])
        dec, tmp = sb("dec", [NS, MH, NS]), sb("tmpm", [NS, MH, NS])
        num, sq = sb("num", [NS, MH, MD + 1]), sb("sqm", [NS, MH, MD])
        inter = sb("inter", [P, MH, NS])
        slrow, slb = sb("slrow", [NS, NSEQ, MH]), sb("slb", [P, NSEQ, MH])
        M, Mb, ML = sb("M", [NS, MH]), sb("Mb", [NS, 2 * MH]), sb("ML", [NS, 2 * MH])
        sc, wl, sl, emt, r1, r2, nq = (sb(n, [NS, MH]) for n in ("sc", "wl", "sl", "emt", "r1", "r2", "nq"))
        names = ("loaded", "qk_ready", "qk_copied", "diag_a_ready", "arow_ready", "steps", "diag_m_ready", "mrow_ready",
                 "last_ready", "exponents_ready", "exps_ready", "differences_ready", "scores_ready", "weighted_ready",
                 "intra_ready", "inter_ready", "inter_copied", "inter_turned", "scale_ready", "scale_spread",
                 "masked_ready", "update_ready", "updated", "norm_ready", "square_ready", "root_ready", "gated_ready",
                 "turned", "stored")
        S = {n: sem(n) for n in names}
        block = ctx.enter_context(nc.Block())
        last = NTILE
        a, b = sm["a"][0:NS, last, :], sm["b"][0:NS, last, :]
        ones, ident = K["ones"], K["ident"]
        small = lambda bank: psum[0:NS, bank, 0:MH * NS].rearrange("p (h t) -> p h t", h=MH)
        wide = lambda bank: psum[0:NS, bank:bank + 2, :].rearrange("p b (h t) -> p (b h) t", h=2)[:, :, 0:MD + 1]
        per_head = lambda v, n: v.unsqueeze(2).to_broadcast([NS, MH, n])
        per_all = lambda v: v.unsqueeze(1).to_broadcast([NS, MH, NS])

        @block.sync
        def _(sp):
            sp.dma_start(wqk[:, :, :, :], A["m_wqk"]).then_inc(S["loaded"], 16)
            sp.dma_start(mnorm[:, :, :], A["m_norm"].partition_broadcast(NS)).then_inc(S["loaded"], 16)
            sp.dma_start(C[:, :, :, :], A["s_C0"]).then_inc(S["loaded"], 16)
            sp.dma_start(n0[:, :, :], A["s_n0t"]).then_inc(S["loaded"], 16)
            sp.dma_start(n8[:, :, :], A["s_n0"]).then_inc(S["loaded"], 16)
            sp.dma_start(m0[:, :], A["s_m0t"]).then_inc(S["loaded"], 16)
            sp.wait_ge(S["updated"], NSEQ)
            sp.dma_start(O["s_C"], C[:, :, :, :]).then_inc(S["stored"], 16)
            sp.wait_ge(S["norm_ready"], 1)
            sp.dma_start(O["s_n"], n8[:, :, :]).then_inc(S["stored"], 16)
            sp.dma_start(O["s_m"], sl8[:, MH:2 * MH]).then_inc(S["stored"], 16)
            sp.wait_ge(S["stored"], 48)

        @block.tensor
        def _(pe):
            pe.wait_ge(S["loaded"], 96)
            for h in range(MH):
                x = hm[:, h, TP:T]
                nc.tensor.matmul(psum[:, 0, h * NS:(h + 1) * NS], wqk[:, 0, h, :], x, start=True, stop=True)
                nc.tensor.matmul(psum[:, 1, h * NS:(h + 1) * NS], wqk[:, 1, h, :], x, start=True, stop=True)
                nc.tensor.matmul(psum[0:NS, 2, h * MD:(h + 1) * MD], x, wqk[:, 1, h, :], start=True, stop=True)
                mm = nc.tensor.matmul(psum[0:NS, 3, h * MD:(h + 1) * MD], x, wqk[:, 0, h, :], start=True, stop=True)
            mm.then_inc(S["qk_ready"], 1)
            pe.wait_ge(S["diag_a_ready"], 1)
            nc.tensor.matmul(psum[0:NS, 4, 0:MH * NS], ones[0:NS, 0:NS], tmp[:, :, :].rearrange("p h t -> p (h t)"),
                             start=True, stop=True).then_inc(S["arow_ready"], 1)
            pe.wait_ge(S["qk_copied"], 4)
            for h in range(MH):
                mm = nc.tensor.matmul(psum[0:NS, 5, h * NS:(h + 1) * NS], kT[:, h, :], qT[:, h, :], start=True, stop=True)
            mm.then_inc(S["scores_ready"], 1)
            for h in range(MH):
                for q in range(NSEQ):
                    c = slice(h * NS + q * TS, h * NS + (q + 1) * TS)
                    mm = nc.tensor.matmul(psum[:, 6, c], C[:, q, h, :], qT[:, h, q * TS:(q + 1) * TS], start=True, stop=True)
            mm.then_inc(S["inter_ready"], 1)
            pe.wait_ge(S["diag_m_ready"], 1)
            nc.tensor.matmul(psum[0:NS, 4, 0:MH * NS], ones[0:NS, 0:NS], tmp[:, :, :].rearrange("p h t -> p (h t)"),
                             start=True, stop=True).then_inc(S["mrow_ready"], 1)
            nc.tensor.matmul(psum[0:NS, 7, 0:2 * MH], K["slast"][0:NS, 0:NS], Mb[:, :], start=True, stop=True
                             ).then_inc(S["last_ready"], 1)
            pe.wait_ge(S["inter_copied"], 1)
            for h in range(MH):
                mm = nc.tensor.transpose(psum[0:NS, 6, h * MD:(h + 1) * MD], inter[:, h, :], ident[:, :])
            mm.then_inc(S["inter_turned"], 1)
            pe.wait_ge(S["weighted_ready"], 1)
            for h in range(MH):
                mm = nc.tensor.matmul(wide(0)[:, h, :], dec[:, h, :], va[:, h, :], start=True, stop=True)
            mm.then_inc(S["intra_ready"], 1)
            pe.wait_ge(S["scale_ready"], 1)
            nc.tensor.matmul(psum[:, 4, 0:NSEQ * MH], ones[0:NS, :], slrow[:, :, :].rearrange("p b h -> p (b h)"),
                             start=True, stop=True)
            nc.tensor.matmul(psum[0:NSEQ, 7, 0:MH], K["slast8"][0:NS, 0:NSEQ], sl[:, :], start=True, stop=True)
            nc.tensor.matmul(psum[0:NSEQ, 7, MH:2 * MH], K["slast8"][0:NS, 0:NSEQ], Mb[:, MH:2 * MH], start=True, stop=True)
            nc.tensor.matmul(psum[0:NSEQ, 5, :], K["sseq8"][0:NS, 0:NSEQ], kw[:, :, :].rearrange("p h k -> p (h k)"),
                             start=True, stop=True).then_inc(S["scale_spread"], 1)
            for q in range(NSEQ):
                pe.wait_ge(S["masked_ready"], q + 1)
                if q >= 2:
                    pe.wait_ge(S["updated"], q - 1)
                for h in range(MH):
                    mm = nc.tensor.matmul(psum[:, 2 + q % 2, h * MD:(h + 1) * MD], kwm[:, q, h * MD:(h + 1) * MD],
                                          va[:, h, 0:MD], start=True, stop=True)
                mm.then_inc(S["update_ready"], 1)
            pe.wait_ge(S["gated_ready"], 1)
            for h in range(MH):
                mm = nc.tensor.transpose(psum[:, 0, h * NS:(h + 1) * NS], num[:, h, 0:MD], ident[0:NS, 0:NS])
            mm.then_inc(S["turned"], 1)

        @block.scalar
        def _(act):
            act.wait_ge(S["qk_ready"], 1)
            k = MD ** -0.5
            nc.scalar.activation(qT[:, :, :], psum[:, 0, 0:MH * NS].rearrange("p (h t) -> p h t", h=MH), ACT.Copy
                                 ).then_inc(S["qk_copied"], 1)
            nc.scalar.activation(kT[:, :, :], psum[:, 1, 0:MH * NS].rearrange("p (h t) -> p h t", h=MH), ACT.Copy, scale=k
                                 ).then_inc(S["qk_copied"], 1)
            nc.scalar.activation(kt[:, :, :], psum[0:NS, 2, :].rearrange("p (h t) -> p h t", h=MH), ACT.Copy, scale=k
                                 ).then_inc(S["qk_copied"], 1)
            nc.scalar.activation(qt[:, :, :], psum[0:NS, 3, :].rearrange("p (h t) -> p h t", h=MH), ACT.Copy
                                 ).then_inc(S["qk_copied"], 1)
            act.wait_ge(S["exponents_ready"], 1)
            for h in range(MH):
                nc.scalar.activation(dec[:, h, :], dec[:, h, :], ACT.Exp, bias=sm["a"][0:NS, last, h:h + 1]
                                     ).then_inc(S["exps_ready"], 1)
            act.wait_ge(S["differences_ready"], 1)
            for v in (sc, emt, wl, sl):
                nc.scalar.activation(v[:, :], v[:, :], ACT.Exp).then_inc(S["exps_ready"], 1)
            act.wait_ge(S["inter_ready"], 1)
            nc.scalar.activation(inter[:, :, :], psum[:, 6, 0:MH * NS].rearrange("p (h t) -> p h t", h=MH), ACT.Copy
                                 ).then_inc(S["inter_copied"], 1)
            act.wait_ge(S["square_ready"], 1)
            nc.scalar.activation(r1[:, :], r1[:, :], ACT.Sqrt).then_inc(S["root_ready"], 1)

        @block.vector
        def _(ve):
            ch = Chain(ve, S["steps"])

            def signal(ins, name):
                ins.then_inc(S[name], 1)
                ve.wait_ge(S[name], 1)

            nc.vector.memset(va[:, :, MD:MD + 1], 1.0)
            nc.vector.tensor_tensor(tmp[:, :, :], per_all(ident[0:NS, 0:NS]), per_head(a, NS), ALU.mult
                                    ).then_inc(S["diag_a_ready"], 1)
            nc.vector.tensor_copy(va[:, :, 0:MD], tokm[0:NS, last, C_V:C_V + 512].rearrange("p (h v) -> p h v", h=MH))
            ve.wait_ge(S["loaded"], 96)
            ve.wait_ge(S["arow_ready"], 1)
            ch.link(nc.vector.tensor_tensor(dec[:, :, :], small(4), per_all(K["scausal"][0:NS, 0:NS]), ALU.add))
            ch.link(nc.vector.tensor_reduce(M[:, :], dec[:, :, :], AX.X, ALU.max))
            ch.link(nc.vector.tensor_tensor(M[:, :], M[:, :], m0[:, :], ALU.max))
            nc.vector.tensor_copy(Mb[:, 0:MH], M[:, :])
            ch.link(nc.vector.tensor_tensor(Mb[:, MH:2 * MH], M[:, :], b, ALU.add))
            nc.vector.tensor_tensor(tmp[:, :, :], per_all(ident[0:NS, 0:NS]), per_head(M[:, :], NS), ALU.mult
                                    ).then_inc(S["diag_m_ready"], 1)
            nc.vector.tensor_tensor(sc[:, :], m0[:, :], M[:, :], ALU.subtract)
            nc.vector.tensor_scalar(emt[:, :], Mb[:, MH:2 * MH], -1.0, None, ALU.mult)
            ve.wait_ge(S["mrow_ready"], 1)
            nc.vector.tensor_tensor(dec[:, :, :], per_all(K["scausal_t"][0:NS, 0:NS]), small(4), ALU.subtract
                                    ).then_inc(S["exponents_ready"], 1)
            ve.wait_ge(S["last_ready"], 1)
            ch.link(nc.vector.tensor_copy(ML[:, :], psum[0:NS, 7, 0:2 * MH]))
            nc.vector.tensor_tensor(wl[:, :], a, ML[:, 0:MH], ALU.subtract)
            signal(nc.vector.tensor_tensor(sl[:, :], m0[:, :], ML[:, 0:MH], ALU.subtract), "differences_ready")
            ve.wait_ge(S["scores_ready"], 1)
            ve.wait_ge(S["exps_ready"], 8)
            ve.wait_ge(S["qk_copied"], 4)
            ch.link(nc.vector.tensor_tensor(sq[:, :, :], qt[:, :, :], n0[:, :, :], ALU.mult))
            ch.link(nc.vector.tensor_reduce(nq[:, :], sq[:, :, :], AX.X, ALU.add))
            ch.link(nc.vector.tensor_tensor(nq[:, :], nq[:, :], sc[:, :], ALU.mult))
            nc.vector.tensor_tensor(dec[:, :, :], dec[:, :, :], small(5), ALU.mult)
            signal(nc.vector.tensor_tensor(kw[:, :, :], kt[:, :, :], per_head(wl[:, :], MD), ALU.mult), "weighted_ready")
            signal(nc.vector.tensor_tensor(slrow[:, :, :], K["slast8"][0:NS, 0:NSEQ].unsqueeze(2).to_broadcast([NS, NSEQ, MH]),
                                           sl[:, :].unsqueeze(1).to_broadcast([NS, NSEQ, MH]), ALU.mult), "scale_ready")
            for q in range(NSEQ):
                nc.vector.tensor_scalar(kwm[:, q, :], kw[:, :, :].rearrange("p h k -> p (h k)"), K["sseq8"][0:NS, q:q + 1],
                                        None, ALU.mult).then_inc(S["masked_ready"], 1)
            ve.wait_ge(S["inter_turned"], 1)
            ve.wait_ge(S["intra_ready"], 1)
            ch.link(nc.vector.tensor_tensor(num[:, :, 0:MD], psum[0:NS, 6, :].rearrange("p (h v) -> p h v", h=MH),
                                            per_head(sc[:, :], MD), ALU.mult))
            ch.link(nc.vector.tensor_tensor(num[:, :, 0:MD], num[:, :, 0:MD], wide(0)[:, :, 0:MD], ALU.add))
            ch.link(nc.vector.tensor_tensor(nq[:, :], nq[:, :], wide(0)[:, :, MD], ALU.add))
            ch.link(nc.vector.scalar_tensor_tensor(out=r2[:, :], in0=nq[:, :], scalar=-1.0, in1=nq[:, :], op0=ALU.mult, op1=ALU.max))
            ch.link(nc.vector.tensor_tensor(r2[:, :], r2[:, :], emt[:, :], ALU.max))
            ch.link(nc.vector.reciprocal(r2[:, :], r2[:, :]))
            ch.link(nc.vector.tensor_tensor(num[:, :, 0:MD], num[:, :, 0:MD], per_head(r2[:, :], MD), ALU.mult))
            ch.link(nc.vector.tensor_tensor(sq[:, :, :], num[:, :, 0:MD], num[:, :, 0:MD], ALU.mult))
            ch.link(nc.vector.tensor_reduce(r1[:, :], sq[:, :, :], AX.X, ALU.add))
            signal(nc.vector.tensor_scalar(r1[:, :], r1[:, :], 1.0 / MD, EPS, ALU.mult, ALU.add), "square_ready")
            ve.wait_ge(S["scale_spread"], 1)
            ch.link(nc.vector.tensor_copy(slb[:, :, :], psum[:, 4, 0:NSEQ * MH].rearrange("p (b h) -> p b h", h=MH)))
            ch.link(nc.vector.tensor_copy(sl8[:, :], psum[0:NSEQ, 7, 0:2 * MH]))
            ch.link(nc.vector.tensor_tensor(n8[:, :, :], n8[:, :, :], sl8[:, 0:MH].unsqueeze(2).to_broadcast([NSEQ, MH, MD]), ALU.mult))
            signal(nc.vector.tensor_tensor(n8[:, :, :], n8[:, :, :], psum[0:NSEQ, 5, :].rearrange("p (h k) -> p h k", h=MH),
                                           ALU.add), "norm_ready")
            for q in range(NSEQ):
                ve.wait_ge(S["update_ready"], q + 1)
                ve.wait_ge(S["inter_ready"], 1)
                ch.link(nc.vector.tensor_tensor(C[:, q, :, :], C[:, q, :, :], slb[:, q, :].unsqueeze(2).to_broadcast([P, MH, MD]), ALU.mult))
                nc.vector.tensor_tensor(C[:, q, :, :], C[:, q, :, :], psum[:, 2 + q % 2, :].rearrange("p (h v) -> p h v", h=MH),
                                        ALU.add).then_inc(S["updated"], 1)
            ve.wait_ge(S["root_ready"], 1)
            ch.link(nc.vector.reciprocal(r1[:, :], r1[:, :]))
            ch.link(nc.vector.tensor_tensor(num[:, :, 0:MD], num[:, :, 0:MD], per_head(r1[:, :], MD), ALU.mult))
            ch.link(nc.vector.tensor_tensor(num[:, :, 0:MD], num[:, :, 0:MD], mnorm[:, :, :], ALU.mult))
            signal(nc.vector.tensor_tensor(num[:, :, 0:MD], num[:, :, 0:MD],
                                           tokm[0:NS, last, C_OG:C_OG + 512].rearrange("p (h v) -> p h v", h=MH), ALU.mult),
                   "gated_ready")
            ve.wait_ge(S["turned"], 1)
            nc.vector.tensor_copy(hm[:, :, TP:T], psum[:, 0, 0:MH * NS].rearrange("p (h t) -> p h t", h=MH))


HEADS_AT_ONCE = 2
BRANCHES = CMP, SEL, SLIDE = range(3)
NCMP = TP // CB
RAWW = 1920
STRIPW, CSTRIPW, WSTRIPW = TP, NCMP + 4 * (NTILE - 1), WIN + P


def compress_setup(nc, A, K, N, zn, psum):
    with stage(nc, "cmp") as (ctx, sem):
        sb = lambda n, s: ctx.enter_context(nc.sbuf_tensor("cmp_" + n, s, F32))
        pe_in = sb("pe", [P, 2, CB])
        act_out = sb("act", [P, 2, NCMP])
        rel, onehot, rmask, rv = sb("rel", [NBUCKET, NH]), sb("onehot", [NBUCKET, 2048]), sb("rmask", [NH, 2048]), sb("rv", [NH, 2048])
        loaded, layer1_ready, bias_ready, act_ready, layer2_ready, copied, vec_ready, vec_masked, stored = map(sem, (
            "loaded", "layer1_ready", "bias_ready", "act_ready", "layer2_ready", "copied", "vec_ready", "vec_masked", "stored"))
        block = ctx.enter_context(nc.Block())

        @block.sync
        def _(sp):
            for dst, src in ((N["w1"][:, :, :, :], A["cmp_w1"]), (N["w2"][:, :, :], A["cmp_w2"]), (pe_in[:, :, :], A["cmp_pe"]),
                             (rel[:, :], A["rel"]), (onehot[:, :], A["onehot"]), (rmask[:, :], A["rmask"])):
                sp.dma_start(dst, src).then_inc(loaded, 16)
            sp.wait_ge(vec_masked, 4)
            sp.dma_start(A["bias_vec"], rv[:, :]).then_inc(stored, 16)
            sp.wait_ge(stored, 16)

        @block.tensor
        def _(pe):
            pe.wait_ge(loaded, 96)
            for q in range(4):
                nc.tensor.matmul(psum[0:NH, q, :], rel[:, :], onehot[:, q * 512:(q + 1) * 512], start=True, stop=True
                                 ).then_inc(vec_ready, 1)
            for kv in range(2):
                for j in range(CB):
                    nc.tensor.matmul(psum[:, 4 + kv, 0:1], N["w1"][:, kv, j, :], pe_in[:, kv, j:j + 1],
                                     start=(j == 0), stop=(j == CB - 1))
                for j in range(CB):
                    last = nc.tensor.matmul(psum[:, 6 + kv, 0:NCMP], N["w1"][:, kv, j, :],
                                            zn[:, Q_KCMP - 4 + kv, j:TP:CB], start=(j == 0), stop=(j == CB - 1))
            last.then_inc(layer1_ready, 1)
            pe.wait_ge(act_ready, 2)
            nc.tensor.matmul(psum[:, 4, 0:NCMP], N["w2"][:, 0, :], act_out[:, 0, :], start=True, stop=True)
            nc.tensor.matmul(psum[0:NCMP, 5, 0:P], act_out[:, 1, :], N["w2"][:, 1, :], start=True, stop=True
                             ).then_inc(layer2_ready, 1)

        @block.vector
        def _(ve):
            ve.wait_ge(loaded, 96)
            for q in range(4):
                ve.wait_ge(vec_ready, q + 1)
                c = slice(q * 512, (q + 1) * 512)
                nc.vector.tensor_tensor(rv[:, c], psum[0:NH, q, :], rmask[:, c], ALU.add).then_inc(vec_masked, 1)
            ve.wait_ge(layer1_ready, 1)
            nc.vector.tensor_copy(N["pb"][:, :], psum[:, 4:6, 0]).then_inc(bias_ready, 1)
            ve.wait_ge(layer2_ready, 1)
            nc.vector.tensor_copy(N["kcmp"][:, :], psum[:, 4, 0:NCMP])
            nc.vector.tensor_copy(N["vcmp"][:, :], psum[0:NCMP, 5, 0:P])

        @block.scalar
        def _(act):
            act.wait_ge(bias_ready, 1)
            for kv in range(2):
                nc.scalar.activation(act_out[:, kv, :], psum[:, 6 + kv, 0:NCMP], ACT.Gelu_apprx_tanh,
                                     bias=N["pb"][:, kv:kv + 1]).then_inc(act_ready, 1)


def nsa_prompt(nc, A, K, N, zn, tokn, gates, on, psum):
    units = [(br, t, g) for t in range(NTILE) for br in BRANCHES for g in range(HEADS_AT_ONCE)]
    U = len(units)
    PER_TILE = len(BRANCHES) * HEADS_AT_ONCE
    NBUF = 4

    def keys(u):
        br, t, _ = units[u]
        if br == CMP:
            return 0, NCMP
        first = 0 if br == SEL else max(0, t - WIN // P)
        return first, (t + 1 - first) * P

    turns = []
    for u in range(U):
        nt = -(-keys(u)[1] // P)
        turns += [(u, k, min(4, nt - k)) for k in range(0, nt, 4)]
    by_unit = [[q for q, x in enumerate(turns) if x[0] == u] for u in range(U)]
    NT = len(turns)

    with stage(nc, "nsap") as (ctx, sem):
        sb = lambda n, s: ctx.enter_context(nc.sbuf_tensor("np_" + n, s, F32))
        raw = sb("raw", [P, 2, RAWW])
        strip, wstrip, cstrip = sb("strip", [P, 2, STRIPW]), sb("wstrip", [P, 2, WSTRIPW]), sb("cstrip", [P, 2, CSTRIPW])
        qs = sb("qs", [P, TP])
        pb = sb("p", [P, NBUF, TP])
        pt = sb("pt", [P, 2, NTILE, P])
        diag = sb("diag", [P, 2, P])
        gp = sb("gp", [P, 2, NTILE, 3])
        nm, sums, rs = sb("nm", [P, NBUF]), sb("sums", [P, NBUF]), sb("rs", [P, NBUF])
        names = ("raw_loaded", "flipped", "setup_ready", "scores_ready", "logits_ready", "max_ready", "exp_ready", "inverted",
                 "diag_ready", "turn_ready", "copied", "pv_ready", "on_stored", "gates_ready")
        S = {n: sem(n) for n in names}
        block = ctx.enter_context(nc.Block())

        @block.sync
        def _(sp):
            for p in range(NPAIR):
                if p:
                    sp.wait_ge(S["flipped"], p)
                for g in range(2):
                    h = p + NPAIR * g
                    src = A["bias_vec"][h:h + 1, 0:RAWW]
                    src = bass.AP(tensor=src.tensor, offset=src.offset, ap=[[1, P], [1, RAWW]])
                    sp.dma_start(raw[:, g, :], src).then_inc(S["raw_loaded"], 16)

        @block.tensor
        def _(pe):
            def scores(i, u):
                br, t, g = units[u]
                k0, nk = keys(u)
                if u >= 2:
                    pe.wait_ge(S["logits_ready"], i * U + u - 1)
                hs = slice(g * HD, (g + 1) * HD)
                src = {CMP: N["kcmp"], SEL: zn[:, Q_KSEL - 4, :], SLIDE: zn[:, Q_KWIN - 4, :]}[br]
                for c in range(0, nk, 512):
                    w = min(512, nk - c)
                    last = nc.tensor.matmul(psum[:, 2 * (u % 2) + c // 512, 0:w], qs[hs, t * P:(t + 1) * P],
                                            src[hs, k0 * P + c:k0 * P + c + w], start=True, stop=True)
                last.then_inc(S["scores_ready"], 1)

            def turn(i, u):
                pe.wait_ge(S["exp_ready"], i * U + u + 1)
                pe.wait_ge(S["diag_ready"], i * U + u + 1)
                nk = keys(u)[1]
                for q in by_unit[u]:
                    _, k, n = turns[q]
                    if q >= 2:
                        pe.wait_ge(S["copied"], i * NT + q - 1)
                    for j in range(n):
                        w = min(P, nk - (k + j) * P)
                        last = nc.tensor.matmul(psum[0:w, 4 + q % 2, j * P:(j + 1) * P],
                                                pb[:, u % NBUF, (k + j) * P:(k + j) * P + w], diag[:, u % 2, :],
                                                start=True, stop=True)
                    last.then_inc(S["turn_ready"], 1)

            def values(i, u):
                br, t, g = units[u]
                k0, nk = keys(u)
                pe.wait_ge(S["copied"], i * NT + by_unit[u][-1] + 1)
                if t >= 2 and br == BRANCHES[0]:
                    pe.wait_ge(S["on_stored"], i * NTILE + t + 1)
                nt = -(-nk // P)
                for j in range(nt):
                    if br == CMP:
                        v = N["vcmp"][0:NCMP, g * HD:(g + 1) * HD]
                    else:
                        c = (N_VSEL if br == SEL else N_VWIN) + g * HD
                        v = tokn[:, k0 + j, c:c + HD]
                    w = min(P, nk)
                    last = nc.tensor.matmul(psum[g * HD:(g + 1) * HD, 6 + t % 2, 0:P], v, pt[0:w, u % 2, j, :],
                                            start=(br == BRANCHES[0] and j == 0), stop=(br == BRANCHES[-1] and j == nt - 1))
                last.then_inc(S["pv_ready"], 1)

            with pe.Fori(0, NPAIR) as i:
                pe.wait_ge(S["on_stored"], i * NTILE + 2)
                pe.wait_ge(S["raw_loaded"], 32 * i + 32)
                for g in range(2):
                    for c in range(2):
                        nc.tensor.matmul(psum[:, 2 * g + c, :], K["flip"][:, :], raw[:, g, c * 512:(c + 1) * 512], start=True, stop=True)
                for g in range(2):
                    last = nc.tensor.matmul(psum[:, 4, g * 64:g * 64 + CSTRIPW], K["flip"][:, :],
                                            raw[:, g, CB - 1:CB - 1 + CB * (CSTRIPW - 1) + 1:CB], start=True, stop=True)
                last.then_inc(S["flipped"], 1)
                pe.wait_ge(S["setup_ready"], i + 1)
                for u in range(3):
                    scores(i, u)
                turn(i, 0)
                for u in range(U):
                    if u + 3 < U:
                        scores(i, u + 3)
                    if u + 1 < U:
                        turn(i, u + 1)
                    values(i, u)

        @block.scalar
        def _(act):
            def exp(i, u):
                x = pb[:, u % NBUF, 0:keys(u)[1]]
                act.wait_ge(S["max_ready"], i * U + u + 1)
                if u >= NBUF:
                    act.wait_ge(S["inverted"], i * U + u - NBUF + 1)
                nc.scalar.activation(x, x, ACT.Exp, bias=nm[:, u % NBUF:u % NBUF + 1],
                                     accum_out=sums[:, u % NBUF:u % NBUF + 1]).then_inc(S["exp_ready"], 1)

            def copies(i, u):
                if u >= 2:
                    act.wait_ge(S["pv_ready"], i * U + u - 1)
                w = min(P, keys(u)[1])
                for q in by_unit[u]:
                    _, k, n = turns[q]
                    act.wait_ge(S["turn_ready"], i * NT + q + 1)
                    nc.scalar.activation(pt[0:w, u % 2, k:k + n, :], psum[0:w, 4 + q % 2, 0:n * P].rearrange("p (n q) -> p n q", n=n),
                                         ACT.Copy).then_inc(S["copied"], 1)

            with act.Fori(0, NPAIR) as i:
                exp(i, 0)
                exp(i, 1)
                copies(i, 0)
                for u in range(U):
                    if u + 2 < U:
                        exp(i, u + 2)
                    if u + 1 < U:
                        copies(i, u + 1)

        @block.vector
        def _(ve):
            def logits(i, u):
                br, t, g = units[u]
                k0, nk = keys(u)
                if br == CMP:
                    bias = cstrip[:, g, 4 * (NTILE - 1 - t):4 * (NTILE - 1 - t) + nk]
                elif br == SEL or t < WIN // P:
                    bias = strip[:, g, (NTILE - 1 - t) * P:TP]
                else:
                    bias = wstrip[:, g, :]
                ve.wait_ge(S["scores_ready"], i * U + u + 1)
                if u >= NBUF:
                    ve.wait_ge(S["turn_ready"], i * NT + by_unit[u - NBUF][-1] + 1)
                x = pb[:, u % NBUF, 0:nk]
                s = psum[:, 2 * (u % 2):2 * (u % 2) + 2, :].rearrange("p a b -> p (a b)")[:, 0:nk]
                nc.vector.tensor_tensor(x, s, bias, ALU.add).then_inc(S["logits_ready"], 1)
                ve.wait_ge(S["logits_ready"], i * U + u + 1)
                nc.vector.tensor_reduce(nm[:, u % NBUF:u % NBUF + 1], x, AX.X, ALU.max, negate=True).then_inc(S["max_ready"], 1)

            def factors(i, u):
                br, t, g = units[u]
                r = rs[:, u % NBUF:u % NBUF + 1]
                ve.wait_ge(S["exp_ready"], i * U + u + 1)
                nc.vector.reciprocal(r, sums[:, u % NBUF:u % NBUF + 1]).then_inc(S["inverted"], 1)
                ve.wait_ge(S["inverted"], i * U + u + 1)
                if u >= 2:
                    ve.wait_ge(S["turn_ready"], i * NT + by_unit[u - 2][-1] + 1)
                nc.vector.tensor_scalar(diag[:, u % 2, :], K["ident"][:, :], r, gp[:, g, t, br:br + 1], ALU.mult, ALU.mult
                                        ).then_inc(S["diag_ready"], 1)

            def store(i, t):
                ve.wait_ge(S["pv_ready"], i * U + (t + 1) * PER_TILE)
                nc.vector.tensor_scalar(on[:, ds(i, 1), t * P:(t + 1) * P].rearrange("p a t -> p (a t)"),
                                        psum[:, 6 + t % 2, 0:P], 1.0, None, ALU.mult).then_inc(S["on_stored"], 1)

            ve.sem_inc(S["on_stored"], 2)
            with ve.Fori(0, NPAIR) as i:
                nc.vector.tensor_scalar(qs[:, :], zn[:, ds(i, 1), 0:TP].rearrange("p a t -> p (a t)"), CMP_SCALE, None, ALU.mult)
                ch = Chain(ve, S["gates_ready"], 4 * i)
                for g in range(2):
                    ch.link(nc.vector.tensor_copy(gp[:, g, :, :], gates[:, 0:NTILE, ds(3 * (i + NPAIR * g), 3)]))
                for g in range(2):
                    ch.link(nc.vector.tensor_tensor(gp[:, g, 0, CMP:CMP + 1], gp[:, g, 0, CMP:CMP + 1], K["seen"][:, :], ALU.mult))
                ve.wait_ge(S["flipped"], i + 1)
                for g in range(2):
                    full = psum[:, 2 * g:2 * g + 2, :].rearrange("p a b -> p (a b)")
                    nc.vector.tensor_copy(strip[:, g, :], full)
                    nc.vector.tensor_copy(wstrip[:, g, P:WSTRIPW], full[:, TP - WIN:TP])
                    nc.vector.tensor_tensor(wstrip[:, g, 0:P], full[:, TP - WSTRIPW:TP - WIN], K["wmask"][:, :], ALU.add)
                nc.vector.tensor_copy(cstrip[:, :, :], psum[:, 4, 0:128].rearrange("p (g x) -> p g x", g=2)[:, :, 0:CSTRIPW]
                                      ).then_inc(S["setup_ready"], 1)
                ve.wait_ge(S["setup_ready"], i + 1)
                for u in range(3):
                    logits(i, u)
                    if u < 2:
                        factors(i, u)
                for u in range(U):
                    if u + 3 < U:
                        logits(i, u + 3)
                    if u + 2 < U:
                        factors(i, u + 2)
                    if u % PER_TILE == PER_TILE - 1:
                        store(i, u // PER_TILE)


def compress_sample(nc, A, K, N, pages, psum):
    with stage(nc, "cmps") as (ctx, sem):
        sb = lambda n, s: ctx.enter_context(nc.sbuf_tensor("cs_" + n, s, F32))
        kv_in = sb("kv", [P, 2, NPAGE, 2 * PAGE])
        act_out = sb("act", [P, 2, P])
        loaded = [sem("loaded0"), sem("loaded1")]
        loaded_soft = [N["soft"][n] for n in ("c0", "c1")]
        layer1_ready, act_ready, layer2_ready, copied = map(sem, ("layer1_ready", "act_ready", "layer2_ready", "copied"))
        block = ctx.enter_context(nc.Block())
        NB = PAST // CB

        def load(eng, first, step, i, j, done):
            n = NPAGE // step // 4
            with eng.Fori(0, n) as p:
                if i is not None:
                    eng.wait_ge(layer1_ready, 2 * i + j - 1)
                at = [(p * 4 + e) * step + first for e in range(4)]
                base = ((2 * i if i is not None else 0) + j) * NPAGE
                page = [eng.value_load(pages[0:1, ds(base + a, 1)], min_val=0, max_val=N["n_pool"] - 1) for a in at]
                for e in range(4):
                    eng.dma_start(kv_in[:, j, ds(at[e], 1), :].rearrange("p a x -> p (a x)"),
                                  A["pool"][ds(page[e], 1), :, 0:2 * PAGE].rearrange("a p x -> (a p) x")).then_inc(done[j], 16)

        @block.sync
        def _(sp):
            for j in range(2):
                load(sp, 0, 2, None, j, loaded)
            with sp.Fori(1, NSEQ // 2) as i:
                for j in range(2):
                    load(sp, 0, 2, i, j, loaded)

        @block.gpsimd
        def _(pool):
            for j in range(2):
                load(pool, 1, 2, None, j, loaded_soft)
            with pool.Fori(1, NSEQ // 2) as i:
                for j in range(2):
                    load(pool, 1, 2, i, j, loaded_soft)

        @block.tensor
        def _(pe):
            with pe.Fori(0, NSEQ // 2) as i:
                for j in range(2):
                    pe.wait_ge(loaded[j], 8 * NPAGE * i + 8 * NPAGE)
                    pe.wait_ge(loaded_soft[j], 8 * NPAGE * i + 8 * NPAGE)
                    pe.wait_ge(copied, 2 * i + j + 1)
                    for kv in range(2):
                        for r in range(CB):
                            last = nc.tensor.matmul(psum[:, kv, 0:NB], N["w1"][:, kv, r, :],
                                                    kv_in[:, j, :, kv * PAGE + r:(kv + 1) * PAGE:CB],
                                                    start=(r == 0), stop=(r == CB - 1))
                    last.then_inc(layer1_ready, 1)
                    pe.wait_ge(act_ready, 4 * i + 2 * j + 2)
                    nc.tensor.matmul(psum[:, 2, 0:NB], N["w2"][:, 0, :], act_out[:, 0, :], start=True, stop=True)
                    nc.tensor.matmul(psum[:, 3, 0:P], act_out[:, 1, :], N["w2"][:, 1, :], start=True, stop=True
                                     ).then_inc(layer2_ready, 1)

        @block.scalar
        def _(act):
            with act.Fori(0, NSEQ // 2) as i:
                for j in range(2):
                    act.wait_ge(layer1_ready, 2 * i + j + 1)
                    for kv in range(2):
                        nc.scalar.activation(act_out[:, kv, :], psum[:, kv, 0:NB], ACT.Gelu_apprx_tanh,
                                             bias=N["pb"][:, kv:kv + 1]).then_inc(act_ready, 1)

        @block.vector
        def _(ve):
            ve.sem_inc(copied, 1)
            with ve.Fori(0, NSEQ // 2) as i:
                for j in range(2):
                    ve.wait_ge(layer2_ready, 2 * i + j + 1)
                    nc.vector.tensor_scalar(N["kc"][:, ds(2 * i + j, 1), :].rearrange("p a x -> p (a x)"), psum[:, 2, 0:NB],
                                            1.0, None, ALU.mult)
                    nc.vector.tensor_scalar(N["vc"][:, ds(2 * i + j, 1), :].rearrange("p a x -> p (a x)"), psum[:, 3, 0:P],
                                            1.0, None, ALU.mult).then_inc(copied, 1)


CMPC, TAILC = 1024, 1152
BW = TAILC + NS


def nsa_sample(nc, A, O, K, N, zn, tokn, gates, pages, on, psum):
    with stage(nc, "nsas") as (ctx, sem):
        sb = lambda n, s: ctx.enter_context(nc.sbuf_tensor("ns_" + n, s, F32))
        qf, qz = sb("qf", [P, 2, P]), sb("qz", [P, NSEQ, P])
        relq, onehot, delta = sb("relq", [P, NH]), sb("onehot", [P, BW]), sb("delta", [P, TS])
        relr = sb("relr", [P, 4, NH, TS])
        bias = sb("bias", [P, BW])
        group, tmask, wmask = sb("group", [P, P]), sb("tmask", [P, 2, NS]), sb("wmask", [P, TS])
        gr = sb("gr", [P, 2, 3])
        kbuf, vbuf = sb("kbuf", [P, 2, 4, 4 * PAGE]), sb("vbuf", [P, 2, 4, 4 * PAGE])
        win = sb("win", [P, 4, 2, WIN])
        ss = sb("ss", [P, PAST + NS])
        ws = sb("ws", [P, WIN + NS])
        pc, pcg = sb("pc", [P, P]), sb("pcg", [P, P])
        imp, top, bmask = sb("imp", [P, SB + 1]), sb("top", [P, 16]), sb("bmask", [P, SB + 1])
        nm, sums, rs = sb("nm", [P, 3]), sb("sums", [P, 3]), sb("rs", [P, 3])
        pt = sb("pt", [P, 2, 4, P])
        names = ("loaded", "win_loaded0", "win_loaded1", "gates_stored", "gates_loaded", "k_loaded0", "k_loaded1", "v_loaded0", "v_loaded1",
                 "q_ready", "rel_ready", "bias_ready", "bias_copied", "score_ready", "score_drained", "pc_ready", "max_ready",
                 "exp_ready", "scale_ready", "probs_ready", "turn_ready", "turn_copied", "pv_ready", "out_copied", "steps",
                 "kept", "gpass")
        S = {n: sem(n) for n in names}
        S.update(N["soft"])
        block = ctx.enter_context(nc.Block())
        CMPJ, WINJ, WTAIL, IMP, SEL0, STAIL = 0, 1, 2, 3, 4, 12
        NJ = 13
        TC, TW, TWT, TS0, TST, NT = 0, 1, 2, 3, 11, 12
        NBLK = PAST // SB

        def load_pages(eng, s, sequences, kind):
            def load(buf, at, done, j, c):
                for b in sequences:
                    n = (4 * s + b) * NPAGE
                    page = [eng.value_load(pages[0:1, ds(4 * c + n + p, 1)], min_val=0, max_val=N["n_pool"] - 1) for p in range(4)]
                    for p in range(4):
                        eng.dma_start(buf[:, j, b, p * PAGE:(p + 1) * PAGE],
                                      A["pool"][ds(page[p], 1), :, at:at + PAGE].rearrange("a p x -> (a p) x")).then_inc(done[j], 16)

            kd, vd = (S[f"k_{kind}0"], S[f"k_{kind}1"]), (S[f"v_{kind}0"], S[f"v_{kind}1"])
            with eng.Fori(0, 4) as i:
                for j in range(2):
                    eng.wait_ge(S["score_ready"], 2 * i + j + s * NJ + SEL0 - 1)
                    load(kbuf, 2 * PAGE, kd, j, 2 * i + j)
            with eng.Fori(0, 4) as i:
                for j in range(2):
                    eng.wait_ge(S["pv_ready"], 2 * i + j + s * NT + TS0 - 1)
                    load(vbuf, 3 * PAGE, vd, j, 2 * i + j)

        @block.gpsimd
        def _(pool):
            for s in range(2):
                load_pages(pool, s, (2, 3), "soft")

        @block.sync
        def _(sp):
            for dst, src in ((relq[:, :], A["relq"]), (onehot[:, :], A["onehot_s"]), (delta[:, :], A["delta"]),
                             (group[:, :], A["group"]), (tmask[:, :, :], A["tmask"]), (wmask[:, :], A["wmask_s"])):
                sp.dma_start(dst, src).then_inc(S["loaded"], 16)
            sp.dma_start(A["gate_rows"], gates[0:NS, NTILE, :]).then_inc(S["gates_stored"], 16)
            sp.dma_start(O["winp"], A["winp"]).then_inc(S["kept"], 16)
            sp.dma_start(O["zkv"], zn[:, 4:8, :]).then_inc(S["kept"], 16)
            sp.dma_start(O["tkv"], tokn[:, :, 0:2 * P]).then_inc(S["kept"], 16)
            sp.wait_ge(S["gates_stored"], 16)
            for q in range(NSEQ):
                src = A["gate_rows"][q * TS:(q + 1) * TS, :].rearrange("q (h r) -> h q r", r=3)
                for h in range(NH):
                    r = (q % 4) * 32 + h * TS
                    sp.dma_start(gr[r:r + TS, q // 4, :], src[h, :, :]).then_inc(S["gates_loaded"], 16)
            for s in range(2):
                if s:
                    sp.wait_ge(S["pv_ready"], TWT + 1)
                for b in range(4):
                    sp.dma_start(win[:, b, :, :], A["winp"][4 * s + b]).then_inc(S[f"win_loaded{s}"], 16)
                load_pages(sp, s, (0, 1), "loaded")
            sp.wait_ge(S["kept"], 48)

        @block.tensor
        def _(pe):
            pe.wait_ge(S["rel_ready"], 1)
            for n, c in enumerate(range(0, BW, 512)):
                w = min(512, BW - c)
                last = nc.tensor.matmul(psum[:, 5 + n, 0:w], relr[:, :, :, :].rearrange("p b h q -> p (b h q)"),
                                        onehot[:, c:c + w], start=True, stop=True)
            last.then_inc(S["bias_ready"], 1)
            pe.wait_ge(S["q_ready"], 1)
            for s in range(2):
                def job(n):
                    n += s * NJ
                    if n >= 2:
                        pe.wait_ge(S["score_drained"], n - 1)
                    return psum[:, n % 2, :]

                def per_sequence(n, rhs, w):
                    out = job(n)
                    for b in range(4):
                        last = nc.tensor.matmul(out[:, 0:w], qz[:, 4 * s + b, :], rhs(b), start=(b == 0), stop=(b == 3))
                    last.then_inc(S["score_ready"], 1)

                per_sequence(CMPJ, lambda b: N["kc"][:, 4 * s + b, :], P)
                pe.wait_ge(S[f"win_loaded{s}"], 64)
                per_sequence(WINJ, lambda b: win[:, b, 0, :], WIN)
                nc.tensor.matmul(job(WTAIL)[:, 0:NS], qf[:, s, :], zn[:, Q_KWIN - 4, TP:T], start=True, stop=True
                                 ).then_inc(S["score_ready"], 1)
                out = job(IMP)
                pe.wait_ge(S["pc_ready"], s + 1)
                nc.tensor.matmul(out[:, 0:P], group[:, :], pc[:, :], start=True, stop=True).then_inc(S["score_ready"], 1)
                for c in range(8):
                    pe.wait_ge(S[f"k_loaded{c % 2}"], 128 * (4 * s + c // 2 + 1))
                    pe.wait_ge(S[f"k_soft{c % 2}"], 128 * (4 * s + c // 2 + 1))
                    per_sequence(SEL0 + c, lambda b: kbuf[:, c % 2, b, :], 4 * PAGE)
                nc.tensor.matmul(job(STAIL)[:, 0:NS], qf[:, s, :], zn[:, Q_KSEL - 4, TP:T], start=True, stop=True
                                 ).then_inc(S["score_ready"], 1)

                def turn(n, src, w, k):
                    n += s * NT
                    if n >= 2:
                        pe.wait_ge(S["turn_copied"], n - 1)
                    for j in range(k):
                        last = nc.tensor.transpose(psum[0:w, 2 + n % 2, j * P:(j + 1) * P], src[:, j * w:(j + 1) * w], K["ident"][:, :])
                    last.then_inc(S["turn_ready"], 1)

                def products(n, w, k, value):
                    first, last_job = n == TC, n == TST
                    n += s * NT
                    pe.wait_ge(S["turn_copied"], n + 1)
                    if first:
                        pe.wait_ge(S["out_copied"], s + 1)
                    for j in range(k):
                        for b in range(4):
                            last = nc.tensor.matmul(psum[:, 4 + b, 0:32], value(b, j), pt[0:w, n % 2, j, b * 32:(b + 1) * 32],
                                                    start=first and j == 0, stop=last_job and j == k - 1)
                    last.then_inc(S["pv_ready"], 1)

                pe.wait_ge(S["probs_ready"], 3 * s + 1)
                turn(TC, pcg[:, :], P, 1)
                products(TC, P, 1, lambda b, j: N["vc"][:, 4 * s + b, :])
                pe.wait_ge(S["probs_ready"], 3 * s + 2)
                turn(TW, ws[:, 0:WIN], P, 4)
                products(TW, P, 4, lambda b, j: win[:, b, 1, j * P:(j + 1) * P])
                turn(TWT, ws[:, WIN:WIN + NS], NS, 1)
                products(TWT, NS, 1, lambda b, j: tokn[0:NS, NTILE, N_VWIN:N_VWIN + P])
                pe.wait_ge(S["probs_ready"], 3 * s + 3)
                turn(TS0, ss[:, 0:4 * P], P, 4)
                for c in range(8):
                    if c < 7:
                        turn(TS0 + c + 1, ss[:, (c + 1) * 4 * P:(c + 2) * 4 * P], P, 4)
                    pe.wait_ge(S[f"v_loaded{c % 2}"], 128 * (4 * s + c // 2 + 1))
                    pe.wait_ge(S[f"v_soft{c % 2}"], 128 * (4 * s + c // 2 + 1))
                    products(TS0 + c, P, 4, lambda b, j: vbuf[:, c % 2, b, j * P:(j + 1) * P])
                turn(TST, ss[:, PAST:PAST + NS], NS, 1)
                products(TST, NS, 1, lambda b, j: tokn[0:NS, NTILE, N_VSEL:N_VSEL + P])

        @block.scalar
        def _(act):
            for s in range(2):
                def exp(k, x):
                    act.wait_ge(S["max_ready"], 3 * s + k + 1)
                    nc.scalar.activation(x, x, ACT.Exp, bias=nm[:, k:k + 1], accum_out=sums[:, k:k + 1]).then_inc(S["exp_ready"], 1)

                def gate(k, dst, x):
                    act.wait_ge(S["scale_ready"], 3 * s + k + 1)
                    act.wait_ge(S["exp_ready"], 3 * s + k + 1)
                    nc.scalar.activation(dst, x, ACT.Copy, scale=rs[:, k:k + 1]).then_inc(S["probs_ready"], 1)

                def copy(n, w, k):
                    n += s * NT
                    act.wait_ge(S["turn_ready"], n + 1)
                    if n >= 2:
                        act.wait_ge(S["pv_ready"], n - 1)
                    nc.scalar.activation(pt[0:w, n % 2, 0:k, :], psum[0:w, 2 + n % 2, 0:k * P].rearrange("p (k r) -> p k r", k=k),
                                         ACT.Copy).then_inc(S["turn_copied"], 1)

                exp(0, pc[:, :])
                exp(1, ws[:, :])
                gate(0, pcg[:, :], pc[:, :])
                gate(1, ws[:, :], ws[:, :])
                exp(2, ss[:, :])
                gate(2, ss[:, :], ss[:, :])
                copy(TC, P, 1)
                copy(TW, P, 4)
                copy(TWT, NS, 1)
                for c in range(8):
                    copy(TS0 + c, P, 4)
                copy(TST, NS, 1)

        @block.vector
        def _(ve):
            ch = Chain(ve, S["steps"])
            ve.wait_ge(S["loaded"], 96)
            dst = relr[:, :, :, :].rearrange("p b h q -> p b (h q)")
            ch.link(nc.vector.tensor_copy(relr[:, 0, :, :], relq[:, :].unsqueeze(2).to_broadcast([P, NH, TS])))
            ch.link(nc.vector.tensor_tensor(relr[:, 0, :, :], relr[:, 0, :, :], delta[:, :].unsqueeze(1).to_broadcast([P, NH, TS]), ALU.mult))
            nc.vector.tensor_copy(relr[:, 1:4, :, :].rearrange("p b h q -> p b (h q)"),
                                  relr[:, 0, :, :].rearrange("p h q -> p (h q)").unsqueeze(1).to_broadcast([P, 3, NH * TS])
                                  ).then_inc(S["rel_ready"], 1)
            nc.vector.memset(qz[:, :, :], 0.0)
            ch.link(nc.vector.memset(qf[:, :, :], 0.0))
            for s in range(2):
                for g in range(2):
                    half = slice(g * HD, (g + 1) * HD)
                    for b in range(4):
                        q = 4 * s + b
                        last = nc.vector.tensor_scalar(
                            qf[half, s, b * 32 + g * 16:b * 32 + (g + 1) * 16].rearrange("p (i q) -> p i q", q=TS),
                            zn[half, 0:NPAIR, TP + q * TS:TP + (q + 1) * TS], CMP_SCALE, None, ALU.mult)
            ch.link(last)
            for q in range(NSEQ):
                c = slice((q % 4) * 32, (q % 4 + 1) * 32)
                last = nc.vector.tensor_copy(qz[:, q, c], qf[:, q // 4, c])
            last.then_inc(S["q_ready"], 1)
            ve.wait_ge(S["bias_ready"], 1)
            for n, c in enumerate(range(0, BW, 512)):
                w = min(512, BW - c)
                last = nc.vector.tensor_copy(bias[:, c:c + w], psum[:, 5 + n, 0:w])
            last.then_inc(S["out_copied"], 1)
            ve.wait_ge(S["out_copied"], 1)
            ve.wait_ge(S["gates_loaded"], 16 * 64)
            for s in range(2):
                def job(n):
                    n += s * NJ
                    ve.wait_ge(S["score_ready"], n + 1)
                    return psum[:, n % 2, :]

                def most(k, x):
                    nc.vector.tensor_reduce(nm[:, k:k + 1], x, AX.X, ALU.max, negate=True).then_inc(S["max_ready"], 1)

                def scale(k, g):
                    ve.wait_ge(S["exp_ready"], 3 * s + k + 1)
                    ch.link(nc.vector.reciprocal(rs[:, k:k + 1], sums[:, k:k + 1]))
                    if k == 0:
                        ch.link(nc.vector.tensor_scalar(pc[:, :], pc[:, :], rs[:, 0:1], None, ALU.mult))
                        nc.vector.tensor_copy(rs[:, 0:1], gr[:, s, 0:1]).then_inc(S["scale_ready"], 1)
                    else:
                        nc.vector.tensor_tensor(rs[:, k:k + 1], rs[:, k:k + 1], gr[:, s, g:g + 1], ALU.mult).then_inc(S["scale_ready"], 1)

                def drained(ins, n):
                    ins.then_inc(S["score_drained"], 1)
                    ve.wait_ge(S["score_drained"], s * NJ + n + 1)

                if s:
                    ve.wait_ge(S["turn_ready"], NT)
                x = job(CMPJ)
                drained(nc.vector.tensor_tensor(pc[:, :], x[:, 0:P], bias[:, CMPC:CMPC + P], ALU.add), CMPJ)
                most(0, pc[:, :])
                x = job(WINJ)
                drained(nc.vector.tensor_tensor(ws[:, 0:WIN], x, bias[:, WIN:2 * WIN], ALU.add), WINJ)
                ch.link(nc.vector.tensor_tensor(ws[:, 0:TS], ws[:, 0:TS], wmask[:, :], ALU.add))
                x = job(WTAIL)
                drained(nc.vector.tensor_tensor(ws[:, WIN:WIN + NS], x[:, 0:NS], bias[:, TAILC:BW], ALU.add), WTAIL)
                ch.link(nc.vector.tensor_tensor(ws[:, WIN:WIN + NS], ws[:, WIN:WIN + NS], tmask[:, s, :], ALU.add))
                most(1, ws[:, :])
                scale(0, 0)
                nc.vector.memset(imp[:, NBLK:NBLK + 1], 1.0e4).then_inc(S["pc_ready"], 1)
                x = job(IMP)
                drained(nc.vector.tensor_reduce(imp[:, 0:NBLK], x[:, 0:P].rearrange("p (b c) -> p b c", c=SB // CB), AX.X, ALU.add), IMP)
                ch.link(nc.vector.memset(imp[:, 0:1], 1.0e4))
                for r in range(TOPK // 8):
                    ch.link(nc.vector.max(top[:, 8 * r:8 * r + 8], imp[:, :]))
                    ch.link(nc.vector.match_replace(imp[:, :], top[:, 8 * r:8 * r + 8], imp[:, :], -4.0))
                ch.link(nc.vector.tensor_scalar(bmask[:, :], imp[:, :], -2.0, NEG, ALU.is_gt, ALU.mult))
                for c in range(8):
                    x = job(SEL0 + c)
                    out = ss[:, c * 512:(c + 1) * 512].rearrange("p (b t) -> p b t", t=SB)
                    mask = bmask[:, 8 * c:8 * c + 8].unsqueeze(2).to_broadcast([P, 8, SB])
                    x3 = x.rearrange("p (b t) -> p b t", t=SB)
                    if c < 6:
                        drained(nc.vector.scalar_tensor_tensor(out=out, in0=x3, scalar=bias[:, 0:1], in1=mask,
                                                               op0=ALU.add, op1=ALU.add), SEL0 + c)
                    else:
                        drained(nc.vector.tensor_tensor(ss[:, c * 512:(c + 1) * 512], x, bias[:, (c - 6) * 512:(c - 5) * 512],
                                                        ALU.add), SEL0 + c)
                        ch.link(nc.vector.tensor_tensor(out, out, mask, ALU.add))
                x = job(STAIL)
                drained(nc.vector.tensor_tensor(ss[:, PAST:PAST + NS], x[:, 0:NS], bias[:, TAILC:BW], ALU.add), STAIL)
                ch.link(nc.vector.tensor_tensor(ss[:, PAST:PAST + NS], ss[:, PAST:PAST + NS], tmask[:, s, :], ALU.add))
                scale(1, 2)
                most(2, ss[:, :])
                scale(2, 1)
                ve.wait_ge(S["pv_ready"], (s + 1) * NT)
                for g in range(2):
                    half = slice(g * HD, (g + 1) * HD)
                    for b in range(4):
                        q = 4 * s + b
                        last = nc.vector.tensor_copy(on[half, 0:NPAIR, TP + q * TS:TP + (q + 1) * TS],
                                                     psum[half, 4 + b, g * 16:(g + 1) * 16].rearrange("p (i q) -> p i q", q=TS))
                last.then_inc(S["out_copied"], 1)


def merge(nc, A, h, hm, on, dst, acc):
    SPAN = 2 * (KD + 4) * P
    with stage(nc, "merge") as (ctx, sem):
        ring = ctx.enter_context(nc.sbuf_tensor("mg_ring", [P, 2, SPAN], F32))
        sg = ctx.enter_context(nc.sbuf_tensor("mg_gate", [P, 2, T], F32))
        part = ctx.enter_context(nc.sbuf_tensor("mg_part", [P, T], F32))
        w_loaded = [sem("w_loaded0"), sem("w_loaded1")]
        gate_ready, branch_ready, gate_drained, branch_drained, parts = map(
            sem, ("gate_ready", "branch_ready", "gate_drained", "branch_drained", "parts"))
        h_loaded = [sem(f"h_loaded{g}") for g in range(NG)]
        block = ctx.enter_context(nc.Block())
        n_chunks = D // P

        @block.sync
        def _(sp):
            for j in range(2):
                sp.dma_start(ring[:, j, :], A["w_merge"][j]).then_inc(w_loaded[j], 16)
            with sp.Fori(1, n_chunks // 2) as i:
                for j in range(2):
                    sp.wait_ge(branch_ready, 4 * i + 2 * j - 2)
                    sp.dma_start(ring[:, j, :], A["w_merge"][ds(2 * i + j, 1), :, :].rearrange("a p k -> p (a k)")
                                 ).then_inc(w_loaded[j], 16)

        @block.tensor
        def _(pe):
            with pe.Fori(0, n_chunks // 2) as i:
                for j in range(2):
                    pe.wait_ge(w_loaded[j], 16 * i + 16)
                    for r, (branch, x) in enumerate(((0, hm), (1, on))):
                        base = r * (KD + 4) * P
                        pe.wait_ge(gate_drained, 4 * i + 2 * j + r + 1)
                        for g in range(NG):
                            pe.wait_ge(h_loaded[g], 16)
                            for k in range(KD):
                                last = nc.tensor.matmul(acc[:, g, 0:GW], ring[:, j, base + k * P:base + (k + 1) * P],
                                                        h[:, k, g * GW:(g + 1) * GW], start=(k == 0), stop=(k == KD - 1))
                        last.then_inc(gate_ready, 1)
                        base += KD * P
                        pe.wait_ge(branch_drained, 4 * i + 2 * j + r + 2)
                        for g in range(NG):
                            for k in range(4):
                                last = nc.tensor.matmul(acc[:, 3 + g, 0:GW], ring[:, j, base + k * P:base + (k + 1) * P],
                                                        x[:, k, g * GW:(g + 1) * GW], start=(k == 0), stop=(k == 3))
                        last.then_inc(branch_ready, 1)

        @block.scalar
        def _(act):
            for g in range(NG):
                c = slice(g * GW, (g + 1) * GW)
                act.dma_start(h[:, :, c], A["h_spill"][:, :, c]).then_inc(h_loaded[g], 16)
            act.sem_inc(gate_drained, 1)
            with act.Fori(0, n_chunks) as i:
                for r in range(2):
                    act.wait_ge(gate_ready, 2 * i + r + 1)
                    if r == 0:
                        act.wait_ge(branch_drained, 2 * i + 1)
                    else:
                        act.wait_ge(parts, i + 1)
                    nc.scalar.activation(sg[:, r, :].rearrange("p (g t) -> p g t", g=NG), acc[:, 0:NG, 0:GW], ACT.Sigmoid
                                         ).then_inc(gate_drained, 1)

        @block.vector
        def _(ve):
            ve.sem_inc(branch_drained, 2)
            ve.sem_inc(parts, 1)
            with ve.Fori(0, n_chunks) as i:
                for r in range(2):
                    ve.wait_ge(gate_drained, 2 * i + r + 2)
                    ve.wait_ge(branch_ready, 2 * i + r + 1)
                    gate = sg[:, r, :].rearrange("p (g t) -> p g t", g=NG)
                    if r == 0:
                        ve.wait_ge(parts, i + 1)
                    dst_r = part[:, :].rearrange("p (g t) -> p g t", g=NG) if r == 0 else gate
                    nc.vector.tensor_tensor(dst_r, acc[:, NG:2 * NG, 0:GW], gate, ALU.mult).then_inc(branch_drained, 1)
                    ve.wait_ge(branch_drained, 2 * i + r + 3)
                nc.vector.tensor_tensor(dst[:, ds(i, 1), :].rearrange("p a t -> p (a t)"), part[:, :], sg[:, 1, :], ALU.add
                                        ).then_inc(parts, 1)


def cross_prompt(nc, O, K, qx, mk, mv, ox, psum):
    with stage(nc, "xp") as (ctx, sem):
        sb = lambda n, s: ctx.enter_context(nc.sbuf_tensor("xp_" + n, s, F32))
        q = sb("q", [P, KD, P])
        p, pt = sb("p", [P, 2, MEM]), sb("pt", [P, 2, 2, P])
        nm, sums = sb("nm", [P, 2]), sb("sums", [P, 2])
        names = ("q_ready", "score_ready", "max_ready", "exp_ready", "inverted", "probs_ready", "turn_ready", "turn_copied",
                 "pv_ready", "out_ready", "stored")
        S = {n: sem(n) for n in names}
        block = ctx.enter_context(nc.Block())
        DC = KD // XH

        @block.sync
        def _(sp):
            sp.dma_start(O["mk"], mk[:, :, :]).then_inc(S["stored"], 16)
            sp.dma_start(O["mv"], mv[:, :, :]).then_inc(S["stored"], 16)
            sp.wait_ge(S["stored"], 32)

        @block.tensor
        def _(pe):
            def scores(i, h):
                for c in range(DC):
                    last = nc.tensor.matmul(psum[:, h % 2, 0:MEM], q[:, DC * h + c, :], mk[:, DC * h + c, :],
                                            start=(c == 0), stop=(c == DC - 1))
                last.then_inc(S["score_ready"], 1)

            with pe.Fori(0, NTILE) as i:
                pe.wait_ge(S["q_ready"], i + 1)
                scores(i, 0)
                for h in range(XH):
                    if h + 1 < XH:
                        if h >= 1:
                            pe.wait_ge(S["exp_ready"], XH * i + h)
                        scores(i, h + 1)
                    pe.wait_ge(S["probs_ready"], XH * i + h + 1)
                    for m in range(2):
                        last = nc.tensor.transpose(psum[:, 2 + h % 2, m * P:(m + 1) * P], p[:, h % 2, m * P:(m + 1) * P], K["ident"][:, :])
                    last.then_inc(S["turn_ready"], 1)
                    pe.wait_ge(S["turn_copied"], XH * i + h + 1)
                    for c in range(DC):
                        for m in range(2):
                            last = nc.tensor.matmul(psum[:, 4 + h % 2, c * P:(c + 1) * P], mv[:, m, (DC * h + c) * P:(DC * h + c + 1) * P],
                                                    pt[:, h % 2, m, :], start=(m == 0), stop=(m == 1))
                    last.then_inc(S["pv_ready"], 1)

        @block.scalar
        def _(act):
            with act.Fori(0, NTILE) as i:
                for h in range(XH):
                    act.wait_ge(S["max_ready"], XH * i + h + 1)
                    nc.scalar.activation(p[:, h % 2, :], psum[:, h % 2, 0:MEM], ACT.Exp, bias=nm[:, h % 2:h % 2 + 1],
                                         accum_out=sums[:, h % 2:h % 2 + 1]).then_inc(S["exp_ready"], 1)
                    act.wait_ge(S["turn_ready"], XH * i + h + 1)
                    nc.scalar.activation(pt[:, h % 2, :, :], psum[:, 2 + h % 2, 0:2 * P].rearrange("p (m q) -> p m q", m=2), ACT.Copy
                                         ).then_inc(S["turn_copied"], 1)

        @block.vector
        def _(ve):
            with ve.Fori(0, NTILE) as i:
                nc.vector.tensor_scalar(q[:, :, :], qx[:, :, ds(i * P, P)], float(D // XH) ** -0.5, None, ALU.mult
                                        ).then_inc(S["q_ready"], 1)

                def most(h):
                    ve.wait_ge(S["score_ready"], XH * i + h + 1)
                    nc.vector.tensor_reduce(nm[:, h % 2:h % 2 + 1], psum[:, h % 2, 0:MEM], AX.X, ALU.max, negate=True
                                            ).then_inc(S["max_ready"], 1)

                most(0)
                for h in range(XH):
                    s = sums[:, h % 2:h % 2 + 1]
                    ve.wait_ge(S["exp_ready"], XH * i + h + 1)
                    nc.vector.reciprocal(s, s).then_inc(S["inverted"], 1)
                    ve.wait_ge(S["inverted"], XH * i + h + 1)
                    nc.vector.tensor_scalar(p[:, h % 2, :], p[:, h % 2, :], s, None, ALU.mult).then_inc(S["probs_ready"], 1)
                    if h + 1 < XH:
                        most(h + 1)
                    ve.wait_ge(S["pv_ready"], XH * i + h + 1)
                    nc.vector.tensor_scalar(ox[:, DC * h:DC * (h + 1), ds(i * P, P)],
                                            psum[:, 4 + h % 2, 0:DC * P].rearrange("p (c q) -> p c q", c=DC), 1.0, None, ALU.mult
                                            ).then_inc(S["out_ready"], 1)
                ve.wait_ge(S["out_ready"], XH * i + XH)


def cross_sample(nc, A, K, qx, ox, psum):
    with stage(nc, "xs") as (ctx, sem):
        sb = lambda n, s: ctx.enter_context(nc.sbuf_tensor("xs_" + n, s, F32))
        qz = sb("qz", [P, NSEQ, KD, P])
        kv = sb("kv", [P, 2, KD * MEM])
        p, pt = sb("p", [P, MEM]), sb("pt", [P, 2, P])
        nm, sums = sb("nm", [P, 1]), sb("sums", [P, 1])
        cleared, q_ready, k_used, score_ready, max_ready, exp_ready, inverted, probs_ready, turn_ready, turn_copied, v_used = map(sem, (
            "cleared", "q_ready", "k_used", "score_ready", "max_ready", "exp_ready", "inverted", "probs_ready", "turn_ready",
            "turn_copied", "v_used"))
        loaded = [sem("loaded0"), sem("loaded1")]
        block = ctx.enter_context(nc.Block())
        DC = KD // XH

        @block.sync
        def _(sp):
            for n in range(2 * NSEQ):
                if n >= 2:
                    used, at = (k_used, n - 1) if n - 2 < NSEQ else (v_used, n - 1 - NSEQ)
                    sp.wait_ge(used, at)
                src = A["mem_k"][n] if n < NSEQ else A["mem_v"][n - NSEQ]
                sp.dma_start(kv[:, n % 2, :], src).then_inc(loaded[n % 2], 16)

        @block.gpsimd
        def _(pool):
            nc.gpsimd.memset(qz[:, :, :, :], 0.0).then_inc(cleared, 1)

        @block.vector
        def _(ve):
            ve.wait_ge(cleared, 1)
            for b in range(NSEQ):
                for h in range(XH):
                    r = b * XH * TS + h * TS
                    nc.vector.tensor_scalar(qz[:, b, DC * h:DC * (h + 1), r:r + TS],
                                            qx[:, DC * h:DC * (h + 1), TP + b * TS:TP + (b + 1) * TS],
                                            float(D // XH) ** -0.5, None, ALU.mult).then_inc(q_ready, 1)
            ve.wait_ge(k_used, NSEQ)
            nc.vector.tensor_reduce(nm[:, :], psum[:, 0, 0:MEM], AX.X, ALU.max, negate=True).then_inc(max_ready, 1)
            ve.wait_ge(exp_ready, 1)
            nc.vector.reciprocal(sums[:, :], sums[:, :]).then_inc(inverted, 1)
            ve.wait_ge(inverted, 1)
            nc.vector.tensor_scalar(p[:, :], p[:, :], sums[:, 0:1], None, ALU.mult).then_inc(probs_ready, 1)
            ve.wait_ge(v_used, NSEQ)
            nc.vector.tensor_copy(ox[:, :, TP:T], psum[:, 2, 0:KD * NS].rearrange("p (c t) -> p c t", c=KD))

        @block.scalar
        def _(act):
            act.wait_ge(max_ready, 1)
            nc.scalar.activation(p[:, :], psum[:, 0, 0:MEM], ACT.Exp, bias=nm[:, 0:1], accum_out=sums[:, 0:1]).then_inc(exp_ready, 1)
            act.wait_ge(turn_ready, 1)
            nc.scalar.activation(pt[:, :, :], psum[:, 1, 0:2 * P].rearrange("p (m q) -> p m q", m=2), ACT.Copy).then_inc(turn_copied, 1)

        @block.tensor
        def _(pe):
            pe.wait_ge(q_ready, NSEQ * XH)
            for b in range(NSEQ):
                pe.wait_ge(loaded[b % 2], 16 * (b // 2 + 1))
                for c in range(KD):
                    last = nc.tensor.matmul(psum[:, 0, 0:MEM], qz[:, b, c, :], kv[:, b % 2, c * MEM:(c + 1) * MEM],
                                            start=(b == 0 and c == 0), stop=(b == NSEQ - 1 and c == KD - 1))
                last.then_inc(k_used, 1)
            pe.wait_ge(probs_ready, 1)
            for m in range(2):
                last = nc.tensor.transpose(psum[:, 1, m * P:(m + 1) * P], p[:, m * P:(m + 1) * P], K["ident"][:, :])
            last.then_inc(turn_ready, 1)
            pe.wait_ge(turn_copied, 1)
            for b in range(NSEQ):
                n = NSEQ + b
                pe.wait_ge(loaded[n % 2], 16 * (n // 2 + 1))
                for c in range(KD):
                    r = b * XH * TS + (c // DC) * TS
                    for m in range(2):
                        last = nc.tensor.matmul(psum[:, 2, c * NS + b * TS:c * NS + (b + 1) * TS],
                                                kv[:, n % 2, m * D + c * P:m * D + (c + 1) * P], pt[:, m, r:r + TS],
                                                start=(m == 0), stop=(m == 1))
                last.then_inc(v_used, 1)


def ffn(nc, A, O, h, mid, ring, acc):
    with stage(nc, "ffn") as (ctx, sem):
        sb = lambda n, s: ctx.enter_context(nc.sbuf_tensor("ff_" + n, s, F32))
        taps = sb("taps", [P, KF, 4])
        state = sb("state", [P, KF, NSEQ, 2])
        pstate = sb("pstate", [P, KF, 2])
        tap = sb("tap", [P, 4])
        u, cv = sb("u", [P, T]), sb("cv", [P, T])
        us, cs = sb("us", [P, NSEQ, 2 + TS]), sb("cs", [P, NSEQ, TS])
        names = ("loaded", "wu_loaded", "wg_loaded", "u_ready", "u_copied", "gate_ready", "conv_ready", "gelu_ready", "mid_ready",
                 "steps", "stored")
        S = {n: sem(n) for n in names}
        block = ctx.enter_context(nc.Block())

        @block.sync
        def _(sp):
            sp.dma_start(taps[:, :, :], A["f_conv"]).then_inc(S["loaded"], 16)
            sp.dma_start(state[:, :, :, :], A["f_state"]).then_inc(S["loaded"], 16)
            sp.dma_start(ring[:, 0, :], A["f_wu"][0]).then_inc(S["wu_loaded"], 16)
            sp.dma_start(ring[:, 1, :], A["f_wg"][0]).then_inc(S["wg_loaded"], 16)
            with sp.Fori(1, KF) as i:
                sp.wait_ge(S["u_ready"], i)
                sp.dma_start(ring[:, 0, :], A["f_wu"][ds(i, 1), :, :].rearrange("a p k -> p (a k)")).then_inc(S["wu_loaded"], 16)
                sp.wait_ge(S["gate_ready"], i)
                sp.dma_start(ring[:, 1, :], A["f_wg"][ds(i, 1), :, :].rearrange("a p k -> p (a k)")).then_inc(S["wg_loaded"], 16)
            sp.wait_ge(S["mid_ready"], KF + 1)
            sp.dma_start(O["p_fconv"], pstate[:, :, :]).then_inc(S["stored"], 16)
            sp.dma_start(O["s_fconv"], state[:, :, :, :]).then_inc(S["stored"], 16)
            sp.wait_ge(S["stored"], 32)

        @block.tensor
        def _(pe):
            with pe.Fori(0, KF) as i:
                for j, (wl, ready, free) in enumerate((("wu_loaded", "u_ready", "u_copied"), ("wg_loaded", "gate_ready", "mid_ready"))):
                    pe.wait_ge(S[wl], 16 * i + 16)
                    pe.wait_ge(S[free], i + 1)
                    for g in range(NG):
                        for k in range(KD):
                            last = nc.tensor.matmul(acc[:, 3 * j + g, 0:GW], ring[:, j, k * P:(k + 1) * P],
                                                    h[:, k, g * GW:(g + 1) * GW], start=(k == 0), stop=(k == KD - 1))
                    last.then_inc(S[ready], 1)

        @block.scalar
        def _(act):
            act.sem_inc(S["u_copied"], 1)
            with act.Fori(0, KF) as i:
                act.wait_ge(S["u_ready"], i + 1)
                act.wait_ge(S["mid_ready"], i + 1)
                nc.scalar.activation(u[:, :].rearrange("p (g t) -> p g t", g=NG), acc[:, 0:NG, 0:GW], ACT.Copy
                                     ).then_inc(S["u_copied"], 1)
                act.wait_ge(S["conv_ready"], i + 1)
                nc.scalar.activation(cv[:, :], cv[:, :], ACT.Gelu_apprx_tanh).then_inc(S["gelu_ready"], 1)

        @block.vector
        def _(ve):
            STEPS = 7
            ve.wait_ge(S["loaded"], 32)
            ve.sem_inc(S["mid_ready"], 1)
            with ve.Fori(0, KF) as i:
                ch = Chain(ve, S["steps"], i * STEPS)
                nc.vector.tensor_copy(us[:, :, 0:2], state[:, ds(i, 1), :, :].rearrange("p a b t -> p (a b) t"))
                ch.link(nc.vector.tensor_copy(tap[:, :], taps[:, ds(i, 1), :].rearrange("p a k -> p (a k)")))
                ve.wait_ge(S["u_copied"], i + 2)
                nc.vector.tensor_scalar(cv[:, 0:TP], u[:, 0:TP], tap[:, 2:3], tap[:, 3:4], ALU.mult, ALU.add)
                ch.link(nc.vector.tensor_copy(us[:, :, 2:2 + TS], u[:, TP:T].rearrange("p (b t) -> p b t", t=TS)))
                nc.vector.tensor_scalar(pstate[:, ds(i, 1), :].rearrange("p a t -> p (a t)"), u[:, TP - 2:TP], 1.0, None, ALU.mult)
                nc.vector.tensor_scalar(state[:, ds(i, 1), :, :].rearrange("p a b t -> p (a b) t"), us[:, :, TS:TS + 2], 1.0, None, ALU.mult)
                ch.link(nc.vector.tensor_scalar(cs[:, :, :], us[:, :, 2:2 + TS], tap[:, 2:3], tap[:, 3:4], ALU.mult, ALU.add))
                for k in (1, 0):
                    d = 2 - k
                    ch.link(nc.vector.scalar_tensor_tensor(out=cv[:, d:TP], in0=u[:, 0:TP - d], scalar=tap[:, k:k + 1],
                                                           in1=cv[:, d:TP], op0=ALU.mult, op1=ALU.add))
                    ch.link(nc.vector.scalar_tensor_tensor(out=cs[:, :, :], in0=us[:, :, k:k + TS], scalar=tap[:, k:k + 1],
                                                           in1=cs[:, :, :], op0=ALU.mult, op1=ALU.add))
                nc.vector.tensor_copy(cv[:, TP:T].rearrange("p (b t) -> p b t", t=TS), cs[:, :, :]).then_inc(S["conv_ready"], 1)
                ve.wait_ge(S["gelu_ready"], i + 1)
                ve.wait_ge(S["gate_ready"], i + 1)
                nc.vector.tensor_tensor(mid[:, ds(i, 1), :].rearrange("p a (g t) -> p (a g) t", g=NG), acc[:, NG:2 * NG, 0:GW],
                                        cv[:, :].rearrange("p (g t) -> p g t", g=NG), ALU.mult).then_inc(S["mid_ready"], 1)
                ve.wait_ge(S["mid_ready"], i + 2)
                assert ch.n == STEPS, ch.n


def build(nc, A, O):
    with ExitStack() as ctx:
        K = {}

        def sb(name, shape, c=ctx):
            return c.enter_context(nc.sbuf_tensor(name, shape, F32))

        psum = ctx.enter_context(nc.psum_tensor("psum", [P, 8, 512], F32))
        consts = sb("consts", [P, N_CONST])
        for n, (a, w) in CONST_AT.items():
            K[n] = consts[:, a:a + w]
        gains = sb("gains", [P, 6, KD])
        ring = sb("ring", [P, 2, KD * P])
        pages = ctx.enter_context(nc.sbuf_tensor("pages", [1, NSEQ * NPAGE], I32))
        low = sb("low", [P, KD, T])
        hm, zm = low[:, 0:4, :], low[:, 4:8, :]
        x = low
        late = ctx.enter_context(ExitStack())
        zn = sb("zn", [P, NFEAT - 4, T], late)
        tokn = sb("tokn", [P, NTILE + 1, N_END], late)
        branch_gates = sb("branch_gates", [P, NTILE + 1, 3 * NH], late)
        early = ctx.enter_context(ExitStack())
        tokm = sb("tokm", [P, NTILE + 1, C_OG + 512], early)
        with stage(nc, "load") as (c, sem):
            loaded = sem("loaded")
            block = c.enter_context(nc.Block())

            @block.sync
            def _(sp):
                sp.dma_start(consts[:, :], A["consts"]).then_inc(loaded, 16)
                sp.dma_start(gains[:, :, :], A["gains"]).then_inc(loaded, 16)
                sp.dma_start(pages[:, :], A["page_table"]).then_inc(loaded, 16)
                sp.wait_ge(loaded, 48)

        with ExitStack() as c:
            h = sb("h", [P, KD, T], c)
            with ExitStack() as c2:
                sq = sb("sq", [P, 2, T], c2)
                rstd = sb("rstd", [P, T], c2)
                rms_norm(nc, "norm0", K, h, gains[:, 0, :], h, sq, rstd, psum[:, 0:3, :], A["x"], tokn[:, NTILE, :])
            project(nc, "inm", A["w_in"][0:4], 4, KD, h, zm, ring, psum)
            project(nc, "inn", A["w_in"][4:12], 8, KD, h, zn, ring, psum, aside=[(A["h_spill"], h[:, :, :])])
            project_tokens(nc, "int", A["w_tok"], h, [(0, 512, tokm[:, :, 0:512]), (512, 512, tokm[:, :, 512:1024]),
                                                      (1024, TOKW - 1024, tokn)], psum)

        with ExitStack() as c:
            n = NTILE + 1
            sm = {m: sb("s_" + m, [P, n, w], c) for m, w in (("lf", MH), ("b", MH), ("a", MH), ("tmp", MH))}
            sm["g"] = branch_gates
            conv_mlstm(nc, A, O, K, zm, hm)
            gates(nc, A, K, tokm, tokn, sm, psum)
            mlstm(nc, A, O, K, hm, tokm, sm, psum)
            mlstm_sample(nc, A, O, K, hm, tokm, sm, psum)
        early.close()
        with ExitStack() as c:
            N = {"kcmp": sb("kcmp", [P, NCMP], c), "vcmp": sb("vcmp", [NCMP, P], c),
                 "kc": sb("kc", [P, NSEQ, P], c), "vc": sb("vc", [P, NSEQ, P], c), "n_pool": A["pool"].shape[0],
                 "soft": {n: ctx.enter_context(nc.semaphore(n)) for n in ("c0", "c1", "k_soft0", "k_soft1", "v_soft0", "v_soft1")}}
            with ExitStack() as c2:
                N.update({"w1": sb("w1", [P, 2, CB, P], c2), "w2": sb("w2", [P, 2, P], c2), "pb": sb("pb", [P, 2], c2)})
                compress_setup(nc, A, K, N, zn, psum)
                compress_sample(nc, A, K, N, pages, psum)
            nsa_prompt(nc, A, K, N, zn, tokn, branch_gates, zm, psum)
            nsa_sample(nc, A, O, K, N, zn, tokn, branch_gates, pages, zm, psum)

        late.close()
        h = sb("h_again", [P, KD, T])
        with ExitStack() as c:
            dst = sb("merged", [P, KD, T], c)
            merge(nc, A, h, hm, zm, dst, psum)
            project(nc, "wout", A["w_out"], KD, KD, dst, h, ring, psum, aside=[(x[:, :, :], A["x"])])

        def norms(name, g, src, store=None):
            with ExitStack() as c:
                sq, rstd = sb(name + "_sq", [P, 2, T], c), sb(name + "_rstd", [P, 2, T], c)
                residual_norm(nc, name, K, src, gains, g, x, h, sq, rstd, psum[:, 0:3, :], store)

        norms("norm1", 1, h)
        with ExitStack() as c:
            qx = sb("qx", [P, KD, T], c)
            with ExitStack() as c2:
                mk, mv = sb("mk", [P, KD, MEM], c2), sb("mv", [P, 2, D], c2)
                with ExitStack() as c3:
                    mem = sb("mem", [P, KD, MEM], c3)
                    project(nc, "xq", A["x_wq"], KD, KD, h, qx, ring, psum, aside=[(mem[:, :, :], A["mem"])])
                    project(nc, "xk", A["x_wk"], KD, KD, mem, mk, ring, psum, width=MEM, groups=1)
                    project_tokens(nc, "xv", A["x_wv"], mem, [(0, 512, mv[:, :, 0:512]), (512, 512, mv[:, :, 512:1024])], psum, (P, P))
                cross_prompt(nc, O, K, qx, mk, mv, h, psum)
            cross_sample(nc, A, K, qx, h, psum)
            project(nc, "xo", A["x_wo"], KD, KD, h, qx, ring, psum)
            norms("norm2", 3, qx)
        with ExitStack() as c:
            mid = sb("mid", [P, KF, T], c)
            ffn(nc, A, O, h, mid, ring, psum)
            with ExitStack() as c2:
                wide = sb("wide_ring", [P, 2, KF * P], c2)
                project(nc, "down", A["f_wd"], KD, KF, mid, h, wide, psum)
        norms("norm3", 5, h, O["y"])




def shape_constants():
    i = np.arange(P)
    c = {}
    c["ident"] = np.eye(P)
    c["ones"] = np.ones((P, P))
    c["tri"] = (i[:, None] <= i[None, :]) * 1.0
    same = (i[:, None] // TS == i[None, :] // TS) & (i[:, None] < NS) & (i[None, :] < NS)
    c["stri"] = same * c["tri"]
    c["last"] = (i[:, None] == P - 1) * np.ones((1, P))
    seq = np.arange(NSEQ)
    c["slast"] = same * (i[:, None] % TS == TS - 1)
    c["slast8"] = (i[:, None] == seq[None, :] * TS + TS - 1) * 1.0
    c["sseq8"] = (i[:, None] // TS == seq[None, :]) * 1.0
    c["scausal"] = np.where(c["stri"].T > 0, 0.0, NEG)[:, 0:NS]
    c["scausal_t"] = np.where(c["stri"] > 0, 0.0, NEG)[:, 0:NS]
    c["flip"] = np.eye(P)[::-1]
    c["seen"] = (i[:, None] >= CB - 1) * 1.0
    c["wmask"] = np.where(i[None, :] <= i[:, None], NEG, 0.0)
    c["causal"] = np.where(i[None, :] <= i[:, None], 0.0, NEG)
    c["causal_t"] = np.ascontiguousarray(c["causal"].T)
    return c


CONST = shape_constants()
CONST_AT, N_CONST = {}, 0
for _n, _v in CONST.items():
    CONST_AT[_n] = (N_CONST, _v.shape[1])
    N_CONST += _v.shape[1]


def chunked(w):
    k, m = w.shape
    return np.ascontiguousarray(w.reshape(k // P, P, m // P, P).transpose(2, 1, 0, 3)).reshape(m // P, P, k)


def feature_rows(a):
    return np.ascontiguousarray(a.reshape(a.shape[0], -1, P).transpose(2, 1, 0))


def lay_out(v):
    L = {}
    x = np.concatenate([v["x_prompt"].reshape(TP, D), v["x_sample"].reshape(NS, D)])
    L["x"] = feature_rows(x)
    L["consts"] = np.concatenate([CONST[n] for n in CONST_AT], axis=1).astype(np.float32)
    L["gains"] = np.ascontiguousarray(v["norms"][0].reshape(6, KD, P).transpose(2, 0, 1))
    w = v["w_in"][0]
    at, parts = 0, []
    for n in (512, 512, 4, 4, 512, 512, 256, 256, 256, 24, 1024, 1024):
        parts.append(w[:, at:at + n])
        at += n
    xm, val, ig, fg, og, qn, kvc, kvs, kvw, gn, ga, gb = parts
    pair = np.array([h * HD + e for i in range(NPAIR) for h in (i, NPAIR + i) for e in range(HD)])
    L["w_in"] = chunked(np.concatenate([xm, qn[:, pair], kvc, kvs[:, 0:128], kvw[:, 0:128]], axis=1))
    tok = np.concatenate([val, og, kvs[:, 128:], kvw[:, 128:], ig, fg, gn], axis=1)
    L["w_tok"] = np.ascontiguousarray(tok.reshape(KD, P, TOKW).transpose(1, 0, 2))
    L["m_conv"] = np.ascontiguousarray(np.concatenate([v["m_conv_w"][0], v["m_conv_b"]]).reshape(5, 4, P).transpose(2, 1, 0))
    L["m_state"] = np.ascontiguousarray(v["state_mlstm_conv"][0].reshape(NSEQ, 3, 4, P).transpose(3, 2, 0, 1))
    L["gate_b"] = v["m_gate_b"].reshape(8)
    L["m_wqk"] = np.ascontiguousarray(np.stack([v["m_wq"][0], v["m_wk"][0]]).transpose(2, 0, 1, 3))
    L["m_norm"] = v["m_norm"][0]
    dist = TP - 1 - np.arange(2048)
    L["onehot"] = (bias_buckets(dist)[None, :] == np.arange(NBUCKET)[:, None]).astype(np.float32)
    L["rmask"] = np.tile(np.where(dist >= 0, 0.0, NEG), (NH, 1)).astype(np.float32)
    L["rel"] = v["rel_bias"]
    w1 = v["cmp_w1"][0].reshape(2, CB, HD, HD)
    w2 = v["cmp_w2"][0]
    both = np.zeros((P, 2, CB, P), np.float32)
    both2 = np.zeros((P, 2, P), np.float32)
    for g in range(2):
        half = slice(g * HD, (g + 1) * HD)
        both[half, :, :, half] = w1.transpose(2, 0, 1, 3)
        both2[half, :, half] = w2.transpose(1, 0, 2)
    L["cmp_w1"], L["cmp_w2"] = both, both2
    pe = v["cmp_pe"][0].transpose(2, 0, 1)
    L["cmp_pe"] = np.ascontiguousarray(np.concatenate([pe, pe]))
    cache = v["cache_nsa_kv"][0].reshape(-1, PAGE, 4, P)
    pool = cache.transpose(0, 3, 2, 1).copy()
    pool[:, :, 3, :] = cache[:, :, 3, :]
    L["pool"] = pool.reshape(-1, P, 4 * PAGE)
    L["page_table"] = v["page_table"].reshape(1, NSEQ * NPAGE)
    w = v["cache_win_kv"][0].reshape(NSEQ, WIN, 2, P)
    winp = np.empty((NSEQ, P, 2, WIN), np.float32)
    winp[:, :, 0] = w[:, :, 0].transpose(0, 2, 1)
    winp[:, :, 1] = w[:, :, 1].reshape(NSEQ, 4, P, P).transpose(0, 2, 1, 3).reshape(NSEQ, P, WIN)
    L["winp"] = winp
    L["relq"] = np.tile(v["rel_bias"], (TS, 1))
    qd = np.arange(P) // NBUCKET
    near = PAST + qd[:, None] - (PAST - 1024 + np.arange(1024))[None, :]
    blocks = PAST + qd[:, None] - (np.arange(P) * CB + CB - 1)[None, :]
    tail = qd[:, None] - (np.arange(NS) % TS)[None, :]
    dist = np.concatenate([near, blocks, tail], axis=1)
    L["onehot_s"] = (bias_buckets(dist) == (np.arange(P) % NBUCKET)[:, None]).astype(np.float32)
    L["delta"] = (qd[:, None] == np.arange(TS)[None, :]).astype(np.float32)
    row = np.arange(P)
    rb, rg, rq = row // 32, row // 16 % 2, row % TS
    L["group"] = ((rb[:, None] == rb) & (rg[:, None] == rg) & (rq[:, None] == rq)).astype(np.float32)
    tok = np.arange(NS)
    ok = [(tok // TS == 4 * s + rb[:, None]) & (tok % TS <= rq[:, None]) for s in range(2)]
    L["tmask"] = np.where(np.stack(ok, 1), 0.0, NEG).astype(np.float32)
    L["wmask_s"] = np.where(np.arange(TS) <= rq[:, None], NEG, 0.0).astype(np.float32)
    ca, cb = chunked(ga), chunked(gb)
    um, un = chunked(v["w_up_m"][0]), chunked(v["w_up_n"][0][pair])
    L["w_merge"] = np.concatenate([ca, um, cb, un], axis=2)
    L["w_out"] = chunked(v["w_out"][0])
    L["x_wq"], L["x_wo"] = chunked(v["x_wq"][0]), chunked(v["x_wo"][0])
    L["mem"] = feature_rows(v["mem_prompt"][0])
    L["x_wk"] = chunked(v["x_wkv"][0][:, 0:D])
    L["x_wv"] = np.ascontiguousarray(v["x_wkv"][0][:, D:].reshape(KD, P, D).transpose(1, 0, 2))
    mem = v["cache_mem_kv"][0].reshape(NSEQ, MEM, 2, KD, P)
    L["mem_k"] = np.ascontiguousarray(mem[:, :, 0].transpose(0, 3, 2, 1)).reshape(NSEQ, P, KD * MEM)
    L["mem_v"] = np.ascontiguousarray(mem[:, :, 1].reshape(NSEQ, 2, P, D).transpose(0, 2, 1, 3)).reshape(NSEQ, P, 2 * D)
    L["f_wu"], L["f_wg"], L["f_wd"] = chunked(v["f_wu"][0]), chunked(v["f_wg"][0]), chunked(v["f_wd"][0])
    L["f_conv"] = np.ascontiguousarray(np.concatenate([v["f_conv_w"][0], v["f_conv_b"]]).reshape(4, KF, P).transpose(2, 1, 0))
    L["f_state"] = np.ascontiguousarray(v["state_ffn_conv"][0].reshape(NSEQ, 2, KF, P).transpose(3, 2, 0, 1))
    L["s_C0"] = np.ascontiguousarray(v["state_mlstm_C"][0].transpose(3, 0, 1, 2))
    L["s_n0"] = v["state_mlstm_n"][0]
    L["s_n0t"] = np.repeat(v["state_mlstm_n"][0], TS, axis=0)
    L["s_m0t"] = np.repeat(v["state_mlstm_m"][0], TS, axis=0)
    return L


SCRATCH = {"gate_rows": (NS, 3 * NH), "bias_vec": (NH, 2048), "h_spill": (P, KD, T)}
OUTS = {"y": (P, KD, T), "p_mconv": (P, 4, 3), "s_mconv": (P, 4, NSEQ, 3), "p_C": (P, MH, MD), "p_n": (P, MH),
        "p_m": (1, MH), "s_C": (P, NSEQ, MH, MD), "s_n": (NSEQ, MH, MD), "s_m": (NSEQ, MH), "winp": (NSEQ, P, 2, WIN),
        "mk": (P, KD, MEM), "mv": (P, 2, D), "p_fconv": (P, KF, 2), "s_fconv": (P, KF, NSEQ, 2), "zkv": (P, 4, T), "tkv": (P, NTILE + 1, 2 * P)}


def kernel(**inputs):
    import concourse.bacc as bacc
    from concourse.bass_utils import run_bass_kernel_spmd

    v = {n: np.asarray(a) for n, a in inputs.items()}
    nc = bacc.Bacc("TRN2", target_bir_lowering=False, num_devices=1)
    L = lay_out(v)
    A = {n: nc.dram_tensor("in_" + n, a.shape, mybir.dt.from_np(a.dtype), kind="ExternalInput").ap() for n, a in L.items()}
    for n, s in SCRATCH.items():
        A[n] = nc.dram_tensor(n, s, F32, kind="Internal").ap()
    O = {n: nc.dram_tensor("out_" + n, s, F32, kind="ExternalOutput").ap() for n, s in OUTS.items()}
    build(nc, A, O)
    r = run_bass_kernel_spmd(nc, [{"in_" + n: a for n, a in L.items()}], core_ids=[0]).results[0]
    R = {n: r["out_" + n] for n in OUTS}

    y = R["y"].transpose(2, 1, 0).reshape(T, D)
    kz, kt = R["zkv"].transpose(2, 1, 0), R["tkv"].transpose(1, 0, 2).reshape(-1, 2, P)[:T]
    rows = np.stack([kz[:, 0], kz[:, 1], kz[:, 2], kt[:, 0]], axis=1).reshape(T, 4, 2, HD)
    wnew = np.stack([kz[:, 3], kt[:, 1]], axis=1).reshape(T, 2, 2, HD)
    wold = np.stack([R["winp"][:, :, 0].transpose(0, 2, 1),
                     R["winp"][:, :, 1].reshape(NSEQ, P, 4, P).transpose(0, 2, 1, 3).reshape(NSEQ, WIN, P)], axis=2)
    swin = np.concatenate([wold.reshape(NSEQ, WIN, 2, 2, HD)[:, TS:], wnew[TP:].reshape(NSEQ, TS, 2, 2, HD)], axis=1)
    mkv = np.stack([R["mk"].transpose(2, 1, 0).reshape(MEM, D), R["mv"].transpose(1, 0, 2).reshape(MEM, D)], axis=1)
    fix = lambda a: np.ascontiguousarray(a)
    return tuple(fix(a) for a in (
        y[None, :TP], y[TP:].reshape(NSEQ, TS, D),
        rows[None, None, :TP], wnew[None, None, TP - WIN:TP],
        R["p_C"].transpose(1, 0, 2)[None, None], R["p_n"].T[None, None], R["p_m"][None],
        R["p_mconv"].transpose(2, 1, 0).reshape(1, 1, 3, MH * MD), R["p_fconv"].transpose(2, 1, 0).reshape(1, 1, 2, DFF),
        mkv.reshape(1, 1, MEM, 2, XH, D // XH),
        rows[TP:].reshape(1, NSEQ, TS, 4, 2, HD), swin[None],
        R["s_C"].transpose(1, 2, 3, 0)[None], R["s_n"][None], R["s_m"][None],
        R["s_mconv"].transpose(2, 3, 1, 0).reshape(1, NSEQ, 3, MH * MD), R["s_fconv"].transpose(2, 3, 1, 0).reshape(1, NSEQ, 2, DFF)))
```

```python
from contextlib import ExitStack, contextmanager

import concourse.bass as bass
import numpy as np
from concourse import mybir

F32 = mybir.dt.float32
I32 = mybir.dt.int32
F32R = mybir.dt.float32r
ACT = mybir.ActivationFunctionType
ALU = mybir.AluOpType
AX = mybir.AxisListType
ds = bass.ds

P = 128
D = 1024
KD = D // P
TP = 1024
NTILE = TP // P
NSEQ, TS = 8, 4
NS = NSEQ * TS
T = TP + NS
NG = 3
GW = T // NG
EPS = 1e-6
MH, MD = 4, 128
NH, HD = 8, 64
NPAIR = NH // 2
CB = 32
SB = 64
TOPK = 16
WIN = 512
PAST, PAGE = 4096, 128
NPAGE = PAST // PAGE
NBUCKET, MAX_DIST = 32, 1024
MEM = 256
XH = 4
DFF = 2816
KF = DFF // P
NEG = -1.0e30
CMP_SCALE = float(HD) ** -0.5
C_V, C_OG = 0, 512
N_VSEL, N_VWIN, N_IG, N_FG, N_GN, N_END = 0, 128, 256, 260, 264, 288
TOKW = 1312
Q_KCMP, Q_KSEL, Q_KWIN = 8, 10, 11
NFEAT = 12




def high_part(nc, high, x):
    return nc.vector.tensor_copy(high, x)


def low_part(engine, low, x, high):
    return engine.tensor_tensor(low, x, high.bitcast(F32), ALU.subtract)


def high_columns(nc, high, x, c, kc, x_high):
    for k in range(kc):
        nc.scalar.activation(high[:, k, c], x[:, k, c], ACT.Copy).then_inc(x_high, 1)


def low_columns(nc, ve, low, x, high, c, kc, g, x_high, x_low):
    for k in range(kc):
        ve.wait_ge(x_high, g * kc + k + 1)
        low_part(nc.vector, low[:, k, c], x[:, k, c], high[:, k, c]).then_inc(x_low, 1)


def split_product(nc, out, w, x, first, last):
    for n, (a, b) in enumerate(((0, 0), (0, 1), (1, 0))):
        ins = nc.tensor.matmul(out, w[a], x[b], start=first and n == 0, stop=last and n == 2)
    return ins


class Chain:

    def __init__(self, eng, sem, base=0):
        self.eng, self.sem, self.base, self.n = eng, sem, base, 0

    def link(self, ins):
        self.n += 1
        ins.then_inc(self.sem, 1)
        self.eng.wait_ge(self.sem, self.base + self.n)


def bias_buckets(dist):
    d = np.maximum(dist, 0)
    exact = NBUCKET // 2
    ratio = np.log(np.maximum(d, 1).astype(np.float32) / np.float32(exact)) / np.float32(np.log(MAX_DIST / exact))
    large = np.minimum(exact + (ratio * np.float32(NBUCKET - exact)).astype(np.int32), NBUCKET - 1)
    return np.where(d < exact, d, large)


@contextmanager
def stage(nc, name):
    with ExitStack() as outer:
        used = []

        def sem(n):
            used.append(outer.enter_context(nc.semaphore(f"{name}_{n}")))
            return used[-1]

        with ExitStack() as ctx:
            yield ctx, sem
        for s in used:
            nc.sync.sem_clear(s)
        nc.all_engine_barrier(sem_only=True)




def rms_norm(nc, name, K, src, gain, out, sq, rstd, ss, load=None, clear=None):
    with stage(nc, name) as (ctx, sem):
        sq_ready, sq_used, out_ready, rstd_ready, mean_ready, root_ready = map(
            sem, ("sq_ready", "sq_used", "out_ready", "rstd_ready", "mean_ready", "root_ready"))
        loaded = [sem(f"loaded{c}") for c in range(KD)]
        block = ctx.enter_context(nc.Block())

        @block.sync
        def _(sp):
            for c in range(KD):
                sp.dma_start(src[:, c, :], load[:, c, :]).then_inc(loaded[c], 16)

        @block.gpsimd
        def _(pool):
            nc.gpsimd.memset(clear, 0.0)

        @block.scalar
        def _(act):
            for c in range(KD):
                act.wait_ge(loaded[c], 16)
                if c >= 2:
                    act.wait_ge(sq_used, c - 1)
                nc.scalar.activation(sq[:, c % 2, :], src[:, c, :], ACT.Square).then_inc(sq_ready, 1)
            act.wait_ge(mean_ready, 1)
            nc.scalar.activation(rstd[:, :], rstd[:, :], ACT.Sqrt).then_inc(root_ready, 1)

        @block.tensor
        def _(pe):
            for c in range(KD):
                pe.wait_ge(sq_ready, c + 1)
                for g in range(NG):
                    last = nc.tensor.matmul(ss[:, g, 0:GW], K["ones"][:, :], sq[:, c % 2, g * GW:(g + 1) * GW],
                                            start=(c == 0), stop=(c == KD - 1))
                last.then_inc(sq_used, 1)

        @block.vector
        def _(ve):
            ve.wait_ge(sq_used, KD)
            nc.vector.tensor_scalar(rstd[:, :].rearrange("p (g t) -> p g t", g=NG), ss[:, :, 0:GW], 1.0 / D, EPS,
                                    ALU.mult, ALU.add).then_inc(mean_ready, 1)
            ve.wait_ge(root_ready, 1)
            nc.vector.reciprocal(rstd[:, :], rstd[:, :]).then_inc(rstd_ready, 1)
            ve.wait_ge(rstd_ready, 1)
            for c in range(KD):
                nc.vector.scalar_tensor_tensor(out=out[:, c, :], in0=src[:, c, :], scalar=gain[:, c:c + 1],
                                               in1=rstd[:, :], op0=ALU.mult, op1=ALU.mult).then_inc(out_ready, 1)


def residual_norm(nc, name, K, src, gains, g, x, h, sq, rstd, ss, store=None, high=None, low=None, keep=None):
    with stage(nc, name) as (ctx, sem):
        sq_ready, sq_used, rstd_ready, mean_ready, root_ready, scaled, out_ready, stored = map(
            sem, ("sq_ready", "sq_used", "rstd_ready", "mean_ready", "root_ready", "scaled", "out_ready", "stored"))
        summed_pool, summed_dve = sem("summed_pool"), sem("summed_dve")
        pool_chunks = [c for c in range(KD) if c % 3 != 2 and c != KD - 1]
        dve_chunks = [c for c in range(KD) if c not in pool_chunks]

        def wait_summed(eng, c):
            if c in pool_chunks:
                eng.wait_ge(summed_pool, pool_chunks.index(c) + 1)
            else:
                eng.wait_ge(summed_dve, dve_chunks.index(c) + 1)

        high_ready, low_ready = sem("high_ready"), sem("low_ready")
        rounds = 1 if store is not None else 2
        block = ctx.enter_context(nc.Block())

        @block.sync
        def _(sp):
            if store is not None:
                for c in range(KD):
                    wait_summed(sp, c)
                    sp.dma_start(store[:, c, :], x[:, c, :]).then_inc(stored, 16)
                sp.wait_ge(stored, 16 * KD)
            if keep is not None:
                for c in range(KD):
                    wait_summed(sp, c)
                    sp.dma_start(keep[:, c, :], x[:, c, :]).then_inc(stored, 16)
                sp.wait_ge(stored, 16 * KD)

        @block.scalar
        def _(act):
            for r in range(rounds):
                for c in range(KD):
                    n = r * KD + c
                    if n >= 2:
                        act.wait_ge(sq_used, n - 1)
                    if r:
                        wait_summed(act, c)
                    nc.scalar.activation(sq[:, c % 2, :], (src, x)[r][:, c, :], ACT.Square).then_inc(sq_ready, 1)
                act.wait_ge(mean_ready, r + 1)
                nc.scalar.activation(rstd[:, r, :], rstd[:, r, :], ACT.Sqrt).then_inc(root_ready, 1)
            if high is not None:
                for c in range(KD):
                    act.wait_ge(out_ready, c + 1)
                    nc.scalar.activation(high[:, c, :], h[:, c, :], ACT.Copy).then_inc(high_ready, 1)

        @block.tensor
        def _(pe):
            for n in range(rounds * KD):
                c = n % KD
                pe.wait_ge(sq_ready, n + 1)
                if n == KD:
                    pe.wait_ge(mean_ready, 1)
                for q in range(NG):
                    last = nc.tensor.matmul(ss[:, q, 0:GW], K["ones"][:, :], sq[:, c % 2, q * GW:(q + 1) * GW],
                                            start=(c == 0), stop=(c == KD - 1))
                last.then_inc(sq_used, 1)

        @block.vector
        def _(ve):
            for r in range(rounds):
                ve.wait_ge(sq_used, KD * (r + 1))
                nc.vector.tensor_scalar(rstd[:, r, :].rearrange("p (g t) -> p g t", g=NG), ss[:, :, 0:GW], 1.0 / D, EPS,
                                        ALU.mult, ALU.add).then_inc(mean_ready, 1)
                ve.wait_ge(root_ready, r + 1)
                nc.vector.reciprocal(rstd[:, r, :], rstd[:, r, :]).then_inc(rstd_ready, 1)
                ve.wait_ge(rstd_ready, r + 1)
                if r:
                    for c in range(KD):
                        wait_summed(ve, c)
                if r and keep is not None:
                    ve.wait_ge(stored, 16 * KD)
                for c in range(KD):
                    nc.vector.scalar_tensor_tensor(out=(src, h)[r][:, c, :], in0=(src, x)[r][:, c, :],
                                                   scalar=gains[:, g + r, c:c + 1], in1=rstd[:, r, :], op0=ALU.mult,
                                                   op1=ALU.mult).then_inc((scaled, out_ready)[r], 1)
                    if r == 0 and c in dve_chunks:
                        ve.wait_ge(scaled, c + 1)
                        nc.vector.tensor_tensor(x[:, c, :], x[:, c, :], src[:, c, :], ALU.add).then_inc(summed_dve, 1)
                    if r and high is not None:
                        if c >= 2 and (c - 2) % 3:
                            ve.wait_ge(high_ready, c - 1)
                            low_part(nc.vector, low[:, c - 2, :], h[:, c - 2, :], high[:, c - 2, :]).then_inc(low_ready, 1)
                if r and high is not None:
                    for c in (KD - 2, KD - 1):
                        if c % 3:
                            ve.wait_ge(high_ready, c + 1)
                            low_part(nc.vector, low[:, c, :], h[:, c, :], high[:, c, :]).then_inc(low_ready, 1)

        @block.gpsimd
        def _(pool):
            for c in pool_chunks:
                pool.wait_ge(scaled, c + 1)
                nc.gpsimd.tensor_tensor(x[:, c, :], x[:, c, :], src[:, c, :], ALU.add).then_inc(summed_pool, 1)
            if high is not None:
                for c in range(0, KD, 3):
                    pool.wait_ge(high_ready, c + 1)
                    low_part(nc.gpsimd, low[:, c, :], h[:, c, :], high[:, c, :]).then_inc(low_ready, 1)


def project(nc, name, w, n_chunks, kc, rhs, dst, ring, acc, width=T, groups=NG, aside=()):
    gw = width // groups
    with stage(nc, name) as (ctx, sem):
        w_loaded = [sem("w_loaded0"), sem("w_loaded1")]
        acc_ready, acc_free, moved = map(sem, ("acc_ready", "acc_free", "moved"))
        block = ctx.enter_context(nc.Block())
        assert n_chunks % 2 == 0

        @block.scalar
        def _(act):
            if aside:
                for to, src in aside:
                    act.dma_start(to, src).then_inc(moved, 16)
                act.wait_ge(moved, 16 * len(aside))

        @block.sync
        def _(sp):
            for j in range(2):
                sp.dma_start(ring[:, j, 0:kc * P], w[j]).then_inc(w_loaded[j], 16)
            with sp.Fori(1, n_chunks // 2) as i:
                for j in range(2):
                    sp.wait_ge(acc_ready, 2 * i + j - 1)
                    sp.dma_start(ring[:, j, 0:kc * P], w[ds(2 * i + j, 1), :, :].rearrange("a p k -> p (a k)")
                                 ).then_inc(w_loaded[j], 16)

        @block.tensor
        def _(pe):
            with pe.Fori(0, n_chunks // 2) as i:
                for j in range(2):
                    pe.wait_ge(w_loaded[j], 16 * i + 16)
                    pe.wait_ge(acc_free, 2 * i + j + 1)
                    for g in range(groups):
                        for k in range(kc):
                            last = nc.tensor.matmul(acc[:, 3 * j + g, 0:gw], ring[:, j, k * P:(k + 1) * P],
                                                    rhs[:, k, g * gw:(g + 1) * gw], start=(k == 0), stop=(k == kc - 1))
                    last.then_inc(acc_ready, 1)

        @block.vector
        def _(ve):
            ve.sem_inc(acc_free, 2)
            with ve.Fori(0, n_chunks // 2) as i:
                for j in range(2):
                    ve.wait_ge(acc_ready, 2 * i + j + 1)
                    out = dst[:, ds(2 * i + j, 1), :].rearrange("p a (g t) -> p (a g) t", g=groups)
                    nc.vector.tensor_scalar(out, acc[:, 3 * j:3 * j + groups, 0:gw], 1.0, None, ALU.mult
                                            ).then_inc(acc_free, 1)


def project_split(nc, name, w, n_chunks, kc, rhs, high, low, dst, ring, acc, split_here=True, add=False, aside=(), half=None):
    with stage(nc, name) as (ctx, sem):
        if half is None:
            half = ctx.enter_context(nc.sbuf_tensor(name + "_half", [P, 2 * 2 * kc * P], F32R))
        half = half.rearrange("p (j n k) -> p j n k", j=2, n=2)
        w_loaded = [sem("w_loaded0"), sem("w_loaded1")]
        w_high, w_low, acc_ready, acc_free, moved, x_high, x_low = map(
            sem, ("w_high", "w_low", "acc_ready", "acc_free", "moved", "x_high", "x_low"))
        block = ctx.enter_context(nc.Block())
        assert n_chunks % 2 == 0

        @block.scalar
        def _(act):
            for to, src in aside:
                act.dma_start(to, src).then_inc(moved, 16)
            if split_here:
                for g in range(NG):
                    high_columns(nc, high, rhs, slice(g * GW, (g + 1) * GW), kc, x_high)
            if aside:
                act.wait_ge(moved, 16 * len(aside))

        @block.sync
        def _(sp):
            for j in range(2):
                sp.dma_start(ring[:, j, 0:kc * P], w[j]).then_inc(w_loaded[j], 16)
            with sp.Fori(1, n_chunks // 2) as i:
                for j in range(2):
                    sp.wait_ge(w_low, 2 * i + j - 1)
                    sp.dma_start(ring[:, j, 0:kc * P], w[ds(2 * i + j, 1), :, :].rearrange("a p k -> p (a k)")
                                 ).then_inc(w_loaded[j], 16)

        @block.gpsimd
        def _(pool):
            with pool.Fori(0, n_chunks // 2) as i:
                for j in range(2):
                    pool.wait_ge(w_high, 2 * i + j + 1)
                    low_part(nc.gpsimd, half[:, j, 1, :], ring[:, j, 0:kc * P], half[:, j, 0, :]).then_inc(w_low, 1)

        @block.tensor
        def _(pe):
            with pe.Fori(0, n_chunks // 2) as i:
                for j in range(2):
                    pe.wait_ge(w_low, 2 * i + j + 1)
                    pe.wait_ge(acc_free, 2 * i + j + 1)
                    for g in range(NG):
                        c = slice(g * GW, (g + 1) * GW)
                        for k in range(kc):
                            if split_here and j == 0:
                                pe.wait_ge(x_low, g * kc + k + 1)
                            ks = slice(k * P, (k + 1) * P)
                            last = split_product(nc, acc[:, 3 * j + g, 0:GW], (half[:, j, 0, ks], half[:, j, 1, ks]),
                                                 (high[:, k, c], low[:, k, c]), k == 0, k == kc - 1)
                    last.then_inc(acc_ready, 1)

        @block.vector
        def _(ve):
            def split_weights(j, i, first=False):
                ve.wait_ge(w_loaded[j], 16 * i + 16)
                if not first:
                    ve.wait_ge(acc_ready, 2 * i + j - 1)
                high_part(nc, half[:, j, 0, :], ring[:, j, 0:kc * P]).then_inc(w_high, 1)

            def drain(i, j):
                ve.wait_ge(acc_ready, 2 * i + j + 1)
                out = dst[:, ds(2 * i + j, 1), :].rearrange("p a (g t) -> p (a g) t", g=NG)
                x = acc[:, 3 * j:3 * j + NG, 0:GW]
                if add:
                    nc.vector.tensor_tensor(out, x, out, ALU.add).then_inc(acc_free, 1)
                else:
                    nc.vector.tensor_scalar(out, x, 1.0, None, ALU.mult).then_inc(acc_free, 1)

            ve.sem_inc(acc_free, 2)
            split_weights(0, 0, True)
            split_weights(1, 0, True)
            if split_here:
                for g in range(NG):
                    low_columns(nc, ve, low, rhs, high, slice(g * GW, (g + 1) * GW), kc, g, x_high, x_low)
            with ve.Fori(0, n_chunks // 2 - 1) as i:
                for j in range(2):
                    drain(i, j)
                    split_weights(j, i + 1)
            for j in range(2):
                drain(n_chunks // 2 - 1, j)


def project_tokens(nc, name, w, h, outs, acc, sizes=(P,) * NTILE + (NS,), aside=()):
    with stage(nc, name) as (ctx, sem):
        wt = ctx.enter_context(nc.sbuf_tensor(name + "_wt", [P, 2, KD, max(n for _, n, _ in outs)], F32))
        w_loaded = [sem("w_loaded0"), sem("w_loaded1")]
        acc_ready, acc_free, moved = map(sem, ("acc_ready", "acc_free", "moved"))
        block = ctx.enter_context(nc.Block())
        n = len(sizes)

        @block.scalar
        def _(act):
            if aside:
                for to, src in aside:
                    act.dma_start(to, src).then_inc(moved, 16)
                act.wait_ge(moved, 16 * len(aside))

        @block.sync
        def _(sp):
            for j, (c, width, _) in enumerate(outs):
                if j >= 2:
                    sp.wait_ge(acc_ready, (j - 1) * n)
                sp.dma_start(wt[:, j % 2, :, 0:width], w[:, :, c:c + width]).then_inc(w_loaded[j % 2], 16)

        @block.tensor
        def _(pe):
            for j, (_, width, _) in enumerate(outs):
                pe.wait_ge(w_loaded[j % 2], 16 * (j // 2 + 1))
                for t in range(n):
                    m = sizes[t]
                    u = j * n + t
                    if u >= 2:
                        pe.wait_ge(acc_free, u - 1)
                    for k in range(KD):
                        last = nc.tensor.matmul(acc[0:m, u % 2, 0:width], h[:, k, t * P:t * P + m],
                                                wt[:, j % 2, k, 0:width], start=(k == 0), stop=(k == KD - 1))
                    last.then_inc(acc_ready, 1)

        @block.vector
        def _(ve):
            for j, (c, width, dst) in enumerate(outs):
                for t in range(n):
                    m = sizes[t]
                    u = j * n + t
                    ve.wait_ge(acc_ready, u + 1)
                    nc.vector.tensor_copy(dst[0:m, t, :], acc[0:m, u % 2, 0:width]).then_inc(acc_free, 1)



def conv_mlstm(nc, A, O, zm, hm):
    with stage(nc, "mconv") as (ctx, sem):
        sb = lambda n, s: ctx.enter_context(nc.sbuf_tensor(n, s, F32))
        cw = sb("cw", [P, 4, 5])
        xs = sb("xs", [P, 4, NSEQ, 3 + TS])
        ys = sb("ys", [P, 4, NSEQ, TS])
        loaded, staged, steps, conv_ready, stored, act_done = map(
            sem, ("loaded", "staged", "steps", "conv_ready", "stored", "act_done"))
        block = ctx.enter_context(nc.Block())

        @block.sync
        def _(sp):
            sp.dma_start(cw[:, :, :], A["m_conv"]).then_inc(loaded, 16)
            sp.dma_start(xs[:, :, :, 0:3], A["m_state"]).then_inc(loaded, 16)
            sp.dma_start(O["p_mconv"], zm[:, :, TP - 3:TP]).then_inc(stored, 16)
            sp.wait_ge(staged, 4)
            sp.dma_start(O["s_mconv"], xs[:, :, :, TS:TS + 3]).then_inc(stored, 16)
            sp.wait_ge(stored, 32)

        @block.vector
        def _(ve):
            ve.wait_ge(loaded, 32)
            for c in range(4):
                nc.vector.tensor_copy(xs[:, c, :, 3:3 + TS],
                                      zm[:, c, TP:T].rearrange("p (b t) -> p b t", t=TS)).then_inc(staged, 1)
            ve.wait_ge(staged, 4)
            chain = Chain(ve, steps)
            for c in range(4):
                nc.vector.tensor_scalar(hm[:, c, 0:TP], zm[:, c, 0:TP], cw[:, c, 3:4], cw[:, c, 4:5],
                                        ALU.mult, ALU.add)
                chain.link(nc.vector.tensor_scalar(ys[:, c, :, :], xs[:, c, :, 3:3 + TS], cw[:, c, 3:4],
                                                   cw[:, c, 4:5], ALU.mult, ALU.add))
            for k in range(3):
                d = 3 - k
                for c in range(4):
                    nc.vector.scalar_tensor_tensor(out=hm[:, c, d:TP], in0=zm[:, c, 0:TP - d], scalar=cw[:, c, k:k + 1],
                                                   in1=hm[:, c, d:TP], op0=ALU.mult, op1=ALU.add)
                    chain.link(nc.vector.scalar_tensor_tensor(
                        out=ys[:, c, :, :], in0=xs[:, c, :, k:k + TS], scalar=cw[:, c, k:k + 1],
                        in1=ys[:, c, :, :], op0=ALU.mult, op1=ALU.add))
            for c in range(4):
                nc.vector.tensor_copy(hm[:, c, TP:T].rearrange("p (b t) -> p b t", t=TS), ys[:, c, :, :]
                                      ).then_inc(conv_ready, 1)

        @block.scalar
        def _(act):
            for c in range(4):
                act.wait_ge(conv_ready, c + 1)
                nc.scalar.activation(hm[:, c, :], hm[:, c, :], ACT.Silu).then_inc(act_done, 1)


def gates(nc, A, K, tokm, tokn, sm, psum):
    lf, b, a, g, tmp = sm["lf"], sm["b"], sm["a"], sm["g"], sm["tmp"]
    n = NTILE + 1
    with stage(nc, "gates") as (ctx, sem):
        gb = ctx.enter_context(nc.sbuf_tensor("gb", [P, 8], F32))
        loaded, steps, act_steps, cum_ready, og_done = map(sem, ("loaded", "steps", "act_steps", "cum_ready", "og_done"))
        block = ctx.enter_context(nc.Block())
        fg = tokn[:, :, N_FG:N_FG + MH]

        @block.sync
        def _(sp):
            sp.dma_start(gb[:, :], A["gate_b"].partition_broadcast(P)).then_inc(loaded, 16)

        @block.vector
        def _(ve):
            ve.wait_ge(loaded, 16)
            chain = Chain(ve, steps)
            chain.link(nc.vector.tensor_tensor(tokn[:, :, N_IG:N_IG + 8], tokn[:, :, N_IG:N_IG + 8],
                                               gb[:, :].unsqueeze(1).to_broadcast([P, n, 8]), ALU.add))
            nc.vector.tensor_scalar(lf[:, :, :], fg, 0.0, None, ALU.min)
            chain.link(nc.vector.scalar_tensor_tensor(out=tmp[:, :, :], in0=fg, scalar=-1.0, in1=fg,
                                                      op0=ALU.mult, op1=ALU.min))
            ve.wait_ge(act_steps, 1)
            chain.link(nc.vector.tensor_scalar(tmp[:, :, :], tmp[:, :, :], 1.0, None, ALU.add))
            ve.wait_ge(act_steps, 2)
            chain.link(nc.vector.tensor_tensor(lf[:, :, :], lf[:, :, :], tmp[:, :, :], ALU.subtract))
            ve.wait_ge(cum_ready, 2)
            nc.vector.tensor_copy(b[:, 0:NTILE, :], psum[:, 0, 0:NTILE * MH].rearrange("p (t h) -> p t h", h=MH))
            chain.link(nc.vector.tensor_copy(b[:, NTILE, :], psum[:, 1, 0:MH]))
            chain.link(nc.vector.tensor_tensor(a[:, :, :], tokn[:, :, N_IG:N_IG + MH], b[:, :, :], ALU.subtract))

        @block.scalar
        def _(act):
            act.wait_ge(steps, 2)
            nc.scalar.activation(tmp[:, :, :], tmp[:, :, :], ACT.Exp).then_inc(act_steps, 1)
            act.wait_ge(steps, 3)
            nc.scalar.activation(tmp[:, :, :], tmp[:, :, :], ACT.Ln).then_inc(act_steps, 1)
            nc.scalar.activation(g[:, :, :], tokn[:, :, N_GN:N_END], ACT.Sigmoid).then_inc(act_steps, 1)
            for t in range(n):
                m = P if t < NTILE else NS
                nc.scalar.activation(tokm[0:m, t, C_OG:C_OG + 512], tokm[0:m, t, C_OG:C_OG + 512], ACT.Sigmoid
                                     ).then_inc(og_done, 1)

        @block.tensor
        def _(pe):
            pe.wait_ge(steps, 4)
            nc.tensor.matmul(psum[:, 0, 0:NTILE * MH], K["tri"][:, :], lf[:, 0:NTILE, :].rearrange("p t h -> p (t h)"),
                             start=True, stop=True).then_inc(cum_ready, 1)
            nc.tensor.matmul(psum[:, 1, 0:MH], K["stri"][:, :], lf[:, NTILE, :], start=True, stop=True
                             ).then_inc(cum_ready, 1)


def mlstm(nc, A, O, K, hm, tokm, sm, psum):
    with stage(nc, "mlstm") as (ctx, sem):
        sb = lambda n, s: ctx.enter_context(nc.sbuf_tensor(n, s, F32))
        wqk = sb("wqk", [P, 2, MH, MD])
        mnorm = sb("mnorm", [P, MH, MD])
        xc = sb("xc", [P, MH, P])
        qT, kT, kt = sb("qT", [P, MH, P]), sb("kT", [P, MH, P]), sb("kt", [P, MH, P])
        va = sb("va", [P, MH, MD + 1])
        kw = sb("kw", [P, MH, MD])
        dec = sb("dec", [P, MH, P])
        num = sb("num", [P, MH, MD + 1])
        C = sb("C", [P, MH, MD + 1])
        mc, M, Mb, ML = sb("mc", [P, MH]), sb("M", [P, MH]), sb("Mb", [P, 2 * MH]), sb("ML", [P, 2 * MH])
        sc, wl, sl, emt, r1, r2 = (sb(n, [P, MH]) for n in ("sc", "wl", "sl", "emt", "r1", "r2"))
        tmp = sb("tmpm", [P, MH, P])
        ac = sb("ac", [P, MH])
        names = ("loaded", "xc_ready", "qk_ready", "qk_copied", "arow_ready", "steps", "mrow_ready", "last_ready",
                 "exps_ready", "scores_ready", "inter_ready", "intra_ready", "update_ready", "turned", "h_stored",
                 "finished", "diag_a_ready", "diag_m_ready", "exponents_ready", "differences_ready", "weighted_ready",
                 "square_ready", "root_ready", "gated_ready", "stored")
        S = {n: sem(n) for n in names}
        block = ctx.enter_context(nc.Block())
        row4 = lambda bank: psum[:, bank, :].rearrange("p (h t) -> p h t", h=MH)
        wide = lambda bank: psum[:, bank:bank + 2, :].rearrange("p b (h t) -> p (b h) t", h=2)[:, :, 0:MD + 1]
        per_head = lambda v, n: v.unsqueeze(2).to_broadcast([P, MH, n])
        per_all = lambda v: v.unsqueeze(1).to_broadcast([P, MH, P])
        STEPS = 19

        @block.sync
        def _(sp):
            sp.dma_start(wqk[:, :, :, :], A["m_wqk"]).then_inc(S["loaded"], 16)
            sp.dma_start(mnorm[:, :, :], A["m_norm"].partition_broadcast(P)).then_inc(S["loaded"], 16)
            sp.wait_ge(S["finished"], 2)
            sp.dma_start(O["p_C"], tmp[:, :, :]).then_inc(S["stored"], 16)
            sp.dma_start(O["p_n"], r1[:, :]).then_inc(S["stored"], 16)
            sp.dma_start(O["p_m"], mc[0:1, :]).then_inc(S["stored"], 16)
            sp.wait_ge(S["stored"], 48)

        @block.scalar
        def _(act):
            act.wait_ge(S["loaded"], 32)
            with act.Fori(0, NTILE) as i:
                act.wait_ge(S["h_stored"], i + 1)
                nc.scalar.activation(xc[:, :, :], hm[:, :, ds(i * P, P)], ACT.Copy).then_inc(S["xc_ready"], 1)
                act.wait_ge(S["qk_ready"], i + 1)
                nc.scalar.activation(qT[:, :, :], row4(0), ACT.Copy).then_inc(S["qk_copied"], 1)
                nc.scalar.activation(kT[:, :, :], row4(1), ACT.Copy, scale=MD ** -0.5).then_inc(S["qk_copied"], 1)
                nc.scalar.activation(kt[:, :, :], row4(2), ACT.Copy, scale=MD ** -0.5).then_inc(S["qk_copied"], 1)
                act.wait_ge(S["exponents_ready"], i + 1)
                for h in range(MH):
                    nc.scalar.activation(dec[:, h, :], dec[:, h, :], ACT.Exp,
                                         bias=ac[:, h:h + 1]
                                         ).then_inc(S["exps_ready"], 1)
                act.wait_ge(S["differences_ready"], i + 1)
                for v in (sc, emt, wl, sl):
                    nc.scalar.activation(v[:, :], v[:, :], ACT.Exp).then_inc(S["exps_ready"], 1)
                act.wait_ge(S["square_ready"], i + 1)
                nc.scalar.activation(r1[:, :], r1[:, :], ACT.Sqrt).then_inc(S["root_ready"], 1)

        @block.tensor
        def _(pe):
            pe.wait_ge(S["loaded"], 32)
            with pe.Fori(0, NTILE) as i:
                pe.wait_ge(S["h_stored"], i + 1)
                pe.wait_ge(S["xc_ready"], i + 1)
                for h in range(MH):
                    hs = slice(h * P, (h + 1) * P)
                    nc.tensor.matmul(psum[:, 0, hs], wqk[:, 0, h, :], xc[:, h, :], start=True, stop=True)
                    nc.tensor.matmul(psum[:, 1, hs], wqk[:, 1, h, :], xc[:, h, :], start=True, stop=True)
                    last = nc.tensor.matmul(psum[:, 2, hs], xc[:, h, :], wqk[:, 1, h, :], start=True, stop=True)
                last.then_inc(S["qk_ready"], 1)
                pe.wait_ge(S["diag_a_ready"], i + 1)
                nc.tensor.matmul(psum[:, 4, :], K["ones"][:, :], tmp[:, :, :].rearrange("p h t -> p (h t)"),
                                 start=True, stop=True).then_inc(S["arow_ready"], 1)
                pe.wait_ge(S["qk_copied"], 3 * i + 3)
                for h in range(MH):
                    last = nc.tensor.matmul(psum[:, 3, h * P:(h + 1) * P], kT[:, h, :], qT[:, h, :], start=True, stop=True)
                last.then_inc(S["scores_ready"], 1)
                for h in range(MH):
                    last = nc.tensor.matmul(wide(5)[:, h, :], qT[:, h, :], C[:, h, :], start=True, stop=True)
                last.then_inc(S["inter_ready"], 1)
                pe.wait_ge(S["diag_m_ready"], i + 1)
                nc.tensor.matmul(psum[:, 4, :], K["ones"][:, :], tmp[:, :, :].rearrange("p h t -> p (h t)"),
                                 start=True, stop=True).then_inc(S["mrow_ready"], 1)
                nc.tensor.matmul(psum[:, 7, 0:2 * MH], K["last"][:, :], Mb[:, :], start=True, stop=True
                                 ).then_inc(S["last_ready"], 1)
                pe.wait_ge(S["weighted_ready"], i + 1)
                for h in range(MH):
                    last = nc.tensor.matmul(wide(0)[:, h, :], dec[:, h, :], va[:, h, :], start=True, stop=True)
                last.then_inc(S["intra_ready"], 1)
                for h in range(MH):
                    last = nc.tensor.matmul(wide(2)[:, h, :], kw[:, h, :], va[:, h, :], start=True, stop=True)
                last.then_inc(S["update_ready"], 1)
                pe.wait_ge(S["gated_ready"], i + 1)
                for h in range(MH):
                    last = nc.tensor.transpose(psum[:, 4, h * P:(h + 1) * P], num[:, h, 0:MD], K["ident"][:, :])
                last.then_inc(S["turned"], 1)
            pe.wait_ge(S["h_stored"], NTILE + 1)
            for h in range(MH):
                last = nc.tensor.transpose(psum[:, 4, h * P:(h + 1) * P], C[:, h, 0:MD], K["ident"][:, :])
            last.then_inc(S["turned"], 1)

        @block.vector
        def _(ve):
            ve.wait_ge(S["loaded"], 32)
            pre = Chain(ve, S["finished"])
            nc.vector.memset(C[:, :, :], 0.0)
            nc.vector.memset(va[:, :, MD:MD + 1], 1.0)
            pre.link(nc.vector.memset(mc[:, :], 0.0))
            ve.sem_inc(S["h_stored"], 1)
            with ve.Fori(0, NTILE) as i:
                ch = Chain(ve, S["steps"], i * STEPS)

                def signal(ins, name):
                    ins.then_inc(S[name], 1)
                    ve.wait_ge(S[name], i + 1)

                a = ac[:, :]
                ch.link(nc.vector.tensor_copy(a, sm["a"][:, ds(i, 1), :].rearrange("p a h -> p (a h)")))
                b = sm["b"][:, ds(i, 1), :].rearrange("p a h -> p (a h)")
                nc.vector.tensor_tensor(tmp[:, :, :], per_all(K["ident"][:, :]), per_head(a, P), ALU.mult
                                        ).then_inc(S["diag_a_ready"], 1)
                nc.vector.tensor_copy(va[:, :, 0:MD], tokm[:, ds(i, 1), C_V:C_V + 512].rearrange("p a (h v) -> p (a h) v", h=MH))
                ve.wait_ge(S["arow_ready"], i + 1)
                ch.link(nc.vector.tensor_tensor(dec[:, :, :], row4(4), per_all(K["causal"][:, :]), ALU.add))
                ch.link(nc.vector.tensor_reduce(M[:, :], dec[:, :, :], AX.X, ALU.max))
                ch.link(nc.vector.tensor_tensor(M[:, :], M[:, :], mc[:, :], ALU.max))
                nc.vector.tensor_copy(Mb[:, 0:MH], M[:, :])
                ch.link(nc.vector.tensor_tensor(Mb[:, MH:2 * MH], M[:, :], b, ALU.add))
                nc.vector.tensor_tensor(tmp[:, :, :], per_all(K["ident"][:, :]), per_head(M[:, :], P), ALU.mult
                                        ).then_inc(S["diag_m_ready"], 1)
                nc.vector.tensor_tensor(sc[:, :], mc[:, :], M[:, :], ALU.subtract)
                nc.vector.tensor_scalar(emt[:, :], Mb[:, MH:2 * MH], -1.0, None, ALU.mult)
                ve.wait_ge(S["mrow_ready"], i + 1)
                nc.vector.tensor_tensor(dec[:, :, :], per_all(K["causal_t"][:, :]), row4(4), ALU.subtract
                                        ).then_inc(S["exponents_ready"], 1)
                ve.wait_ge(S["last_ready"], i + 1)
                ch.link(nc.vector.tensor_copy(ML[:, :], psum[:, 7, 0:2 * MH]))
                nc.vector.tensor_tensor(wl[:, :], a, ML[:, 0:MH], ALU.subtract)
                ch.link(nc.vector.tensor_tensor(sl[:, :], mc[:, :], ML[:, 0:MH], ALU.subtract))
                signal(nc.vector.tensor_copy(mc[:, :], ML[:, MH:2 * MH]), "differences_ready")
                ve.wait_ge(S["scores_ready"], i + 1)
                ve.wait_ge(S["exps_ready"], 8 * i + 8)
                nc.vector.tensor_tensor(dec[:, :, :], dec[:, :, :], row4(3), ALU.mult)
                signal(nc.vector.tensor_tensor(kw[:, :, :], kt[:, :, :], per_head(wl[:, :], MD), ALU.mult), "weighted_ready")
                ve.wait_ge(S["inter_ready"], i + 1)
                ch.link(nc.vector.tensor_tensor(num[:, :, :], wide(5), per_head(sc[:, :], MD + 1), ALU.mult))
                ve.wait_ge(S["intra_ready"], i + 1)
                ch.link(nc.vector.tensor_tensor(num[:, :, :], num[:, :, :], wide(0), ALU.add))
                den = num[:, :, MD]
                ch.link(nc.vector.scalar_tensor_tensor(out=r2[:, :], in0=den, scalar=-1.0, in1=den, op0=ALU.mult, op1=ALU.max))
                ch.link(nc.vector.tensor_tensor(r2[:, :], r2[:, :], emt[:, :], ALU.max))
                ch.link(nc.vector.reciprocal(r2[:, :], r2[:, :]))
                ch.link(nc.vector.tensor_tensor(num[:, :, 0:MD], num[:, :, 0:MD], per_head(r2[:, :], MD), ALU.mult))
                ch.link(nc.vector.tensor_tensor(tmp[:, :, :], num[:, :, 0:MD], num[:, :, 0:MD], ALU.mult))
                ch.link(nc.vector.tensor_reduce(r1[:, :], tmp[:, :, :], AX.X, ALU.add))
                signal(nc.vector.tensor_scalar(r1[:, :], r1[:, :], 1.0 / MD, EPS, ALU.mult, ALU.add), "square_ready")
                ve.wait_ge(S["root_ready"], i + 1)
                ch.link(nc.vector.reciprocal(r1[:, :], r1[:, :]))
                ch.link(nc.vector.tensor_tensor(num[:, :, 0:MD], num[:, :, 0:MD], per_head(r1[:, :], MD), ALU.mult))
                ch.link(nc.vector.tensor_tensor(num[:, :, 0:MD], num[:, :, 0:MD], mnorm[:, :, :], ALU.mult))
                signal(nc.vector.tensor_tensor(
                    num[:, :, 0:MD], num[:, :, 0:MD],
                    tokm[:, ds(i, 1), C_OG:C_OG + 512].rearrange("p a (h v) -> p (a h) v", h=MH), ALU.mult), "gated_ready")
                ve.wait_ge(S["update_ready"], i + 1)
                for h in range(MH):
                    last = nc.vector.scalar_tensor_tensor(out=C[:, h, :], in0=C[:, h, :], scalar=sl[:, h:h + 1],
                                                          in1=wide(2)[:, h, :], op0=ALU.mult, op1=ALU.add)
                ch.link(last)
                assert ch.n == STEPS, ch.n
                ve.wait_ge(S["turned"], i + 1)
                nc.vector.tensor_scalar(hm[:, :, ds(i * P, P)], row4(4), 1.0, None, ALU.mult).then_inc(S["h_stored"], 1)
            ve.wait_ge(S["turned"], NTILE + 1)
            nc.vector.tensor_copy(r1[:, :], C[:, :, MD])
            pre.link(nc.vector.tensor_copy(tmp[:, :, :], row4(4)))


def mlstm_sample(nc, A, O, K, hm, tokm, sm, psum):
    with stage(nc, "smlstm") as (ctx, sem):
        sb = lambda n, s: ctx.enter_context(nc.sbuf_tensor("sm_" + n, s, F32))
        wqk = sb("wqk", [P, 2, MH, MD])
        mnorm = sb("mnorm", [NS, MH, MD])
        C = sb("C", [P, NSEQ, MH, MD])
        n0, m0 = sb("n0", [NS, MH, MD]), sb("m0", [NS, MH])
        n8, sl8 = sb("n8", [NSEQ, MH, MD]), sb("sl8", [NSEQ, 2 * MH])
        qT, kT = sb("qT", [P, MH, NS]), sb("kT", [P, MH, NS])
        kt, qt = sb("kt", [NS, MH, MD]), sb("qt", [NS, MH, MD])
        kw, kwm = sb("kw", [NS, MH, MD]), sb("kwm", [NS, NSEQ, MH * MD])
        va = sb("va", [NS, MH, MD + 1])
        dec, tmp = sb("dec", [NS, MH, NS]), sb("tmpm", [NS, MH, NS])
        num, sq = sb("num", [NS, MH, MD + 1]), sb("sqm", [NS, MH, MD])
        inter = sb("inter", [P, MH, NS])
        slrow, slb = sb("slrow", [NS, NSEQ, MH]), sb("slb", [P, NSEQ, MH])
        M, Mb, ML = sb("M", [NS, MH]), sb("Mb", [NS, 2 * MH]), sb("ML", [NS, 2 * MH])
        sc, wl, sl, emt, r1, r2, nq = (sb(n, [NS, MH]) for n in ("sc", "wl", "sl", "emt", "r1", "r2", "nq"))
        names = ("loaded", "qk_ready", "qk_copied", "diag_a_ready", "arow_ready", "steps", "diag_m_ready", "mrow_ready",
                 "last_ready", "exponents_ready", "exps_ready", "differences_ready", "scores_ready", "weighted_ready",
                 "intra_ready", "inter_ready", "inter_copied", "inter_turned", "scale_ready", "scale_spread",
                 "masked_ready", "update_ready", "updated", "norm_ready", "square_ready", "root_ready", "gated_ready",
                 "turned", "stored")
        S = {n: sem(n) for n in names}
        block = ctx.enter_context(nc.Block())
        last = NTILE
        a, b = sm["a"][0:NS, last, :], sm["b"][0:NS, last, :]
        ones, ident = K["ones"], K["ident"]
        small = lambda bank: psum[0:NS, bank, 0:MH * NS].rearrange("p (h t) -> p h t", h=MH)
        wide = lambda bank: psum[0:NS, bank:bank + 2, :].rearrange("p b (h t) -> p (b h) t", h=2)[:, :, 0:MD + 1]
        per_head = lambda v, n: v.unsqueeze(2).to_broadcast([NS, MH, n])
        per_all = lambda v: v.unsqueeze(1).to_broadcast([NS, MH, NS])

        @block.sync
        def _(sp):
            sp.dma_start(wqk[:, :, :, :], A["m_wqk"]).then_inc(S["loaded"], 16)
            sp.dma_start(mnorm[:, :, :], A["m_norm"].partition_broadcast(NS)).then_inc(S["loaded"], 16)
            sp.dma_start(C[:, :, :, :], A["s_C0"]).then_inc(S["loaded"], 16)
            sp.dma_start(n0[:, :, :], A["s_n0t"]).then_inc(S["loaded"], 16)
            sp.dma_start(n8[:, :, :], A["s_n0"]).then_inc(S["loaded"], 16)
            sp.dma_start(m0[:, :], A["s_m0t"]).then_inc(S["loaded"], 16)
            sp.wait_ge(S["updated"], NSEQ)
            sp.dma_start(O["s_C"], C[:, :, :, :]).then_inc(S["stored"], 16)
            sp.wait_ge(S["norm_ready"], 1)
            sp.dma_start(O["s_n"], n8[:, :, :]).then_inc(S["stored"], 16)
            sp.dma_start(O["s_m"], sl8[:, MH:2 * MH]).then_inc(S["stored"], 16)
            sp.wait_ge(S["stored"], 48)

        @block.tensor
        def _(pe):
            pe.wait_ge(S["loaded"], 96)
            for h in range(MH):
                x = hm[:, h, TP:T]
                nc.tensor.matmul(psum[:, 0, h * NS:(h + 1) * NS], wqk[:, 0, h, :], x, start=True, stop=True)
                nc.tensor.matmul(psum[:, 1, h * NS:(h + 1) * NS], wqk[:, 1, h, :], x, start=True, stop=True)
                nc.tensor.matmul(psum[0:NS, 2, h * MD:(h + 1) * MD], x, wqk[:, 1, h, :], start=True, stop=True)
                mm = nc.tensor.matmul(psum[0:NS, 3, h * MD:(h + 1) * MD], x, wqk[:, 0, h, :], start=True, stop=True)
            mm.then_inc(S["qk_ready"], 1)
            pe.wait_ge(S["diag_a_ready"], 1)
            nc.tensor.matmul(psum[0:NS, 4, 0:MH * NS], ones[0:NS, 0:NS], tmp[:, :, :].rearrange("p h t -> p (h t)"),
                             start=True, stop=True).then_inc(S["arow_ready"], 1)
            pe.wait_ge(S["qk_copied"], 4)
            for h in range(MH):
                mm = nc.tensor.matmul(psum[0:NS, 5, h * NS:(h + 1) * NS], kT[:, h, :], qT[:, h, :], start=True, stop=True)
            mm.then_inc(S["scores_ready"], 1)
            for h in range(MH):
                for q in range(NSEQ):
                    c = slice(h * NS + q * TS, h * NS + (q + 1) * TS)
                    mm = nc.tensor.matmul(psum[:, 6, c], C[:, q, h, :], qT[:, h, q * TS:(q + 1) * TS], start=True, stop=True)
            mm.then_inc(S["inter_ready"], 1)
            pe.wait_ge(S["diag_m_ready"], 1)
            nc.tensor.matmul(psum[0:NS, 4, 0:MH * NS], ones[0:NS, 0:NS], tmp[:, :, :].rearrange("p h t -> p (h t)"),
                             start=True, stop=True).then_inc(S["mrow_ready"], 1)
            nc.tensor.matmul(psum[0:NS, 7, 0:2 * MH], K["slast"][0:NS, 0:NS], Mb[:, :], start=True, stop=True
                             ).then_inc(S["last_ready"], 1)
            pe.wait_ge(S["inter_copied"], 1)
            for h in range(MH):
                mm = nc.tensor.transpose(psum[0:NS, 6, h * MD:(h + 1) * MD], inter[:, h, :], ident[:, :])
            mm.then_inc(S["inter_turned"], 1)
            pe.wait_ge(S["weighted_ready"], 1)
            for h in range(MH):
                mm = nc.tensor.matmul(wide(0)[:, h, :], dec[:, h, :], va[:, h, :], start=True, stop=True)
            mm.then_inc(S["intra_ready"], 1)
            pe.wait_ge(S["scale_ready"], 1)
            nc.tensor.matmul(psum[:, 4, 0:NSEQ * MH], ones[0:NS, :], slrow[:, :, :].rearrange("p b h -> p (b h)"),
                             start=True, stop=True)
            nc.tensor.matmul(psum[0:NSEQ, 7, 0:MH], K["slast8"][0:NS, 0:NSEQ], sl[:, :], start=True, stop=True)
            nc.tensor.matmul(psum[0:NSEQ, 7, MH:2 * MH], K["slast8"][0:NS, 0:NSEQ], Mb[:, MH:2 * MH], start=True, stop=True)
            nc.tensor.matmul(psum[0:NSEQ, 5, :], K["sseq8"][0:NS, 0:NSEQ], kw[:, :, :].rearrange("p h k -> p (h k)"),
                             start=True, stop=True).then_inc(S["scale_spread"], 1)
            for q in range(NSEQ):
                pe.wait_ge(S["masked_ready"], q + 1)
                if q >= 2:
                    pe.wait_ge(S["updated"], q - 1)
                for h in range(MH):
                    mm = nc.tensor.matmul(psum[:, 2 + q % 2, h * MD:(h + 1) * MD], kwm[:, q, h * MD:(h + 1) * MD],
                                          va[:, h, 0:MD], start=True, stop=True)
                mm.then_inc(S["update_ready"], 1)
            pe.wait_ge(S["gated_ready"], 1)
            for h in range(MH):
                mm = nc.tensor.transpose(psum[:, 0, h * NS:(h + 1) * NS], num[:, h, 0:MD], ident[0:NS, 0:NS])
            mm.then_inc(S["turned"], 1)

        @block.scalar
        def _(act):
            act.wait_ge(S["qk_ready"], 1)
            k = MD ** -0.5
            nc.scalar.activation(qT[:, :, :], psum[:, 0, 0:MH * NS].rearrange("p (h t) -> p h t", h=MH), ACT.Copy
                                 ).then_inc(S["qk_copied"], 1)
            nc.scalar.activation(kT[:, :, :], psum[:, 1, 0:MH * NS].rearrange("p (h t) -> p h t", h=MH), ACT.Copy, scale=k
                                 ).then_inc(S["qk_copied"], 1)
            nc.scalar.activation(kt[:, :, :], psum[0:NS, 2, :].rearrange("p (h t) -> p h t", h=MH), ACT.Copy, scale=k
                                 ).then_inc(S["qk_copied"], 1)
            nc.scalar.activation(qt[:, :, :], psum[0:NS, 3, :].rearrange("p (h t) -> p h t", h=MH), ACT.Copy
                                 ).then_inc(S["qk_copied"], 1)
            act.wait_ge(S["exponents_ready"], 1)
            for h in range(MH):
                nc.scalar.activation(dec[:, h, :], dec[:, h, :], ACT.Exp, bias=sm["a"][0:NS, last, h:h + 1]
                                     ).then_inc(S["exps_ready"], 1)
            act.wait_ge(S["differences_ready"], 1)
            for v in (sc, emt, wl, sl):
                nc.scalar.activation(v[:, :], v[:, :], ACT.Exp).then_inc(S["exps_ready"], 1)
            act.wait_ge(S["inter_ready"], 1)
            nc.scalar.activation(inter[:, :, :], psum[:, 6, 0:MH * NS].rearrange("p (h t) -> p h t", h=MH), ACT.Copy
                                 ).then_inc(S["inter_copied"], 1)
            act.wait_ge(S["square_ready"], 1)
            nc.scalar.activation(r1[:, :], r1[:, :], ACT.Sqrt).then_inc(S["root_ready"], 1)

        @block.vector
        def _(ve):
            ch = Chain(ve, S["steps"])

            def signal(ins, name):
                ins.then_inc(S[name], 1)
                ve.wait_ge(S[name], 1)

            nc.vector.memset(va[:, :, MD:MD + 1], 1.0)
            nc.vector.tensor_tensor(tmp[:, :, :], per_all(ident[0:NS, 0:NS]), per_head(a, NS), ALU.mult
                                    ).then_inc(S["diag_a_ready"], 1)
            nc.vector.tensor_copy(va[:, :, 0:MD], tokm[0:NS, last, C_V:C_V + 512].rearrange("p (h v) -> p h v", h=MH))
            ve.wait_ge(S["loaded"], 96)
            ve.wait_ge(S["arow_ready"], 1)
            ch.link(nc.vector.tensor_tensor(dec[:, :, :], small(4), per_all(K["scausal"][0:NS, 0:NS]), ALU.add))
            ch.link(nc.vector.tensor_reduce(M[:, :], dec[:, :, :], AX.X, ALU.max))
            ch.link(nc.vector.tensor_tensor(M[:, :], M[:, :], m0[:, :], ALU.max))
            nc.vector.tensor_copy(Mb[:, 0:MH], M[:, :])
            ch.link(nc.vector.tensor_tensor(Mb[:, MH:2 * MH], M[:, :], b, ALU.add))
            nc.vector.tensor_tensor(tmp[:, :, :], per_all(ident[0:NS, 0:NS]), per_head(M[:, :], NS), ALU.mult
                                    ).then_inc(S["diag_m_ready"], 1)
            nc.vector.tensor_tensor(sc[:, :], m0[:, :], M[:, :], ALU.subtract)
            nc.vector.tensor_scalar(emt[:, :], Mb[:, MH:2 * MH], -1.0, None, ALU.mult)
            ve.wait_ge(S["mrow_ready"], 1)
            nc.vector.tensor_tensor(dec[:, :, :], per_all(K["scausal_t"][0:NS, 0:NS]), small(4), ALU.subtract
                                    ).then_inc(S["exponents_ready"], 1)
            ve.wait_ge(S["last_ready"], 1)
            ch.link(nc.vector.tensor_copy(ML[:, :], psum[0:NS, 7, 0:2 * MH]))
            nc.vector.tensor_tensor(wl[:, :], a, ML[:, 0:MH], ALU.subtract)
            signal(nc.vector.tensor_tensor(sl[:, :], m0[:, :], ML[:, 0:MH], ALU.subtract), "differences_ready")
            ve.wait_ge(S["scores_ready"], 1)
            ve.wait_ge(S["exps_ready"], 8)
            ve.wait_ge(S["qk_copied"], 4)
            ch.link(nc.vector.tensor_tensor(sq[:, :, :], qt[:, :, :], n0[:, :, :], ALU.mult))
            ch.link(nc.vector.tensor_reduce(nq[:, :], sq[:, :, :], AX.X, ALU.add))
            ch.link(nc.vector.tensor_tensor(nq[:, :], nq[:, :], sc[:, :], ALU.mult))
            nc.vector.tensor_tensor(dec[:, :, :], dec[:, :, :], small(5), ALU.mult)
            signal(nc.vector.tensor_tensor(kw[:, :, :], kt[:, :, :], per_head(wl[:, :], MD), ALU.mult), "weighted_ready")
            signal(nc.vector.tensor_tensor(slrow[:, :, :], K["slast8"][0:NS, 0:NSEQ].unsqueeze(2).to_broadcast([NS, NSEQ, MH]),
                                           sl[:, :].unsqueeze(1).to_broadcast([NS, NSEQ, MH]), ALU.mult), "scale_ready")
            for q in range(NSEQ):
                nc.vector.tensor_scalar(kwm[:, q, :], kw[:, :, :].rearrange("p h k -> p (h k)"), K["sseq8"][0:NS, q:q + 1],
                                        None, ALU.mult).then_inc(S["masked_ready"], 1)
            ve.wait_ge(S["inter_turned"], 1)
            ve.wait_ge(S["intra_ready"], 1)
            ch.link(nc.vector.tensor_tensor(num[:, :, 0:MD], psum[0:NS, 6, :].rearrange("p (h v) -> p h v", h=MH),
                                            per_head(sc[:, :], MD), ALU.mult))
            ch.link(nc.vector.tensor_tensor(num[:, :, 0:MD], num[:, :, 0:MD], wide(0)[:, :, 0:MD], ALU.add))
            ch.link(nc.vector.tensor_tensor(nq[:, :], nq[:, :], wide(0)[:, :, MD], ALU.add))
            ch.link(nc.vector.scalar_tensor_tensor(out=r2[:, :], in0=nq[:, :], scalar=-1.0, in1=nq[:, :], op0=ALU.mult, op1=ALU.max))
            ch.link(nc.vector.tensor_tensor(r2[:, :], r2[:, :], emt[:, :], ALU.max))
            ch.link(nc.vector.reciprocal(r2[:, :], r2[:, :]))
            ch.link(nc.vector.tensor_tensor(num[:, :, 0:MD], num[:, :, 0:MD], per_head(r2[:, :], MD), ALU.mult))
            ch.link(nc.vector.tensor_tensor(sq[:, :, :], num[:, :, 0:MD], num[:, :, 0:MD], ALU.mult))
            ch.link(nc.vector.tensor_reduce(r1[:, :], sq[:, :, :], AX.X, ALU.add))
            signal(nc.vector.tensor_scalar(r1[:, :], r1[:, :], 1.0 / MD, EPS, ALU.mult, ALU.add), "square_ready")
            ve.wait_ge(S["scale_spread"], 1)
            ch.link(nc.vector.tensor_copy(slb[:, :, :], psum[:, 4, 0:NSEQ * MH].rearrange("p (b h) -> p b h", h=MH)))
            ch.link(nc.vector.tensor_copy(sl8[:, :], psum[0:NSEQ, 7, 0:2 * MH]))
            ch.link(nc.vector.tensor_tensor(n8[:, :, :], n8[:, :, :], sl8[:, 0:MH].unsqueeze(2).to_broadcast([NSEQ, MH, MD]), ALU.mult))
            signal(nc.vector.tensor_tensor(n8[:, :, :], n8[:, :, :], psum[0:NSEQ, 5, :].rearrange("p (h k) -> p h k", h=MH),
                                           ALU.add), "norm_ready")
            for q in range(NSEQ):
                ve.wait_ge(S["update_ready"], q + 1)
                ve.wait_ge(S["inter_ready"], 1)
                ch.link(nc.vector.tensor_tensor(C[:, q, :, :], C[:, q, :, :], slb[:, q, :].unsqueeze(2).to_broadcast([P, MH, MD]), ALU.mult))
                nc.vector.tensor_tensor(C[:, q, :, :], C[:, q, :, :], psum[:, 2 + q % 2, :].rearrange("p (h v) -> p h v", h=MH),
                                        ALU.add).then_inc(S["updated"], 1)
            ve.wait_ge(S["root_ready"], 1)
            ch.link(nc.vector.reciprocal(r1[:, :], r1[:, :]))
            ch.link(nc.vector.tensor_tensor(num[:, :, 0:MD], num[:, :, 0:MD], per_head(r1[:, :], MD), ALU.mult))
            ch.link(nc.vector.tensor_tensor(num[:, :, 0:MD], num[:, :, 0:MD], mnorm[:, :, :], ALU.mult))
            signal(nc.vector.tensor_tensor(num[:, :, 0:MD], num[:, :, 0:MD],
                                           tokm[0:NS, last, C_OG:C_OG + 512].rearrange("p (h v) -> p h v", h=MH), ALU.mult),
                   "gated_ready")
            ve.wait_ge(S["turned"], 1)
            nc.vector.tensor_copy(hm[:, :, TP:T], psum[:, 0, 0:MH * NS].rearrange("p (h t) -> p h t", h=MH))


HEADS_AT_ONCE = 2
BRANCHES = CMP, SEL, SLIDE = range(3)
NCMP = TP // CB
RAWW = 1920
STRIPW, CSTRIPW, WSTRIPW = TP, NCMP + 4 * (NTILE - 1), WIN + P


def compress_setup(nc, A, N, zn, psum):
    with stage(nc, "cmp") as (ctx, sem):
        sb = lambda n, s: ctx.enter_context(nc.sbuf_tensor("cmp_" + n, s, F32))
        pe_in = sb("pe", [P, 2, CB])
        act_out = sb("act", [P, 2, NCMP])
        rel, onehot, rmask, rv = sb("rel", [NBUCKET, NH]), sb("onehot", [NBUCKET, 2048]), sb("rmask", [NH, 2048]), sb("rv", [NH, 2048])
        loaded, layer1_ready, bias_ready, act_ready, layer2_ready, copied, vec_ready, vec_masked, stored = map(sem, (
            "loaded", "layer1_ready", "bias_ready", "act_ready", "layer2_ready", "copied", "vec_ready", "vec_masked", "stored"))
        block = ctx.enter_context(nc.Block())

        @block.sync
        def _(sp):
            for dst, src in ((N["w1"][:, :, :, :], A["cmp_w1"]), (N["w2"][:, :, :], A["cmp_w2"]), (pe_in[:, :, :], A["cmp_pe"]),
                             (rel[:, :], A["rel"]), (onehot[:, :], A["onehot"]), (rmask[:, :], A["rmask"])):
                sp.dma_start(dst, src).then_inc(loaded, 16)
            sp.wait_ge(vec_masked, 4)
            sp.dma_start(A["bias_vec"], rv[:, :]).then_inc(stored, 16)
            sp.wait_ge(stored, 16)

        @block.tensor
        def _(pe):
            pe.wait_ge(loaded, 96)
            for q in range(4):
                nc.tensor.matmul(psum[0:NH, q, :], rel[:, :], onehot[:, q * 512:(q + 1) * 512], start=True, stop=True
                                 ).then_inc(vec_ready, 1)
            for kv in range(2):
                for j in range(CB):
                    nc.tensor.matmul(psum[:, 4 + kv, 0:1], N["w1"][:, kv, j, :], pe_in[:, kv, j:j + 1],
                                     start=(j == 0), stop=(j == CB - 1))
                for j in range(CB):
                    last = nc.tensor.matmul(psum[:, 6 + kv, 0:NCMP], N["w1"][:, kv, j, :],
                                            zn[:, Q_KCMP - 4 + kv, j:TP:CB], start=(j == 0), stop=(j == CB - 1))
            last.then_inc(layer1_ready, 1)
            pe.wait_ge(act_ready, 2)
            nc.tensor.matmul(psum[:, 4, 0:NCMP], N["w2"][:, 0, :], act_out[:, 0, :], start=True, stop=True)
            nc.tensor.matmul(psum[0:NCMP, 5, 0:P], act_out[:, 1, :], N["w2"][:, 1, :], start=True, stop=True
                             ).then_inc(layer2_ready, 1)

        @block.vector
        def _(ve):
            ve.wait_ge(loaded, 96)
            for q in range(4):
                ve.wait_ge(vec_ready, q + 1)
                c = slice(q * 512, (q + 1) * 512)
                nc.vector.tensor_tensor(rv[:, c], psum[0:NH, q, :], rmask[:, c], ALU.add).then_inc(vec_masked, 1)
            ve.wait_ge(layer1_ready, 1)
            nc.vector.tensor_copy(N["pb"][:, :], psum[:, 4:6, 0]).then_inc(bias_ready, 1)
            ve.wait_ge(layer2_ready, 1)
            nc.vector.tensor_copy(N["kcmp"][:, :], psum[:, 4, 0:NCMP])
            nc.vector.tensor_copy(N["vcmp"][:, :], psum[0:NCMP, 5, 0:P])

        @block.scalar
        def _(act):
            act.wait_ge(bias_ready, 1)
            for kv in range(2):
                nc.scalar.activation(act_out[:, kv, :], psum[:, 6 + kv, 0:NCMP], ACT.Gelu_apprx_tanh,
                                     bias=N["pb"][:, kv:kv + 1]).then_inc(act_ready, 1)


def nsa_prompt(nc, A, O, K, N, zn, tokn, gates, on, psum):
    units = [(br, t, g) for t in range(NTILE) for br in BRANCHES for g in range(HEADS_AT_ONCE)]
    U = len(units)
    PER_TILE = len(BRANCHES) * HEADS_AT_ONCE
    NBUF = 4

    def keys(u):
        br, t, _ = units[u]
        if br == CMP:
            return 0, NCMP
        first = 0 if br == SEL else max(0, t - WIN // P)
        return first, (t + 1 - first) * P

    turns = []
    for u in range(U):
        nt = -(-keys(u)[1] // P)
        turns += [(u, k, min(4, nt - k)) for k in range(0, nt, 4)]
    by_unit = [[q for q, x in enumerate(turns) if x[0] == u] for u in range(U)]
    NT = len(turns)

    with stage(nc, "nsap") as (ctx, sem):
        sb = lambda n, s: ctx.enter_context(nc.sbuf_tensor("np_" + n, s, F32))
        raw = sb("raw", [P, 2, RAWW])
        strip, wstrip, cstrip = sb("strip", [P, 2, STRIPW]), sb("wstrip", [P, 2, WSTRIPW]), sb("cstrip", [P, 2, CSTRIPW])
        qs = sb("qs", [P, TP])
        pb = sb("p", [P, NBUF, TP])
        pt = sb("pt", [P, 2, NTILE, P])
        gp = sb("gp", [P, 2, NTILE, 3])
        nm, sums, rs = sb("nm", [P, NBUF]), sb("sums", [P, NBUF]), sb("rs", [P, NBUF])
        names = ("raw_loaded", "flipped", "setup_ready", "scores_ready", "logits_ready", "max_ready", "exp_ready", "inverted",
                 "scaled", "turn_ready", "copied", "pv_ready", "on_stored", "gates_ready", "kept")
        S = {n: sem(n) for n in names}
        block = ctx.enter_context(nc.Block())

        @block.sync
        def _(sp):
            for p in range(NPAIR):
                if p:
                    sp.wait_ge(S["flipped"], p)
                for g in range(2):
                    h = p + NPAIR * g
                    src = A["bias_vec"][h:h + 1, 0:RAWW]
                    src = bass.AP(tensor=src.tensor, offset=src.offset, ap=[[1, P], [1, RAWW]])
                    sp.dma_start(raw[:, g, :], src).then_inc(S["raw_loaded"], 16)
            sp.dma_start(O["winp"], A["winp"]).then_inc(S["kept"], 16)
            sp.dma_start(O["zkv"], zn[:, 4:8, :]).then_inc(S["kept"], 16)
            sp.dma_start(O["tkv"], tokn[:, :, 0:2 * P]).then_inc(S["kept"], 16)
            sp.wait_ge(S["kept"], 48)

        @block.tensor
        def _(pe):
            def scores(i, u):
                br, t, g = units[u]
                k0, nk = keys(u)
                if u >= 2:
                    pe.wait_ge(S["logits_ready"], i * U + u - 1)
                hs = slice(g * HD, (g + 1) * HD)
                src = {CMP: N["kcmp"], SEL: zn[:, Q_KSEL - 4, :], SLIDE: zn[:, Q_KWIN - 4, :]}[br]
                for c in range(0, nk, 512):
                    w = min(512, nk - c)
                    last = nc.tensor.matmul(psum[:, 2 * (u % 2) + c // 512, 0:w], qs[hs, t * P:(t + 1) * P],
                                            src[hs, k0 * P + c:k0 * P + c + w], start=True, stop=True)
                last.then_inc(S["scores_ready"], 1)

            def turn(i, u):
                pe.wait_ge(S["scaled"], i * U + u + 1)
                nk = keys(u)[1]
                for q in by_unit[u]:
                    _, k, n = turns[q]
                    if q >= 2:
                        pe.wait_ge(S["copied"], i * NT + q - 1)
                    for j in range(n):
                        w = min(P, nk - (k + j) * P)
                        last = nc.tensor.transpose(psum[0:w, 4 + q % 2, j * P:(j + 1) * P],
                                                   pb[:, u % NBUF, (k + j) * P:(k + j) * P + w], K["ident"][:, :])
                    last.then_inc(S["turn_ready"], 1)

            def values(i, u):
                br, t, g = units[u]
                k0, nk = keys(u)
                pe.wait_ge(S["copied"], i * NT + by_unit[u][-1] + 1)
                if t >= 2 and br == BRANCHES[0]:
                    pe.wait_ge(S["on_stored"], i * NTILE + t + 1)
                nt = -(-nk // P)
                for j in range(nt):
                    if br == CMP:
                        v = N["vcmp"][0:NCMP, g * HD:(g + 1) * HD]
                    else:
                        c = (N_VSEL if br == SEL else N_VWIN) + g * HD
                        v = tokn[:, k0 + j, c:c + HD]
                    w = min(P, nk)
                    last = nc.tensor.matmul(psum[g * HD:(g + 1) * HD, 6 + t % 2, 0:P], v, pt[0:w, u % 2, j, :],
                                            start=(br == BRANCHES[0] and j == 0), stop=(br == BRANCHES[-1] and j == nt - 1))
                last.then_inc(S["pv_ready"], 1)

            with pe.Fori(0, NPAIR) as i:
                pe.wait_ge(S["on_stored"], i * NTILE + 2)
                pe.wait_ge(S["raw_loaded"], 32 * i + 32)
                for g in range(2):
                    for c in range(2):
                        nc.tensor.matmul(psum[:, 2 * g + c, :], K["flip"][:, :], raw[:, g, c * 512:(c + 1) * 512], start=True, stop=True)
                for g in range(2):
                    last = nc.tensor.matmul(psum[:, 4, g * 64:g * 64 + CSTRIPW], K["flip"][:, :],
                                            raw[:, g, CB - 1:CB - 1 + CB * (CSTRIPW - 1) + 1:CB], start=True, stop=True)
                last.then_inc(S["flipped"], 1)
                pe.wait_ge(S["setup_ready"], i + 1)
                for u in range(3):
                    scores(i, u)
                turn(i, 0)
                for u in range(U):
                    if u + 3 < U:
                        scores(i, u + 3)
                    if u + 1 < U:
                        turn(i, u + 1)
                    values(i, u)

        @block.scalar
        def _(act):
            def exp(i, u):
                x = pb[:, u % NBUF, 0:keys(u)[1]]
                act.wait_ge(S["max_ready"], i * U + u + 1)
                if u >= NBUF:
                    act.wait_ge(S["inverted"], i * U + u - NBUF + 1)
                nc.scalar.activation(x, x, ACT.Exp, bias=nm[:, u % NBUF:u % NBUF + 1],
                                     accum_out=sums[:, u % NBUF:u % NBUF + 1]).then_inc(S["exp_ready"], 1)

            def copies(i, u):
                if u >= 2:
                    act.wait_ge(S["pv_ready"], i * U + u - 1)
                w = min(P, keys(u)[1])
                for q in by_unit[u]:
                    _, k, n = turns[q]
                    act.wait_ge(S["turn_ready"], i * NT + q + 1)
                    nc.scalar.activation(pt[0:w, u % 2, k:k + n, :], psum[0:w, 4 + q % 2, 0:n * P].rearrange("p (n q) -> p n q", n=n),
                                         ACT.Copy).then_inc(S["copied"], 1)

            with act.Fori(0, NPAIR) as i:
                exp(i, 0)
                exp(i, 1)
                copies(i, 0)
                for u in range(U):
                    if u + 2 < U:
                        exp(i, u + 2)
                    if u + 1 < U:
                        copies(i, u + 1)

        @block.vector
        def _(ve):
            def logits(i, u):
                br, t, g = units[u]
                k0, nk = keys(u)
                if br == CMP:
                    bias = cstrip[:, g, 4 * (NTILE - 1 - t):4 * (NTILE - 1 - t) + nk]
                elif br == SEL or t < WIN // P:
                    bias = strip[:, g, (NTILE - 1 - t) * P:TP]
                else:
                    bias = wstrip[:, g, :]
                ve.wait_ge(S["scores_ready"], i * U + u + 1)
                if u >= NBUF:
                    ve.wait_ge(S["turn_ready"], i * NT + by_unit[u - NBUF][-1] + 1)
                x = pb[:, u % NBUF, 0:nk]
                s = psum[:, 2 * (u % 2):2 * (u % 2) + 2, :].rearrange("p a b -> p (a b)")[:, 0:nk]
                nc.vector.tensor_tensor(x, s, bias, ALU.add).then_inc(S["logits_ready"], 1)
                ve.wait_ge(S["logits_ready"], i * U + u + 1)
                nc.vector.tensor_reduce(nm[:, u % NBUF:u % NBUF + 1], x, AX.X, ALU.max, negate=True).then_inc(S["max_ready"], 1)

            def factors(i, u):
                br, t, g = units[u]
                r = rs[:, u % NBUF:u % NBUF + 1]
                ve.wait_ge(S["exp_ready"], i * U + u + 1)
                nc.vector.reciprocal(r, sums[:, u % NBUF:u % NBUF + 1]).then_inc(S["inverted"], 1)
                ve.wait_ge(S["inverted"], i * U + u + 1)
                x = pb[:, u % NBUF, 0:keys(u)[1]]
                nc.vector.tensor_scalar(x, x, r, gp[:, g, t, br:br + 1], ALU.mult, ALU.mult).then_inc(S["scaled"], 1)

            def store(i, t):
                ve.wait_ge(S["pv_ready"], i * U + (t + 1) * PER_TILE)
                nc.vector.tensor_scalar(on[:, ds(i, 1), t * P:(t + 1) * P].rearrange("p a t -> p (a t)"),
                                        psum[:, 6 + t % 2, 0:P], 1.0, None, ALU.mult).then_inc(S["on_stored"], 1)

            ve.sem_inc(S["on_stored"], 2)
            with ve.Fori(0, NPAIR) as i:
                nc.vector.tensor_scalar(qs[:, :], zn[:, ds(i, 1), 0:TP].rearrange("p a t -> p (a t)"), CMP_SCALE, None, ALU.mult)
                ch = Chain(ve, S["gates_ready"], 4 * i)
                for g in range(2):
                    ch.link(nc.vector.tensor_copy(gp[:, g, :, :], gates[:, 0:NTILE, ds(3 * (i + NPAIR * g), 3)]))
                for g in range(2):
                    ch.link(nc.vector.tensor_tensor(gp[:, g, 0, CMP:CMP + 1], gp[:, g, 0, CMP:CMP + 1], K["seen"][:, :], ALU.mult))
                ve.wait_ge(S["flipped"], i + 1)
                for g in range(2):
                    full = psum[:, 2 * g:2 * g + 2, :].rearrange("p a b -> p (a b)")
                    nc.vector.tensor_copy(strip[:, g, :], full)
                    nc.vector.tensor_copy(wstrip[:, g, P:WSTRIPW], full[:, TP - WIN:TP])
                    nc.vector.tensor_tensor(wstrip[:, g, 0:P], full[:, TP - WSTRIPW:TP - WIN], K["wmask"][:, :], ALU.add)
                nc.vector.tensor_copy(cstrip[:, :, :], psum[:, 4, 0:128].rearrange("p (g x) -> p g x", g=2)[:, :, 0:CSTRIPW]
                                      ).then_inc(S["setup_ready"], 1)
                ve.wait_ge(S["setup_ready"], i + 1)
                for u in range(3):
                    logits(i, u)
                    if u < 2:
                        factors(i, u)
                for u in range(U):
                    if u + 3 < U:
                        logits(i, u + 3)
                    if u + 2 < U:
                        factors(i, u + 2)
                    if u % PER_TILE == PER_TILE - 1:
                        store(i, u // PER_TILE)


def compress_sample(nc, A, N, pages, psum):
    with stage(nc, "cmps") as (ctx, sem):
        sb = lambda n, s: ctx.enter_context(nc.sbuf_tensor("cs_" + n, s, F32))
        kv_in = sb("kv", [P, 2, NPAGE, 2 * PAGE])
        act_out = sb("act", [P, 2, P])
        loaded = [sem("loaded0"), sem("loaded1")]
        loaded_soft = [N["soft"][n] for n in ("c0", "c1")]
        layer1_ready, act_ready, layer2_ready, copied = map(sem, ("layer1_ready", "act_ready", "layer2_ready", "copied"))
        block = ctx.enter_context(nc.Block())
        NB = PAST // CB

        def load(eng, first, count, i, j, done):
            with eng.Fori(0, count // 4) as p:
                if i is not None:
                    eng.wait_ge(layer1_ready, 2 * i + j - 1)
                at = [p * 4 + e + first for e in range(4)]
                base = ((2 * i if i is not None else 0) + j) * NPAGE
                page = [eng.value_load(pages[0:1, ds(base + a, 1)], min_val=0, max_val=N["n_pool"] - 1) for a in at]
                for e in range(4):
                    eng.dma_start(kv_in[:, j, ds(at[e], 1), :].rearrange("p a x -> p (a x)"),
                                  A["pool"][ds(page[e], 1), :, 0:2 * PAGE].rearrange("a p x -> (a p) x")).then_inc(done[j], 16)

        @block.sync
        def _(sp):
            for j in range(2):
                load(sp, 0, 12, None, j, loaded)
            with sp.Fori(1, NSEQ // 2) as i:
                for j in range(2):
                    load(sp, 0, 12, i, j, loaded)

        @block.gpsimd
        def _(pool):
            for j in range(2):
                load(pool, 20, 12, None, j, loaded_soft)
            with pool.Fori(1, NSEQ // 2) as i:
                for j in range(2):
                    load(pool, 20, 12, i, j, loaded_soft)

        @block.tensor
        def _(pe):
            with pe.Fori(0, NSEQ // 2) as i:
                for j in range(2):
                    pe.wait_ge(loaded[j], 16 * 20 * i + 16 * 20)
                    pe.wait_ge(loaded_soft[j], 16 * 12 * i + 16 * 12)
                    pe.wait_ge(copied, 2 * i + j + 1)
                    for kv in range(2):
                        for r in range(CB):
                            last = nc.tensor.matmul(psum[:, kv, 0:NB], N["w1"][:, kv, r, :],
                                                    kv_in[:, j, :, kv * PAGE + r:(kv + 1) * PAGE:CB],
                                                    start=(r == 0), stop=(r == CB - 1))
                    last.then_inc(layer1_ready, 1)
                    pe.wait_ge(act_ready, 4 * i + 2 * j + 2)
                    nc.tensor.matmul(psum[:, 2, 0:NB], N["w2"][:, 0, :], act_out[:, 0, :], start=True, stop=True)
                    nc.tensor.matmul(psum[:, 3, 0:P], act_out[:, 1, :], N["w2"][:, 1, :], start=True, stop=True
                                     ).then_inc(layer2_ready, 1)

        @block.scalar
        def _(act):
            def gelu(i, j):
                act.wait_ge(layer1_ready, 2 * i + j + 1)
                for kv in range(2):
                    nc.scalar.activation(act_out[:, kv, :], psum[:, kv, 0:NB], ACT.Gelu_apprx_tanh,
                                         bias=N["pb"][:, kv:kv + 1]).then_inc(act_ready, 1)

            for j in range(2):
                load(act, 12, 8, None, j, loaded)
            with act.Fori(0, NSEQ // 2 - 1) as i:
                for j in range(2):
                    gelu(i, j)
                    load(act, 12, 8, i + 1, j, loaded)
            for j in range(2):
                gelu(NSEQ // 2 - 1, j)

        @block.vector
        def _(ve):
            ve.sem_inc(copied, 1)
            with ve.Fori(0, NSEQ // 2) as i:
                for j in range(2):
                    ve.wait_ge(layer2_ready, 2 * i + j + 1)
                    nc.vector.tensor_scalar(N["kc"][:, ds(2 * i + j, 1), :].rearrange("p a x -> p (a x)"), psum[:, 2, 0:NB],
                                            1.0, None, ALU.mult)
                    nc.vector.tensor_scalar(N["vc"][:, ds(2 * i + j, 1), :].rearrange("p a x -> p (a x)"), psum[:, 3, 0:P],
                                            1.0, None, ALU.mult).then_inc(copied, 1)


CMPC, TAILC = 1024, 1152
BW = TAILC + NS


def nsa_sample(nc, A, K, N, zn, tokn, gates, pages, on, psum):
    with stage(nc, "nsas") as (ctx, sem):
        sb = lambda n, s: ctx.enter_context(nc.sbuf_tensor("ns_" + n, s, F32))
        qf, qz = sb("qf", [P, 2, P]), sb("qz", [P, NSEQ, P])
        relq, onehot, delta = sb("relq", [P, NH]), sb("onehot", [P, BW]), sb("delta", [P, TS])
        relr = sb("relr", [P, 4, NH, TS])
        bias = sb("bias", [P, BW])
        group, tmask, wmask = sb("group", [P, P]), sb("tmask", [P, 2, NS]), sb("wmask", [P, TS])
        gr = sb("gr", [P, 2, 3])
        row_token, row_head = sb("row_token", [NS, 2, P]), sb("row_head", [P, 3 * NH])
        picked = sb("picked", [P, 2, 3 * NH])
        kbuf, vbuf = sb("kbuf", [P, 2, 4, 4 * PAGE]), sb("vbuf", [P, 2, 4, 4 * PAGE])
        win = sb("win", [P, 4, 2, WIN])
        ss = sb("ss", [P, PAST + NS])
        ws = sb("ws", [P, WIN + NS])
        pc, pcg = sb("pc", [P, P]), sb("pcg", [P, P])
        imp, top, bmask = sb("imp", [P, SB + 1]), sb("top", [P, 16]), sb("bmask", [P, SB + 1])
        nm, sums, rs = sb("nm", [P, 3]), sb("sums", [P, 3]), sb("rs", [P, 3])
        pt = sb("pt", [P, 2, 4, P])
        names = ("loaded", "win_loaded0", "win_loaded1", "k_loaded0", "k_loaded1", "v_loaded0", "v_loaded1",
                 "q_ready", "rel_ready", "bias_ready", "score_ready", "score_drained", "pc_ready", "max_ready",
                 "exp_ready", "scale_ready", "probs_ready", "turn_ready", "turn_copied", "pv_ready", "out_copied", "steps")
        S = {n: sem(n) for n in names}
        S.update(N["soft"])
        block = ctx.enter_context(nc.Block())
        CMPJ, WINJ, WTAIL, IMP, SEL0, STAIL = 0, 1, 2, 3, 4, 12
        NJ = 13
        TC, TW, TWT, TS0, TST, NT = 0, 1, 2, 3, 11, 12
        NBLK = PAST // SB

        def load(eng, kind, s, c, j, mine):
            buf, at = (kbuf, 2 * PAGE) if kind[0] == "k" else (vbuf, 3 * PAGE)
            for first in range(0, len(mine), 4):
                some = mine[first:first + 4]
                page = [eng.value_load(pages[0:1, ds(4 * c + (4 * s + b) * NPAGE + p, 1)], min_val=0, max_val=N["n_pool"] - 1)
                        for b, p in some]
                for (b, p), g in zip(some, page):
                    eng.dma_start(buf[:, j, b, p * PAGE:(p + 1) * PAGE],
                                  A["pool"][ds(g, 1), :, at:at + PAGE].rearrange("a p x -> (a p) x")).then_inc(S[kind + str(j)], 16)

        def first_keys(eng, s, mine, name):
            for c in range(2):
                if s:
                    eng.wait_ge(S["score_ready"], SEL0 + 6 + c + 1)
                load(eng, "k_" + name, s, c, c, mine)

        def first_values(eng, s, mine, name):
            for c in range(2):
                if s:
                    eng.wait_ge(S["pv_ready"], TS0 + 6 + c + 1)
                load(eng, "v_" + name, s, c, c, mine)

        def load_pages(eng, s, mine, name):
            first_keys(eng, s, mine, name)
            with eng.Fori(1, 4) as i:
                for j in range(2):
                    eng.wait_ge(S["score_ready"], 2 * i + j + s * NJ + SEL0 - 1)
                    load(eng, "k_" + name, s, 2 * i + j, j, mine)
            first_values(eng, s, mine, name)
            with eng.Fori(1, 4) as i:
                for j in range(2):
                    eng.wait_ge(S["pv_ready"], 2 * i + j + s * NT + TS0 - 1)
                    load(eng, "v_" + name, s, 2 * i + j, j, mine)

        sp_pages = [(0, p) for p in range(4)] + [(3, 0)]
        pool_pages = [(1, p) for p in range(4)] + [(3, p) for p in range(1, 4)]
        act_pages = [(2, p) for p in range(4)]

        @block.gpsimd
        def _(pool):
            for s in range(2):
                load_pages(pool, s, pool_pages, "soft")

        @block.sync
        def _(sp):
            for dst, src in ((relq[:, :], A["relq"]), (onehot[:, :], A["onehot_s"]), (delta[:, :], A["delta"]),
                             (group[:, :], A["group"]), (tmask[:, :, :], A["tmask"]), (wmask[:, :], A["wmask_s"]),
                             (row_token[:, :, :], A["row_token"]), (row_head[:, :], A["row_head"])):
                sp.dma_start(dst, src).then_inc(S["loaded"], 16)
            for s in range(2):
                if s:
                    sp.wait_ge(S["pv_ready"], TWT + 1)
                for b in range(4):
                    sp.dma_start(win[:, b, :, :], A["winp"][4 * s + b]).then_inc(S[f"win_loaded{s}"], 16)
                load_pages(sp, s, sp_pages, "loaded")

        @block.tensor
        def _(pe):
            pe.wait_ge(S["rel_ready"], 1)
            for n, c in enumerate(range(0, BW, 512)):
                w = min(512, BW - c)
                last = nc.tensor.matmul(psum[:, 5 + n, 0:w], relr[:, :, :, :].rearrange("p b h q -> p (b h q)"),
                                        onehot[:, c:c + w], start=True, stop=True)
            for s in range(2):
                last = nc.tensor.matmul(psum[:, 4, s * 32:s * 32 + 3 * NH], row_token[:, s, :], gates[0:NS, NTILE, :], start=True, stop=True)
            last.then_inc(S["bias_ready"], 1)
            pe.wait_ge(S["q_ready"], 1)
            for s in range(2):
                def job(n):
                    n += s * NJ
                    if n >= 2:
                        pe.wait_ge(S["score_drained"], n - 1)
                    return psum[:, n % 2, :]

                def per_sequence(n, rhs, w):
                    out = job(n)
                    for b in range(4):
                        last = nc.tensor.matmul(out[:, 0:w], qz[:, 4 * s + b, :], rhs(b), start=(b == 0), stop=(b == 3))
                    last.then_inc(S["score_ready"], 1)

                per_sequence(CMPJ, lambda b: N["kc"][:, 4 * s + b, :], P)
                pe.wait_ge(S[f"win_loaded{s}"], 64)
                per_sequence(WINJ, lambda b: win[:, b, 0, :], WIN)
                nc.tensor.matmul(job(WTAIL)[:, 0:NS], qf[:, s, :], zn[:, Q_KWIN - 4, TP:T], start=True, stop=True
                                 ).then_inc(S["score_ready"], 1)
                out = job(IMP)
                pe.wait_ge(S["pc_ready"], s + 1)
                nc.tensor.matmul(out[:, 0:P], group[:, :], pc[:, :], start=True, stop=True).then_inc(S["score_ready"], 1)
                for c in range(8):
                    pe.wait_ge(S[f"k_loaded{c % 2}"], 144 * (4 * s + c // 2 + 1))
                    pe.wait_ge(S[f"k_soft{c % 2}"], 112 * (4 * s + c // 2 + 1))
                    per_sequence(SEL0 + c, lambda b: kbuf[:, c % 2, b, :], 4 * PAGE)
                nc.tensor.matmul(job(STAIL)[:, 0:NS], qf[:, s, :], zn[:, Q_KSEL - 4, TP:T], start=True, stop=True
                                 ).then_inc(S["score_ready"], 1)

                def turn(n, src, w, k):
                    n += s * NT
                    if n >= 2:
                        pe.wait_ge(S["turn_copied"], n - 1)
                    for j in range(k):
                        last = nc.tensor.transpose(psum[0:w, 2 + n % 2, j * P:(j + 1) * P], src[:, j * w:(j + 1) * w], K["ident"][:, :])
                    last.then_inc(S["turn_ready"], 1)

                def products(n, w, k, value):
                    first, last_job = n == TC, n == TST
                    n += s * NT
                    pe.wait_ge(S["turn_copied"], n + 1)
                    if first:
                        pe.wait_ge(S["out_copied"], s + 1)
                    for j in range(k):
                        for b in range(4):
                            last = nc.tensor.matmul(psum[:, 4 + b, 0:32], value(b, j), pt[0:w, n % 2, j, b * 32:(b + 1) * 32],
                                                    start=first and j == 0, stop=last_job and j == k - 1)
                    last.then_inc(S["pv_ready"], 1)

                pe.wait_ge(S["probs_ready"], 3 * s + 1)
                turn(TC, pcg[:, :], P, 1)
                products(TC, P, 1, lambda b, j: N["vc"][:, 4 * s + b, :])
                pe.wait_ge(S["probs_ready"], 3 * s + 2)
                turn(TW, ws[:, 0:WIN], P, 4)
                products(TW, P, 4, lambda b, j: win[:, b, 1, j * P:(j + 1) * P])
                turn(TWT, ws[:, WIN:WIN + NS], NS, 1)
                products(TWT, NS, 1, lambda b, j: tokn[0:NS, NTILE, N_VWIN:N_VWIN + P])
                pe.wait_ge(S["probs_ready"], 3 * s + 3)
                turn(TS0, ss[:, 0:4 * P], P, 4)
                for c in range(8):
                    if c < 7:
                        turn(TS0 + c + 1, ss[:, (c + 1) * 4 * P:(c + 2) * 4 * P], P, 4)
                    pe.wait_ge(S[f"v_loaded{c % 2}"], 144 * (4 * s + c // 2 + 1))
                    pe.wait_ge(S[f"v_soft{c % 2}"], 112 * (4 * s + c // 2 + 1))
                    products(TS0 + c, P, 4, lambda b, j: vbuf[:, c % 2, b, j * P:(j + 1) * P])
                turn(TST, ss[:, PAST:PAST + NS], NS, 1)
                products(TST, NS, 1, lambda b, j: tokn[0:NS, NTILE, N_VSEL:N_VSEL + P])

        @block.scalar
        def _(act):
            for s in range(2):
                def exp(k, x):
                    act.wait_ge(S["max_ready"], 3 * s + k + 1)
                    nc.scalar.activation(x, x, ACT.Exp, bias=nm[:, k:k + 1], accum_out=sums[:, k:k + 1]).then_inc(S["exp_ready"], 1)

                def gate(k, dst, x):
                    act.wait_ge(S["scale_ready"], 3 * s + k + 1)
                    act.wait_ge(S["exp_ready"], 3 * s + k + 1)
                    nc.scalar.activation(dst, x, ACT.Copy, scale=rs[:, k:k + 1]).then_inc(S["probs_ready"], 1)

                def copy(n, w, k):
                    n += s * NT
                    act.wait_ge(S["turn_ready"], n + 1)
                    if n >= 2:
                        act.wait_ge(S["pv_ready"], n - 1)
                    nc.scalar.activation(pt[0:w, n % 2, 0:k, :], psum[0:w, 2 + n % 2, 0:k * P].rearrange("p (k r) -> p k r", k=k),
                                         ACT.Copy).then_inc(S["turn_copied"], 1)

                first_keys(act, s, act_pages, "loaded")
                exp(0, pc[:, :])
                exp(1, ws[:, :])
                gate(0, pcg[:, :], pc[:, :])
                for c in range(2, 8):
                    act.wait_ge(S["score_ready"], c + s * NJ + SEL0 - 1)
                    load(act, "k_loaded", s, c, c % 2, act_pages)
                gate(1, ws[:, :], ws[:, :])
                exp(2, ss[:, :])
                first_values(act, s, act_pages, "loaded")
                gate(2, ss[:, :], ss[:, :])
                copy(TC, P, 1)
                copy(TW, P, 4)
                copy(TWT, NS, 1)
                copy(TS0, P, 4)
                for c in range(8):
                    copy(TS0 + c + 1, *((P, 4) if c < 7 else (NS, 1)))
                    if c < 6:
                        act.wait_ge(S["pv_ready"], c + 2 + s * NT + TS0 - 1)
                        load(act, "v_loaded", s, c + 2, c % 2, act_pages)

        @block.vector
        def _(ve):
            ch = Chain(ve, S["steps"])
            ve.wait_ge(S["loaded"], 128)
            dst = relr[:, :, :, :].rearrange("p b h q -> p b (h q)")
            ch.link(nc.vector.tensor_copy(relr[:, 0, :, :], relq[:, :].unsqueeze(2).to_broadcast([P, NH, TS])))
            ch.link(nc.vector.tensor_tensor(relr[:, 0, :, :], relr[:, 0, :, :], delta[:, :].unsqueeze(1).to_broadcast([P, NH, TS]), ALU.mult))
            nc.vector.tensor_copy(relr[:, 1:4, :, :].rearrange("p b h q -> p b (h q)"),
                                  relr[:, 0, :, :].rearrange("p h q -> p (h q)").unsqueeze(1).to_broadcast([P, 3, NH * TS])
                                  ).then_inc(S["rel_ready"], 1)
            nc.vector.memset(qz[:, :, :], 0.0)
            ch.link(nc.vector.memset(qf[:, :, :], 0.0))
            for s in range(2):
                for g in range(2):
                    half = slice(g * HD, (g + 1) * HD)
                    for b in range(4):
                        q = 4 * s + b
                        last = nc.vector.tensor_scalar(
                            qf[half, s, b * 32 + g * 16:b * 32 + (g + 1) * 16].rearrange("p (i q) -> p i q", q=TS),
                            zn[half, 0:NPAIR, TP + q * TS:TP + (q + 1) * TS], CMP_SCALE, None, ALU.mult)
            ch.link(last)
            for q in range(NSEQ):
                c = slice((q % 4) * 32, (q % 4 + 1) * 32)
                last = nc.vector.tensor_copy(qz[:, q, c], qf[:, q // 4, c])
            last.then_inc(S["q_ready"], 1)
            ve.wait_ge(S["bias_ready"], 1)
            for n, c in enumerate(range(0, BW, 512)):
                w = min(512, BW - c)
                last = nc.vector.tensor_copy(bias[:, c:c + w], psum[:, 5 + n, 0:w])
            for s in range(2):
                ch.link(nc.vector.tensor_tensor(picked[:, s, :], psum[:, 4, s * 32:s * 32 + 3 * NH], row_head[:, :], ALU.mult))
                last = nc.vector.tensor_reduce(gr[:, s, :], picked[:, s, :].rearrange("p (h r) -> p r h", r=3), AX.X, ALU.add)
            last.then_inc(S["out_copied"], 1)
            ve.wait_ge(S["out_copied"], 1)
            for s in range(2):
                def job(n):
                    n += s * NJ
                    ve.wait_ge(S["score_ready"], n + 1)
                    return psum[:, n % 2, :]

                def most(k, x):
                    nc.vector.tensor_reduce(nm[:, k:k + 1], x, AX.X, ALU.max, negate=True).then_inc(S["max_ready"], 1)

                def scale(k, g):
                    ve.wait_ge(S["exp_ready"], 3 * s + k + 1)
                    ch.link(nc.vector.reciprocal(rs[:, k:k + 1], sums[:, k:k + 1]))
                    if k == 0:
                        ch.link(nc.vector.tensor_scalar(pc[:, :], pc[:, :], rs[:, 0:1], None, ALU.mult))
                        nc.vector.tensor_copy(rs[:, 0:1], gr[:, s, 0:1]).then_inc(S["scale_ready"], 1)
                    else:
                        nc.vector.tensor_tensor(rs[:, k:k + 1], rs[:, k:k + 1], gr[:, s, g:g + 1], ALU.mult).then_inc(S["scale_ready"], 1)

                def drained(ins, n):
                    ins.then_inc(S["score_drained"], 1)
                    ve.wait_ge(S["score_drained"], s * NJ + n + 1)

                if s:
                    ve.wait_ge(S["turn_ready"], NT)
                x = job(CMPJ)
                drained(nc.vector.tensor_tensor(pc[:, :], x[:, 0:P], bias[:, CMPC:CMPC + P], ALU.add), CMPJ)
                most(0, pc[:, :])
                x = job(WINJ)
                drained(nc.vector.tensor_tensor(ws[:, 0:WIN], x, bias[:, WIN:2 * WIN], ALU.add), WINJ)
                ch.link(nc.vector.tensor_tensor(ws[:, 0:TS], ws[:, 0:TS], wmask[:, :], ALU.add))
                x = job(WTAIL)
                drained(nc.vector.tensor_tensor(ws[:, WIN:WIN + NS], x[:, 0:NS], bias[:, TAILC:BW], ALU.add), WTAIL)
                ch.link(nc.vector.tensor_tensor(ws[:, WIN:WIN + NS], ws[:, WIN:WIN + NS], tmask[:, s, :], ALU.add))
                most(1, ws[:, :])
                scale(0, 0)
                nc.vector.memset(imp[:, NBLK:NBLK + 1], 1.0e4).then_inc(S["pc_ready"], 1)
                x = job(IMP)
                drained(nc.vector.tensor_reduce(imp[:, 0:NBLK], x[:, 0:P].rearrange("p (b c) -> p b c", c=SB // CB), AX.X, ALU.add), IMP)
                ch.link(nc.vector.memset(imp[:, 0:1], 1.0e4))
                for r in range(TOPK // 8):
                    ch.link(nc.vector.max(top[:, 8 * r:8 * r + 8], imp[:, :]))
                    ch.link(nc.vector.match_replace(imp[:, :], top[:, 8 * r:8 * r + 8], imp[:, :], -4.0))
                ch.link(nc.vector.tensor_scalar(bmask[:, :], imp[:, :], -2.0, NEG, ALU.is_gt, ALU.mult))
                for c in range(8):
                    x = job(SEL0 + c)
                    out = ss[:, c * 512:(c + 1) * 512].rearrange("p (b t) -> p b t", t=SB)
                    mask = bmask[:, 8 * c:8 * c + 8].unsqueeze(2).to_broadcast([P, 8, SB])
                    x3 = x.rearrange("p (b t) -> p b t", t=SB)
                    if c < 6:
                        drained(nc.vector.scalar_tensor_tensor(out=out, in0=x3, scalar=bias[:, 0:1], in1=mask,
                                                               op0=ALU.add, op1=ALU.add), SEL0 + c)
                    else:
                        drained(nc.vector.tensor_tensor(ss[:, c * 512:(c + 1) * 512], x, bias[:, (c - 6) * 512:(c - 5) * 512],
                                                        ALU.add), SEL0 + c)
                        ch.link(nc.vector.tensor_tensor(out, out, mask, ALU.add))
                x = job(STAIL)
                drained(nc.vector.tensor_tensor(ss[:, PAST:PAST + NS], x[:, 0:NS], bias[:, TAILC:BW], ALU.add), STAIL)
                ch.link(nc.vector.tensor_tensor(ss[:, PAST:PAST + NS], ss[:, PAST:PAST + NS], tmask[:, s, :], ALU.add))
                scale(1, 2)
                most(2, ss[:, :])
                scale(2, 1)
                ve.wait_ge(S["pv_ready"], (s + 1) * NT)
                for g in range(2):
                    half = slice(g * HD, (g + 1) * HD)
                    for b in range(4):
                        q = 4 * s + b
                        last = nc.vector.tensor_copy(on[half, 0:NPAIR, TP + q * TS:TP + (q + 1) * TS],
                                                     psum[half, 4 + b, g * 16:(g + 1) * 16].rearrange("p (i q) -> p i q", q=TS))
                last.then_inc(S["out_copied"], 1)


def merge(nc, A, h, high, low, hm, on, dst, acc):
    GATE, BRANCH = KD * P, 4 * P
    with stage(nc, "merge") as (ctx, sem):
        sb = lambda n, s: ctx.enter_context(nc.sbuf_tensor("mg_" + n, s, F32))
        gate_w, branch_w = sb("gate_w", [P, 2, GATE]), sb("branch_w", [P, 2, BRANCH])
        half = ctx.enter_context(nc.sbuf_tensor("mg_half", [P, 2, 2, GATE], F32R))
        sg, part = sb("gate", [P, 2, T]), sb("part", [P, T])
        gate_loaded = [sem("gate_loaded0"), sem("gate_loaded1")]
        branch_loaded = [sem("branch_loaded0"), sem("branch_loaded1")]
        gate_ready, branch_ready, gate_drained, branch_drained, parts, w_high, w_low, x_high, x_low = map(
            sem, ("gate_ready", "branch_ready", "gate_drained", "branch_drained", "parts", "w_high", "w_low", "x_high", "x_low"))
        h_loaded = [sem(f"h_loaded{g}") for g in range(NG)]
        block = ctx.enter_context(nc.Block())
        n_chunks = D // P

        def weights(i, r):
            at = r * (GATE + BRANCH)
            w = A["w_merge"][ds(i, 1), :, :].rearrange("a p k -> p (a k)") if not isinstance(i, int) else A["w_merge"][i]
            return w[:, at:at + GATE], w[:, at + GATE:at + GATE + BRANCH]

        @block.sync
        def _(sp):
            for r in range(2):
                for dst_w, src, done in zip((gate_w, branch_w), weights(0, r), (gate_loaded, branch_loaded)):
                    sp.dma_start(dst_w[:, r, :], src).then_inc(done[r], 16)
            with sp.Fori(1, n_chunks) as i:
                for r in range(2):
                    wg, wb = weights(i, r)
                    sp.wait_ge(w_low, 2 * i + r - 1)
                    sp.dma_start(gate_w[:, r, :], wg).then_inc(gate_loaded[r], 16)
                    sp.wait_ge(branch_ready, 2 * i + r - 1)
                    sp.dma_start(branch_w[:, r, :], wb).then_inc(branch_loaded[r], 16)

        @block.gpsimd
        def _(pool):
            with pool.Fori(0, n_chunks) as i:
                for r in range(2):
                    pool.wait_ge(w_high, 2 * i + r + 1)
                    low_part(nc.gpsimd, half[:, r, 1, :], gate_w[:, r, :], half[:, r, 0, :]).then_inc(w_low, 1)

        @block.tensor
        def _(pe):
            with pe.Fori(0, n_chunks) as i:
                for r, x in enumerate((hm, on)):
                    pe.wait_ge(w_low, 2 * i + r + 1)
                    pe.wait_ge(gate_drained, 2 * i + r + 1)
                    for g in range(NG):
                        c = slice(g * GW, (g + 1) * GW)
                        for k in range(KD):
                            if r == 0:
                                pe.wait_ge(x_low, g * KD + k + 1)
                            ks = slice(k * P, (k + 1) * P)
                            last = split_product(nc, acc[:, g, 0:GW], (half[:, r, 0, ks], half[:, r, 1, ks]),
                                                 (high[:, k, c], low[:, k, c]), k == 0, k == KD - 1)
                    last.then_inc(gate_ready, 1)
                    pe.wait_ge(branch_loaded[r], 16 * i + 16)
                    pe.wait_ge(branch_drained, 2 * i + r + 2)
                    for g in range(NG):
                        for k in range(4):
                            last = nc.tensor.matmul(acc[:, 3 + g, 0:GW], branch_w[:, r, k * P:(k + 1) * P],
                                                    x[:, k, g * GW:(g + 1) * GW], start=(k == 0), stop=(k == 3))
                    last.then_inc(branch_ready, 1)

        @block.scalar
        def _(act):
            for g in range(NG):
                c = slice(g * GW, (g + 1) * GW)
                act.dma_start(h[:, :, c], A["h_spill"][:, :, c]).then_inc(h_loaded[g], 16)
            for g in range(NG):
                act.wait_ge(h_loaded[g], 16)
                high_columns(nc, high, h, slice(g * GW, (g + 1) * GW), KD, x_high)
            act.sem_inc(gate_drained, 1)
            with act.Fori(0, n_chunks) as i:
                for r in range(2):
                    act.wait_ge(gate_ready, 2 * i + r + 1)
                    if r == 0:
                        act.wait_ge(branch_drained, 2 * i + 1)
                    else:
                        act.wait_ge(parts, i + 1)
                    nc.scalar.activation(sg[:, r, :].rearrange("p (g t) -> p g t", g=NG), acc[:, 0:NG, 0:GW], ACT.Sigmoid
                                         ).then_inc(gate_drained, 1)

        @block.vector
        def _(ve):
            def split_weights(r, i):
                ve.wait_ge(gate_loaded[r], 16 * i + 16)
                high_part(nc, half[:, r, 0, :], gate_w[:, r, :]).then_inc(w_high, 1)

            def chunk(i, last):
                for r in range(2):
                    ve.wait_ge(gate_drained, 2 * i + r + 2)
                    if not last:
                        split_weights(r, i + 1)
                    ve.wait_ge(branch_ready, 2 * i + r + 1)
                    gate = sg[:, r, :].rearrange("p (g t) -> p g t", g=NG)
                    if r == 0:
                        ve.wait_ge(parts, i + 1)
                    dst_r = part[:, :].rearrange("p (g t) -> p g t", g=NG) if r == 0 else gate
                    nc.vector.tensor_tensor(dst_r, acc[:, NG:2 * NG, 0:GW], gate, ALU.mult).then_inc(branch_drained, 1)
                    ve.wait_ge(branch_drained, 2 * i + r + 3)
                nc.vector.tensor_tensor(dst[:, ds(i, 1), :].rearrange("p a t -> p (a t)"), part[:, :], sg[:, 1, :], ALU.add
                                        ).then_inc(parts, 1)

            ve.sem_inc(branch_drained, 2)
            ve.sem_inc(parts, 1)
            split_weights(0, 0)
            split_weights(1, 0)
            for g in range(NG):
                low_columns(nc, ve, low, h, high, slice(g * GW, (g + 1) * GW), KD, g, x_high, x_low)
            with ve.Fori(0, n_chunks - 1) as i:
                chunk(i, False)
            chunk(n_chunks - 1, True)


def cross_prompt(nc, O, K, qx, mk, mv, ox, psum):
    with stage(nc, "xp") as (ctx, sem):
        sb = lambda n, s: ctx.enter_context(nc.sbuf_tensor("xp_" + n, s, F32))
        q = sb("q", [P, KD, P])
        p, pt = sb("p", [P, 2, MEM]), sb("pt", [P, 2, 2, P])
        nm, sums = sb("nm", [P, 2]), sb("sums", [P, 2])
        names = ("q_ready", "score_ready", "max_ready", "exp_ready", "inverted", "probs_ready", "turn_ready", "turn_copied",
                 "pv_ready", "out_ready", "stored")
        S = {n: sem(n) for n in names}
        block = ctx.enter_context(nc.Block())
        DC = KD // XH

        @block.sync
        def _(sp):
            sp.dma_start(O["mk"], mk[:, :, :]).then_inc(S["stored"], 16)
            sp.dma_start(O["mv"], mv[:, :, :]).then_inc(S["stored"], 16)
            sp.wait_ge(S["stored"], 32)

        @block.tensor
        def _(pe):
            def scores(i, h):
                for c in range(DC):
                    last = nc.tensor.matmul(psum[:, h % 2, 0:MEM], q[:, DC * h + c, :], mk[:, DC * h + c, :],
                                            start=(c == 0), stop=(c == DC - 1))
                last.then_inc(S["score_ready"], 1)

            with pe.Fori(0, NTILE) as i:
                pe.wait_ge(S["q_ready"], i + 1)
                scores(i, 0)
                for h in range(XH):
                    if h + 1 < XH:
                        if h >= 1:
                            pe.wait_ge(S["exp_ready"], XH * i + h)
                        scores(i, h + 1)
                    pe.wait_ge(S["probs_ready"], XH * i + h + 1)
                    for m in range(2):
                        last = nc.tensor.transpose(psum[:, 2 + h % 2, m * P:(m + 1) * P], p[:, h % 2, m * P:(m + 1) * P], K["ident"][:, :])
                    last.then_inc(S["turn_ready"], 1)
                    pe.wait_ge(S["turn_copied"], XH * i + h + 1)
                    for c in range(DC):
                        for m in range(2):
                            last = nc.tensor.matmul(psum[:, 4 + h % 2, c * P:(c + 1) * P], mv[:, m, (DC * h + c) * P:(DC * h + c + 1) * P],
                                                    pt[:, h % 2, m, :], start=(m == 0), stop=(m == 1))
                    last.then_inc(S["pv_ready"], 1)

        @block.scalar
        def _(act):
            with act.Fori(0, NTILE) as i:
                for h in range(XH):
                    act.wait_ge(S["max_ready"], XH * i + h + 1)
                    nc.scalar.activation(p[:, h % 2, :], psum[:, h % 2, 0:MEM], ACT.Exp, bias=nm[:, h % 2:h % 2 + 1],
                                         accum_out=sums[:, h % 2:h % 2 + 1]).then_inc(S["exp_ready"], 1)
                    act.wait_ge(S["turn_ready"], XH * i + h + 1)
                    nc.scalar.activation(pt[:, h % 2, :, :], psum[:, 2 + h % 2, 0:2 * P].rearrange("p (m q) -> p m q", m=2), ACT.Copy
                                         ).then_inc(S["turn_copied"], 1)

        @block.vector
        def _(ve):
            with ve.Fori(0, NTILE) as i:
                nc.vector.tensor_scalar(q[:, :, :], qx[:, :, ds(i * P, P)], float(D // XH) ** -0.5, None, ALU.mult
                                        ).then_inc(S["q_ready"], 1)

                def most(h):
                    ve.wait_ge(S["score_ready"], XH * i + h + 1)
                    nc.vector.tensor_reduce(nm[:, h % 2:h % 2 + 1], psum[:, h % 2, 0:MEM], AX.X, ALU.max, negate=True
                                            ).then_inc(S["max_ready"], 1)

                most(0)
                for h in range(XH):
                    s = sums[:, h % 2:h % 2 + 1]
                    ve.wait_ge(S["exp_ready"], XH * i + h + 1)
                    nc.vector.reciprocal(s, s).then_inc(S["inverted"], 1)
                    ve.wait_ge(S["inverted"], XH * i + h + 1)
                    nc.vector.tensor_scalar(p[:, h % 2, :], p[:, h % 2, :], s, None, ALU.mult).then_inc(S["probs_ready"], 1)
                    if h + 1 < XH:
                        most(h + 1)
                    ve.wait_ge(S["pv_ready"], XH * i + h + 1)
                    nc.vector.tensor_scalar(ox[:, DC * h:DC * (h + 1), ds(i * P, P)],
                                            psum[:, 4 + h % 2, 0:DC * P].rearrange("p (c q) -> p c q", c=DC), 1.0, None, ALU.mult
                                            ).then_inc(S["out_ready"], 1)
                ve.wait_ge(S["out_ready"], XH * i + XH)


def cross_sample(nc, A, K, qx, ox, psum):
    with stage(nc, "xs") as (ctx, sem):
        sb = lambda n, s: ctx.enter_context(nc.sbuf_tensor("xs_" + n, s, F32))
        qz = sb("qz", [P, NSEQ, KD, P])
        kv = sb("kv", [P, 2, KD * MEM])
        p, pt = sb("p", [P, MEM]), sb("pt", [P, 2, P])
        nm, sums = sb("nm", [P, 1]), sb("sums", [P, 1])
        cleared, q_ready, k_used, score_ready, max_ready, exp_ready, inverted, probs_ready, turn_ready, turn_copied, v_used = map(sem, (
            "cleared", "q_ready", "k_used", "score_ready", "max_ready", "exp_ready", "inverted", "probs_ready", "turn_ready",
            "turn_copied", "v_used"))
        loaded = [sem("loaded0"), sem("loaded1")]
        block = ctx.enter_context(nc.Block())
        DC = KD // XH

        @block.sync
        def _(sp):
            for n in range(2 * NSEQ):
                if n >= 2:
                    used, at = (k_used, n - 1) if n - 2 < NSEQ else (v_used, n - 1 - NSEQ)
                    sp.wait_ge(used, at)
                src = A["mem_k"][n] if n < NSEQ else A["mem_v"][n - NSEQ]
                sp.dma_start(kv[:, n % 2, :], src).then_inc(loaded[n % 2], 16)

        @block.gpsimd
        def _(pool):
            nc.gpsimd.memset(qz[:, :, :, :], 0.0).then_inc(cleared, 1)

        @block.vector
        def _(ve):
            ve.wait_ge(cleared, 1)
            for b in range(NSEQ):
                for h in range(XH):
                    r = b * XH * TS + h * TS
                    nc.vector.tensor_scalar(qz[:, b, DC * h:DC * (h + 1), r:r + TS],
                                            qx[:, DC * h:DC * (h + 1), TP + b * TS:TP + (b + 1) * TS],
                                            float(D // XH) ** -0.5, None, ALU.mult).then_inc(q_ready, 1)
            ve.wait_ge(k_used, NSEQ)
            nc.vector.tensor_reduce(nm[:, :], psum[:, 0, 0:MEM], AX.X, ALU.max, negate=True).then_inc(max_ready, 1)
            ve.wait_ge(exp_ready, 1)
            nc.vector.reciprocal(sums[:, :], sums[:, :]).then_inc(inverted, 1)
            ve.wait_ge(inverted, 1)
            nc.vector.tensor_scalar(p[:, :], p[:, :], sums[:, 0:1], None, ALU.mult).then_inc(probs_ready, 1)
            ve.wait_ge(v_used, NSEQ)
            nc.vector.tensor_copy(ox[:, :, TP:T], psum[:, 2, 0:KD * NS].rearrange("p (c t) -> p c t", c=KD))

        @block.scalar
        def _(act):
            act.wait_ge(max_ready, 1)
            nc.scalar.activation(p[:, :], psum[:, 0, 0:MEM], ACT.Exp, bias=nm[:, 0:1], accum_out=sums[:, 0:1]).then_inc(exp_ready, 1)
            act.wait_ge(turn_ready, 1)
            nc.scalar.activation(pt[:, :, :], psum[:, 1, 0:2 * P].rearrange("p (m q) -> p m q", m=2), ACT.Copy).then_inc(turn_copied, 1)

        @block.tensor
        def _(pe):
            pe.wait_ge(q_ready, NSEQ * XH)
            for b in range(NSEQ):
                pe.wait_ge(loaded[b % 2], 16 * (b // 2 + 1))
                for c in range(KD):
                    last = nc.tensor.matmul(psum[:, 0, 0:MEM], qz[:, b, c, :], kv[:, b % 2, c * MEM:(c + 1) * MEM],
                                            start=(b == 0 and c == 0), stop=(b == NSEQ - 1 and c == KD - 1))
                last.then_inc(k_used, 1)
            pe.wait_ge(probs_ready, 1)
            for m in range(2):
                last = nc.tensor.transpose(psum[:, 1, m * P:(m + 1) * P], p[:, m * P:(m + 1) * P], K["ident"][:, :])
            last.then_inc(turn_ready, 1)
            pe.wait_ge(turn_copied, 1)
            for b in range(NSEQ):
                n = NSEQ + b
                pe.wait_ge(loaded[n % 2], 16 * (n // 2 + 1))
                for c in range(KD):
                    r = b * XH * TS + (c // DC) * TS
                    for m in range(2):
                        last = nc.tensor.matmul(psum[:, 2, c * NS + b * TS:c * NS + (b + 1) * TS],
                                                kv[:, n % 2, m * D + c * P:m * D + (c + 1) * P], pt[:, m, r:r + TS],
                                                start=(m == 0), stop=(m == 1))
                last.then_inc(v_used, 1)


def ffn(nc, A, O, high, low, mid, ring, acc):
    with stage(nc, "ffn") as (ctx, sem):
        sb = lambda n, s: ctx.enter_context(nc.sbuf_tensor("ff_" + n, s, F32))
        taps = sb("taps", [P, KF, 4])
        state = sb("state", [P, KF, NSEQ, 2])
        pstate = sb("pstate", [P, KF, 2])
        tap = sb("tap", [P, 4])
        u, cv = sb("u", [P, T]), sb("cv", [P, T])
        us, cs = sb("us", [P, NSEQ, 2 + TS]), sb("cs", [P, NSEQ, TS])
        half = ctx.enter_context(nc.sbuf_tensor("ff_half", [P, 2, 2, KD * P], F32R))
        names = ("loaded", "wu_loaded", "wg_loaded", "u_ready", "u_copied", "gate_ready", "conv_ready", "gelu_ready", "mid_ready",
                 "steps", "stored", "wu_high", "wg_high", "wu_split", "wg_split")
        S = {n: sem(n) for n in names}
        block = ctx.enter_context(nc.Block())

        @block.sync
        def _(sp):
            sp.dma_start(taps[:, :, :], A["f_conv"]).then_inc(S["loaded"], 16)
            sp.dma_start(state[:, :, :, :], A["f_state"]).then_inc(S["loaded"], 16)
            sp.dma_start(ring[:, 0, :], A["f_wu"][0]).then_inc(S["wu_loaded"], 16)
            sp.dma_start(ring[:, 1, :], A["f_wg"][0]).then_inc(S["wg_loaded"], 16)
            with sp.Fori(1, KF) as i:
                sp.wait_ge(S["wu_split"], i)
                sp.dma_start(ring[:, 0, :], A["f_wu"][ds(i, 1), :, :].rearrange("a p k -> p (a k)")).then_inc(S["wu_loaded"], 16)
                sp.wait_ge(S["wg_split"], i)
                sp.dma_start(ring[:, 1, :], A["f_wg"][ds(i, 1), :, :].rearrange("a p k -> p (a k)")).then_inc(S["wg_loaded"], 16)
            sp.wait_ge(S["mid_ready"], KF + 1)
            sp.dma_start(O["p_fconv"], pstate[:, :, :]).then_inc(S["stored"], 16)
            sp.dma_start(O["s_fconv"], state[:, :, :, :]).then_inc(S["stored"], 16)
            sp.wait_ge(S["stored"], 32)

        @block.gpsimd
        def _(pool):
            with pool.Fori(0, KF) as i:
                for j, w in enumerate(("wu", "wg")):
                    pool.wait_ge(S[w + "_high"], i + 1)
                    low_part(nc.gpsimd, half[:, j, 1, :], ring[:, j, :], half[:, j, 0, :]).then_inc(S[w + "_split"], 1)

        @block.tensor
        def _(pe):
            with pe.Fori(0, KF) as i:
                for j, (w, ready, free) in enumerate((("wu_split", "u_ready", "u_copied"), ("wg_split", "gate_ready", "mid_ready"))):
                    pe.wait_ge(S[w], i + 1)
                    pe.wait_ge(S[free], i + 1)
                    for g in range(NG):
                        for k in range(KD):
                            c, ks = slice(g * GW, (g + 1) * GW), slice(k * P, (k + 1) * P)
                            last = split_product(nc, acc[:, 3 * j + g, 0:GW], (half[:, j, 0, ks], half[:, j, 1, ks]),
                                                 (high[:, k, c], low[:, k, c]), k == 0, k == KD - 1)
                    last.then_inc(S[ready], 1)

        @block.scalar
        def _(act):
            act.sem_inc(S["u_copied"], 1)
            with act.Fori(0, KF) as i:
                act.wait_ge(S["u_ready"], i + 1)
                act.wait_ge(S["mid_ready"], i + 1)
                nc.scalar.activation(u[:, :].rearrange("p (g t) -> p g t", g=NG), acc[:, 0:NG, 0:GW], ACT.Copy
                                     ).then_inc(S["u_copied"], 1)
                act.wait_ge(S["conv_ready"], i + 1)
                nc.scalar.activation(cv[:, :], cv[:, :], ACT.Gelu_apprx_tanh).then_inc(S["gelu_ready"], 1)

        @block.vector
        def _(ve):
            STEPS = 7
            ve.wait_ge(S["loaded"], 32)
            ve.sem_inc(S["mid_ready"], 1)

            def split_weights(j, w, i):
                ve.wait_ge(S[w + "_loaded"], 16 * i + 16)
                high_part(nc, half[:, j, 0, :], ring[:, j, :]).then_inc(S[w + "_high"], 1)

            def chunk(i, last):
                ch = Chain(ve, S["steps"], i * STEPS)
                nc.vector.tensor_copy(us[:, :, 0:2], state[:, ds(i, 1), :, :].rearrange("p a b t -> p (a b) t"))
                ch.link(nc.vector.tensor_copy(tap[:, :], taps[:, ds(i, 1), :].rearrange("p a k -> p (a k)")))
                ve.wait_ge(S["u_copied"], i + 2)
                if not last:
                    split_weights(0, "wu", i + 1)
                nc.vector.tensor_scalar(cv[:, 0:TP], u[:, 0:TP], tap[:, 2:3], tap[:, 3:4], ALU.mult, ALU.add)
                ch.link(nc.vector.tensor_copy(us[:, :, 2:2 + TS], u[:, TP:T].rearrange("p (b t) -> p b t", t=TS)))
                nc.vector.tensor_scalar(pstate[:, ds(i, 1), :].rearrange("p a t -> p (a t)"), u[:, TP - 2:TP], 1.0, None, ALU.mult)
                nc.vector.tensor_scalar(state[:, ds(i, 1), :, :].rearrange("p a b t -> p (a b) t"), us[:, :, TS:TS + 2], 1.0, None, ALU.mult)
                ch.link(nc.vector.tensor_scalar(cs[:, :, :], us[:, :, 2:2 + TS], tap[:, 2:3], tap[:, 3:4], ALU.mult, ALU.add))
                for k in (1, 0):
                    d = 2 - k
                    ch.link(nc.vector.scalar_tensor_tensor(out=cv[:, d:TP], in0=u[:, 0:TP - d], scalar=tap[:, k:k + 1],
                                                           in1=cv[:, d:TP], op0=ALU.mult, op1=ALU.add))
                    ch.link(nc.vector.scalar_tensor_tensor(out=cs[:, :, :], in0=us[:, :, k:k + TS], scalar=tap[:, k:k + 1],
                                                           in1=cs[:, :, :], op0=ALU.mult, op1=ALU.add))
                nc.vector.tensor_copy(cv[:, TP:T].rearrange("p (b t) -> p b t", t=TS), cs[:, :, :]).then_inc(S["conv_ready"], 1)
                ve.wait_ge(S["gate_ready"], i + 1)
                if not last:
                    split_weights(1, "wg", i + 1)
                ve.wait_ge(S["gelu_ready"], i + 1)
                nc.vector.tensor_tensor(mid[:, ds(i, 1), :].rearrange("p a (g t) -> p (a g) t", g=NG), acc[:, NG:2 * NG, 0:GW],
                                        cv[:, :].rearrange("p (g t) -> p g t", g=NG), ALU.mult).then_inc(S["mid_ready"], 1)
                ve.wait_ge(S["mid_ready"], i + 2)
                assert ch.n == STEPS, ch.n

            split_weights(0, "wu", 0)
            split_weights(1, "wg", 0)
            with ve.Fori(0, KF - 1) as i:
                chunk(i, False)
            chunk(KF - 1, True)


def build(nc, A, O):
    with ExitStack() as ctx:
        K, place = {}, {}

        def sb(name, shape, c=ctx):
            t = c.enter_context(nc.sbuf_tensor(name, shape, F32))
            place[name] = nc.sbuf_base - 4 * int(np.prod(shape[1:]))
            return t

        def over(name, at, shape):
            return nc.alloc_sbuf_tensor_at(name, shape, F32R, offset=place[at])

        psum = ctx.enter_context(nc.psum_tensor("psum", [P, 8, 512], F32))
        consts = sb("consts", [P, N_CONST])
        for n, (a, w) in CONST_AT.items():
            K[n] = consts[:, a:a + w]
        gains = sb("gains", [P, 6, KD])
        ring = sb("ring", [P, 2, KD * P])
        pages = ctx.enter_context(nc.sbuf_tensor("pages", [1, NSEQ * NPAGE], I32))
        low = sb("low", [P, KD, T])
        hm, zm = low[:, 0:4, :], low[:, 4:8, :]
        x = low
        late = ctx.enter_context(ExitStack())
        zn = sb("zn", [P, NFEAT - 4, T], late)
        tokn = sb("tokn", [P, NTILE + 1, N_END], late)
        branch_gates = sb("branch_gates", [P, NTILE + 1, 3 * NH], late)
        early = ctx.enter_context(ExitStack())
        tokm = sb("tokm", [P, NTILE + 1, C_OG + 512], early)
        with stage(nc, "load") as (c, sem):
            loaded = sem("loaded")
            block = c.enter_context(nc.Block())

            @block.sync
            def _(sp):
                sp.dma_start(consts[:, :], A["consts"]).then_inc(loaded, 16)
                sp.dma_start(gains[:, :, :], A["gains"]).then_inc(loaded, 16)
                sp.dma_start(pages[:, :], A["page_table"]).then_inc(loaded, 16)
                sp.wait_ge(loaded, 48)

        with ExitStack() as c:
            h = sb("h", [P, KD, T], c)
            with ExitStack() as c2:
                sq = sb("sq", [P, 2, T], c2)
                rstd = sb("rstd", [P, T], c2)
                rms_norm(nc, "norm0", K, h, gains[:, 0, :], h, sq, rstd, psum[:, 0:3, :], A["x"], tokn[:, NTILE, :])
            project_tokens(nc, "int", A["w_tok"], h, [(0, 512, tokm[:, :, 0:512]), (512, 512, tokm[:, :, 512:1024]),
                                                      (1024, TOKW - 1024, tokn)], psum, aside=[(A["h_spill"], h[:, :, :])])
            high = c.enter_context(nc.sbuf_tensor("h_high", [P, KD, T], F32R))
            low_h = over("h_low", "h", [P, KD, T])
            half = over("in_half", "low", [P, 4 * KD * P])
            project_split(nc, "inm", A["w_in"][0:4], 4, KD, h, high, low_h, zm, ring, psum, half=half)
            project_split(nc, "inn", A["w_in"][4:12], 8, KD, h, high, low_h, zn, ring, psum, split_here=False, half=half)

        with ExitStack() as c:
            n = NTILE + 1
            sm = {m: sb("s_" + m, [P, n, w], c) for m, w in (("lf", MH), ("b", MH), ("a", MH), ("tmp", MH))}
            sm["g"] = branch_gates
            conv_mlstm(nc, A, O, zm, hm)
            gates(nc, A, K, tokm, tokn, sm, psum)
            mlstm(nc, A, O, K, hm, tokm, sm, psum)
            mlstm_sample(nc, A, O, K, hm, tokm, sm, psum)
        early.close()
        with ExitStack() as c:
            N = {"kcmp": sb("kcmp", [P, NCMP], c), "vcmp": sb("vcmp", [NCMP, P], c),
                 "kc": sb("kc", [P, NSEQ, P], c), "vc": sb("vc", [P, NSEQ, P], c), "n_pool": A["pool"].shape[0],
                 "soft": {n: ctx.enter_context(nc.semaphore(n)) for n in ("c0", "c1", "k_soft0", "k_soft1", "v_soft0", "v_soft1")}}
            with ExitStack() as c2:
                N.update({"w1": sb("w1", [P, 2, CB, P], c2), "w2": sb("w2", [P, 2, P], c2), "pb": sb("pb", [P, 2], c2)})
                compress_setup(nc, A, N, zn, psum)
                compress_sample(nc, A, N, pages, psum)
            nsa_prompt(nc, A, O, K, N, zn, tokn, branch_gates, zm, psum)
            nsa_sample(nc, A, K, N, zn, tokn, branch_gates, pages, zm, psum)

        late.close()
        h = sb("h_again", [P, KD, T])
        h_low = over("h_again_low", "h_again", [P, KD, T])
        with ExitStack() as c:
            dst = sb("merged", [P, KD, T], c)
            high = c.enter_context(nc.sbuf_tensor("merge_high", [P, KD, T], F32R))
            merge(nc, A, h, high, h_low, hm, zm, dst, psum)
            project_split(nc, "wout", A["w_out"], KD, KD, dst, high, over("merged_low", "merged", [P, KD, T]), h, ring, psum, aside=[(x[:, :, :], A["x"])])

        def norms(name, g, src, store=None, high=None, keep=None, x=x):
            with ExitStack() as c:
                sq, rstd = sb(name + "_sq", [P, 2, T], c), sb(name + "_rstd", [P, 2, T], c)
                residual_norm(nc, name, K, src, gains, g, x, h, sq, rstd, psum[:, 0:3, :], store, high, h_low, keep)

        with ExitStack() as c:
            high = c.enter_context(nc.sbuf_tensor("cross_high", [P, KD, T], F32R))
            norms("norm1", 1, h, high=high)
            qx = sb("qx", [P, KD, T], c)
            with ExitStack() as c2:
                mk, mv = sb("mk", [P, KD, MEM], c2), sb("mv", [P, 2, D], c2)
                with ExitStack() as c3:
                    mem = sb("mem", [P, KD, MEM], c3)
                    project_split(nc, "xq", A["x_wq"], KD, KD, h, high, h_low, qx, ring, psum, split_here=False, aside=[(mem[:, :, :], A["mem"])])
                    project(nc, "xk", A["x_wk"], KD, KD, mem, mk, ring, psum, width=MEM, groups=1)
                    project_tokens(nc, "xv", A["x_wv"], mem, [(0, 512, mv[:, :, 0:512]), (512, 512, mv[:, :, 512:1024])], psum, (P, P))
                cross_prompt(nc, O, K, qx, mk, mv, h, psum)
            cross_sample(nc, A, K, qx, h, psum)
            project_split(nc, "xo", A["x_wo"], KD, KD, h, high, h_low, qx, ring, psum)
            x_high = over("x_high", "low", [P, KD, T])
            norms("norm2", 3, qx, high=x_high, keep=A["x_spill"])
        with ExitStack() as c:
            mid = sb("mid", [P, KF, T], c)
            mid_low = over("mid_low", "mid", [P, KF, T])
            ffn(nc, A, O, x_high, h_low, mid, ring, psum)
            parts = [(0, 8), (8, 8), (16, 6)]
            for n, (k0, kc) in enumerate(parts):
                aside = [(mid[:, 0:KD, :], A["x_spill"])] if n == len(parts) - 1 else ()
                project_split(nc, f"down{n}", A["f_wd"][:, :, k0 * P:(k0 + kc) * P], KD, kc, mid[:, k0:k0 + kc, :], x_high,
                              mid_low[:, k0:k0 + kc, :], h,
                              ring, psum, add=n > 0, aside=aside)
            norms("norm3", 5, h, O["y"], x=mid[:, 0:KD, :])




def shape_constants():
    i = np.arange(P)
    c = {}
    c["ident"] = np.eye(P)
    c["ones"] = np.ones((P, P))
    c["tri"] = (i[:, None] <= i[None, :]) * 1.0
    same = (i[:, None] // TS == i[None, :] // TS) & (i[:, None] < NS) & (i[None, :] < NS)
    c["stri"] = same * c["tri"]
    c["last"] = (i[:, None] == P - 1) * np.ones((1, P))
    seq = np.arange(NSEQ)
    c["slast"] = same * (i[:, None] % TS == TS - 1)
    c["slast8"] = (i[:, None] == seq[None, :] * TS + TS - 1) * 1.0
    c["sseq8"] = (i[:, None] // TS == seq[None, :]) * 1.0
    c["scausal"] = np.where(c["stri"].T > 0, 0.0, NEG)[:, 0:NS]
    c["scausal_t"] = np.where(c["stri"] > 0, 0.0, NEG)[:, 0:NS]
    c["flip"] = np.eye(P)[::-1]
    c["seen"] = (i[:, None] >= CB - 1) * 1.0
    c["wmask"] = np.where(i[None, :] <= i[:, None], NEG, 0.0)
    c["causal"] = np.where(i[None, :] <= i[:, None], 0.0, NEG)
    c["causal_t"] = np.ascontiguousarray(c["causal"].T)
    return c


CONST = shape_constants()
CONST_AT, N_CONST = {}, 0
for _n, _v in CONST.items():
    CONST_AT[_n] = (N_CONST, _v.shape[1])
    N_CONST += _v.shape[1]


def chunked(w):
    k, m = w.shape
    return np.ascontiguousarray(w.reshape(k // P, P, m // P, P).transpose(2, 1, 0, 3)).reshape(m // P, P, k)


def feature_rows(a):
    return np.ascontiguousarray(a.reshape(a.shape[0], -1, P).transpose(2, 1, 0))


def lay_out(v):
    L = {}
    x = np.concatenate([v["x_prompt"].reshape(TP, D), v["x_sample"].reshape(NS, D)])
    L["x"] = feature_rows(x)
    L["consts"] = np.concatenate([CONST[n] for n in CONST_AT], axis=1).astype(np.float32)
    L["gains"] = np.ascontiguousarray(v["norms"][0].reshape(6, KD, P).transpose(2, 0, 1))
    w = v["w_in"][0]
    at, parts = 0, []
    for n in (512, 512, 4, 4, 512, 512, 256, 256, 256, 24, 1024, 1024):
        parts.append(w[:, at:at + n])
        at += n
    xm, val, ig, fg, og, qn, kvc, kvs, kvw, gn, ga, gb = parts
    pair = np.array([h * HD + e for i in range(NPAIR) for h in (i, NPAIR + i) for e in range(HD)])
    L["w_in"] = chunked(np.concatenate([xm, qn[:, pair], kvc, kvs[:, 0:128], kvw[:, 0:128]], axis=1))
    tok = np.concatenate([val, og, kvs[:, 128:], kvw[:, 128:], ig, fg, gn], axis=1)
    L["w_tok"] = np.ascontiguousarray(tok.reshape(KD, P, TOKW).transpose(1, 0, 2))
    L["m_conv"] = np.ascontiguousarray(np.concatenate([v["m_conv_w"][0], v["m_conv_b"]]).reshape(5, 4, P).transpose(2, 1, 0))
    L["m_state"] = np.ascontiguousarray(v["state_mlstm_conv"][0].reshape(NSEQ, 3, 4, P).transpose(3, 2, 0, 1))
    L["gate_b"] = v["m_gate_b"].reshape(8)
    L["m_wqk"] = np.ascontiguousarray(np.stack([v["m_wq"][0], v["m_wk"][0]]).transpose(2, 0, 1, 3))
    L["m_norm"] = v["m_norm"][0]
    dist = TP - 1 - np.arange(2048)
    L["onehot"] = (bias_buckets(dist)[None, :] == np.arange(NBUCKET)[:, None]).astype(np.float32)
    L["rmask"] = np.tile(np.where(dist >= 0, 0.0, NEG), (NH, 1)).astype(np.float32)
    L["rel"] = v["rel_bias"]
    w1 = v["cmp_w1"][0].reshape(2, CB, HD, HD)
    w2 = v["cmp_w2"][0]
    both = np.zeros((P, 2, CB, P), np.float32)
    both2 = np.zeros((P, 2, P), np.float32)
    for g in range(2):
        half = slice(g * HD, (g + 1) * HD)
        both[half, :, :, half] = w1.transpose(2, 0, 1, 3)
        both2[half, :, half] = w2.transpose(1, 0, 2)
    L["cmp_w1"], L["cmp_w2"] = both, both2
    pe = v["cmp_pe"][0].transpose(2, 0, 1)
    L["cmp_pe"] = np.ascontiguousarray(np.concatenate([pe, pe]))
    cache = v["cache_nsa_kv"][0].reshape(-1, PAGE, 4, P)
    pool = cache.transpose(0, 3, 2, 1).copy()
    pool[:, :, 3, :] = cache[:, :, 3, :]
    L["pool"] = pool.reshape(-1, P, 4 * PAGE)
    L["page_table"] = v["page_table"].reshape(1, NSEQ * NPAGE)
    w = v["cache_win_kv"][0].reshape(NSEQ, WIN, 2, P)
    winp = np.empty((NSEQ, P, 2, WIN), np.float32)
    winp[:, :, 0] = w[:, :, 0].transpose(0, 2, 1)
    winp[:, :, 1] = w[:, :, 1].reshape(NSEQ, 4, P, P).transpose(0, 2, 1, 3).reshape(NSEQ, P, WIN)
    L["winp"] = winp
    L["relq"] = np.tile(v["rel_bias"], (TS, 1))
    qd = np.arange(P) // NBUCKET
    near = PAST + qd[:, None] - (PAST - 1024 + np.arange(1024))[None, :]
    blocks = PAST + qd[:, None] - (np.arange(P) * CB + CB - 1)[None, :]
    tail = qd[:, None] - (np.arange(NS) % TS)[None, :]
    dist = np.concatenate([near, blocks, tail], axis=1)
    L["onehot_s"] = (bias_buckets(dist) == (np.arange(P) % NBUCKET)[:, None]).astype(np.float32)
    L["delta"] = (qd[:, None] == np.arange(TS)[None, :]).astype(np.float32)
    row = np.arange(P)
    rb, rg, rq = row // 32, row // 16 % 2, row % TS
    L["group"] = ((rb[:, None] == rb) & (rg[:, None] == rg) & (rq[:, None] == rq)).astype(np.float32)
    tok = np.arange(NS)
    ok = [(tok // TS == 4 * s + rb[:, None]) & (tok % TS <= rq[:, None]) for s in range(2)]
    L["row_token"] = np.stack([(np.arange(NS)[:, None] == (4 * s + rb[None, :]) * TS + rq[None, :]) for s in range(2)], 1).astype(np.float32)
    L["row_head"] = (row[:, None] // TS % NH == np.arange(3 * NH)[None, :] // 3).astype(np.float32)
    L["tmask"] = np.where(np.stack(ok, 1), 0.0, NEG).astype(np.float32)
    L["wmask_s"] = np.where(np.arange(TS) <= rq[:, None], NEG, 0.0).astype(np.float32)
    ca, cb = chunked(ga), chunked(gb)
    um, un = chunked(v["w_up_m"][0]), chunked(v["w_up_n"][0][pair])
    L["w_merge"] = np.concatenate([ca, um, cb, un], axis=2)
    L["w_out"] = chunked(v["w_out"][0])
    L["x_wq"], L["x_wo"] = chunked(v["x_wq"][0]), chunked(v["x_wo"][0])
    L["mem"] = feature_rows(v["mem_prompt"][0])
    L["x_wk"] = chunked(v["x_wkv"][0][:, 0:D])
    L["x_wv"] = np.ascontiguousarray(v["x_wkv"][0][:, D:].reshape(KD, P, D).transpose(1, 0, 2))
    mem = v["cache_mem_kv"][0].reshape(NSEQ, MEM, 2, KD, P)
    L["mem_k"] = np.ascontiguousarray(mem[:, :, 0].transpose(0, 3, 2, 1)).reshape(NSEQ, P, KD * MEM)
    L["mem_v"] = np.ascontiguousarray(mem[:, :, 1].reshape(NSEQ, 2, P, D).transpose(0, 2, 1, 3)).reshape(NSEQ, P, 2 * D)
    L["f_wu"], L["f_wg"], L["f_wd"] = chunked(v["f_wu"][0]), chunked(v["f_wg"][0]), chunked(v["f_wd"][0])
    L["f_conv"] = np.ascontiguousarray(np.concatenate([v["f_conv_w"][0], v["f_conv_b"]]).reshape(4, KF, P).transpose(2, 1, 0))
    L["f_state"] = np.ascontiguousarray(v["state_ffn_conv"][0].reshape(NSEQ, 2, KF, P).transpose(3, 2, 0, 1))
    L["s_C0"] = np.ascontiguousarray(v["state_mlstm_C"][0].transpose(3, 0, 1, 2))
    L["s_n0"] = v["state_mlstm_n"][0]
    L["s_n0t"] = np.repeat(v["state_mlstm_n"][0], TS, axis=0)
    L["s_m0t"] = np.repeat(v["state_mlstm_m"][0], TS, axis=0)
    return L


SCRATCH = {"bias_vec": (NH, 2048), "h_spill": (P, KD, T), "x_spill": (P, KD, T)}
OUTS = {"y": (P, KD, T), "p_mconv": (P, 4, 3), "s_mconv": (P, 4, NSEQ, 3), "p_C": (P, MH, MD), "p_n": (P, MH),
        "p_m": (1, MH), "s_C": (P, NSEQ, MH, MD), "s_n": (NSEQ, MH, MD), "s_m": (NSEQ, MH), "winp": (NSEQ, P, 2, WIN),
        "mk": (P, KD, MEM), "mv": (P, 2, D), "p_fconv": (P, KF, 2), "s_fconv": (P, KF, NSEQ, 2), "zkv": (P, 4, T), "tkv": (P, NTILE + 1, 2 * P)}


def kernel(**inputs):
    import concourse.bacc as bacc
    from concourse.bass_utils import run_bass_kernel_spmd

    v = {n: np.asarray(a) for n, a in inputs.items()}
    nc = bacc.Bacc("TRN2", target_bir_lowering=False, num_devices=1)
    L = lay_out(v)
    A = {n: nc.dram_tensor("in_" + n, a.shape, mybir.dt.from_np(a.dtype), kind="ExternalInput").ap() for n, a in L.items()}
    for n, s in SCRATCH.items():
        A[n] = nc.dram_tensor(n, s, F32, kind="Internal").ap()
    O = {n: nc.dram_tensor("out_" + n, s, F32, kind="ExternalOutput").ap() for n, s in OUTS.items()}
    build(nc, A, O)
    r = run_bass_kernel_spmd(nc, [{"in_" + n: a for n, a in L.items()}], core_ids=[0]).results[0]
    R = {n: r["out_" + n] for n in OUTS}

    y = R["y"].transpose(2, 1, 0).reshape(T, D)
    kz, kt = R["zkv"].transpose(2, 1, 0), R["tkv"].transpose(1, 0, 2).reshape(-1, 2, P)[:T]
    rows = np.stack([kz[:, 0], kz[:, 1], kz[:, 2], kt[:, 0]], axis=1).reshape(T, 4, 2, HD)
    wnew = np.stack([kz[:, 3], kt[:, 1]], axis=1).reshape(T, 2, 2, HD)
    wold = np.stack([R["winp"][:, :, 0].transpose(0, 2, 1),
                     R["winp"][:, :, 1].reshape(NSEQ, P, 4, P).transpose(0, 2, 1, 3).reshape(NSEQ, WIN, P)], axis=2)
    swin = np.concatenate([wold.reshape(NSEQ, WIN, 2, 2, HD)[:, TS:], wnew[TP:].reshape(NSEQ, TS, 2, 2, HD)], axis=1)
    mkv = np.stack([R["mk"].transpose(2, 1, 0).reshape(MEM, D), R["mv"].transpose(1, 0, 2).reshape(MEM, D)], axis=1)
    fix = lambda a: np.ascontiguousarray(a)
    return tuple(fix(a) for a in (
        y[None, :TP], y[TP:].reshape(NSEQ, TS, D),
        rows[None, None, :TP], wnew[None, None, TP - WIN:TP],
        R["p_C"].transpose(1, 0, 2)[None, None], R["p_n"].T[None, None], R["p_m"][None],
        R["p_mconv"].transpose(2, 1, 0).reshape(1, 1, 3, MH * MD), R["p_fconv"].transpose(2, 1, 0).reshape(1, 1, 2, DFF),
        mkv.reshape(1, 1, MEM, 2, XH, D // XH),
        rows[TP:].reshape(1, NSEQ, TS, 4, 2, HD), swin[None],
        R["s_C"].transpose(1, 2, 3, 0)[None], R["s_n"][None], R["s_m"][None],
        R["s_mconv"].transpose(2, 3, 1, 0).reshape(1, NSEQ, 3, MH * MD), R["s_fconv"].transpose(2, 3, 1, 0).reshape(1, NSEQ, 2, DFF)))
```
